# Optimizing a Trainium2 kernel written in Bass

```python
import math
import jax, jax.numpy as jnp
from jax import lax
import numpy as np

D_MODEL = 1024
BATCH = 1
SEQ = 2048
DEPTH = 1

RW_HEADS = 8
RW_HEAD_DIM = 64
RW_WIDTH = RW_HEADS * RW_HEAD_DIM
DECAY_LORA = 64
AAA_LORA = 64
GATE_LORA = 128
GN_EPS = 64e-5

NSA_HEADS = 8
NSA_KV_HEADS = 2
NSA_HEAD_DIM = 64
NSA_WIDTH = NSA_HEADS * NSA_HEAD_DIM
NSA_KV_WIDTH = NSA_KV_HEADS * NSA_HEAD_DIM
CMP_BLOCK = 32
CMP_STRIDE = 16
SEL_BLOCK = 64
N_SELECT = 8
WINDOW = 512
Q_BLOCK = 128
N_NSA_BRANCH = 3
FORCE_SCORE = 1e6
NEG_INF = -1e30

N_GROUPS = 4
EXPERTS_PER_GROUP = 8
N_EXPERTS = N_GROUPS * EXPERTS_PER_GROUP
TOP_K = 2
D_EXPERT = 512
ROW_BLOCK = 128

PLE_DIM = 256
NORM_EPS = 1e-6

RW_SIZES = (RW_WIDTH, RW_WIDTH, RW_WIDTH, DECAY_LORA, AAA_LORA, GATE_LORA)
REST_SIZES = (NSA_WIDTH, NSA_KV_WIDTH, NSA_KV_WIDTH, NSA_KV_WIDTH, NSA_KV_WIDTH,
              NSA_KV_WIDTH, NSA_KV_WIDTH, N_NSA_BRANCH * NSA_HEADS, D_MODEL, D_MODEL)
RW_IN = 3 * RW_WIDTH + DECAY_LORA + AAA_LORA + GATE_LORA
N_IN = RW_IN + NSA_WIDTH + 6 * NSA_KV_WIDTH + N_NSA_BRANCH * NSA_HEADS + 2 * D_MODEL

kernel_name = 'hybrid_rwkv7_nsa_hiermoe_block'

def _rmsnorm(x, g):
    xf = x.astype(jnp.float32)
    y = xf * lax.rsqrt(jnp.mean(xf * xf, axis=-1, keepdims=True) + NORM_EPS)
    return (y * g.astype(jnp.float32)).astype(x.dtype)

def _split(z, sizes):
    offs = np.cumsum(sizes)[:-1].tolist()
    return jnp.split(z, offs, axis=-1)

def _token_shift(z, mu):
    prev = jnp.pad(z, ((0, 0), (1, 0), (0, 0)))[:, :-1]
    return z + (prev - z) * mu

def _rwkv7_time_mix(zr, zk, zv, zw, za, zg, w0, w2, a0, a2, g2, k_k, k_a, r_k, ln_w, ln_b):
    B, S, _ = zr.shape
    f32 = jnp.float32
    heads = lambda t: t.reshape(B, S, RW_HEADS, RW_HEAD_DIM)
    tm = lambda t: jnp.moveaxis(t, 1, 0)
    w_raw = (w0 + jnp.tanh(zw) @ w2).astype(f32)
    decay = jnp.exp(-jnp.exp(-jax.nn.softplus(-w_raw) - 0.5))
    a = jax.nn.sigmoid((a0 + za @ a2).astype(f32))
    g = jax.nn.sigmoid(zg) @ g2
    kk = heads(zk * k_k).astype(f32)
    kk = kk / jnp.maximum(jnp.sqrt(jnp.sum(kk * kk, axis=-1, keepdims=True)), 1e-12)
    k = zk * (1 + (a - 1) * k_a)
    r_h, k_h, v_h = heads(zr).astype(f32), heads(k).astype(f32), heads(zv).astype(f32)
    a_h, w_h = heads(a), heads(decay)

    def step(state, inp):
        r_t, w_t, k_t, v_t, kk_t, a_t = inp
        sa = jnp.einsum('bhij,bhj->bhi', state, -kk_t)
        state = (state * w_t[:, :, None, :]
                 + sa[..., None] * (kk_t * a_t)[:, :, None, :]
                 + v_t[..., None] * k_t[:, :, None, :])
        return state, jnp.einsum('bhij,bhj->bhi', state, r_t)

    state0 = jnp.zeros((B, RW_HEADS, RW_HEAD_DIM, RW_HEAD_DIM), f32)
    _, o = lax.scan(step, state0, (tm(r_h), tm(w_h), tm(k_h), tm(v_h), tm(kk), tm(a_h)))
    o = jnp.moveaxis(o, 0, 1)
    mu = jnp.mean(o, axis=-1, keepdims=True)
    var = jnp.mean(jnp.square(o - mu), axis=-1, keepdims=True)
    o = ((o - mu) * lax.rsqrt(var + GN_EPS)).reshape(B, S, RW_WIDTH) * ln_w + ln_b
    bonus = jnp.sum(r_h * k_h * r_k, axis=-1, keepdims=True) * v_h
    o = (o + bonus.reshape(B, S, RW_WIDTH)) * g
    return o.astype(zr.dtype)

def _nsa(q, kc, vc, ks, vs, kw, vw, gate_logits, cmp_pos_k, cmp_pos_v,
         cmp_k_w1, cmp_k_w2, cmp_v_w1, cmp_v_w2, gate_b):
    B, S, _ = q.shape
    f32 = jnp.float32
    G, R, Dh = NSA_KV_HEADS, NSA_HEADS // NSA_KV_HEADS, NSA_HEAD_DIM
    out_dtype = q.dtype
    q = q.reshape(B, S, G, R, Dh).astype(f32) * (Dh ** -0.5)
    kv = lambda t: t.reshape(B, S, G, Dh).astype(f32)
    kc, vc, ks, vs, kw, vw = kv(kc), kv(vc), kv(ks), kv(vs), kv(kw), kv(vw)
    slopes = jnp.asarray((2.0 ** (-8.0 * np.arange(1, NSA_HEADS + 1) / NSA_HEADS))
                         .astype(np.float32).reshape(G, R))
    t_pos = jnp.arange(S)

    n_cmp = (S - CMP_BLOCK) // CMP_STRIDE + 1
    cmp_start = np.arange(n_cmp) * CMP_STRIDE
    win = cmp_start[:, None] + np.arange(CMP_BLOCK)[None, :]

    def compress(t, pos_emb, w1, w2):
        blocks = t[:, win] + pos_emb[None, None, :, None, :]
        blocks = jnp.moveaxis(blocks, 3, 2).reshape(B, n_cmp, G, CMP_BLOCK * Dh)
        return jax.nn.gelu(blocks @ w1.astype(f32)) @ w2.astype(f32)

    kcmp = compress(kc, cmp_pos_k.astype(f32), cmp_k_w1, cmp_k_w2)
    vcmp = compress(vc, cmp_pos_v.astype(f32), cmp_v_w1, cmp_v_w2)
    cmp_end = jnp.asarray(cmp_start + CMP_BLOCK - 1)
    cmp_ctr = jnp.asarray((cmp_start + 0.5 * (CMP_BLOCK - 1)).astype(np.float32))
    dist_c = t_pos.astype(f32)[:, None] - cmp_ctr[None, :]
    mask_c = cmp_end[None, :] <= t_pos[:, None]
    s_c = jnp.einsum('bqgrd,bjgd->bgrqj', q, kcmp) - slopes[..., None, None] * dist_c
    p_c = jax.nn.softmax(jnp.where(mask_c, s_c, NEG_INF), axis=-1) * mask_c
    o_cmp = jnp.einsum('bgrqj,bjgd->bqgrd', p_c, vcmp)

    n_sel = S // SEL_BLOCK
    n_pick = min(N_SELECT, n_sel)
    sel_start = np.arange(n_sel) * SEL_BLOCK
    overlap = np.clip(np.minimum(cmp_start[:, None] + CMP_BLOCK, sel_start[None, :] + SEL_BLOCK)
                      - np.maximum(cmp_start[:, None], sel_start[None, :]), 0, None) / CMP_BLOCK
    imp = jnp.einsum('bgrqj,jk->bgqk', p_c, jnp.asarray(overlap.astype(np.float32)))
    blk_t = (t_pos // SEL_BLOCK)[:, None]
    sel_blk = jnp.arange(n_sel)[None, :]
    forced = (sel_blk == 0) | (sel_blk == blk_t) | (sel_blk == blk_t - 1)
    imp = jnp.where(forced, FORCE_SCORE, jnp.where(sel_blk <= blk_t, imp, -FORCE_SCORE))
    _, sel_idx = lax.top_k(imp, n_pick)

    ks_blocks = jnp.moveaxis(ks.reshape(B, n_sel, SEL_BLOCK, G, Dh), 3, 1)
    vs_blocks = jnp.moveaxis(vs.reshape(B, n_sel, SEL_BLOCK, G, Dh), 3, 1)
    kw_pad = jnp.pad(kw, ((0, 0), (WINDOW, 0), (0, 0), (0, 0)))
    vw_pad = jnp.pad(vw, ((0, 0), (WINDOW, 0), (0, 0), (0, 0)))
    bidx = jnp.arange(B)[:, None, None, None]
    gidx = jnp.arange(G)[None, :, None, None]
    n_keys = n_pick * SEL_BLOCK

    def query_block(i):
        qs = i * Q_BLOCK
        qb = lax.dynamic_slice_in_dim(q, qs, Q_BLOCK, axis=1)
        tq = qs + jnp.arange(Q_BLOCK)
        idx = lax.dynamic_slice_in_dim(sel_idx, qs, Q_BLOCK, axis=2)
        kg = ks_blocks[bidx, gidx, idx].reshape(B, G, Q_BLOCK, n_keys, Dh)
        vg = vs_blocks[bidx, gidx, idx].reshape(B, G, Q_BLOCK, n_keys, Dh)
        kpos = (idx[..., None] * SEL_BLOCK + jnp.arange(SEL_BLOCK)).reshape(B, G, Q_BLOCK, n_keys)
        dist = (tq[None, None, :, None] - kpos)[:, :, None]
        s = (jnp.einsum('bqgrd,bgqkd->bgrqk', qb, kg)
             - slopes[None, :, :, None, None] * dist.astype(f32))
        p = jax.nn.softmax(jnp.where(dist >= 0, s, NEG_INF), axis=-1)
        o_sel = jnp.einsum('bgrqk,bgqkd->bqgrd', p, vg)
        kwb = lax.dynamic_slice_in_dim(kw_pad, qs, Q_BLOCK + WINDOW, axis=1)
        vwb = lax.dynamic_slice_in_dim(vw_pad, qs, Q_BLOCK + WINDOW, axis=1)
        kp = qs - WINDOW + jnp.arange(Q_BLOCK + WINDOW)
        dw = tq[:, None] - kp[None, :]
        mw = (dw >= 0) & (dw < WINDOW) & (kp[None, :] >= 0)
        sw = jnp.einsum('bqgrd,bkgd->bgrqk', qb, kwb) - slopes[..., None, None] * dw.astype(f32)
        pw = jax.nn.softmax(jnp.where(mw, sw, NEG_INF), axis=-1)
        o_win = jnp.einsum('bgrqk,bkgd->bqgrd', pw, vwb)
        return o_sel, o_win

    o_sel, o_win = lax.map(query_block, jnp.arange(S // Q_BLOCK))
    o_sel = jnp.moveaxis(o_sel, 0, 1).reshape(B, S, G, R, Dh)
    o_win = jnp.moveaxis(o_win, 0, 1).reshape(B, S, G, R, Dh)

    gate = jax.nn.sigmoid((gate_logits + gate_b).astype(f32)).reshape(B, S, G, R, N_NSA_BRANCH)
    o = gate[..., 0:1] * o_cmp + gate[..., 1:2] * o_sel + gate[..., 2:3] * o_win
    return o.reshape(B, S, NSA_WIDTH).astype(out_dtype)

def _hier_moe(h, w_group, b_group, w_router, b_router, w_gate_up, w_down):
    B, S, D = h.shape
    T = B * S
    A = T * TOP_K
    f32 = jnp.float32
    hf = h.reshape(T, D)
    g_logits = (hf @ w_group).astype(f32) + b_group
    g_sel = jnp.argmax(g_logits, axis=-1)
    p_group = jnp.take_along_axis(jax.nn.softmax(g_logits, axis=-1), g_sel[:, None], axis=1)
    e_logits = ((hf @ w_router).astype(f32) + b_router).reshape(T, N_GROUPS, EXPERTS_PER_GROUP)
    e_logits = jnp.take_along_axis(e_logits, g_sel[:, None, None], axis=1)[:, 0]
    top_p, top_i = lax.top_k(jax.nn.softmax(e_logits, axis=-1), TOP_K)
    gate = p_group * top_p / jnp.sum(top_p, axis=-1, keepdims=True)
    expert = g_sel[:, None] * EXPERTS_PER_GROUP + top_i

    e_flat = expert.reshape(A)
    order = jnp.argsort(e_flat)
    e_sorted = e_flat[order]
    tok_sorted = order // TOP_K
    counts = jnp.bincount(e_flat, length=N_EXPERTS)
    starts = jnp.cumsum(counts) - counts
    padded = (counts + ROW_BLOCK - 1) // ROW_BLOCK * ROW_BLOCK
    pends = jnp.cumsum(padded)
    dest = (pends - padded)[e_sorted] + jnp.arange(A) - starts[e_sorted]
    n_rows = A + N_EXPERTS * ROW_BLOCK
    n_blk = n_rows // ROW_BLOCK
    rows = jnp.zeros((n_rows, D), h.dtype).at[dest].set(hf[tok_sorted])
    blk_expert = jnp.minimum(jnp.searchsorted(pends, jnp.arange(n_blk) * ROW_BLOCK, side='right'),
                             N_EXPERTS - 1)

    def expert_block(args):
        xb, e = args
        gate_h, up_h = jnp.split(xb @ w_gate_up[e], 2, axis=-1)
        return (jax.nn.silu(gate_h) * up_h) @ w_down[e]

    out_rows = lax.map(expert_block, (rows.reshape(n_blk, ROW_BLOCK, D), blk_expert)).reshape(n_rows, D)
    contrib = out_rows[dest].astype(f32) * gate.reshape(A)[order][:, None]
    y = jax.ops.segment_sum(contrib, tok_sorted, num_segments=T)
    return y.astype(h.dtype).reshape(B, S, D)

def setup_inputs(seed: int = 0) -> dict:
    key = jax.random.key(seed)
    keys = iter(jax.random.split(key, 48))
    f32 = jnp.float32
    nrm = lambda shape, scale: jax.random.normal(next(keys), shape, f32) * scale
    gain = lambda shape: 1.0 + nrm(shape, 0.05)
    L, Dh = DEPTH, NSA_HEAD_DIM
    return {
        'x': nrm((BATCH, SEQ, D_MODEL), 1.0),
        'p': nrm((DEPTH, BATCH, SEQ, PLE_DIM), 1.0),
        'g_mix': gain((L, D_MODEL)),
        'w_in': nrm((L, D_MODEL, N_IN), D_MODEL ** -0.5),
        'mu_shift': jax.random.uniform(next(keys), (L, RW_IN), f32, 0.1, 0.9),
        'rw_w0': jax.random.uniform(next(keys), (L, RW_WIDTH), f32, -6.0, 1.0),
        'rw_w2': nrm((L, DECAY_LORA, RW_WIDTH), 0.1 * DECAY_LORA ** -0.5),
        'rw_a0': nrm((L, RW_WIDTH), 0.1),
        'rw_a2': nrm((L, AAA_LORA, RW_WIDTH), 0.3 * AAA_LORA ** -0.5),
        'rw_g2': nrm((L, GATE_LORA, RW_WIDTH), GATE_LORA ** -0.5),
        'rw_k_k': 0.85 + nrm((L, RW_WIDTH), 0.05),
        'rw_k_a': 1.0 + nrm((L, RW_WIDTH), 0.05),
        'rw_r_k': nrm((L, RW_HEADS, RW_HEAD_DIM), 0.1),
        'rw_ln_w': gain((L, RW_WIDTH)),
        'rw_ln_b': nrm((L, RW_WIDTH), 0.02),
        'cmp_pos_k': nrm((L, CMP_BLOCK, Dh), 0.1),
        'cmp_pos_v': nrm((L, CMP_BLOCK, Dh), 0.1),
        'cmp_k_w1': nrm((L, CMP_BLOCK * Dh, Dh), (CMP_BLOCK * Dh) ** -0.5),
        'cmp_k_w2': nrm((L, Dh, Dh), Dh ** -0.5),
        'cmp_v_w1': nrm((L, CMP_BLOCK * Dh, Dh), (CMP_BLOCK * Dh) ** -0.5),
        'cmp_v_w2': nrm((L, Dh, Dh), Dh ** -0.5),
        'nsa_gate_b': nrm((L, N_NSA_BRANCH * NSA_HEADS), 0.1),
        'w_up_rwkv': nrm((L, RW_WIDTH, D_MODEL), RW_WIDTH ** -0.5),
        'w_up_nsa': nrm((L, NSA_WIDTH, D_MODEL), NSA_WIDTH ** -0.5),
        'w_out': nrm((L, D_MODEL, D_MODEL), D_MODEL ** -0.5),
        'g_ffn': gain((L, D_MODEL)),
        'w_group': nrm((L, D_MODEL, N_GROUPS), D_MODEL ** -0.5),
        'b_group': nrm((L, N_GROUPS), 0.01),
        'w_router': nrm((L, D_MODEL, N_EXPERTS), D_MODEL ** -0.5),
        'b_router': nrm((L, N_EXPERTS), 0.01),
        'w_exp_gate_up': nrm((L, N_EXPERTS, D_MODEL, 2 * D_EXPERT), D_MODEL ** -0.5),
        'w_exp_down': nrm((L, N_EXPERTS, D_EXPERT, D_MODEL), D_EXPERT ** -0.5),
        'w_ple_proj': nrm((L, PLE_DIM, D_MODEL), PLE_DIM ** -0.5),
        'g_ple_norm': gain((L, D_MODEL)),
        'g_ple_gate_in': gain((L, D_MODEL)),
        'w_ple_gate': nrm((L, D_MODEL, D_MODEL), D_MODEL ** -0.5),
        'g_final': gain((D_MODEL,)),
    }

def reference(x, p, g_mix, w_in, mu_shift, rw_w0, rw_w2, rw_a0, rw_a2, rw_g2, rw_k_k, rw_k_a,
              rw_r_k, rw_ln_w, rw_ln_b, cmp_pos_k, cmp_pos_v, cmp_k_w1, cmp_k_w2, cmp_v_w1,
              cmp_v_w2, nsa_gate_b, w_up_rwkv, w_up_nsa, w_out, g_ffn, w_group, b_group,
              w_router, b_router, w_exp_gate_up, w_exp_down, w_ple_proj, g_ple_norm,
              g_ple_gate_in, w_ple_gate, g_final):
    for i in range(DEPTH):
        h = _rmsnorm(x, g_mix[i])
        z = h @ w_in[i]
        zr, zk, zv, zw, za, zg = _split(_token_shift(z[..., :RW_IN], mu_shift[i]), RW_SIZES)
        zq, zkc, zvc, zks, zvs, zkw, zvw, zgate, zmr, zmn = _split(z[..., RW_IN:], REST_SIZES)
        y_rw = _rwkv7_time_mix(zr, zk, zv, zw, za, zg, rw_w0[i], rw_w2[i], rw_a0[i], rw_a2[i],
                               rw_g2[i], rw_k_k[i], rw_k_a[i], rw_r_k[i], rw_ln_w[i], rw_ln_b[i])
        y_nsa = _nsa(zq, zkc, zvc, zks, zvs, zkw, zvw, zgate, cmp_pos_k[i], cmp_pos_v[i],
                     cmp_k_w1[i], cmp_k_w2[i], cmp_v_w1[i], cmp_v_w2[i], nsa_gate_b[i])
        mixed = (jax.nn.sigmoid(zmr) * (y_rw @ w_up_rwkv[i])
                 + jax.nn.sigmoid(zmn) * (y_nsa @ w_up_nsa[i]))
        x = x + mixed @ w_out[i]
        x = x + _hier_moe(_rmsnorm(x, g_ffn[i]), w_group[i], b_group[i], w_router[i],
                          b_router[i], w_exp_gate_up[i], w_exp_down[i])
        e = _rmsnorm(p[i] @ w_ple_proj[i], g_ple_norm[i])
        x = x + jax.nn.sigmoid(_rmsnorm(x, g_ple_gate_in[i]) @ w_ple_gate[i]) * e
    return _rmsnorm(x, g_final)


_drawn_inputs = setup_inputs


def setup_inputs(seed=0):
    import zlib

    import numpy as np

    out = dict(_drawn_inputs(seed))
    spreads = {}
    factors = {'rw_w2': 21.576,
     'rw_a0': 3.059,
     'rw_ln_b': 6.035,
     'cmp_pos_k': 8.0,
     'nsa_gate_b': 4.96,
     'b_group': 4.328,
     'b_router': 4.374,
     'g_ple_gate_in': 6.561}
    for name, (base, spread) in spreads.items():
        noise = np.random.default_rng([zlib.crc32(name.encode()), seed]).standard_normal(out[name].shape)
        drawn = base * np.exp(spread * noise) if base else spread * noise
        out[name] = __import__('jax').numpy.asarray(drawn.astype(out[name].dtype))
    for name, factor in factors.items():
        out[name] = (out[name] * factor).astype(out[name].dtype)
    return out
```

```python
from contextlib import ExitStack
import math

import numpy as np

import concourse.bass as bass
from concourse import mybir

F32 = mybir.dt.float32
I32 = mybir.dt.int32
ALU = mybir.AluOpType
ACT = mybir.ActivationFunctionType
AX = mybir.AxisListType

P = 128
D = 1024
S = 2048
DC = D // P
NT = S // P
NB = S // 512
HD = 64
RW_HEADS, RW_W = 8, 512
LORA, GATE_LORA = 64, 128
GN_EPS = 64e-5
NORM_EPS = 1e-6
RW_IN = 3 * RW_W + 2 * LORA + GATE_LORA
NSA_HEADS, KV_HEADS = 8, 2
Q_PER_KV = NSA_HEADS // KV_HEADS
NSA_W = 512
N_IN = RW_IN + NSA_W + 6 * KV_HEADS * HD + 3 * NSA_HEADS + 2 * D
GATE_ROW = RW_IN + NSA_W + 6 * KV_HEADS * HD
N_GATE = 3 * NSA_HEADS
MERGE_COL = GATE_ROW + N_GATE
NEG = -1e30
FORCE = 1e6
DECAY_SCALE = math.exp(-0.5)

ROW_R, ROW_K, ROW_V = 0, RW_W, 2 * RW_W
ROW_W, ROW_A, ROW_G = 3 * RW_W, 3 * RW_W + LORA, 3 * RW_W + 2 * LORA
ROW_Q = RW_IN
ROW_KC, ROW_VC, ROW_KS, ROW_VS, ROW_KW, ROW_VW = (RW_IN + NSA_W + 128 * n for n in range(6))
ROW_MERGE = GATE_ROW
Z_ROWS = ROW_MERGE + 2 * D


class Chain:

    def __init__(self, eng, sem):
        self.eng, self.sem, self.base, self.n = eng, sem, 0, 0

    def mark(self, ins):
        ins.then_inc(self.sem, 1)
        self.n += 1
        return ins

    def wait(self):
        self.eng.wait_ge(self.sem, self.base + self.n)

    def link(self, ins):
        self.mark(ins)
        self.wait()

    def loop(self, i, per):
        self.before, self.per = self.n, per
        self.base, self.n = i * per + self.n, 0

    def end(self, trips):
        assert self.n == self.per, (self.n, self.per)
        self.base, self.n = 0, self.before + trips * self.per


class Stage:

    def __init__(self, nc, ctx, name):
        self.nc, self.ctx, self.name, self.numbers = nc, ctx, name, []

    def sb(self, name, shape, dt=F32):
        return self.ctx.enter_context(self.nc.sbuf_tensor(f"{self.name}_{name}", shape, dt))

    def ps(self, name, shape, dt=F32):
        return self.ctx.enter_context(self.nc.psum_tensor(f"{self.name}_{name}", shape, dt))

    def sem(self, name):
        sem = self.ctx.enter_context(self.nc.semaphore(f"{self.name}_{name}"))
        self.numbers.append(sem.num)
        return sem

    def lasting_sem(self, name, whole):
        return whole.enter_context(self.nc.semaphore(f"{self.name}_{name}"))

    def sems(self, name, n):
        return [self.sem(f"{name}{k}") for k in range(n)]

    def zero(self):
        numbers = sorted(self.numbers)
        firsts = [n for n in numbers if n - 1 not in numbers]
        lasts = [n for n in numbers if n + 1 not in numbers]
        with self.nc.Block() as block:
            @block.gpsimd
            def _(pool):
                for first, last in zip(firsts, lasts):
                    pool.sem_clear(range(first, last + 1))

    def block(self):
        self.ctx.callback(self.zero)
        return self.ctx.enter_context(self.nc.Block())


def steady(eng, Z):
    eng.sem_inc(Z["passed"], 1)


def cols(v, c):
    return v.rearrange("(c p) -> p c", c=c)


def build_identity(pool, ident, seen):
    pool.memset(ident[:, :], 0.0).then_inc(seen, 1)
    pool.wait_ge(seen, 1)
    pool.affine_select(out=ident[:, :], in_=ident[:, :], compare_op=ALU.not_equal, fill=1.0, base=0,
                       pattern=[[-1, P]], channel_multiplier=1).then_inc(seen, 1)


def stage_project(nc, A, Z):
    outer = ExitStack()
    with outer:
        keep = Stage(nc, outer, "pr")
        hT = keep.sb("hT", [P, DC, S])

        with ExitStack() as ctx:
            st = Stage(nc, ctx, "nm")
            x_t = st.sb("x", [P, 2, D])
            sq = st.sb("sq", [P, D])
            stat = st.sb("stat", [P, 2, 4])
            xn = st.sb("xn", [P, 2, D])
            g_c = st.sb("g", [P, DC])
            ident = st.sb("ident", [P, P])
            tp = st.ps("tp", [P, 2, 2, 512])
            x_in = st.sems("x_in", 2)
            x_free, g_in, id_ok = (st.sem(n) for n in ("x_free", "g_in", "id_ok"))
            squares, roots, steps = (st.sem(n) for n in ("squares", "roots", "steps"))
            ms_ok, xn_ok, turned, taken = (st.sem(n) for n in ("ms_ok", "xn_ok", "turned", "taken"))
            block = st.block()

            @block.sync
            def _(sync):
                sync.dma_start(g_c[:, :], cols(A["g_mix"][0], DC)).then_inc(g_in, 16)
                with sync.Fori(0, NT // 2) as i:
                    for k in range(2):
                        sync.wait_ge(x_free, 2 * i + k + 1)
                        sync.dma_start(x_t[:, k, :], A["x"][0][bass.ds((2 * i + k) * P, P), :]).then_inc(x_in[k], 16)

            @block.gpsimd
            def _(pool):
                build_identity(pool, ident, id_ok)

            @block.scalar
            def _(act):
                with act.Fori(0, NT // 2) as i:
                    for k in range(2):
                        act.wait_ge(x_in[k], (i + 1) * 16)
                        act.wait_ge(squares, 2 * i + k)
                        act.activation(sq[:, :], x_t[:, k, :], ACT.Square,
                                       accum_out=stat[:, k, 0:1]).then_inc(squares, 1)
                    for k in range(2):
                        act.wait_ge(ms_ok, 2 * i + k + 1)
                        act.activation(stat[:, k, 2:3], stat[:, k, 1:2], ACT.Sqrt).then_inc(roots, 1)

            @block.vector
            def _(dve):
                v = Chain(dve, steps)
                dve.sem_inc(x_free, 2)
                dve.sem_inc(taken, 2)
                dve.wait_ge(g_in, 16)
                with dve.Fori(0, NT // 2) as i:
                    v.loop(i, 2)
                    for k in range(2):
                        dve.wait_ge(squares, 2 * i + k + 1)
                        dve.tensor_scalar(stat[:, k, 1:2], stat[:, k, 0:1], 1.0 / D, NORM_EPS,
                                          ALU.mult, ALU.add).then_inc(ms_ok, 1)
                    for k in range(2):
                        dve.wait_ge(roots, 2 * i + k + 1)
                        v.link(dve.reciprocal(stat[:, k, 3:4], stat[:, k, 2:3]))
                        dve.wait_ge(turned, 2 * i + k)
                        dve.tensor_scalar(xn[:, k, :], x_t[:, k, :], stat[:, k, 3:4], None,
                                          ALU.mult).then_inc(xn_ok, 1)
                        dve.wait_ge(xn_ok, 2 * i + k + 1)
                        dve.sem_inc(x_free, 1)
                    for k in range(2):
                        dve.wait_ge(turned, 2 * i + k + 1)
                        for c in range(2):
                            ins = dve.tensor_tensor(
                                hT[:, 4 * c:4 * c + 4, bass.ds((2 * i + k) * P, P)],
                                tp[:, k, c, :].rearrange("p (c t) -> p c t", c=4),
                                g_c[:, 4 * c:4 * c + 4].rearrange("p (c o) -> p c o", o=1).to_broadcast([P, 4, P]),
                                ALU.mult)
                        ins.then_inc(taken, 1)
                    v.end(NT // 2)

            @block.tensor
            def _(pe):
                pe.wait_ge(id_ok, 2)
                with pe.Fori(0, NT // 2) as i:
                    for k in range(2):
                        pe.wait_ge(xn_ok, 2 * i + k + 1)
                        pe.wait_ge(taken, 2 * i + k + 1)
                        for c in range(DC):
                            ins = pe.transpose(tp[:, k, c // 4, (c % 4) * P:(c % 4 + 1) * P],
                                               xn[:, k, c * P:(c + 1) * P], ident[:, :])
                        ins.then_inc(turned, 1)

        with ExitStack() as ctx:
            st = Stage(nc, ctx, "zp")
            w = st.sb("w", [P, 2, DC, P])
            zs = st.sb("zs", [P, 2, S])
            acc = st.ps("acc", [P, 2, NB, 512])
            w_in, z_out = st.sems("w_in", 2), [st.lasting_sem(f"z_out{k}", Z["whole"]) for k in range(2)]
            w_free, made, half_a, half_v = (st.sem(n) for n in ("w_free", "made", "half_a", "half_v"))
            n_lead = GATE_ROW // P
            n_all = Z_ROWS // P
            W = A["w_in"][0].rearrange("(c p) n -> p c n", p=P)
            block = st.block()

            @block.sync
            def _(sync):
                def load(i, k, col):
                    sync.wait_ge(w_free, 2 * i + k + 1)
                    sync.dma_start(w[:, k, :, :], W[:, :, bass.ds(col, P)]).then_inc(w_in[k], 16)

                with sync.Fori(0, n_lead // 2) as i:
                    for k in range(2):
                        load(i, k, (2 * i + k) * P)
                with sync.Fori(n_lead // 2, n_all // 2) as i:
                    for k in range(2):
                        load(i, k, (2 * i + k) * P + N_GATE)
                sync.wait_ge(w_free, n_all + 1)
                sync.dma_start(w[:, 0, :, 0:N_GATE], W[:, :, GATE_ROW:MERGE_COL]).then_inc(w_in[0], 16)

            @block.tensor
            def _(pe):
                pe.sem_inc(w_free, 2)
                with pe.Fori(0, n_all // 2) as i:
                    for k in range(2):
                        pe.wait_ge(w_in[k], (i + 1) * 16)
                        pe.wait_ge(half_a, 2 * i + k + 1)
                        pe.wait_ge(half_v, 2 * i + k + 1)
                        for n in range(NB):
                            for c in range(DC):
                                ins = pe.matmul(acc[:, k, n, :], w[:, k, c, :], hT[:, c, n * 512:(n + 1) * 512],
                                                start=(c == 0), stop=(c == DC - 1))
                        ins.then_inc(made, 1)
                        pe.wait_ge(made, 2 * i + k + 1)
                        pe.sem_inc(w_free, 1)
                pe.wait_ge(w_in[0], (n_all // 2 + 1) * 16)
                pe.wait_ge(half_a, n_all + 1)
                pe.wait_ge(half_v, n_all + 1)
                for n in range(NB):
                    for c in range(DC):
                        ins = pe.matmul(acc[0:N_GATE, 0, n, :], w[:, 0, c, 0:N_GATE],
                                        hT[:, c, n * 512:(n + 1) * 512], start=(c == 0), stop=(c == DC - 1))
                ins.then_inc(made, 1)

            @block.scalar
            def _(act):
                act.sem_inc(half_a, 2)
                with act.Fori(0, n_all // 2) as i:
                    for k in range(2):
                        act.wait_ge(made, 2 * i + k + 1)
                        act.wait_ge(z_out[k], i * 16)
                        act.copy(zs[:, k, 0:1024].rearrange("p (n t) -> p n t", n=2),
                                 acc[:, k, 0:2, :]).then_inc(half_a, 1)
                act.wait_ge(made, n_all + 1)
                act.wait_ge(z_out[0], n_all // 2 * 16)
                act.copy(zs[0:N_GATE, 0, 0:1024].rearrange("p (n t) -> p n t", n=2),
                         acc[0:N_GATE, 0, 0:2, :]).then_inc(half_a, 1)

            @block.vector
            def _(dve):
                dve.sem_inc(half_v, 2)
                with dve.Fori(0, n_all // 2) as i:
                    for k in range(2):
                        dve.wait_ge(made, 2 * i + k + 1)
                        dve.wait_ge(z_out[k], i * 16)
                        dve.tensor_copy(zs[:, k, 1024:2048].rearrange("p (n t) -> p n t", n=2),
                                        acc[:, k, 2:4, :]).then_inc(half_v, 1)
                dve.wait_ge(made, n_all + 1)
                dve.wait_ge(z_out[0], n_all // 2 * 16)
                dve.tensor_copy(zs[0:N_GATE, 0, 1024:2048].rearrange("p (n t) -> p n t", n=2),
                                acc[0:N_GATE, 0, 2:4, :]).then_inc(half_v, 1)

            @block.gpsimd
            def _(pool):
                with pool.Fori(0, n_all // 2) as i:
                    for k in range(2):
                        pool.wait_ge(half_a, 2 * i + k + 3)
                        pool.wait_ge(half_v, 2 * i + k + 3)
                        pool.dma_start(Z["z"][bass.ds((2 * i + k) * P, P), :], zs[:, k, :]).then_inc(z_out[k], 16)
                pool.wait_ge(half_a, n_all + 3)
                pool.wait_ge(half_v, n_all + 3)
                pool.dma_start(Z["gate"], zs[0:N_GATE, 0, :]).then_inc(z_out[0], 16)
                pool.wait_ge(z_out[0], (n_all // 2 + 1) * 16)
                pool.wait_ge(z_out[1], n_all // 2 * 16)


CH = P
NCH = S // CH
PAIRS = RW_W // P


def stage_rwkv_prep(nc, A, Z):
    with ExitStack() as ctx:
        st = Stage(nc, ctx, "rp")
        z3 = [st.sb(f"z{n}", [P, 1 + S]) for n in range(3)]
        dif = st.sb("dif", [P, S])
        zk, tw, zas, sg = (st.sb(n, [P, S]) for n in ("zk", "tw", "zas", "sg"))
        lw, cum, cm, aa, e1, e2 = (st.sb(n, [P, S]) for n in ("lw", "cum", "cm", "aa", "e1", "e2"))
        kk, sq = st.sb("kk", [P, S]), st.sb("sq", [P, S])
        ar = st.sb("ar", [P, NCH, 2, CH])
        bt, kt, vt = (st.sb(n, [P, S]) for n in ("bt", "kt", "vt"))
        go = sq
        same = st.sb("same", [P, P])
        reset = st.sb("reset", [P, S])
        dec = st.sb("dec", [P, 2, NCH])
        wl = st.sb("wl", [P, 3, P])
        mu = st.sb("mu", [P, RW_IN // P])
        mu_l = st.sb("mu_l", [HD, 2])
        par = st.sb("par", [P, 5, PAIRS])
        psW, psA = st.ps("psW", [P, NB, 512]), st.ps("psA", [P, NB, 512])
        lora_in, par_in, loads, z_used, w_used = (
            st.sem(n) for n in ("lora_in", "par_in", "loads", "z_used", "w_used"))
        init, lora_ok, lora_act, made, acts, vec = (
            st.sem(n) for n in ("init", "lora_ok", "lora_act", "made", "acts", "vec"))
        kk0_ok, rk_ok, cm_ok, out_ok, stored, act_self = (
            st.sem(n) for n in ("kk0_ok", "rk_ok", "cm_ok", "out_ok", "stored", "act_self"))
        bon_ok, small, g_free = st.sem("bon_ok"), st.sem("small"), st.sem("g_free")
        MADE, ACTS, STORES = 5, 9, 6
        W0, A0, K_K, K_A, R_K = range(5)
        z, Zc = Z["z"], lambda row: Z["z"][bass.ds(row, P), :]
        block = st.block()

        @block.sync
        def _(sync):
            sync.wait_ge(init, 4)
            sync.dma_start(z3[0][0:LORA, 1:1 + S], z[ROW_W:ROW_W + LORA, :]).then_inc(lora_in, 16)
            sync.dma_start(z3[1][0:LORA, 1:1 + S], z[ROW_A:ROW_A + LORA, :]).then_inc(lora_in, 16)
            sync.dma_start(z3[2][:, 1:1 + S], z[ROW_G:ROW_G + P, :]).then_inc(lora_in, 16)
            sync.dma_start(mu[:, :], cols(A["mu_shift"][0], RW_IN // P)).then_inc(par_in, 16)
            sync.dma_start(mu_l[:, :], A["mu_shift"][0][ROW_W:ROW_G].rearrange("(c p) -> p c", c=2)).then_inc(par_in, 16)
            for n, name in enumerate(("rw_w0", "rw_a0", "rw_k_k", "rw_k_a")):
                sync.dma_start(par[:, n, :], cols(A[name][0], PAIRS)).then_inc(par_in, 16)
            sync.dma_start(par[:, R_K, :], cols(A["rw_r_k"][0].rearrange("h d -> (h d)"), PAIRS)).then_inc(par_in, 16)
            with sync.Fori(0, PAIRS) as i:
                sync.wait_ge(z_used, i + 1)
                for n, row in enumerate((ROW_R, ROW_K, ROW_V)):
                    sync.dma_start(z3[n][:, 1:1 + S], Zc(i * P + row)).then_inc(loads, 16)
                sync.wait_ge(w_used, i + 1)
                steady(sync, Z)
                sync.dma_start(wl[0:LORA, 0, :], A["rw_w2"][0][:, bass.ds(i * P, P)]).then_inc(loads, 16)
                sync.dma_start(wl[0:LORA, 1, :], A["rw_a2"][0][:, bass.ds(i * P, P)]).then_inc(loads, 16)
                sync.dma_start(wl[:, 2, :], A["rw_g2"][0][:, bass.ds(i * P, P)]).then_inc(loads, 16)
                sync.wait_ge(out_ok, i + 1)
                steady(sync, Z)
                sync.dma_start(Z["rar"][bass.ds(i * P, P), :, :, :], ar[:, :, :, :]).then_inc(stored, 16)
                sync.dma_start(Z["rb"][bass.ds(i * P, P), :], bt[:, :]).then_inc(stored, 16)
                sync.dma_start(Z["rk"][bass.ds(i * P, P), :], kt[:, :]).then_inc(stored, 16)
                sync.dma_start(Z["rv"][bass.ds(i * P, P), :], vt[:, :]).then_inc(stored, 16)
                sync.dma_start(Z["rdec"][bass.ds(i * P, P), :, :], dec[:, :, :]).then_inc(stored, 16)
                sync.dma_start(Z["rbonus"][bass.ds(i * P, P), :], dif[:, :]).then_inc(stored, 16)
                sync.wait_ge(stored, (i + 1) * 16 * STORES)
                steady(sync, Z)
            sync.wait_ge(g_free, PAIRS * 16)

        @block.gpsimd
        def _(pool):
            for t in z3:
                pool.memset(t[:, 0:1], 0.0).then_inc(init, 1)
            pool.memset(reset[:, :], 1.0).then_inc(small, 1)
            pool.wait_ge(small, 1)
            pool.memset(reset[:, :].rearrange("p (c t) -> p c t", t=CH)[:, :, 0:1], 0.0).then_inc(init, 1)
            pool.memset(same[:, :], 0.0).then_inc(small, 1)
            pool.wait_ge(small, 2)
            pool.memset(same[0:HD, 0:HD], 1.0).then_inc(init, 1)
            pool.memset(same[HD:P, HD:P], 1.0).then_inc(init, 1)

        @block.tensor
        def _(pe):
            def product(dst, lhsT, rhs, k):
                for n in range(NB):
                    ins = pe.matmul(dst[:, n, :], lhsT, rhs[0:k, n * 512:(n + 1) * 512], start=True, stop=True)
                ins.then_inc(made, 1)

            pe.sem_inc(w_used, 1)
            pe.wait_ge(init, 6)
            pe.wait_ge(lora_act, 2)
            pe.wait_ge(lora_ok, 3)
            with pe.Fori(0, PAIRS) as i:
                pe.wait_ge(loads, (i + 1) * 96)
                pe.wait_ge(bon_ok, i)
                product(psW, wl[0:LORA, 0, :], tw, LORA)
                product(psA, wl[0:LORA, 1, :], zas, LORA)
                pe.wait_ge(acts, i * ACTS + 1)
                product(psW, wl[:, 2, :], sg, P)
                pe.wait_ge(acts, i * ACTS + 4)
                product(psA, same[:, :], sq, P)
                pe.wait_ge(made, i * MADE + 4)
                pe.sem_inc(w_used, 1)
                pe.wait_ge(rk_ok, i + 1)
                product(psW, same[:, :], cum, P)

        @block.scalar
        def _(act):
            a = Chain(act, acts)
            act.wait_ge(lora_ok, 1)
            act.activation(tw[0:LORA, :], tw[0:LORA, :], ACT.Tanh).then_inc(lora_act, 1)
            act.wait_ge(lora_ok, 3)
            act.activation(sg[:, :], sg[:, :], ACT.Sigmoid).then_inc(lora_act, 1)
            banks = lambda t: t[:, :].rearrange("p (n t) -> p n t", n=NB)
            with act.Fori(0, PAIRS) as i:
                a.loop(i, ACTS)
                act.wait_ge(made, i * MADE + 1)
                a.mark(act.activation(banks(lw), psW[:, :, :], ACT.Sigmoid, bias=par[:, W0, bass.ds(i, 1)]))
                act.wait_ge(made, i * MADE + 2)
                a.mark(act.activation(banks(aa), psA[:, :, :], ACT.Sigmoid, bias=par[:, A0, bass.ds(i, 1)]))
                act.wait_ge(made, i * MADE + 3)
                act.wait_ge(g_free, i * 16)
                a.link(act.copy(banks(go), psW[:, :, :]))
                act.dma_start(Z["rg"][bass.ds(i * P, P), :], go[:, :]).then_inc(g_free, 16)
                act.wait_ge(kk0_ok, i + 1)
                act.wait_ge(g_free, (i + 1) * 16)
                a.mark(act.activation(sq[:, :], kk[:, :], ACT.Square))
                act.wait_ge(made, i * MADE + 4)
                a.link(act.activation(banks(e1), psA[:, :, :], ACT.Sqrt))
                act.wait_ge(cm_ok, i + 1)
                a.mark(act.activation(e1[:, :], cm[:, :], ACT.Exp))
                a.mark(act.activation(e2[:, :], cm[:, :], ACT.Exp, scale=-1.0))
                a.mark(act.activation(lw[:, :], lw[:, :], ACT.Exp))
                act.activation(dec[:, 0, :], dec[:, 0, :], ACT.Exp)
                a.mark(act.activation(dec[:, 1, :], dec[:, 1, :], ACT.Exp))
                a.end(PAIRS)

        @block.vector
        def _(dve):
            v = Chain(dve, vec)

            def shift(out, src, m, n=P):
                v.link(dve.tensor_tensor(dif[0:n, :], src[0:n, 0:S], src[0:n, 1:1 + S], ALU.subtract))
                v.link(dve.scalar_tensor_tensor(out=out[0:n, :], in0=dif[0:n, :], scalar=m,
                                                in1=src[0:n, 1:1 + S], op0=ALU.mult, op1=ALU.add))

            dve.wait_ge(init, 6)
            dve.wait_ge(lora_in, 48)
            dve.wait_ge(par_in, 16 * 7)
            shift(tw, z3[0], mu_l[:, 0:1], LORA)
            dve.sem_inc(lora_ok, 1)
            shift(zas, z3[1], mu_l[:, 1:2], LORA)
            shift(sg, z3[2], mu[:, RW_IN // P - 1:RW_IN // P])
            dve.sem_inc(lora_ok, 2)
            dve.sem_inc(z_used, 1)
            chunks = lambda t: t[:, :].rearrange("p (c t) -> p c t", t=CH)
            with dve.Fori(0, PAIRS) as i:
                v.loop(i, 20)
                dve.wait_ge(loads, (i + 1) * 96)
                dve.wait_ge(stored, i * 16 * STORES)
                shift(cum, z3[0], mu[:, bass.ds(i, 1)])
                shift(zk, z3[1], mu[:, bass.ds(i + PAIRS, 1)])
                shift(vt, z3[2], mu[:, bass.ds(i + 2 * PAIRS, 1)])
                v.link(dve.tensor_copy(ar[:, :, 1, :], chunks(cum)))
                dve.sem_inc(z_used, 1)
                v.link(dve.tensor_scalar(kk[:, :], zk[:, :], par[:, K_K, bass.ds(i, 1)], None, ALU.mult))
                dve.sem_inc(kk0_ok, 1)
                dve.wait_ge(acts, i * ACTS + 1)
                v.link(dve.tensor_scalar(lw[:, :], lw[:, :], -DECAY_SCALE, None, ALU.mult))
                v.link(dve.tensor_tensor_scan(cum[:, :], reset[:, :], lw[:, :], 0.0, ALU.mult, ALU.add))
                mid = chunks(cum)[:, :, CH // 2 - 1:CH // 2]
                v.link(dve.tensor_tensor(chunks(cm), chunks(cum), mid.to_broadcast([P, NCH, CH]), ALU.subtract))
                dve.tensor_copy(dec[:, 0, :].rearrange("p (c o) -> p c o", o=1), mid)
                dve.tensor_copy(dec[:, 1, :].rearrange("p (c o) -> p c o", o=1), chunks(cm)[:, :, CH - 1:CH])
                v.link(dve.tensor_tensor(lw[:, :], cm[:, :], lw[:, :], ALU.subtract))
                dve.wait_ge(acts, i * ACTS + 5)
                v.link(dve.tensor_scalar(dif[:, :], e1[:, :], 1e-12, None, ALU.max))
                dve.sem_inc(cm_ok, 1)
                v.link(dve.reciprocal(dif[:, :], dif[:, :]))
                v.link(dve.tensor_tensor(kk[:, :], kk[:, :], dif[:, :], ALU.mult))
                dve.wait_ge(acts, i * ACTS + 2)
                v.link(dve.tensor_scalar(dif[:, :], aa[:, :], -1.0, par[:, K_A, bass.ds(i, 1)], ALU.add, ALU.mult))
                v.link(dve.scalar_tensor_tensor(out=zk[:, :], in0=dif[:, :], scalar=1.0, in1=zk[:, :],
                                                op0=ALU.add, op1=ALU.mult))
                v.link(dve.scalar_tensor_tensor(out=chunks(cum), in0=ar[:, :, 1, :], scalar=par[:, R_K, bass.ds(i, 1)],
                                                in1=chunks(zk), op0=ALU.mult, op1=ALU.mult))
                dve.wait_ge(acts, i * ACTS + 3)
                dve.sem_inc(rk_ok, 1)
                v.mark(dve.tensor_tensor(aa[:, :], kk[:, :], aa[:, :], ALU.mult))
                dve.wait_ge(acts, i * ACTS + 9)
                v.wait()
                dve.tensor_tensor(bt[:, :], aa[:, :], e2[:, :], ALU.mult)
                dve.tensor_tensor(kt[:, :], zk[:, :], e2[:, :], ALU.mult)
                dve.scalar_tensor_tensor(out=ar[:, :, 0, :], in0=chunks(kk), scalar=-1.0, in1=chunks(lw),
                                         op0=ALU.mult, op1=ALU.mult)
                dve.tensor_tensor(ar[:, :, 1, :], ar[:, :, 1, :], chunks(e1), ALU.mult)
                dve.wait_ge(made, (i + 1) * MADE)
                v.link(dve.tensor_tensor(dif[:, :].rearrange("p (n t) -> p n t", n=NB), psW[:, :, :],
                                         vt[:, :].rearrange("p (n t) -> p n t", n=NB), ALU.mult))
                dve.sem_inc(bon_ok, 1)
                dve.sem_inc(out_ok, 1)
                v.end(PAIRS)


LEVELS = 7


def stage_rwkv_scan(nc, A, Z):
    H, HG = RW_HEADS, 4
    with ExitStack() as ctx:
        st = Stage(nc, ctx, "rs")
        ar = st.sb("ar", [HD, 2, H, 2, CH])
        bkv = st.sb("bkv", [HD, 2, 3, H, CH])
        tok = st.sb("tok", [P, 3, H, HD])
        M = st.sb("M", [P, H, 4, CH])
        Lm = st.sb("Lm", [P, 2, HG, CH])
        X = st.sb("X", [P, 2, HG, CH])
        inv = st.sb("inv", [P, 2, HG, CH])
        invT = st.sb("invT", [P, 2, HG, CH])
        Wt, U = st.sb("W", [P, H, HD]), st.sb("U", [P, H, HD])
        state, mid = st.sb("state", [HD, H, HD]), st.sb("mid", [HD, H, HD])
        o = st.sb("o", [HD, H, CH])
        dec = st.sb("dec", [HD, H, 2, NCH])
        ident = st.sb("ident", [P, P])
        row, col, row_s, col_s = (st.sb(n, [P, P], I32) for n in ("row", "col", "row_s", "col_s"))
        upper = st.sb("upper", [P, 4, CH])
        block_of = st.sb("block_of", [P, LEVELS + 1, CH])
        join = st.sb("join", [P, LEVELS, CH])
        bank = st.ps("bank", [P, 8, 512])
        XB, DB, EB, SCORE, WB, UB, OB, SB = (0, 1), (2, 3), (4, 5), (3, 4, 5), 6, 7, (0, 1), 2
        loads = st.sems("loads", 2)
        ld_used, dec_in, id_ok, setup, tables, turned, scored = (
            st.sem(n) for n in ("ld_used", "dec_in", "id_ok", "setup", "tables", "turned", "scored"))
        x_made, d_made, e_made, w_made, u_made, o_made, s_made = (
            st.sem(n) for n in ("x_made", "d_made", "e_made", "w_made", "u_made", "o_made", "s_made"))
        tok_ok, m_ok, l_ok, x_ok, d_ok, e_ok, w_ok, u_ok, o_ok, s_ok, mid_ok = (
            st.sem(n) for n in ("tok_ok", "m_ok", "l_ok", "x_ok", "d_ok", "e_ok", "w_ok", "u_ok", "o_ok", "s_ok", "mid_ok"))
        o_out = st.sem("o_out")
        block = st.block()
        heads = lambda t: t.rearrange("(h d) s -> d h s", h=H)

        @block.sync
        def _(sync):
            sync.dma_start(dec[:, :, :, :], Z["rdec"].rearrange("(h d) a c -> d h a c", h=H)).then_inc(dec_in, 16)
            with sync.Fori(0, NCH // 2) as i:
                for k in range(2):
                    c = 2 * i + k
                    sync.wait_ge(ld_used, c + 1)
                    for h2 in range(2):
                        sync.dma_start(ar[:, k, 4 * h2:4 * h2 + 4, :, :],
                                       Z["rar"].rearrange("(h d) c a t -> d h c a t", h=H)[:, 4 * h2:4 * h2 + 4, bass.ds(c, 1), :, :]
                                       .rearrange("d h c a t -> d h (c a t)")).then_inc(loads[k], 16)
                    for n, name in enumerate(("rb", "rk", "rv")):
                        sync.dma_start(bkv[:, k, n, :, :], heads(Z[name])[:, :, bass.ds(c * CH, CH)]).then_inc(loads[k], 16)

        @block.gpsimd
        def _(pool):
            build_identity(pool, ident, id_ok)
            pool.iota(row[:, :], [[0, P]], base=0, channel_multiplier=1).then_inc(setup, 1)
            pool.iota(col[:, :], [[1, P]], base=0, channel_multiplier=0).then_inc(setup, 1)
            pool.wait_ge(tables, 1)
            with pool.Fori(0, NCH // 2) as i:
                for k in range(2):
                    c = 2 * i + k
                    for lev in range(LEVELS):
                        for g in range(2):
                            if lev == 0:
                                pool.wait_ge(m_ok, 8 * c + 4 * g + 4)
                            pool.wait_ge(x_made, 14 * c + 2 * lev + g)
                            if lev == 1:
                                pool.wait_ge(e_ok, 14 * c + g + 1)
                            pool.tensor_tensor(Lm[:, g, :, :], M[:, 4 * g:4 * g + 4, 0, :],
                                               join[:, lev:lev + 1, :].to_broadcast([P, HG, CH]),
                                               ALU.mult).then_inc(l_ok, 1)

        @block.tensor
        def _(pe):
            pe.sem_inc(ld_used, 2)
            pe.wait_ge(id_ok, 2)
            with pe.Fori(0, NCH // 2) as i:
                for k in range(2):
                    c = 2 * i + k
                    pe.wait_ge(loads[k], (i + 1) * 80)
                    pe.wait_ge(o_ok, c)
                    pe.wait_ge(s_ok, c + 1)
                    steady(pe, Z)
                    for n in range(3):
                        for h in range(H):
                            ins = pe.transpose(bank[:, n, h * HD:(h + 1) * HD], bkv[:, k, n, h, :], ident[0:HD, 0:HD])
                        ins.then_inc(turned, 1)
                    for h in range(H):
                        if h >= 3:
                            pe.wait_ge(m_ok, 8 * c + h - 2)
                        b = SCORE[h % 3]
                        arh = ar[:, k, h, :, :].rearrange("d a t -> d (a t)")
                        pe.matmul(bank[:, b, 0:2 * CH], bkv[:, k, 0, h, :], arh, start=True, stop=True)
                        pe.matmul(bank[:, b, 2 * CH:4 * CH], bkv[:, k, 1, h, :], arh, start=True, stop=True).then_inc(scored, 1)
                    pe.wait_ge(m_ok, 8 * c + 8)
                    for g in range(2):
                        pe.wait_ge(l_ok, 14 * c + g + 1)
                        if g == 0:
                            pe.wait_ge(tok_ok, 3 * c + 3)
                        for h in range(HG):
                            ins = pe.matmul(bank[:, DB[g], h * CH:(h + 1) * CH], Lm[:, g, h, :], ident[:, :],
                                            start=True, stop=True)
                        ins.then_inc(d_made, 1)
                        pe.wait_ge(d_made, 12 * c + g + 1)
                        pe.sem_inc(x_made, 1)
                    for lev in range(1, LEVELS):
                        for g in range(2):
                            pe.wait_ge(l_ok, 14 * c + 2 * lev + g + 1)
                            pe.wait_ge(d_ok, 12 * c + 2 * lev + g - 1)
                            for h in range(HG):
                                ins = pe.matmul(bank[:, XB[g], h * CH:(h + 1) * CH], Lm[:, g, h, :], inv[:, g, h, :],
                                                start=True, stop=True)
                            ins.then_inc(x_made, 1)
                        for g in range(2):
                            pe.wait_ge(x_ok, 12 * c + 2 * lev + g - 1)
                            pe.wait_ge(e_ok, 14 * c + 2 * lev + g - 1)
                            if lev < LEVELS - 1:
                                for h in range(HG):
                                    ins = pe.matmul(bank[:, DB[g], h * CH:(h + 1) * CH], invT[:, g, h, :], X[:, g, h, :],
                                                    start=True, stop=True)
                                ins.then_inc(d_made, 1)
                            for h in range(HG):
                                ins = pe.matmul(bank[:, EB[g], h * CH:(h + 1) * CH], X[:, g, h, :], invT[:, g, h, :],
                                                start=True, stop=True)
                            ins.then_inc(e_made, 1)
                    pe.wait_ge(mid_ok, c + 1)
                    for h in range(H):
                        pe.matmul(bank[:, WB, h * HD:(h + 1) * HD], ar[:, k, h, 0, :], mid[:, h, :], start=True, stop=False)
                        ins = pe.matmul(bank[:, WB, h * HD:(h + 1) * HD], M[:, h, 2, :], tok[:, 2, h, :],
                                        start=False, stop=True)
                    ins.then_inc(w_made, 1)
                    pe.wait_ge(w_ok, c + 1)
                    pe.wait_ge(e_ok, 14 * c + 14)
                    for h in range(H):
                        ins = pe.matmul(bank[:, UB, h * HD:(h + 1) * HD], invT[:, h // HG, h % HG, :], Wt[:, h, :],
                                        start=True, stop=True)
                    ins.then_inc(u_made, 1)
                    pe.wait_ge(u_ok, c + 1)
                    for h in range(H):
                        pe.matmul(bank[0:HD, SB, h * HD:(h + 1) * HD], tok[:, 0, h, :], U[:, h, :], start=True, stop=False)
                        ins = pe.matmul(bank[0:HD, SB, h * HD:(h + 1) * HD], tok[:, 1, h, :], tok[:, 2, h, :],
                                        start=False, stop=True)
                    ins.then_inc(s_made, 1)
                    for h in range(H):
                        dst = bank[0:HD, OB[h // HG], (h % HG) * CH:(h % HG + 1) * CH]
                        pe.matmul(dst, mid[:, h, :], ar[:, k, h, 1, :], start=True, stop=False)
                        pe.matmul(dst, U[:, h, :], M[:, h, 1, :], start=False, stop=False)
                        ins = pe.matmul(dst, tok[:, 2, h, :], M[:, h, 3, :], start=False, stop=True)
                    ins.then_inc(o_made, 1)
                    pe.wait_ge(o_made, c + 1)
                    pe.sem_inc(ld_used, 1)

        @block.scalar
        def _(act):
            with act.Fori(0, NCH // 2) as i:
                for k in range(2):
                    c = 2 * i + k
                    act.wait_ge(o_made, c)
                    for n in range(3):
                        act.wait_ge(turned, 3 * c + n + 1)
                        act.copy(tok[:, n, :, :].rearrange("p h d -> p (h d)"), bank[:, n, :]).then_inc(tok_ok, 1)
                    for lev in range(1, LEVELS):
                        for g in range(2):
                            act.wait_ge(x_made, 14 * c + 2 * lev + g + 1)
                            act.wait_ge(e_made, 12 * c + 2 * lev - 2 + g)
                            act.copy(X[:, g, :, :].rearrange("p h t -> p (h t)"), bank[:, XB[g], :]).then_inc(x_ok, 1)
                    act.wait_ge(w_made, c + 1)
                    act.copy(Wt[:, :, :].rearrange("p h d -> p (h d)"), bank[:, WB, :]).then_inc(w_ok, 1)
                    act.wait_ge(o_made, c + 1)
                    act.wait_ge(o_out, c * 16)
                    act.copy(o[:, :, :].rearrange("p (b h) t -> p b (h t)", b=2), bank[0:HD, 0:2, :]).then_inc(o_ok, 1)
                    act.wait_ge(o_ok, c + 1)
                    act.dma_start(heads(Z["ro"])[:, :, bass.ds(c * CH, CH)], o[:, :, :]).then_inc(o_out, 16)
            act.wait_ge(o_out, NCH * 16)

        @block.vector
        def _(dve):
            v = Chain(dve, setup)
            v.n = 2
            dve.wait_ge(setup, 2)
            for lev in range(LEVELS + 1):
                v.mark(dve.tensor_scalar(row_s[:, :], row[:, :], lev, None, ALU.arith_shift_right))
                v.link(dve.tensor_scalar(col_s[:, :], col[:, :], lev, None, ALU.arith_shift_right))
                v.link(dve.tensor_tensor(block_of[:, lev, :], row_s[:, :], col_s[:, :], ALU.is_equal))
            for n in range(4):
                v.link(dve.tensor_tensor(upper[:, n, :], col[:, :], row[:, :], ALU.is_ge if n % 2 else ALU.is_gt))
            for lev in range(LEVELS):
                v.link(dve.tensor_tensor(join[:, lev, :], block_of[:, lev + 1, :], block_of[:, lev, :], ALU.subtract))
                v.link(dve.tensor_tensor(join[:, lev, :], join[:, lev, :], upper[:, 0, :], ALU.mult))
            v.link(dve.memset(state[:, :, :], 0.0))
            dve.sem_inc(tables, 1)
            dve.sem_inc(s_ok, 1)
            dve.wait_ge(dec_in, 16)
            dve.wait_ge(id_ok, 2)
            eye = ident[:, :].rearrange("p (o t) -> p o t", o=1).to_broadcast([P, HG, CH])
            flat = lambda t: t.rearrange("p h t -> p (h t)")
            in_bank = lambda b: bank[:, b, :].rearrange("p (h t) -> p h t", h=HG)
            with dve.Fori(0, NCH // 2) as i:
                for k in range(2):
                    c = 2 * i + k
                    dve.wait_ge(s_ok, c + 1)
                    dve.wait_ge(o_made, c)
                    dve.tensor_tensor(mid[:, :, :], state[:, :, :],
                                      dec[:, :, 0, bass.ds(c, 1)].to_broadcast([HD, H, HD]), ALU.mult).then_inc(mid_ok, 1)
                    for h in range(H):
                        dve.wait_ge(scored, 8 * c + h + 1)
                        dve.tensor_tensor(M[:, h, :, :].rearrange("p a t -> p (a t)"), bank[:, SCORE[h % 3], :],
                                          upper[:, :, :].rearrange("p a t -> p (a t)"), ALU.mult).then_inc(m_ok, 1)
                    for g in range(2):
                        dve.wait_ge(l_ok, 14 * c + g + 1)
                        dve.tensor_tensor(invT[:, g, :, :], Lm[:, g, :, :], eye, ALU.add).then_inc(e_ok, 1)
                        dve.wait_ge(d_made, 12 * c + g + 1)
                        dve.tensor_tensor(inv[:, g, :, :], in_bank(DB[g]), eye, ALU.add).then_inc(d_ok, 1)
                    for lev in range(1, LEVELS):
                        for g in range(2):
                            dve.wait_ge(d_ok, 12 * c + 2 * lev + g - 1)
                            dve.wait_ge(e_ok, 14 * c + 2 * lev + g - 1)
                            dve.wait_ge(e_made, 12 * c + 2 * lev + g - 1)
                            if lev < LEVELS - 1:
                                dve.tensor_tensor(inv[:, g, :, :], in_bank(DB[g]), inv[:, g, :, :],
                                                  ALU.add).then_inc(d_ok, 1)
                            dve.tensor_tensor(invT[:, g, :, :], in_bank(EB[g]), invT[:, g, :, :],
                                              ALU.add).then_inc(e_ok, 1)
                    dve.wait_ge(u_made, c + 1)
                    dve.tensor_copy(U[:, :, :].rearrange("p h d -> p (h d)"), bank[:, UB, :]).then_inc(u_ok, 1)
                    dve.wait_ge(s_made, c + 1)
                    dve.tensor_tensor(state[:, :, :].rearrange("p h d -> p (h d)"),
                                      mid[:, :, :].rearrange("p h d -> p (h d)"), bank[0:HD, SB, :], ALU.add).then_inc(tables, 1)
                    dve.wait_ge(tables, c + 2)
                    dve.tensor_tensor(state[:, :, :], state[:, :, :],
                                      dec[:, :, 1, bass.ds(c, 1)].to_broadcast([HD, H, HD]), ALU.mult).then_inc(s_ok, 1)


def stage_rwkv_post(nc, A, Z):
    with ExitStack() as ctx:
        st = Stage(nc, ctx, "rn")
        o, bonus, g, sd = (st.sb(n, [P, 2, S]) for n in ("o", "bonus", "g", "sd"))
        sq = st.sb("sq", [P, S])
        average = st.sb("average", [P, P])
        eps = st.sb("eps", [P, 1])
        par = st.sb("par", [P, 2, PAIRS])
        mean, var = st.ps("mean", [P, NB, 512]), st.ps("var", [P, NB, 512])
        loads, stored = st.sems("loads", 2), st.sems("stored", 2)
        init, par_in, mean_made, var_made, centred, squared, rooted, y_ok, steps = (
            st.sem(n) for n in ("init", "par_in", "mean_made", "var_made", "centred", "squared", "rooted", "y_ok", "steps"))
        block = st.block()
        rows = lambda t, c: t[bass.ds(c * P, P), :]
        banks = lambda t: t.rearrange("p (n t) -> p n t", n=NB)

        @block.sync
        def _(sync):
            for n, name in enumerate(("rw_ln_w", "rw_ln_b")):
                sync.dma_start(par[:, n, :], cols(A[name][0], PAIRS)).then_inc(par_in, 16)
            with sync.Fori(0, PAIRS // 2) as i:
                for k in range(2):
                    sync.wait_ge(stored[k], i * 16)
                    for t, name in ((o, "ro"), (bonus, "rbonus"), (g, "rg")):
                        sync.dma_start(t[:, k, :], rows(Z[name], 2 * i + k)).then_inc(loads[k], 16)

        @block.gpsimd
        def _(pool):
            pool.memset(average[:, :], 0.0).then_inc(init, 1)
            pool.wait_ge(init, 1)
            pool.memset(average[0:HD, 0:HD], 1.0 / HD).then_inc(init, 1)
            pool.memset(average[HD:P, HD:P], 1.0 / HD).then_inc(init, 1)
            pool.wait_ge(init, 3)
            pool.memset(eps[:, :], GN_EPS).then_inc(init, 1)
            with pool.Fori(0, PAIRS // 2) as i:
                for k in range(2):
                    pool.wait_ge(y_ok, 2 * i + k + 1)
                    pool.dma_start(rows(Z["yr"], 2 * i + k), o[:, k, :]).then_inc(stored[k], 16)
            for k in range(2):
                pool.wait_ge(stored[k], PAIRS // 2 * 16)

        @block.tensor
        def _(pe):
            pe.wait_ge(init, 4)
            with pe.Fori(0, PAIRS // 2) as i:
                for k in range(2):
                    pe.wait_ge(loads[k], (i + 1) * 48)
                    pe.wait_ge(centred, 2 * i + k)
                    for n in range(NB):
                        ins = pe.matmul(mean[:, n, :], average[:, :], o[:, k, n * 512:(n + 1) * 512], start=True, stop=True)
                    ins.then_inc(mean_made, 1)
                    pe.wait_ge(squared, 2 * i + k + 1)
                    pe.wait_ge(rooted, 2 * i + k)
                    for n in range(NB):
                        ins = pe.matmul(var[:, n, :], average[:, :], sq[:, n * 512:(n + 1) * 512], start=True, stop=True)
                    ins.then_inc(var_made, 1)

        @block.scalar
        def _(act):
            act.wait_ge(init, 4)
            with act.Fori(0, PAIRS // 2) as i:
                for k in range(2):
                    act.wait_ge(centred, 2 * i + k + 1)
                    act.wait_ge(var_made, 2 * i + k)
                    act.activation(sq[:, :], o[:, k, :], ACT.Square).then_inc(squared, 1)
                    act.wait_ge(var_made, 2 * i + k + 1)
                    act.activation(banks(sd[:, k, :]), var[:, :, :], ACT.Sqrt, bias=eps[:, 0:1]).then_inc(rooted, 1)

        @block.vector
        def _(dve):
            v = Chain(dve, steps)
            dve.wait_ge(par_in, 32)
            with dve.Fori(0, PAIRS // 2) as i:
                v.loop(i, 8)
                for k in range(2):
                    dve.wait_ge(mean_made, 2 * i + k + 1)
                    dve.tensor_tensor(banks(o[:, k, :]), banks(o[:, k, :]), mean[:, :, :], ALU.subtract).then_inc(centred, 1)
                    dve.wait_ge(rooted, 2 * i + k + 1)
                    v.link(dve.reciprocal(sd[:, k, :], sd[:, k, :]))
                    v.link(dve.tensor_tensor(o[:, k, :], o[:, k, :], sd[:, k, :], ALU.mult))
                    v.link(dve.tensor_scalar(o[:, k, :], o[:, k, :], par[:, 0, bass.ds(2 * i + k, 1)],
                                             par[:, 1, bass.ds(2 * i + k, 1)], ALU.mult, ALU.add))
                    v.link(dve.tensor_tensor(o[:, k, :], o[:, k, :], bonus[:, k, :], ALU.add))
                    dve.tensor_tensor(o[:, k, :], o[:, k, :], g[:, k, :], ALU.mult).then_inc(y_ok, 1)
                v.end(PAIRS // 2)


CMP_BLOCK, CMP_STRIDE, SEL_BLOCK, N_SELECT, WINDOW = 32, 16, 64, 8, 512
N_CMP = (S - CMP_BLOCK) // CMP_STRIDE + 1
N_SEL = S // SEL_BLOCK
LOWEST = -3e38
STEPS = 62
SLOPES = [2.0 ** (-8.0 * (h + 1) / NSA_HEADS) for h in range(NSA_HEADS)]


def stage_nsa(nc, A, Z):
    G, R = KV_HEADS, Q_PER_KV
    outer = ExitStack()
    with outer:
        kp = Stage(nc, outer, "at")
        ks_t = kp.sb("ks_t", [HD, G, S])
        kw_t = kp.sb("kw_t", [HD, G, WINDOW + S])
        vs = kp.sb("vs", [P, NT, P])
        vw = kp.sb("vw", [P, WINDOW // P + NT, P])
        kcmp = kp.sb("kcmp", [HD, G, P])
        vcmp = kp.sb("vcmp", [P, G, HD])
        ident = kp.sb("ident", [P, P])

        with ExitStack() as ctx:
            st = Stage(nc, ctx, "cp")
            kv = st.sb("kv", [HD, 2, G, S])
            w1 = st.sb("w1", [HD, 2, CMP_BLOCK, HD])
            w2 = st.sb("w2", [HD, 2, HD])
            pos = st.sb("pos", [HD, 2, CMP_BLOCK])
            pos_p = st.sb("pos_p", [HD, 2])
            hid = st.sb("hid", [HD, 2, G, N_CMP])
            v_raw = st.sb("v_raw", [P, 2, S])
            acc = st.ps("acc", [P, 2, 512])
            out = st.ps("out", [P, 512])
            tp = st.ps("tp", [P, 4, 512])
            in_k, in_v, in_w, id_ok, hid_made, pos_ok, hid_ok, out_made, out_ok, turned, tok_ok, zeros = (
                st.sem(n) for n in ("in_k", "in_v", "in_w", "id_ok", "hid_made", "pos_ok", "hid_ok", "out_made",
                                    "out_ok", "turned", "tok_ok", "zeros"))
            block = st.block()

            @block.sync
            def _(sync):
                for a, (row, n) in enumerate(((ROW_KC, "k"), (ROW_VC, "v"))):
                    sync.dma_start(w1[:, a, :, :], A[f"cmp_{n}_w1"][0].rearrange("(l d) e -> d l e", d=HD)).then_inc(in_w, 16)
                    sync.dma_start(w2[:, a, :], A[f"cmp_{n}_w2"][0]).then_inc(in_w, 16)
                    sync.dma_start(pos[:, a, :], A[f"cmp_pos_{n}"][0].rearrange("l d -> d l")).then_inc(in_w, 16)
                    sync.dma_start(kv[:, a, :, :], Z["z"][row:row + P, :].rearrange("(g d) s -> d g s", g=G)).then_inc(in_w, 16)
                sync.dma_start(v_raw[:, 0, :], Z["z"][ROW_VS:ROW_VS + P, :]).then_inc(in_v, 16)
                sync.dma_start(v_raw[:, 1, :], Z["z"][ROW_VW:ROW_VW + P, :]).then_inc(in_v, 16)
                sync.dma_start(ks_t[:, :, :], Z["z"][ROW_KS:ROW_KS + P, :].rearrange("(g d) s -> d g s", g=G)).then_inc(in_k, 16)
                sync.dma_start(kw_t[:, :, WINDOW:WINDOW + S],
                               Z["z"][ROW_KW:ROW_KW + P, :].rearrange("(g d) s -> d g s", g=G)).then_inc(in_k, 16)
                sync.wait_ge(in_k, 32)

            @block.gpsimd
            def _(pool):
                build_identity(pool, ident, id_ok)
                pool.memset(kw_t[:, :, 0:WINDOW], 0.0).then_inc(zeros, 1)
                pool.wait_ge(zeros, 1)
                pool.memset(vw[:, 0:WINDOW // P, :], 0.0).then_inc(zeros, 1)
                pool.wait_ge(zeros, 2)

            @block.tensor
            def _(pe):
                pe.wait_ge(in_w, 16 * 8)
                for a in range(2):
                    for g in range(G):
                        for l in range(CMP_BLOCK):
                            pe.matmul(acc[0:HD, a, g * P:g * P + N_CMP], w1[:, a, l, :],
                                      kv[:, a, g, l:l + CMP_STRIDE * (N_CMP - 1) + 1:CMP_STRIDE],
                                      start=(l == 0), stop=(l == CMP_BLOCK - 1))
                    for l in range(CMP_BLOCK):
                        ins = pe.matmul(acc[0:HD, a, 2 * P:2 * P + 1], w1[:, a, l, :], pos[:, a, l:l + 1],
                                        start=(l == 0), stop=(l == CMP_BLOCK - 1))
                    ins.then_inc(hid_made, 1)
                pe.wait_ge(id_ok, 2)
                pe.wait_ge(in_v, 32)
                for n in range(8):
                    if n >= 4:
                        pe.wait_ge(tok_ok, n - 3)
                    for t in range(4):
                        ins = pe.transpose(tp[:, n % 4, t * P:(t + 1) * P],
                                           v_raw[:, n // 4, (n % 4 * 4 + t) * P:(n % 4 * 4 + t + 1) * P], ident[:, :])
                    ins.then_inc(turned, 1)
                pe.wait_ge(hid_ok, 2 * G)
                for g in range(G):
                    pe.matmul(out[0:HD, g * P:g * P + N_CMP], w2[:, 0, :], hid[:, 0, g, :], start=True, stop=True)
                    ins = pe.matmul(out[0:N_CMP, (2 + g) * P:(2 + g) * P + HD], hid[:, 1, g, :], w2[:, 1, :],
                                    start=True, stop=True)
                ins.then_inc(out_made, 1)

            @block.scalar
            def _(act):
                for a in range(2):
                    act.wait_ge(hid_made, a + 1)
                    act.copy(pos_p[:, a:a + 1], acc[0:HD, a, 2 * P:2 * P + 1]).then_inc(pos_ok, 1)
                    act.wait_ge(pos_ok, a + 1)
                    for g in range(G):
                        act.activation(hid[:, a, g, :], acc[0:HD, a, g * P:g * P + N_CMP], ACT.Gelu_apprx_tanh,
                                       bias=pos_p[:, a:a + 1]).then_inc(hid_ok, 1)

            @block.vector
            def _(dve):
                for n in range(8):
                    dve.wait_ge(turned, n + 1)
                    dst = vs[:, n * 4:n * 4 + 4, :] if n < 4 else vw[:, n * 4 - 12:n * 4 - 8, :]
                    dve.tensor_copy(dst, tp[:, n % 4, :].rearrange("p (t c) -> p t c", t=4)).then_inc(tok_ok, 1)
                dve.wait_ge(out_made, 1)
                for g in range(G):
                    dve.tensor_copy(kcmp[:, g, 0:N_CMP], out[0:HD, g * P:g * P + N_CMP]).then_inc(out_ok, 1)
                    dve.tensor_copy(vcmp[0:N_CMP, g, :], out[0:N_CMP, (2 + g) * P:(2 + g) * P + HD]).then_inc(out_ok, 1)
                dve.wait_ge(out_ok, 4)

        with ExitStack() as ctx:
            st = Stage(nc, ctx, "aq")
            KT = S - P
            WK = WINDOW + P
            U = G * 2 * R
            t_sel = st.sb("t_sel", [P, KT + 512])
            t_win, t_win0 = st.sb("t_win", [P, WK]), st.sb("t_win0", [P, WK])
            t_pad = st.sb("t_pad", [P, 2 * WINDOW])
            t_cmp, t_cmp_t = st.sb("t_cmp", [P, 248]), st.sb("t_cmp_t", [P, N_CMP])
            rows_ok = st.sb("rows_ok", [P, NT])
            keep_t, force_t = st.sb("keep_t", [P, 64]), st.sb("force_t", [P, 64])
            q_scale = st.sb("q_scale", [HD, NSA_HEADS])
            gate_b = st.sb("gate_b", [P, N_GATE])
            q_raw, q = st.sb("q_raw", [HD, NSA_HEADS, P]), st.sb("q", [HD, NSA_HEADS, P])
            g_raw, gates = st.sb("g_raw", [N_GATE, P]), st.sb("gates", [P, N_GATE])
            pc = st.sb("pc", [P, R, P])
            pct = st.sb("pct", [P, R, P])
            oc = st.sb("oc", [P, R, HD])
            cst = st.sb("cst", [P, 4, R])
            psum_c = st.sb("psum_c", [P, P + 4])
            imp, imp2, sel = (st.sb(n, [P, N_SEL]) for n in ("imp", "imp2", "sel"))
            top = st.sb("top", [P, 8])
            tg = st.sb("tg", [P, S])
            sc = st.sb("sc", [P, 2, S])
            mxc = st.sb("mxc", [P, U, 4])
            ust = st.sb("ust", [P, 3, U])
            pt = st.sb("pt", [P, 4, 4, P])
            y, yT = st.sb("y", [P, NSA_W]), st.sb("yT", [P, NSA_W // P, P])
            s_bank, t_bank = st.ps("s_bank", [P, 3, 512]), st.ps("t_bank", [P, 2, 512])
            o_bank, misc = st.ps("o_bank", [P, 2, 512]), st.ps("misc", [P, 512])
            tabs, tab_ok, small_in, q_in, q_used, q_ok = (
                st.sem(n) for n in ("tabs", "tab_ok", "small_in", "q_in", "q_used", "q_ok"))
            s_made, s_read, max_ok, exp_ok, turned, pt_a, pt_v, o_made = (
                st.sem(n) for n in ("s_made", "s_read", "max_ok", "exp_ok", "turned", "pt_a", "pt_v", "o_made"))
            misc_made, misc_read, cmax_ok, cexp_ok, pc_ok, y_ok, y_out, vec = (
                st.sem(n) for n in ("misc_made", "misc_read", "cmax_ok", "cexp_ok", "pc_ok", "y_ok", "y_out", "vec"))
            gate_ok, gated, win0_ok, tg_ok = (st.sem(n) for n in ("gate_ok", "gated", "win0_ok", "tg_ok"))
            block = st.block()

            def kind(u):
                return u // (2 * R), u % (2 * R) >= R, u % R

            def widths(u, grp):
                return [512] * (grp + 1) if kind(u)[1] else [WINDOW, P]

            def plan(grp):
                first, at = [], 0
                for u in range(U):
                    first.append(at)
                    at += len(widths(u, grp))
                return first, at

            class Runs:

                def __init__(self, grp, tau):
                    per = [plan(g)[1] for g in range(grp + 1)]
                    self.all = 4 * sum(per[:-1]) + tau * per[-1]
                    self.even = 4 * sum((n + 1) // 2 for n in per[:-1]) + tau * ((per[-1] + 1) // 2)
                    self.odd = 4 * sum(n // 2 for n in per[:-1]) + tau * (per[-1] // 2)

            MISC = 2 + 3 * G

            @block.sync
            def _(sync):
                sync.dma_start(gate_b[:, :], A["nsa_gate_b"][0].partition_broadcast(P)).then_inc(small_in, 16)
                qz = Z["z"][ROW_Q:ROW_Q + NSA_W, :].rearrange("(h d) s -> d h s", d=HD)
                with sync.Fori(0, NT) as t:
                    sync.wait_ge(q_used, t + 1)
                    sync.dma_start(q_raw[:, :, :], qz[:, :, bass.ds(t * P, P)]).then_inc(q_in, 16)
                    sync.dma_start(g_raw[:, :], Z["gate"][:, bass.ds(t * P, P)]).then_inc(q_in, 16)

            @block.gpsimd
            def _(pool):
                n = [0]

                def step(ins):
                    ins.then_inc(tabs, 1)
                    n[0] += 1
                    pool.wait_ge(tabs, n[0])

                def masked(t, pattern, base, cm, fill, op=ALU.is_ge, part=slice(0, P)):
                    step(pool.affine_select(out=t[part, :], in_=t[part, :], compare_op=op, fill=fill, base=base,
                                            pattern=pattern, channel_multiplier=cm))

                w = KT + 512
                step(pool.iota(t_sel[:, :], [[1, w]], base=-KT, channel_multiplier=-1, allow_small_or_imprecise_dtypes=True))
                masked(t_sel, [[-1, w]], KT, 1, NEG)
                step(pool.iota(t_win[:, :], [[1, WK]], base=-WINDOW, channel_multiplier=-1, allow_small_or_imprecise_dtypes=True))
                masked(t_win, [[-1, WK]], WINDOW, 1, NEG)
                masked(t_win, [[1, WK]], -1, -1, NEG)
                step(pool.memset(t_pad[:, 0:WINDOW], NEG))
                step(pool.memset(t_pad[:, WINDOW:2 * WINDOW], 0.0))
                step(pool.iota(t_cmp[:, :], [[CMP_STRIDE, 248]], base=-KT, channel_multiplier=-1, allow_small_or_imprecise_dtypes=True))
                step(pool.tensor_scalar(t_cmp[:, :], t_cmp[:, :], 0.5 * (CMP_BLOCK - 1), 1.0, ALU.add, ALU.mult))
                masked(t_cmp, [[-CMP_STRIDE, 248]], KT - (CMP_BLOCK - 1), 1, NEG)
                step(pool.memset(rows_ok[:, :], 1.0))
                masked(rows_ok, [[P, NT]], -(CMP_BLOCK - 1), 1, 0.0)
                step(pool.memset(keep_t[:, :], 1.0))
                step(pool.memset(force_t[:, :], -FORCE))
                for h in range(2):
                    part = slice(h * 64, h * 64 + 64)
                    masked(keep_t, [[-1, 64]], 28 + h, 0, 0.0, part=part)
                    masked(force_t, [[1, 64]], -31 - h, 0, FORCE, part=part)
                    masked(force_t, [[1, 64]], -29 - h, 0, 0.0, part=part)
                for h in range(NSA_HEADS):
                    step(pool.memset(q_scale[:, h:h + 1], HD ** -0.5 / SLOPES[h]))
                step(pool.memset(psum_c[:, :], 0.0))
                pool.sem_inc(tab_ok, 1)

            @block.tensor
            def _(pe):
                pe.wait_ge(tab_ok, 1)
                for grp in range(NT // 4):
                    first, per_tile = plan(grp)
                    with pe.Fori(0, 4) as tau:
                        t, runs = tau + 4 * grp, Runs(grp, tau)

                        def evacuated(j, more):
                            if j % 2 == 0:
                                pe.wait_ge(pt_a, runs.even + j // 2 + more)
                            else:
                                pe.wait_ge(pt_v, runs.odd + j // 2 + more)

                        def use_misc(n):
                            pe.wait_ge(misc_read, t * MISC + n)

                        def scores(u):
                            g, selected, h = kind(u)
                            for r, wd in enumerate(widths(u, grp)):
                                j = first[u] + r
                                pe.wait_ge(s_read, runs.all + max(j - 2, 0))
                                keys = ks_t[:, g, r * 512:r * 512 + wd] if selected else \
                                    kw_t[:, g, bass.ds(t * P + r * 512, wd)]
                                if not selected:
                                    steady(pe, Z)
                                pe.matmul(s_bank[:, j % 3, 0:wd], q[:, g * R + h, :], keys,
                                          start=True, stop=True).then_inc(s_made, 1)

                        def values(u):
                            g, selected, h = kind(u)
                            ws = widths(u, grp)
                            pe.wait_ge(exp_ok, t * U + u + 1)
                            n_blocks, done = sum(ws) // P, 0

                            def pv(r):
                                nonlocal done
                                j = first[u] + r
                                evacuated(j, 1)
                                for b in range(ws[r] // P):
                                    if selected:
                                        val = vs[:, r * 4 + b, g * HD:(g + 1) * HD]
                                    else:
                                        val = vw[:, bass.ds(t + r * 4 + b, 1), g * HD:(g + 1) * HD].rearrange("p o d -> p (o d)")
                                    ins = pe.matmul(o_bank[:, g, (u % 8) * HD:(u % 8 + 1) * HD], pt[:, j % 4, b, :], val,
                                                    start=(done == 0), stop=(done == n_blocks - 1))
                                    done += 1
                                if done == n_blocks:
                                    ins.then_inc(o_made, 1)

                            for r in range(len(ws)):
                                j = first[u] + r
                                evacuated(j, 0)
                                for b in range(ws[r] // P):
                                    ins = pe.transpose(t_bank[:, j % 2, b * P:(b + 1) * P],
                                                       sc[:, u % 2, r * 512 + b * P:r * 512 + (b + 1) * P], ident[:, :])
                                ins.then_inc(turned, 1)
                                if r >= 1:
                                    pv(r - 1)
                            pv(len(ws) - 1)

                        pe.wait_ge(q_in, t * 32 + 32)
                        use_misc(0)
                        steady(pe, Z)
                        pe.transpose(misc[:, 0:N_GATE], g_raw[:, :], ident[0:N_GATE, 0:N_GATE]).then_inc(misc_made, 1)
                        pe.wait_ge(q_ok, t + 1)
                        for u in range(U + 1):
                            g, j = u // 8, u % 8
                            if j == 0 and u < U:
                                use_misc(1 + 3 * g)
                                for h in range(R):
                                    ins = pe.matmul(misc[:, h * P:h * P + N_CMP], q[:, g * R + h, :], kcmp[:, g, 0:N_CMP],
                                                    start=True, stop=True)
                                ins.then_inc(misc_made, 1)
                            if u < U:
                                scores(u)
                            if u >= 1:
                                values(u - 1)
                            if j == 1:
                                use_misc(2 + 3 * g)
                                pe.wait_ge(pc_ok, t * G + g + 1)
                                for h in range(R):
                                    ins = pe.transpose(misc[0:N_CMP, h * P:(h + 1) * P], pc[:, h, 0:N_CMP], ident[:, :])
                                ins.then_inc(misc_made, 1)
                            if j == 3:
                                use_misc(3 + 3 * g)
                                for h in range(R):
                                    ins = pe.matmul(misc[:, h * HD:(h + 1) * HD], pct[0:N_CMP, h, :], vcmp[0:N_CMP, g, :],
                                                    start=True, stop=True)
                                ins.then_inc(misc_made, 1)
                        use_misc(MISC - 1)
                        pe.wait_ge(y_ok, t * G + G)
                        for c in range(NSA_W // P):
                            ins = pe.transpose(misc[:, c * P:(c + 1) * P], y[:, c * P:(c + 1) * P], ident[:, :])
                        ins.then_inc(misc_made, 1)


            def unit_of(j, grp):
                first = plan(grp)[0]
                return max(u for u in range(U) if first[u] <= j)

            def pt_free(eng, j, grp, t):
                eng.wait_ge(o_made, t * U + (unit_of(j - 4, grp) + 1 if j >= 4 else 0))

            @block.scalar
            def _(act):
                act.wait_ge(tab_ok, 1)
                act.wait_ge(small_in, 16)
                for grp in range(NT // 4):
                    first, per_tile = plan(grp)
                    with act.Fori(0, 4) as tau:
                        t, runs = tau + 4 * grp, Runs(grp, tau)
                        act.wait_ge(gate_ok, t + 1)
                        act.activation(gates[:, :], gates[:, :], ACT.Tanh, scale=0.5).then_inc(gated, 1)
                        for u in range(U + 1):
                            g, j = u // 8, u % 8
                            if j == 0 and u < U:
                                act.wait_ge(cmax_ok, t * G + g + 1)
                                for h in range(R):
                                    ins = act.activation(pc[:, h, 0:N_CMP], pc[:, h, 0:N_CMP], ACT.Exp,
                                                         bias=cst[:, 1, h:h + 1], accum_out=cst[:, 2, h:h + 1])
                                ins.then_inc(cexp_ok, 1)
                            if u < U:
                                n = sum(widths(u, grp))
                                act.wait_ge(max_ok, t * U + u + 1)
                                act.activation(sc[:, u % 2, 0:n], sc[:, u % 2, 0:n], ACT.Exp, bias=ust[:, 0, u:u + 1],
                                               accum_out=ust[:, 1, u:u + 1]).then_inc(exp_ok, 1)
                            if u >= 1:
                                for r, wd in enumerate(widths(u - 1, grp)):
                                    run = first[u - 1] + r
                                    if run % 2 == 0:
                                        act.wait_ge(turned, runs.all + run + 1)
                                        pt_free(act, run, grp, t)
                                        act.copy(pt[:, run % 4, 0:wd // P, :].rearrange("p b t -> p (b t)"),
                                                 t_bank[:, 0, 0:wd]).then_inc(pt_a, 1)
                            if j == 1:
                                act.wait_ge(misc_made, t * MISC + 3 + 3 * g)
                                act.copy(pct[0:N_CMP, :, :].rearrange("p h t -> p (h t)"), misc[0:N_CMP, :]).then_inc(misc_read, 1)
                        act.wait_ge(misc_made, t * MISC + MISC)
                        act.wait_ge(y_out, t * 16)
                        act.copy(yT[:, :, :].rearrange("p c t -> p (c t)"), misc[:, :]).then_inc(misc_read, 1)
                        act.wait_ge(misc_read, t * MISC + MISC)
                        act.dma_start(Z["yn"].rearrange("(c p) s -> p c s", p=P)[:, :, bass.ds(t * P, P)],
                                      yT[:, :, :]).then_inc(y_out, 16)
                act.wait_ge(y_out, NT * 16)

            @block.vector
            def _(dve):
                v = Chain(dve, vec)
                dve.wait_ge(tab_ok, 1)
                dve.wait_ge(small_in, 16)
                dve.sem_inc(q_used, 1)
                for grp in range(NT // 4):
                    first, per_tile = plan(grp)
                    keys = 512 * (grp + 1)
                    with dve.Fori(0, 4) as tau:
                        v.loop(tau, STEPS + (1 if grp == 0 else 0))
                        t, runs = tau + 4 * grp, Runs(grp, tau)
                        dve.wait_ge(q_in, t * 32 + 32)
                        dve.wait_ge(s_made, runs.all)
                        dve.tensor_tensor(q[:, :, :], q_raw[:, :, :],
                                          q_scale[:, :].rearrange("p (h o) -> p h o", o=1).to_broadcast([HD, NSA_HEADS, P]),
                                          ALU.mult).then_inc(q_ok, 1)
                        dve.wait_ge(misc_made, t * MISC + 1)
                        dve.tensor_tensor(gates[:, :], misc[:, 0:N_GATE], gate_b[:, :], ALU.add).then_inc(gate_ok, 1)
                        dve.wait_ge(gate_ok, t + 1)
                        dve.sem_inc(misc_read, 1)
                        dve.wait_ge(q_ok, t + 1)
                        dve.sem_inc(q_used, 1)
                        dve.wait_ge(gated, t + 1)
                        v.link(dve.tensor_scalar(gates[:, :], gates[:, :], 0.5, 0.5, ALU.mult, ALU.add))
                        steady(dve, Z)
                        v.link(dve.tensor_copy(t_cmp_t[:, :], t_cmp[:, bass.ds(120 - t * (P // CMP_STRIDE), N_CMP)]))
                        win = t_win
                        if grp == 0:
                            win = t_win0
                            v.link(dve.tensor_tensor(t_win0[:, :], t_win[:, :], t_pad[:, bass.ds(t * P, WK)], ALU.add))

                        def compressed_scores(g):
                            dve.wait_ge(misc_made, t * MISC + 2 + 3 * g)
                            steady(dve, Z)
                            for h in range(R):
                                ins = dve.tensor_tensor_reduce(
                                    out=pc[:, h, 0:N_CMP], in0=misc[:, h * P:h * P + N_CMP],
                                    in1=t_cmp_t[:, :],
                                    scale=SLOPES[g * R + h], scalar=LOWEST, op0=ALU.add, op1=ALU.max,
                                    accum_out=cst[:, 0, h:h + 1])
                            ins.then_inc(misc_read, 1)
                            dve.wait_ge(misc_read, t * MISC + 2 + 3 * g)
                            dve.tensor_scalar(cst[:, 1, :], cst[:, 0, :], -1.0, None, ALU.mult).then_inc(cmax_ok, 1)

                        def compressed_probs(g):
                            dve.wait_ge(cexp_ok, t * G + g + 1)
                            v.link(dve.reciprocal(cst[:, 3, :], cst[:, 2, :]))
                            v.link(dve.tensor_scalar(cst[:, 3, :], cst[:, 3, :], rows_ok[:, bass.ds(t, 1)], None, ALU.mult))
                            for h in range(R):
                                ins = dve.tensor_scalar(pc[:, h, 0:N_CMP], pc[:, h, 0:N_CMP], cst[:, 3, h:h + 1], None, ALU.mult)
                            ins.then_inc(pc_ok, 1)
                            dve.wait_ge(pc_ok, t * G + g + 1)

                        def select(g):
                            total = psum_c[:, 1:1 + N_CMP]
                            v.link(dve.tensor_tensor(total, pc[:, 0, 0:N_CMP], pc[:, 1, 0:N_CMP], ALU.add))
                            v.link(dve.tensor_tensor(total, total, pc[:, 2, 0:N_CMP], ALU.add))
                            v.link(dve.tensor_tensor(total, total, pc[:, 3, 0:N_CMP], ALU.add))
                            part = lambda n: psum_c[:, n:n + P - 3:4]
                            v.mark(dve.tensor_tensor(imp2[:, :], part(0), part(4), ALU.add))
                            v.link(dve.tensor_tensor(imp[:, :], part(1), part(2), ALU.add))
                            v.link(dve.tensor_tensor(imp[:, :], imp[:, :], part(3), ALU.add))
                            v.link(dve.scalar_tensor_tensor(out=imp[:, :], in0=imp2[:, :], scalar=0.5, in1=imp[:, :],
                                                            op0=ALU.mult, op1=ALU.add))
                            steady(dve, Z)
                            at = bass.ds(30 - 2 * t, N_SEL)
                            v.link(dve.tensor_tensor(imp[:, :], imp[:, :], keep_t[:, at], ALU.mult))
                            v.link(dve.tensor_tensor(imp[:, :], imp[:, :], force_t[:, at], ALU.add))
                            v.link(dve.memset(imp[:, 0:1], FORCE))
                            steady(dve, Z)
                            v.link(dve.max(top[:, :], imp[:, :]))
                            steady(dve, Z)
                            v.link(dve.match_replace(imp2[:, :], top[:, :], imp[:, :], -LOWEST))
                            v.link(dve.tensor_scalar(sel[:, :], imp2[:, :], -LOWEST, NEG, ALU.not_equal, ALU.mult))
                            n = keys // SEL_BLOCK
                            steady(dve, Z)
                            v.link(dve.tensor_tensor(
                                tg[:, 0:keys].rearrange("p (n b) -> p n b", n=n),
                                t_sel[:, bass.ds(KT - t * P, keys)].rearrange("p (n b) -> p n b", n=n),
                                sel[:, 0:n].rearrange("p (n o) -> p n o", o=1).to_broadcast([P, n, SEL_BLOCK]), ALU.add))

                        def combine(g):
                            dve.wait_ge(o_made, t * U + 8 * g + 8)
                            v.link(dve.reciprocal(ust[:, 2, 8 * g:8 * g + 8], ust[:, 1, 8 * g:8 * g + 8]))
                            gate = lambda b: gates[:, 3 * R * g:3 * R * (g + 1)].rearrange("p (h b) -> p b h", b=3)[:, b, :]
                            v.mark(dve.tensor_tensor(ust[:, 2, 8 * g:8 * g + 4], ust[:, 2, 8 * g:8 * g + 4], gate(2), ALU.mult))
                            v.link(dve.tensor_tensor(ust[:, 2, 8 * g + 4:8 * g + 8], ust[:, 2, 8 * g + 4:8 * g + 8], gate(1), ALU.mult))
                            yh = lambda h: y[:, (g * R + h) * HD:(g * R + h + 1) * HD]
                            for h in range(R):
                                n = 3 * (g * R + h)
                                v.mark(dve.tensor_scalar(yh(h), oc[:, h, :], gates[:, n:n + 1], None, ALU.mult))
                            v.wait()
                            for u in range(8):
                                if u == 4:
                                    v.wait()
                                ins = dve.scalar_tensor_tensor(
                                    out=yh(u % 4), in0=o_bank[:, g, u * HD:(u + 1) * HD], scalar=ust[:, 2, 8 * g + u:8 * g + u + 1],
                                    in1=yh(u % 4), op0=ALU.mult, op1=ALU.add)
                                if u < 7:
                                    v.mark(ins)
                            ins.then_inc(y_ok, 1)

                        for u in range(U + 1):
                            g, j = u // 8, u % 8
                            if j == 0 and u < U:
                                compressed_scores(g)
                            if u < U:
                                _, selected, h = kind(u)
                                dve.wait_ge(turned, runs.all + (first[u - 1] if u >= 2 else 0))
                                for r, wd in enumerate(widths(u, grp)):
                                    run = first[u] + r
                                    dve.wait_ge(s_made, runs.all + run + 1)
                                    steady(dve, Z)
                                    dve.tensor_tensor_reduce(
                                        out=sc[:, u % 2, r * 512:r * 512 + wd], in0=s_bank[:, run % 3, 0:wd],
                                        in1=(tg if selected else win)[:, r * 512:r * 512 + wd], scale=SLOPES[g * R + h],
                                        scalar=LOWEST, op0=ALU.add, op1=ALU.max, accum_out=mxc[:, u, r:r + 1]).then_inc(s_read, 1)
                                n = len(widths(u, grp))
                                dve.wait_ge(s_read, runs.all + first[u] + n)
                                dve.tensor_reduce(ust[:, 0, u:u + 1], mxc[:, u, 0:n], AX.X, ALU.max, negate=True).then_inc(max_ok, 1)
                            if u >= 1:
                                for r, wd in enumerate(widths(u - 1, grp)):
                                    run = first[u - 1] + r
                                    if run % 2 == 1:
                                        dve.wait_ge(turned, runs.all + run + 1)
                                        pt_free(dve, run, grp, t)
                                        dve.tensor_copy(pt[:, run % 4, 0:wd // P, :].rearrange("p b t -> p (b t)"),
                                                        t_bank[:, 1, 0:wd]).then_inc(pt_v, 1)
                            if j == 0 and u < U:
                                compressed_probs(g)
                            if j == 1:
                                select(g)
                            if j == 3:
                                dve.wait_ge(misc_made, t * MISC + 4 + 3 * g)
                                dve.tensor_copy(oc[:, :, :].rearrange("p h d -> p (h d)"), misc[:, 0:R * HD]).then_inc(misc_read, 1)
                                dve.wait_ge(misc_read, t * MISC + 4 + 3 * g)
                            if u == 9:
                                combine(0)
                        combine(1)
                        v.end(4)


def stage_mix(nc, A, Z):
    with ExitStack() as ctx:
        st = Stage(nc, ctx, "mx")
        YC = RW_W // P
        up = st.sb("up", [P, 2, YC, D])
        wo = st.sb("wo", [P, DC, D])
        ys = st.sb("ys", [P, 2, YC, 512])
        mg = st.sb("mg", [P, 2, DC, 512])
        res = st.sb("res", [P, 2, D])
        part = st.sb("part", [P, 2, 2, 512])
        mixed = st.sb("mixed", [P, DC, 512])
        ups = st.ps("ups", [P, 2, 2, 512])
        outs = st.ps("outs", [P, 2, 2, 512])
        w_in, y_in, g_in, res_in = st.sem("w_in"), st.sem("y_in"), st.sem("g_in"), st.sems("res_in", 2)
        ups_made, ups_read, sig_ok, mixed_ok, out_made, out_ok, vec = (
            st.sem(n) for n in ("ups_made", "ups_read", "sig_ok", "mixed_ok", "out_made", "out_ok", "vec"))
        stored = st.sems("stored", 2)
        block = st.block()
        TB = 512 // P

        @block.sync
        def _(sync):
            for n, name in enumerate(("w_up_rwkv", "w_up_nsa")):
                sync.dma_start(up[:, n, :, :], A[name][0].rearrange("(c p) n -> p c n", p=P)).then_inc(w_in, 16)
            sync.dma_start(wo[:, :, :], A["w_out"][0].rearrange("(c p) n -> p c n", p=P)).then_inc(w_in, 16)
            with sync.Fori(0, NB) as i:
                sync.wait_ge(ups_made, i * DC)
                for n, name in enumerate(("yr", "yn")):
                    sync.dma_start(ys[:, n, :, :], Z[name].rearrange("(c p) s -> p c s", p=P)[:, :, bass.ds(i * 512, 512)]).then_inc(y_in, 16)
                sync.wait_ge(ups_read, i * DC)
                for n in range(2):
                    sync.dma_start(mg[:, n, :, :], Z["z"][ROW_MERGE + n * D:ROW_MERGE + (n + 1) * D, :]
                                   .rearrange("(c p) s -> p c s", p=P)[:, :, bass.ds(i * 512, 512)]).then_inc(g_in, 16)
                for t in range(TB):
                    tile = i * TB + t
                    sync.wait_ge(stored[t % 2], (i * (TB // 2) + t // 2) * 16)
                    sync.dma_start(res[:, t % 2, :], A["x"][0][bass.ds(tile * P, P), :]).then_inc(res_in[t % 2], 16)

        @block.tensor
        def _(pe):
            pe.wait_ge(w_in, 48)
            with pe.Fori(0, NB) as i:
                pe.wait_ge(y_in, (i + 1) * 32)
                for d in range(DC):
                    pe.wait_ge(ups_read, i * DC + max(d - 1, 0))
                    for n in range(2):
                        for c in range(YC):
                            ins = pe.matmul(ups[:, d % 2, n, :], up[:, n, c, d * P:(d + 1) * P], ys[:, n, c, :],
                                            start=(c == 0), stop=(c == YC - 1))
                    ins.then_inc(ups_made, 1)
                pe.wait_ge(mixed_ok, (i + 1) * DC)
                for t in range(TB):
                    pe.wait_ge(out_ok, i * TB + max(t - 1, 0))
                    for n in range(2):
                        for c in range(DC):
                            ins = pe.matmul(outs[:, t % 2, n, :], mixed[:, c, t * P:(t + 1) * P], wo[:, c, n * 512:(n + 1) * 512],
                                            start=(c == 0), stop=(c == DC - 1))
                    ins.then_inc(out_made, 1)

        @block.scalar
        def _(act):
            with act.Fori(0, NB) as i:
                act.wait_ge(g_in, (i + 1) * 32)
                for d in range(DC):
                    act.activation(mg[:, :, d, :], mg[:, :, d, :], ACT.Sigmoid).then_inc(sig_ok, 1)

        @block.vector
        def _(dve):
            v = Chain(dve, vec)
            with dve.Fori(0, NB) as i:
                v.loop(i, DC)
                for d in range(DC):
                    dve.wait_ge(ups_made, i * DC + d + 1)
                    dve.wait_ge(sig_ok, i * DC + d + 1)
                    dve.wait_ge(mixed_ok, i * DC + max(d - 1, 0))
                    v.link(dve.tensor_tensor(part[:, d % 2, :, :], ups[:, d % 2, :, :], mg[:, :, d, :], ALU.mult))
                    dve.sem_inc(ups_read, 1)
                    if d == 0:
                        dve.wait_ge(out_made, i * TB)
                    dve.tensor_tensor(mixed[:, d, :], part[:, d % 2, 0, :], part[:, d % 2, 1, :], ALU.add).then_inc(mixed_ok, 1)
                for t in range(TB):
                    dve.wait_ge(out_made, i * TB + t + 1)
                    dve.wait_ge(res_in[t % 2], (i * (TB // 2) + t // 2 + 1) * 16)
                    dve.tensor_tensor(res[:, t % 2, :].rearrange("p (n c) -> p n c", n=2), outs[:, t % 2, :, :],
                                      res[:, t % 2, :].rearrange("p (n c) -> p n c", n=2), ALU.add).then_inc(out_ok, 1)
                v.end(NB)

        @block.gpsimd
        def _(pool):
            with pool.Fori(0, NT // 2) as i:
                for k in range(2):
                    pool.wait_ge(out_ok, 2 * i + k + 1)
                    pool.dma_start(Z["x1"][bass.ds((2 * i + k) * P, P), :], res[:, k, :]).then_inc(stored[k], 16)
            for k in range(2):
                pool.wait_ge(stored[k], NT // 2 * 16)


N_GROUPS, PER_GROUP = 4, 8
N_EXPERTS = N_GROUPS * PER_GROUP
D_EXPERT = 512
MAX_BLOCKS = 2 * S // P + N_EXPERTS
N_LOGITS = N_GROUPS + N_EXPERTS


def stage_route(nc, A, Z, keep):
    lg, weight, dest, ends = keep["lg"], keep["weight"], keep["dest"], keep["ends"]
    with ExitStack() as ctx:
        st = Stage(nc, ctx, "ro")
        x_t, xn = st.sb("x", [P, 2, D]), st.sb("xn", [P, 2, D])
        sq = st.sb("sq", [P, D])
        stat = st.sb("stat", [P, 2, 4])
        hT = st.sb("hT", [P, 2, DC, P])
        g_row = st.sb("g", [P, D])
        w_r = st.sb("w_r", [P, DC, N_LOGITS])
        b_r = st.sb("b_r", [P, N_LOGITS])
        ident = st.sb("ident", [P, P])
        zero_i, tok_id = st.sb("zero_i", [P, MAX_BLOCKS + 1], I32), keep["tok_id"]
        tp, lps = st.ps("tp", [P, 2, 2, 512]), st.ps("lps", [P, 2, 512])
        x_in, h_out = st.sems("x_in", 2), st.sems("h_out", 2)
        x_free, w_in, id_ok, squares, roots, ms_ok, vec = (
            st.sem(n) for n in ("x_free", "w_in", "id_ok", "squares", "roots", "ms_ok", "vec"))
        h_ok, turned, ht_ok, l_made, l_ok, cleared, rows_clear = (
            st.sem(n) for n in ("h_ok", "turned", "ht_ok", "l_made", "l_ok", "cleared", "rows_clear"))
        block = st.block()

        @block.sync
        def _(sync):
            sync.dma_start(g_row[:, :], A["g_ffn"][0].partition_broadcast(P)).then_inc(w_in, 16)
            sync.dma_start(w_r[:, :, 0:N_GROUPS], A["w_group"][0].rearrange("(c p) n -> p c n", p=P)).then_inc(w_in, 16)
            sync.dma_start(w_r[:, :, N_GROUPS:N_LOGITS], A["w_router"][0].rearrange("(c p) n -> p c n", p=P)).then_inc(w_in, 16)
            sync.dma_start(b_r[:, 0:N_GROUPS], A["b_group"][0].partition_broadcast(P)).then_inc(w_in, 16)
            sync.dma_start(b_r[:, N_GROUPS:N_LOGITS], A["b_router"][0].partition_broadcast(P)).then_inc(w_in, 16)
            with sync.Fori(0, NT // 2) as i:
                for k in range(2):
                    sync.wait_ge(x_free, 2 * i + k + 1)
                    sync.dma_start(x_t[:, k, :], Z["x1"][bass.ds((2 * i + k) * P, P), :]).then_inc(x_in[k], 16)

        @block.gpsimd
        def _(pool):
            build_identity(pool, ident, id_ok)
            pool.memset(zero_i[:, :], 0).then_inc(cleared, 1)
            pool.iota(tok_id[:, :], [[P, NT]], base=0, channel_multiplier=1).then_inc(cleared, 1)
            pool.wait_ge(cleared, 2)
            pool.dma_start(Z["row_tok"].rearrange("(p b) o -> p (b o)", p=P), zero_i[:, :]).then_inc(rows_clear, 16)
            pool.wait_ge(rows_clear, 16)
            with pool.Fori(0, NT // 2) as i:
                for k in range(2):
                    pool.wait_ge(h_ok, 2 * i + k + 1)
                    pool.dma_start(Z["h2"][bass.ds((2 * i + k) * P, P), :], xn[:, k, :]).then_inc(h_out[k], 16)
            for k in range(2):
                pool.wait_ge(h_out[k], NT // 2 * 16)

        @block.scalar
        def _(act):
            with act.Fori(0, NT // 2) as i:
                for k in range(2):
                    act.wait_ge(x_in[k], (i + 1) * 16)
                    act.wait_ge(squares, 2 * i + k)
                    act.activation(sq[:, :], x_t[:, k, :], ACT.Square, accum_out=stat[:, k, 0:1]).then_inc(squares, 1)
                for k in range(2):
                    act.wait_ge(ms_ok, 2 * i + k + 1)
                    act.activation(stat[:, k, 2:3], stat[:, k, 1:2], ACT.Sqrt).then_inc(roots, 1)
                for k in range(2):
                    act.wait_ge(turned, 2 * i + k + 1)
                    act.wait_ge(l_made, 2 * i + k)
                    act.copy(hT[:, k, :, :].rearrange("p (b c) t -> p b (c t)", b=2), tp[:, k, :, :]).then_inc(ht_ok, 1)

        @block.vector
        def _(dve):
            v = Chain(dve, vec)
            dve.sem_inc(x_free, 2)
            dve.wait_ge(w_in, 80)
            with dve.Fori(0, NT // 2) as i:
                v.loop(i, 4)
                for k in range(2):
                    dve.wait_ge(squares, 2 * i + k + 1)
                    dve.tensor_scalar(stat[:, k, 1:2], stat[:, k, 0:1], 1.0 / D, NORM_EPS, ALU.mult, ALU.add).then_inc(ms_ok, 1)
                for k in range(2):
                    dve.wait_ge(roots, 2 * i + k + 1)
                    v.link(dve.reciprocal(stat[:, k, 3:4], stat[:, k, 2:3]))
                    dve.wait_ge(turned, 2 * i + k)
                    dve.wait_ge(h_out[k], i * 16)
                    v.link(dve.scalar_tensor_tensor(out=xn[:, k, :], in0=x_t[:, k, :], scalar=stat[:, k, 3:4], in1=g_row[:, :],
                                                    op0=ALU.mult, op1=ALU.mult))
                    dve.sem_inc(h_ok, 1)
                    dve.sem_inc(x_free, 1)
                for k in range(2):
                    dve.wait_ge(l_made, 2 * i + k + 1)
                    dve.tensor_tensor(lg[:, bass.ds(2 * i + k, 1), :].rearrange("p o n -> p (o n)"), lps[:, k, 0:N_LOGITS],
                                      b_r[:, :], ALU.add).then_inc(l_ok, 1)
                v.end(NT // 2)
            dve.wait_ge(l_ok, NT)

        @block.tensor
        def _(pe):
            pe.wait_ge(id_ok, 2)
            pe.wait_ge(w_in, 80)
            with pe.Fori(0, NT // 2) as i:
                for k in range(2):
                    pe.wait_ge(h_ok, 2 * i + k + 1)
                    pe.wait_ge(ht_ok, 2 * i)
                    for c in range(DC):
                        ins = pe.transpose(tp[:, k, c // 4, (c % 4) * P:(c % 4 + 1) * P], xn[:, k, c * P:(c + 1) * P], ident[:, :])
                    ins.then_inc(turned, 1)
                for k in range(2):
                    pe.wait_ge(ht_ok, 2 * i + k + 1)
                    pe.wait_ge(l_ok, 2 * i)
                    for c in range(DC):
                        ins = pe.matmul(lps[:, k, 0:N_LOGITS], hT[:, k, c, :], w_r[:, c, :], start=(c == 0), stop=(c == DC - 1))
                    ins.then_inc(l_made, 1)

    with ExitStack() as ctx:
        st = Stage(nc, ctx, "rt")
        E3 = [P, NT, N_EXPERTS]
        small = lambda n: st.sb(n, [P, NT, 1])
        gmax, gsum, g_at, m1, m2, at, ratio, total = (small(n) for n in ("gmax", "gsum", "g_at", "m1", "m2", "at", "ratio", "total"))
        gd, g_one, le, cand, tmp = (st.sb(n, [P, NT, PER_GROUP]) for n in ("gd", "g_one", "le", "cand", "tmp"))
        one = [st.sb(f"one{n}", [P, NT, PER_GROUP]) for n in range(2)]
        hot = [st.sb(f"hot{n}", E3) for n in range(2)]
        both, tot, base, prod = (st.sb(n, E3) for n in ("both", "tot", "base", "prod"))
        count, ends_f, nb_f = (st.sb(n, [P, N_EXPERTS]) for n in ("count", "ends_f", "nb_f"))
        nb_i = st.sb("nb_i", [P, N_EXPERTS], I32)
        ones_e = st.sb("ones_e", [P, N_EXPERTS])
        iota8, col, row = st.sb("iota8", [P, PER_GROUP]), st.sb("col", [P, P]), st.sb("row", [P, P])
        before, ones_m = st.sb("before", [P, P]), st.sb("ones_m", [P, P])
        pos, sums = st.ps("pos", [P, 512]), st.ps("sums", [P, 512])
        vec, init, soft, hots_ok, made = (st.sem(n) for n in ("vec", "init", "soft", "hots_ok", "made"))
        dest_ok, listed = st.sem("dest_ok"), st.sem("listed")
        block = st.block()

        @block.gpsimd
        def _(pool):
            pool.iota(iota8[:, :], [[1, PER_GROUP]], base=0, channel_multiplier=0, allow_small_or_imprecise_dtypes=True).then_inc(init, 1)
            pool.iota(col[:, :], [[1, P]], base=0, channel_multiplier=0, allow_small_or_imprecise_dtypes=True).then_inc(init, 1)
            pool.iota(row[:, :], [[0, P]], base=0, channel_multiplier=1, allow_small_or_imprecise_dtypes=True).then_inc(init, 1)
            pool.memset(ones_e[:, :], 1.0).then_inc(init, 1)
            pool.memset(ones_m[:, :], 1.0).then_inc(init, 1)
            pool.wait_ge(dest_ok, 1)
            for t in range(NT):
                for n in range(2):
                    pool.indirect_dma_start(out=Z["row_tok"], out_offset=bass.IndirectOffsetOnAxis(ap=dest[:, n, t:t + 1], axis=0),
                                            in_=keep["tok_id"][:, t:t + 1], in_offset=None).then_inc(listed, 16)
            pool.wait_ge(listed, 2 * NT * 16)

        @block.tensor
        def _(pe):
            pe.wait_ge(hots_ok, 1)
            flat = both[:, :, :].rearrange("p t e -> p (t e)")
            pe.matmul(pos[:, :], before[:, :], flat, start=True, stop=True)
            pe.matmul(sums[:, :], ones_m[:, :], flat, start=True, stop=True).then_inc(made, 1)

        @block.scalar
        def _(act):
            act.wait_ge(soft, 1)
            act.activation(gd[:, :, 0:N_GROUPS], gd[:, :, 0:N_GROUPS], ACT.Exp).then_inc(soft, 1)
            act.wait_ge(soft, 3)
            act.activation(ratio[:, :, :], ratio[:, :, :], ACT.Exp).then_inc(soft, 1)

        @block.vector
        def _(dve):
            v = Chain(dve, vec)
            dve.wait_ge(init, 5)
            v.link(dve.tensor_tensor(before[:, :], col[:, :], row[:, :], ALU.is_gt))
            wide = lambda t, n: t.to_broadcast([P, NT, n])
            index = lambda n: iota8[:, 0:n].rearrange("p (o n) -> p o n", o=1).to_broadcast([P, NT, n])

            def first_max(values, n, top, out):
                v.link(dve.tensor_reduce(top, values, AX.X, ALU.max))
                v.link(dve.tensor_tensor(cand[:, :, 0:n], values, wide(top, n), ALU.is_ge))
                v.link(dve.tensor_scalar(cand[:, :, 0:n], cand[:, :, 0:n], -64.0, 64.0, ALU.mult, ALU.add))
                v.link(dve.tensor_tensor(cand[:, :, 0:n], cand[:, :, 0:n], index(n), ALU.add))
                v.link(dve.tensor_reduce(at[:, :, :], cand[:, :, 0:n], AX.X, ALU.min))
                v.link(dve.tensor_tensor(out, index(n), wide(at[:, :, :], n), ALU.is_equal))

            groups = lg[:, :, 0:N_GROUPS]
            first_max(groups, N_GROUPS, gmax[:, :, :], g_one[:, :, 0:N_GROUPS])
            v.link(dve.tensor_tensor(gd[:, :, 0:N_GROUPS], groups, wide(gmax[:, :, :], N_GROUPS), ALU.subtract))
            dve.sem_inc(soft, 1)
            for n in range(N_GROUPS):
                e = lg[:, :, N_GROUPS + n * PER_GROUP:N_GROUPS + (n + 1) * PER_GROUP]
                out = le if n == 0 else tmp
                v.link(dve.tensor_tensor(out[:, :, :], e, wide(g_one[:, :, n:n + 1], PER_GROUP), ALU.mult))
                if n:
                    v.link(dve.tensor_tensor(le[:, :, :], le[:, :, :], tmp[:, :, :], ALU.add))
            first_max(le[:, :, :], PER_GROUP, m1[:, :, :], one[0][:, :, :])
            v.link(dve.scalar_tensor_tensor(out=le[:, :, :], in0=one[0][:, :, :], scalar=NEG, in1=le[:, :, :],
                                            op0=ALU.mult, op1=ALU.add))
            first_max(le[:, :, :], PER_GROUP, m2[:, :, :], one[1][:, :, :])
            dve.wait_ge(soft, 2)
            v.link(dve.tensor_tensor(ratio[:, :, :], m2[:, :, :], m1[:, :, :], ALU.subtract))
            dve.sem_inc(soft, 1)
            v.link(dve.tensor_reduce(gsum[:, :, :], gd[:, :, 0:N_GROUPS], AX.X, ALU.add))
            dve.wait_ge(soft, 4)
            v.link(dve.tensor_scalar(total[:, :, :], ratio[:, :, :], 1.0, None, ALU.add))
            v.link(dve.tensor_tensor(total[:, :, :], total[:, :, :], gsum[:, :, :], ALU.mult))
            v.link(dve.reciprocal(weight[:, 0, :].rearrange("p (t o) -> p t o", o=1), total[:, :, :]))
            v.link(dve.tensor_tensor(weight[:, 1, :].rearrange("p (t o) -> p t o", o=1),
                                     weight[:, 0, :].rearrange("p (t o) -> p t o", o=1), ratio[:, :, :], ALU.mult))
            for n in range(2):
                for g in range(N_GROUPS):
                    ins = dve.tensor_tensor(hot[n][:, :, g * PER_GROUP:(g + 1) * PER_GROUP], one[n][:, :, :],
                                            wide(g_one[:, :, g:g + 1], PER_GROUP), ALU.mult)
                v.link(ins)
            v.link(dve.tensor_tensor(both[:, :, :], hot[0][:, :, :], hot[1][:, :, :], ALU.add))
            dve.sem_inc(hots_ok, 1)
            dve.wait_ge(made, 1)
            three = lambda t: t[:, :].rearrange("p (t e) -> p t e", t=NT)
            v.link(dve.tensor_copy(tot[:, :, :], three(sums)))
            v.link(dve.memset(base[:, 0, :], 0.0))
            for t in range(1, NT):
                v.link(dve.tensor_tensor(base[:, t, :], base[:, t - 1, :], tot[:, t - 1, :], ALU.add))
            v.link(dve.tensor_tensor(count[:, :], base[:, NT - 1, :], tot[:, NT - 1, :], ALU.add))
            v.link(dve.tensor_scalar(count[:, :], count[:, :], float(P - 1), float(P), ALU.add, ALU.max))
            v.link(dve.tensor_copy(nb_i[:, :], count[:, :]))
            v.link(dve.tensor_scalar(nb_i[:, :], nb_i[:, :], 7, None, ALU.arith_shift_right))
            v.link(dve.tensor_copy(nb_f[:, :], nb_i[:, :]))
            v.link(dve.tensor_tensor_scan(ends_f[:, :], ones_e[:, :], nb_f[:, :], 0.0, ALU.mult, ALU.add))
            v.link(dve.tensor_copy(ends[:, 1:1 + N_EXPERTS], ends_f[:, :]))
            v.link(dve.memset(ends[:, 0:1], 0))
            v.link(dve.tensor_scalar(ends[:, 1 + N_EXPERTS:2 + N_EXPERTS], ends_f[:, N_EXPERTS - 1:N_EXPERTS], -1.0,
                                     float(MAX_BLOCKS + 1), ALU.mult, ALU.add))
            v.link(dve.tensor_tensor(nb_f[:, :], ends_f[:, :], nb_f[:, :], ALU.subtract))
            v.link(dve.tensor_scalar(nb_f[:, :], nb_f[:, :], float(P), None, ALU.mult))
            v.link(dve.tensor_tensor(base[:, :, :], base[:, :, :], three(pos), ALU.add))
            v.link(dve.tensor_tensor(base[:, :, :], base[:, :, :],
                                     nb_f[:, :].rearrange("p (o e) -> p o e", o=1).to_broadcast(E3), ALU.add))
            for n in range(2):
                v.link(dve.tensor_tensor(prod[:, :, :], base[:, :, :], hot[n][:, :, :], ALU.mult))
                v.link(dve.tensor_reduce(total[:, :, :], prod[:, :, :], AX.X, ALU.add))
                v.link(dve.tensor_copy(dest[:, n, :].rearrange("p (t o) -> p t o", o=1), total[:, :, :]))
            dve.sem_inc(dest_ok, 1)


def stage_experts(nc, A, Z, keep):
    ends = keep["ends"]
    with ExitStack() as ctx:
        st = Stage(nc, ctx, "ex")
        wgu = st.sb("wgu", [P, 2, DC, 2 * D_EXPERT])
        FC = D_EXPERT // P
        wd = st.sb("wd", [P, 2, FC, D])
        idx = st.sb("idx", [P, 1], I32)
        xg = st.sb("xg", [P, D])
        xT = st.sb("xT", [P, DC, P])
        gate = st.sb("gate", [P, D_EXPERT])
        hid = st.sb("hid", [P, D_EXPERT])
        hidT = st.sb("hidT", [P, FC, P])
        y = st.sb("y", [P, D])
        zeros = st.sb("zeros", [P, D])
        ident = st.sb("ident", [P, P])
        tp, gu, tph, yps = st.ps("tp", [P, 2, 512]), st.ps("gu", [P, 2, 512]), st.ps("tph", [P, 512]), st.ps("yps", [P, 2, 512])
        w_in = st.sems("w_in", 2)
        zeros_ok, z_out = st.sem("zeros_ok"), st.sem("z_out")
        w_used, id_ok, idx_in, x_in, turned, xt_ok, gu_made = (
            st.sem(n) for n in ("w_used", "id_ok", "idx_in", "x_in", "turned", "xt_ok", "gu_made"))
        silu_ok, hid_ok, hid_turned, hidt_ok, y_made, y_ok, y_out = (
            st.sem(n) for n in ("silu_ok", "hid_ok", "hid_turned", "hidt_ok", "y_made", "y_ok", "y_out"))
        block = st.block()
        bound = dict(min_val=1, max_val=MAX_BLOCKS)

        @block.sync
        def _(sync):
            WGU = A["w_exp_gate_up"][0].rearrange("e (c p) n -> e p c n", p=P)
            WD = A["w_exp_down"][0].rearrange("e (c p) n -> e p c n", p=P)
            sync.wait_ge(zeros_ok, 1)
            spare = sync.value_load(ends[0:1, 1 + N_EXPERTS:2 + N_EXPERTS], **bound)
            with sync.Fori(0, spare) as b:
                sync.dma_start(Z["rows"][bass.ds((MAX_BLOCKS - b) * P, P), :], zeros[:, :]).then_inc(z_out, 16)
            sync.wait_ge(z_out, spare * 16)
            steady(sync, Z)
            with sync.Fori(0, N_EXPERTS // 2) as i:
                for k in range(2):
                    sync.wait_ge(w_used, 2 * i + k + 1)
                    sync.dma_start(wgu[:, k, :, :], WGU[bass.ds(2 * i + k, 1), :, :, :].rearrange("e p c n -> p (e c) n")).then_inc(w_in[k], 16)
                    sync.dma_start(wd[:, k, :, :], WD[bass.ds(2 * i + k, 1), :, :, :].rearrange("e p c n -> p (e c) n")).then_inc(w_in[k], 16)

        @block.gpsimd
        def _(pool):
            build_identity(pool, ident, id_ok)
            pool.memset(zeros[:, :], 0.0).then_inc(zeros_ok, 1)
            pool.sem_inc(w_used, 2)
            n = pool.value_load(ends[0:1, N_EXPERTS:N_EXPERTS + 1], **bound)
            with pool.Fori(0, n + 1) as b:
                pool.wait_ge(x_in, b * 16)
                pool.dma_start(idx[:, :], Z["row_tok"][bass.ds(b * P, P), :]).then_inc(idx_in, 16)
                pool.wait_ge(idx_in, (b + 1) * 16)
                pool.wait_ge(turned, b)
                steady(pool, Z)
                pool.indirect_dma_start(out=xg[:, :], out_offset=None, in_=Z["h2"],
                                        in_offset=bass.IndirectOffsetOnAxis(ap=idx[:, 0:1], axis=0)).then_inc(x_in, 16)
            pool.wait_ge(turned, n + 1)
            pool.wait_ge(x_in, n * 16 + 16)

        @block.tensor
        def _(pe):
            def turn_rows(b):
                pe.wait_ge(x_in, b * 16 + 16)
                pe.wait_ge(xt_ok, b)
                for c in range(DC):
                    ins = pe.transpose(tp[:, c // 4, (c % 4) * P:(c % 4 + 1) * P], xg[:, c * P:(c + 1) * P], ident[:, :])
                ins.then_inc(turned, 1)

            pe.wait_ge(id_ok, 2)
            turn_rows(0)
            with pe.Fori(0, N_EXPERTS // 2) as i:
                for k in range(2):
                    first = pe.value_load(ends[0:1, bass.ds(2 * i + k, 1)], min_val=0, max_val=MAX_BLOCKS)
                    last = pe.value_load(ends[0:1, bass.ds(2 * i + k + 1, 1)], **bound)
                    pe.wait_ge(w_in[k], (i + 1) * 32)
                    steady(pe, Z)
                    with pe.Fori(first, last) as b:
                        pe.wait_ge(xt_ok, b + 1)
                        pe.wait_ge(hid_ok, b)
                        for n in range(2):
                            for c in range(DC):
                                ins = pe.matmul(gu[:, n, :], xT[:, c, :], wgu[:, k, c, n * 512:(n + 1) * 512],
                                                start=(c == 0), stop=(c == DC - 1))
                            ins.then_inc(gu_made, 1)
                        turn_rows(b + 1)
                        pe.wait_ge(hid_ok, b + 1)
                        pe.wait_ge(hidt_ok, b)
                        for c in range(FC):
                            ins = pe.transpose(tph[:, c * P:(c + 1) * P], hid[:, c * P:(c + 1) * P], ident[:, :])
                        ins.then_inc(hid_turned, 1)
                        pe.wait_ge(hidt_ok, b + 1)
                        pe.wait_ge(y_ok, b)
                        for n in range(2):
                            for c in range(FC):
                                ins = pe.matmul(yps[:, n, :], hidT[:, c, :], wd[:, k, c, n * 512:(n + 1) * 512],
                                                start=(c == 0), stop=(c == FC - 1))
                        ins.then_inc(y_made, 1)
                    pe.wait_ge(y_made, last)
                    pe.sem_inc(w_used, 1)

        @block.scalar
        def _(act):
            n = act.value_load(ends[0:1, N_EXPERTS:N_EXPERTS + 1], **bound)
            with act.Fori(0, n) as b:
                act.wait_ge(gu_made, b * 2 + 1)
                act.wait_ge(hid_ok, b)
                act.activation(gate[:, :], gu[:, 0, :], ACT.Silu).then_inc(silu_ok, 1)
                act.wait_ge(hid_turned, b + 1)
                act.copy(hidT[:, :, :].rearrange("p c t -> p (c t)"), tph[:, :]).then_inc(hidt_ok, 1)
                act.wait_ge(y_made, b + 1)
                act.wait_ge(y_out, b * 16)
                act.copy(y[:, :].rearrange("p (n c) -> p n c", n=2), yps[:, :, :]).then_inc(y_ok, 1)
                act.wait_ge(y_ok, b + 1)
                act.dma_start(Z["rows"][bass.ds(b * P, P), :], y[:, :]).then_inc(y_out, 16)
            act.wait_ge(y_out, n * 16)
            steady(act, Z)

        @block.vector
        def _(dve):
            n = dve.value_load(ends[0:1, N_EXPERTS:N_EXPERTS + 1], **bound)
            dve.wait_ge(turned, 1)
            dve.tensor_copy(xT[:, :, :].rearrange("p (b c) t -> p b (c t)", b=2), tp[:, :, :]).then_inc(xt_ok, 1)
            with dve.Fori(0, n) as b:
                dve.wait_ge(gu_made, b * 2 + 2)
                dve.wait_ge(silu_ok, b + 1)
                dve.wait_ge(hid_turned, b)
                dve.tensor_tensor(hid[:, :], gate[:, :], gu[:, 1, :], ALU.mult).then_inc(hid_ok, 1)
                dve.wait_ge(turned, b + 2)
                dve.tensor_copy(xT[:, :, :].rearrange("p (b c) t -> p b (c t)", b=2), tp[:, :, :]).then_inc(xt_ok, 1)


def stage_moe(nc, A, Z):
    with ExitStack() as ctx:
        st = Stage(nc, ctx, "mo")
        keep = dict(lg=st.sb("lg", [P, NT, N_LOGITS]), weight=st.sb("weight", [P, 2, NT]), dest=st.sb("dest", [P, 2, NT], I32),
                    ends=st.sb("ends", [P, 2 + N_EXPERTS], I32), tok_id=st.sb("tok_id", [P, NT], I32))
        stage_route(nc, A, Z, keep)
        stage_experts(nc, A, Z, keep)
        stage_final(nc, A, Z, keep)


PLE = 256


def stage_final(nc, A, Z, keep):
    dest, weight = keep["dest"], keep["weight"]
    with ExitStack() as ctx:
        st = Stage(nc, ctx, "fi")
        PC = PLE // P
        w_g, w_p = st.sb("w_g", [P, DC, D]), st.sb("w_p", [P, PC, D])
        g_in = st.sb("g_in", [P, DC])
        g_e, g_y = st.sb("g_e", [P, D]), st.sb("g_y", [P, D])
        x = st.sb("x", [P, 2, D])
        r = st.sb("r", [P, 2, 2, D])
        p_t = st.sb("p_t", [P, 2, PLE])
        idx = st.sb("idx", [P, 2, 2], I32)
        xn, sg, e = (st.sb(n, [P, D]) for n in ("xn", "sg", "e"))
        junk = st.sb("junk", [P, D])
        out_t = st.sb("out_t", [P, 2, D])
        xT, pT = st.sb("xT", [P, DC, P]), st.sb("pT", [P, PC, P])
        stat = st.sb("stat", [P, 3, 4])
        ident = st.sb("ident", [P, P])
        tp, gps = st.ps("tp", [P, 2, 512]), st.ps("gps", [P, 2, 512])
        pps, eps = st.ps("pps", [P, 512]), st.ps("eps", [P, 2, 512])
        x_in, r_in, y_out = st.sems("x_in", 2), st.sems("r_in", 2), st.sems("y_out", 2)
        w_in, id_ok, idx_ok, x_used, summed, ms_ok, roots = (
            st.sem(n) for n in ("w_in", "id_ok", "idx_ok", "x_used", "summed", "ms_ok", "roots"))
        xn_ok, turned, xt_ok, made, sig_ok, y_ok, vec = (
            st.sem(n) for n in ("xn_ok", "turned", "xt_ok", "made", "sig_ok", "y_ok", "vec"))
        p_turned, pt_ok, e_made = st.sem("p_turned"), st.sem("pt_ok"), st.sem("e_made")
        block = st.block()
        MIX, EMB, OUT = range(3)

        @block.sync
        def _(sync):
            sync.dma_start(w_g[:, :, :], A["w_ple_gate"][0].rearrange("(c p) n -> p c n", p=P)).then_inc(w_in, 16)
            sync.dma_start(w_p[:, :, :], A["w_ple_proj"][0].rearrange("(c p) n -> p c n", p=P)).then_inc(w_in, 16)
            sync.dma_start(g_in[:, :], cols(A["g_ple_gate_in"][0], DC)).then_inc(w_in, 16)
            sync.dma_start(g_e[:, :], A["g_ple_norm"][0].partition_broadcast(P)).then_inc(w_in, 16)
            sync.dma_start(g_y[:, :], A["g_final"].partition_broadcast(P)).then_inc(w_in, 16)
            with sync.Fori(0, NT // 2) as i:
                for k in range(2):
                    t = 2 * i + k
                    sync.wait_ge(x_used, t + 1)
                    sync.dma_start(x[:, k, :], Z["x1"][bass.ds(t * P, P), :]).then_inc(x_in[k], 16)
                    sync.dma_start(p_t[:, k, :], A["p"][0][0][bass.ds(t * P, P), :]).then_inc(x_in[k], 16)

        @block.gpsimd
        def _(pool):
            build_identity(pool, ident, id_ok)
            with pool.Fori(0, NT // 2) as i:
                for k in range(2):
                    t = 2 * i + k
                    pool.wait_ge(x_used, t + 1)
                    pool.wait_ge(r_in[k], i * 32)
                    pool.tensor_copy(idx[:, k, :].rearrange("p (n o) -> p n o", o=1), dest[:, :, bass.ds(t, 1)]).then_inc(idx_ok, 1)
                    pool.wait_ge(idx_ok, t + 1)
                    steady(pool, Z)
                    for n in range(2):
                        pool.indirect_dma_start(out=r[:, k, n, :], out_offset=None, in_=Z["rows"],
                                                in_offset=bass.IndirectOffsetOnAxis(ap=idx[:, k, n:n + 1], axis=0)).then_inc(r_in[k], 16)

        @block.tensor
        def _(pe):
            pe.wait_ge(id_ok, 2)
            pe.wait_ge(w_in, 80)
            with pe.Fori(0, NT // 2) as i:
                for k in range(2):
                    t = 2 * i + k
                    pe.wait_ge(x_in[k], (i + 1) * 32)
                    pe.wait_ge(pt_ok, t)
                    for c in range(PC):
                        ins = pe.transpose(pps[:, c * P:(c + 1) * P], p_t[:, k, c * P:(c + 1) * P], ident[:, :])
                    ins.then_inc(p_turned, 1)
                    pe.wait_ge(pt_ok, t + 1)
                    pe.wait_ge(y_ok, t)
                    for n in range(2):
                        for c in range(PC):
                            ins = pe.matmul(eps[:, n, :], pT[:, c, :], w_p[:, c, n * 512:(n + 1) * 512],
                                            start=(c == 0), stop=(c == PC - 1))
                    ins.then_inc(e_made, 1)
                    pe.wait_ge(xn_ok, t + 1)
                    for c in range(DC):
                        ins = pe.transpose(tp[:, c // 4, (c % 4) * P:(c % 4 + 1) * P], xn[:, c * P:(c + 1) * P], ident[:, :])
                    ins.then_inc(turned, 1)
                    pe.wait_ge(xt_ok, t + 1)
                    pe.wait_ge(sig_ok, t)
                    for n in range(2):
                        for c in range(DC):
                            ins = pe.matmul(gps[:, n, :], xT[:, c, :], w_g[:, c, n * 512:(n + 1) * 512],
                                            start=(c == 0), stop=(c == DC - 1))
                    ins.then_inc(made, 1)

        @block.scalar
        def _(act):
            def root(which, n):
                act.wait_ge(ms_ok, n)
                act.activation(stat[:, which, 2:3], stat[:, which, 1:2], ACT.Sqrt).then_inc(roots, 1)

            with act.Fori(0, NT // 2) as i:
                for k in range(2):
                    t = 2 * i + k
                    act.wait_ge(p_turned, t + 1)
                    act.wait_ge(e_made, t)
                    act.copy(pT[:, :, :].rearrange("p c t -> p (c t)"), pps[:, 0:PLE]).then_inc(pt_ok, 1)
                    act.wait_ge(e_made, t + 1)
                    act.wait_ge(summed, 3 * t)
                    act.activation(junk[:, :].rearrange("p (n c) -> p n c", n=2), eps[:, :, :], ACT.Square,
                                   accum_out=stat[:, EMB, 0:1]).then_inc(summed, 1)
                    root(EMB, 3 * t + 1)
                    act.wait_ge(vec, t * 8 + 2)
                    act.wait_ge(summed, 3 * t + 1)
                    act.activation(junk[:, :], x[:, k, :], ACT.Square, accum_out=stat[:, MIX, 0:1]).then_inc(summed, 1)
                    root(MIX, 3 * t + 2)
                    act.wait_ge(made, t + 1)
                    act.activation(sg[:, :].rearrange("p (n c) -> p n c", n=2), gps[:, :, :], ACT.Sigmoid).then_inc(sig_ok, 1)
                    act.wait_ge(vec, t * 8 + 7)
                    act.wait_ge(summed, 3 * t + 2)
                    act.activation(junk[:, :], x[:, k, :], ACT.Square, accum_out=stat[:, OUT, 0:1]).then_inc(summed, 1)
                    root(OUT, 3 * t + 3)
                    act.wait_ge(y_ok, t + 1)
                    act.dma_start(Z["y"][0][bass.ds(t * P, P), :], out_t[:, k, :]).then_inc(y_out[k], 16)
            for k in range(2):
                act.wait_ge(y_out[k], NT // 2 * 16)

        @block.vector
        def _(dve):
            v = Chain(dve, vec)

            def mean_square(which, n):
                dve.wait_ge(summed, n)
                dve.tensor_scalar(stat[:, which, 1:2], stat[:, which, 0:1], 1.0 / D, NORM_EPS, ALU.mult, ALU.add).then_inc(ms_ok, 1)
                dve.wait_ge(roots, n)
                v.link(dve.reciprocal(stat[:, which, 3:4], stat[:, which, 2:3]))

            dve.sem_inc(x_used, 2)
            dve.wait_ge(w_in, 80)
            halves = lambda a: a.rearrange("p (n c) -> p n c", n=2)
            with dve.Fori(0, NT // 2) as i:
                v.loop(i, 16)
                for k in range(2):
                    t = 2 * i + k
                    dve.wait_ge(x_in[k], (i + 1) * 32)
                    dve.wait_ge(r_in[k], (i + 1) * 32)
                    for n in range(2):
                        v.link(dve.scalar_tensor_tensor(out=x[:, k, :], in0=r[:, k, n, :], scalar=weight[:, n, bass.ds(t, 1)],
                                                        in1=x[:, k, :], op0=ALU.mult, op1=ALU.add))
                    mean_square(EMB, 3 * t + 1)
                    v.link(dve.scalar_tensor_tensor(out=halves(e[:, :]), in0=eps[:, :, :], scalar=stat[:, EMB, 3:4],
                                                    in1=halves(g_e[:, :]), op0=ALU.mult, op1=ALU.mult))
                    mean_square(MIX, 3 * t + 2)
                    dve.wait_ge(turned, t)
                    dve.tensor_scalar(xn[:, :], x[:, k, :], stat[:, MIX, 3:4], None, ALU.mult).then_inc(xn_ok, 1)
                    dve.wait_ge(turned, t + 1)
                    dve.wait_ge(made, t)
                    for b in range(2):
                        ins = dve.tensor_tensor(xT[:, 4 * b:4 * b + 4, :], tp[:, b, :].rearrange("p (c t) -> p c t", c=4),
                                                g_in[:, 4 * b:4 * b + 4].rearrange("p (c o) -> p c o", o=1).to_broadcast([P, 4, P]),
                                                ALU.mult)
                    ins.then_inc(xt_ok, 1)
                    dve.wait_ge(sig_ok, t + 1)
                    v.link(dve.tensor_tensor(e[:, :], e[:, :], sg[:, :], ALU.mult))
                    v.link(dve.tensor_tensor(x[:, k, :], x[:, k, :], e[:, :], ALU.add))
                    mean_square(OUT, 3 * t + 3)
                    dve.wait_ge(y_out[k], i * 16)
                    dve.scalar_tensor_tensor(out=out_t[:, k, :], in0=x[:, k, :], scalar=stat[:, OUT, 3:4], in1=g_y[:, :],
                                             op0=ALU.mult, op1=ALU.mult).then_inc(y_ok, 1)
                    dve.wait_ge(y_ok, t + 1)
                    dve.sem_inc(x_used, 1)
                v.end(NT // 2)


_IN_NAMES = ["x", "p", "g_mix", "w_in", "mu_shift", "rw_w0", "rw_w2", "rw_a0", "rw_a2", "rw_g2", "rw_k_k", "rw_k_a",
             "rw_r_k", "rw_ln_w", "rw_ln_b", "cmp_pos_k", "cmp_pos_v", "cmp_k_w1", "cmp_k_w2", "cmp_v_w1", "cmp_v_w2",
             "nsa_gate_b", "w_up_rwkv", "w_up_nsa", "w_out", "g_ffn", "w_group", "b_group", "w_router", "b_router",
             "w_exp_gate_up", "w_exp_down", "w_ple_proj", "g_ple_norm", "g_ple_gate_in", "w_ple_gate", "g_final"]

_SCRATCH = {
    "z": ((Z_ROWS, S), F32), "gate": ((N_GATE, S), F32),
    "rar": ((RW_W, NCH, 2, CH), F32), "rb": ((RW_W, S), F32), "rk": ((RW_W, S), F32), "rv": ((RW_W, S), F32),
    "rdec": ((RW_W, 2, NCH), F32), "rbonus": ((RW_W, S), F32), "rg": ((RW_W, S), F32), "ro": ((RW_W, S), F32),
    "yr": ((RW_W, S), F32), "yn": ((NSA_W, S), F32), "x1": ((S, D), F32), "h2": ((S, D), F32),
    "row_tok": (((MAX_BLOCKS + 1) * P, 1), I32), "rows": (((MAX_BLOCKS + 1) * P, D), F32),
}


def build_program(nc, A, out):
    Z = {n: nc.dram_tensor(f"s_{n}", shape, dt).ap() for n, (shape, dt) in _SCRATCH.items()}
    Z["y"] = out
    with ExitStack() as whole, nc.semaphore("passed") as passed, \
            nc.allow_non_contiguous_dma(reason="vectors of parameters, a few KB each"):
        Z["passed"], Z["whole"] = passed, whole
        stage_project(nc, A, Z)
        stage_rwkv_prep(nc, A, Z)
        stage_rwkv_scan(nc, A, Z)
        stage_rwkv_post(nc, A, Z)
        stage_nsa(nc, A, Z)
        stage_mix(nc, A, Z)
        stage_moe(nc, A, Z)


def kernel(**inputs):
    import concourse.bacc as bacc
    from concourse.bass_utils import run_bass_kernel_spmd

    nc = bacc.Bacc("TRN2", target_bir_lowering=False, num_devices=1)
    arrays, A = {}, {}
    for name in _IN_NAMES:
        a = np.ascontiguousarray(inputs[name])
        arrays[f"in_{name}"] = a
        A[name] = nc.dram_tensor(f"in_{name}", a.shape, mybir.dt.from_np(a.dtype), kind="ExternalInput").ap()
    out = nc.dram_tensor("out_y", (1, S, D), F32, kind="ExternalOutput").ap()
    build_program(nc, A, out)
    r = run_bass_kernel_spmd(nc, [arrays], core_ids=[0])
    return r.results[0]["out_y"]
```

```python
from contextlib import ExitStack
import math

import numpy as np

import concourse.bass as bass
from concourse import mybir

F32 = mybir.dt.float32
I32 = mybir.dt.int32
ALU = mybir.AluOpType
ACT = mybir.ActivationFunctionType
AX = mybir.AxisListType

P = 128
D = 1024
S = 2048
DC = D // P
NT = S // P
NB = S // 512
HD = 64
RW_HEADS, RW_W = 8, 512
LORA, GATE_LORA = 64, 128
GN_EPS = 64e-5
NORM_EPS = 1e-6
RW_IN = 3 * RW_W + 2 * LORA + GATE_LORA
NSA_HEADS, KV_HEADS = 8, 2
Q_PER_KV = NSA_HEADS // KV_HEADS
NSA_W = 512
N_IN = RW_IN + NSA_W + 6 * KV_HEADS * HD + 3 * NSA_HEADS + 2 * D
GATE_ROW = RW_IN + NSA_W + 6 * KV_HEADS * HD
N_GATE = 3 * NSA_HEADS
MERGE_COL = GATE_ROW + N_GATE
NEG = -1e30
FORCE = 1e6
DECAY_SCALE = math.exp(-0.5)

ROW_R, ROW_K, ROW_V = 0, RW_W, 2 * RW_W
ROW_W, ROW_A, ROW_G = 3 * RW_W, 3 * RW_W + LORA, 3 * RW_W + 2 * LORA
ROW_Q = RW_IN
ROW_KC, ROW_VC, ROW_KS, ROW_VS, ROW_KW, ROW_VW = (RW_IN + NSA_W + 128 * n for n in range(6))
ROW_MERGE = GATE_ROW
Z_ROWS = ROW_MERGE + 2 * D


class Chain:

    def __init__(self, eng, sem):
        self.eng, self.sem, self.base, self.n = eng, sem, 0, 0

    def mark(self, ins):
        ins.then_inc(self.sem, 1)
        self.n += 1
        return ins

    def wait(self):
        self.eng.wait_ge(self.sem, self.base + self.n)

    def link(self, ins):
        self.mark(ins)
        self.wait()

    def loop(self, i, per):
        self.before, self.per = self.n, per
        self.base, self.n = i * per + self.n, 0

    def end(self, trips):
        assert self.n == self.per, (self.n, self.per)
        self.base, self.n = 0, self.before + trips * self.per


class Stage:

    def __init__(self, nc, ctx, name):
        self.nc, self.ctx, self.name, self.numbers = nc, ctx, name, []

    def sb(self, name, shape, dt=F32):
        return self.ctx.enter_context(self.nc.sbuf_tensor(f"{self.name}_{name}", shape, dt))

    def ps(self, name, shape, dt=F32):
        return self.ctx.enter_context(self.nc.psum_tensor(f"{self.name}_{name}", shape, dt))

    def sem(self, name):
        sem = self.ctx.enter_context(self.nc.semaphore(f"{self.name}_{name}"))
        self.numbers.append(sem.num)
        return sem

    def lasting_sem(self, name, whole):
        return whole.enter_context(self.nc.semaphore(f"{self.name}_{name}"))

    def sems(self, name, n):
        return [self.sem(f"{name}{k}") for k in range(n)]

    def zero(self):
        numbers = sorted(self.numbers)
        firsts = [n for n in numbers if n - 1 not in numbers]
        lasts = [n for n in numbers if n + 1 not in numbers]
        with self.nc.Block() as block:
            @block.gpsimd
            def _(pool):
                for first, last in zip(firsts, lasts):
                    pool.sem_clear(range(first, last + 1))

    def block(self):
        self.ctx.callback(self.zero)
        return self.ctx.enter_context(self.nc.Block())


def steady(eng, Z):
    eng.sem_inc(Z["passed"], 1)


def cols(v, c):
    return v.rearrange("(c p) -> p c", c=c)


def build_identity(pool, ident, seen):
    pool.memset(ident[:, :], 0.0).then_inc(seen, 1)
    pool.wait_ge(seen, 1)
    pool.affine_select(out=ident[:, :], in_=ident[:, :], compare_op=ALU.not_equal, fill=1.0, base=0,
                       pattern=[[-1, P]], channel_multiplier=1).then_inc(seen, 1)


def stage_project(nc, A, Z):
    outer = ExitStack()
    with outer:
        keep = Stage(nc, outer, "pr")
        hT = keep.sb("hT", [P, DC, S])

        with ExitStack() as ctx:
            st = Stage(nc, ctx, "nm")
            x_t = st.sb("x", [P, 2, D])
            sq = st.sb("sq", [P, D])
            stat = st.sb("stat", [P, 2, 4])
            xn = st.sb("xn", [P, 2, D])
            g_c = st.sb("g", [P, DC])
            ident = st.sb("ident", [P, P])
            tp = st.ps("tp", [P, 2, 2, 512])
            x_in = st.sems("x_in", 2)
            x_free, g_in, id_ok = (st.sem(n) for n in ("x_free", "g_in", "id_ok"))
            squares, roots, steps = (st.sem(n) for n in ("squares", "roots", "steps"))
            ms_ok, xn_ok, turned, taken = (st.sem(n) for n in ("ms_ok", "xn_ok", "turned", "taken"))
            block = st.block()

            @block.sync
            def _(sync):
                sync.dma_start(g_c[:, :], cols(A["g_mix"][0], DC)).then_inc(g_in, 16)
                with sync.Fori(0, NT // 2) as i:
                    for k in range(2):
                        sync.wait_ge(x_free, 2 * i + k + 1)
                        sync.dma_start(x_t[:, k, :], A["x"][0][bass.ds((2 * i + k) * P, P), :]).then_inc(x_in[k], 16)

            @block.gpsimd
            def _(pool):
                build_identity(pool, ident, id_ok)

            @block.scalar
            def _(act):
                with act.Fori(0, NT // 2) as i:
                    for k in range(2):
                        act.wait_ge(x_in[k], (i + 1) * 16)
                        act.wait_ge(squares, 2 * i + k)
                        act.activation(sq[:, :], x_t[:, k, :], ACT.Square,
                                       accum_out=stat[:, k, 0:1]).then_inc(squares, 1)
                    for k in range(2):
                        act.wait_ge(ms_ok, 2 * i + k + 1)
                        act.activation(stat[:, k, 2:3], stat[:, k, 1:2], ACT.Sqrt).then_inc(roots, 1)

            @block.vector
            def _(dve):
                v = Chain(dve, steps)
                dve.sem_inc(x_free, 2)
                dve.sem_inc(taken, 2)
                dve.wait_ge(g_in, 16)
                with dve.Fori(0, NT // 2) as i:
                    v.loop(i, 2)
                    for k in range(2):
                        dve.wait_ge(squares, 2 * i + k + 1)
                        dve.tensor_scalar(stat[:, k, 1:2], stat[:, k, 0:1], 1.0 / D, NORM_EPS,
                                          ALU.mult, ALU.add).then_inc(ms_ok, 1)
                    for k in range(2):
                        dve.wait_ge(roots, 2 * i + k + 1)
                        v.link(dve.reciprocal(stat[:, k, 3:4], stat[:, k, 2:3]))
                        dve.wait_ge(turned, 2 * i + k)
                        dve.tensor_scalar(xn[:, k, :], x_t[:, k, :], stat[:, k, 3:4], None,
                                          ALU.mult).then_inc(xn_ok, 1)
                        dve.wait_ge(xn_ok, 2 * i + k + 1)
                        dve.sem_inc(x_free, 1)
                    for k in range(2):
                        dve.wait_ge(turned, 2 * i + k + 1)
                        for c in range(2):
                            ins = dve.tensor_tensor(
                                hT[:, 4 * c:4 * c + 4, bass.ds((2 * i + k) * P, P)],
                                tp[:, k, c, :].rearrange("p (c t) -> p c t", c=4),
                                g_c[:, 4 * c:4 * c + 4].rearrange("p (c o) -> p c o", o=1).to_broadcast([P, 4, P]),
                                ALU.mult)
                        ins.then_inc(taken, 1)
                    v.end(NT // 2)

            @block.tensor
            def _(pe):
                pe.wait_ge(id_ok, 2)
                with pe.Fori(0, NT // 2) as i:
                    for k in range(2):
                        pe.wait_ge(xn_ok, 2 * i + k + 1)
                        pe.wait_ge(taken, 2 * i + k + 1)
                        for c in range(DC):
                            ins = pe.transpose(tp[:, k, c // 4, (c % 4) * P:(c % 4 + 1) * P],
                                               xn[:, k, c * P:(c + 1) * P], ident[:, :])
                        ins.then_inc(turned, 1)

        with ExitStack() as ctx:
            st = Stage(nc, ctx, "zp")
            w = st.sb("w", [P, 2, DC, P])
            zs = st.sb("zs", [P, 2, S])
            acc = st.ps("acc", [P, 2, NB, 512])
            w_in, z_out = st.sems("w_in", 2), [st.lasting_sem(f"z_out{k}", Z["whole"]) for k in range(2)]
            w_free, made, half_a, half_v = (st.sem(n) for n in ("w_free", "made", "half_a", "half_v"))
            n_lead = GATE_ROW // P
            n_all = Z_ROWS // P
            W = A["w_in"][0].rearrange("(c p) n -> p c n", p=P)
            block = st.block()

            @block.sync
            def _(sync):
                def load(i, k, col):
                    sync.wait_ge(w_free, 2 * i + k + 1)
                    sync.dma_start(w[:, k, :, :], W[:, :, bass.ds(col, P)]).then_inc(w_in[k], 16)

                with sync.Fori(0, n_lead // 2) as i:
                    for k in range(2):
                        load(i, k, (2 * i + k) * P)
                with sync.Fori(n_lead // 2, n_all // 2) as i:
                    for k in range(2):
                        load(i, k, (2 * i + k) * P + N_GATE)
                sync.wait_ge(w_free, n_all + 1)
                sync.dma_start(w[:, 0, :, 0:N_GATE], W[:, :, GATE_ROW:MERGE_COL]).then_inc(w_in[0], 16)

            @block.tensor
            def _(pe):
                pe.sem_inc(w_free, 2)
                with pe.Fori(0, n_all // 2) as i:
                    for k in range(2):
                        pe.wait_ge(w_in[k], (i + 1) * 16)
                        pe.wait_ge(half_a, 2 * i + k + 1)
                        pe.wait_ge(half_v, 2 * i + k + 1)
                        for n in range(NB):
                            for c in range(DC):
                                ins = pe.matmul(acc[:, k, n, :], w[:, k, c, :], hT[:, c, n * 512:(n + 1) * 512],
                                                start=(c == 0), stop=(c == DC - 1))
                        ins.then_inc(made, 1)
                        pe.wait_ge(made, 2 * i + k + 1)
                        pe.sem_inc(w_free, 1)
                pe.wait_ge(w_in[0], (n_all // 2 + 1) * 16)
                pe.wait_ge(half_a, n_all + 1)
                pe.wait_ge(half_v, n_all + 1)
                for n in range(NB):
                    for c in range(DC):
                        ins = pe.matmul(acc[0:N_GATE, 0, n, :], w[:, 0, c, 0:N_GATE],
                                        hT[:, c, n * 512:(n + 1) * 512], start=(c == 0), stop=(c == DC - 1))
                ins.then_inc(made, 1)

            @block.scalar
            def _(act):
                act.sem_inc(half_a, 2)
                with act.Fori(0, n_all // 2) as i:
                    for k in range(2):
                        act.wait_ge(made, 2 * i + k + 1)
                        act.wait_ge(z_out[k], i * 16)
                        act.copy(zs[:, k, 0:1024].rearrange("p (n t) -> p n t", n=2),
                                 acc[:, k, 0:2, :]).then_inc(half_a, 1)
                act.wait_ge(made, n_all + 1)
                act.wait_ge(z_out[0], n_all // 2 * 16)
                act.copy(zs[0:N_GATE, 0, 0:1024].rearrange("p (n t) -> p n t", n=2),
                         acc[0:N_GATE, 0, 0:2, :]).then_inc(half_a, 1)

            @block.vector
            def _(dve):
                dve.sem_inc(half_v, 2)
                with dve.Fori(0, n_all // 2) as i:
                    for k in range(2):
                        dve.wait_ge(made, 2 * i + k + 1)
                        dve.wait_ge(z_out[k], i * 16)
                        dve.tensor_copy(zs[:, k, 1024:2048].rearrange("p (n t) -> p n t", n=2),
                                        acc[:, k, 2:4, :]).then_inc(half_v, 1)
                dve.wait_ge(made, n_all + 1)
                dve.wait_ge(z_out[0], n_all // 2 * 16)
                dve.tensor_copy(zs[0:N_GATE, 0, 1024:2048].rearrange("p (n t) -> p n t", n=2),
                                acc[0:N_GATE, 0, 2:4, :]).then_inc(half_v, 1)

            @block.gpsimd
            def _(pool):
                with pool.Fori(0, n_all // 2) as i:
                    for k in range(2):
                        pool.wait_ge(half_a, 2 * i + k + 3)
                        pool.wait_ge(half_v, 2 * i + k + 3)
                        pool.dma_start(Z["z"][bass.ds((2 * i + k) * P, P), :], zs[:, k, :]).then_inc(z_out[k], 16)
                pool.wait_ge(half_a, n_all + 3)
                pool.wait_ge(half_v, n_all + 3)
                pool.dma_start(Z["gate"], zs[0:N_GATE, 0, :]).then_inc(z_out[0], 16)
                pool.wait_ge(z_out[0], (n_all // 2 + 1) * 16)
                pool.wait_ge(z_out[1], n_all // 2 * 16)


CH = P
NCH = S // CH
PAIRS = RW_W // P


def stage_rwkv_prep(nc, A, Z):
    with ExitStack() as ctx:
        st = Stage(nc, ctx, "rp")
        z3 = [st.sb(f"z{n}", [P, 1 + S]) for n in range(3)]
        dif = st.sb("dif", [P, S])
        zk, tw, zas, sg = (st.sb(n, [P, S]) for n in ("zk", "tw", "zas", "sg"))
        lw, cum, cm, aa, e1, e2 = (st.sb(n, [P, S]) for n in ("lw", "cum", "cm", "aa", "e1", "e2"))
        kk, sq = st.sb("kk", [P, S]), st.sb("sq", [P, S])
        ar = st.sb("ar", [P, NCH, 2, CH])
        bt, kt, vt = (st.sb(n, [P, S]) for n in ("bt", "kt", "vt"))
        go = sq
        same = st.sb("same", [P, P])
        reset = st.sb("reset", [P, S])
        dec = st.sb("dec", [P, 2, NCH])
        wl = st.sb("wl", [P, 3, P])
        mu = st.sb("mu", [P, RW_IN // P])
        mu_l = st.sb("mu_l", [HD, 2])
        par = st.sb("par", [P, 5, PAIRS])
        psW, psA = st.ps("psW", [P, NB, 512]), st.ps("psA", [P, NB, 512])
        lora_in, par_in, loads, z_used, w_used = (
            st.sem(n) for n in ("lora_in", "par_in", "loads", "z_used", "w_used"))
        init, lora_ok, lora_act, made, acts, vec = (
            st.sem(n) for n in ("init", "lora_ok", "lora_act", "made", "acts", "vec"))
        kk0_ok, rk_ok, cm_ok, out_ok, stored, act_self = (
            st.sem(n) for n in ("kk0_ok", "rk_ok", "cm_ok", "out_ok", "stored", "act_self"))
        bon_ok, small, g_free = st.sem("bon_ok"), st.sem("small"), st.sem("g_free")
        MADE, ACTS, STORES = 5, 9, 6
        W0, A0, K_K, K_A, R_K = range(5)
        z, Zc = Z["z"], lambda row: Z["z"][bass.ds(row, P), :]
        block = st.block()

        @block.sync
        def _(sync):
            sync.wait_ge(init, 4)
            sync.dma_start(z3[0][0:LORA, 1:1 + S], z[ROW_W:ROW_W + LORA, :]).then_inc(lora_in, 16)
            sync.dma_start(z3[1][0:LORA, 1:1 + S], z[ROW_A:ROW_A + LORA, :]).then_inc(lora_in, 16)
            sync.dma_start(z3[2][:, 1:1 + S], z[ROW_G:ROW_G + P, :]).then_inc(lora_in, 16)
            sync.dma_start(mu[:, :], cols(A["mu_shift"][0], RW_IN // P)).then_inc(par_in, 16)
            sync.dma_start(mu_l[:, :], A["mu_shift"][0][ROW_W:ROW_G].rearrange("(c p) -> p c", c=2)).then_inc(par_in, 16)
            for n, name in enumerate(("rw_w0", "rw_a0", "rw_k_k", "rw_k_a")):
                sync.dma_start(par[:, n, :], cols(A[name][0], PAIRS)).then_inc(par_in, 16)
            sync.dma_start(par[:, R_K, :], cols(A["rw_r_k"][0].rearrange("h d -> (h d)"), PAIRS)).then_inc(par_in, 16)
            with sync.Fori(0, PAIRS) as i:
                sync.wait_ge(z_used, i + 1)
                for n, row in enumerate((ROW_R, ROW_K, ROW_V)):
                    sync.dma_start(z3[n][:, 1:1 + S], Zc(i * P + row)).then_inc(loads, 16)
                sync.wait_ge(w_used, i + 1)
                steady(sync, Z)
                sync.dma_start(wl[0:LORA, 0, :], A["rw_w2"][0][:, bass.ds(i * P, P)]).then_inc(loads, 16)
                sync.dma_start(wl[0:LORA, 1, :], A["rw_a2"][0][:, bass.ds(i * P, P)]).then_inc(loads, 16)
                sync.dma_start(wl[:, 2, :], A["rw_g2"][0][:, bass.ds(i * P, P)]).then_inc(loads, 16)
                sync.wait_ge(out_ok, i + 1)
                steady(sync, Z)
                sync.dma_start(Z["rar"][bass.ds(i * P, P), :, :, :], ar[:, :, :, :]).then_inc(stored, 16)
                sync.dma_start(Z["rb"][bass.ds(i * P, P), :], bt[:, :]).then_inc(stored, 16)
                sync.dma_start(Z["rk"][bass.ds(i * P, P), :], kt[:, :]).then_inc(stored, 16)
                sync.dma_start(Z["rv"][bass.ds(i * P, P), :], vt[:, :]).then_inc(stored, 16)
                sync.dma_start(Z["rdec"][bass.ds(i * P, P), :, :], dec[:, :, :]).then_inc(stored, 16)
                sync.dma_start(Z["rbonus"][bass.ds(i * P, P), :], dif[:, :]).then_inc(stored, 16)
                sync.wait_ge(stored, (i + 1) * 16 * STORES)
                steady(sync, Z)
            sync.wait_ge(g_free, PAIRS * 16)

        @block.gpsimd
        def _(pool):
            for t in z3:
                pool.memset(t[:, 0:1], 0.0).then_inc(init, 1)
            pool.memset(reset[:, :], 1.0).then_inc(small, 1)
            pool.wait_ge(small, 1)
            pool.memset(reset[:, :].rearrange("p (c t) -> p c t", t=CH)[:, :, 0:1], 0.0).then_inc(init, 1)
            pool.memset(same[:, :], 0.0).then_inc(small, 1)
            pool.wait_ge(small, 2)
            pool.memset(same[0:HD, 0:HD], 1.0).then_inc(init, 1)
            pool.memset(same[HD:P, HD:P], 1.0).then_inc(init, 1)

        @block.tensor
        def _(pe):
            def product(dst, lhsT, rhs, k):
                for n in range(NB):
                    ins = pe.matmul(dst[:, n, :], lhsT, rhs[0:k, n * 512:(n + 1) * 512], start=True, stop=True)
                ins.then_inc(made, 1)

            pe.sem_inc(w_used, 1)
            pe.wait_ge(init, 6)
            pe.wait_ge(lora_act, 2)
            pe.wait_ge(lora_ok, 3)
            with pe.Fori(0, PAIRS) as i:
                pe.wait_ge(loads, (i + 1) * 96)
                pe.wait_ge(bon_ok, i)
                product(psW, wl[0:LORA, 0, :], tw, LORA)
                product(psA, wl[0:LORA, 1, :], zas, LORA)
                pe.wait_ge(acts, i * ACTS + 1)
                product(psW, wl[:, 2, :], sg, P)
                pe.wait_ge(acts, i * ACTS + 4)
                product(psA, same[:, :], sq, P)
                pe.wait_ge(made, i * MADE + 4)
                pe.sem_inc(w_used, 1)
                pe.wait_ge(rk_ok, i + 1)
                product(psW, same[:, :], cum, P)

        @block.scalar
        def _(act):
            a = Chain(act, acts)
            act.wait_ge(lora_ok, 1)
            act.activation(tw[0:LORA, :], tw[0:LORA, :], ACT.Tanh).then_inc(lora_act, 1)
            act.wait_ge(lora_ok, 3)
            act.activation(sg[:, :], sg[:, :], ACT.Sigmoid).then_inc(lora_act, 1)
            banks = lambda t: t[:, :].rearrange("p (n t) -> p n t", n=NB)
            with act.Fori(0, PAIRS) as i:
                a.loop(i, ACTS)
                act.wait_ge(made, i * MADE + 1)
                a.mark(act.activation(banks(lw), psW[:, :, :], ACT.Sigmoid, bias=par[:, W0, bass.ds(i, 1)]))
                act.wait_ge(made, i * MADE + 2)
                a.mark(act.activation(banks(aa), psA[:, :, :], ACT.Sigmoid, bias=par[:, A0, bass.ds(i, 1)]))
                act.wait_ge(made, i * MADE + 3)
                act.wait_ge(g_free, i * 16)
                a.link(act.copy(banks(go), psW[:, :, :]))
                act.dma_start(Z["rg"][bass.ds(i * P, P), :], go[:, :]).then_inc(g_free, 16)
                act.wait_ge(kk0_ok, i + 1)
                act.wait_ge(g_free, (i + 1) * 16)
                a.mark(act.activation(sq[:, :], kk[:, :], ACT.Square))
                act.wait_ge(made, i * MADE + 4)
                a.link(act.activation(banks(e1), psA[:, :, :], ACT.Sqrt))
                act.wait_ge(cm_ok, i + 1)
                a.mark(act.activation(e1[:, :], cm[:, :], ACT.Exp))
                a.mark(act.activation(e2[:, :], cm[:, :], ACT.Exp, scale=-1.0))
                a.mark(act.activation(lw[:, :], lw[:, :], ACT.Exp))
                act.activation(dec[:, 0, :], dec[:, 0, :], ACT.Exp)
                a.mark(act.activation(dec[:, 1, :], dec[:, 1, :], ACT.Exp))
                a.end(PAIRS)

        @block.vector
        def _(dve):
            v = Chain(dve, vec)

            def shift(out, src, m, n=P):
                v.link(dve.tensor_tensor(dif[0:n, :], src[0:n, 0:S], src[0:n, 1:1 + S], ALU.subtract))
                v.link(dve.scalar_tensor_tensor(out=out[0:n, :], in0=dif[0:n, :], scalar=m,
                                                in1=src[0:n, 1:1 + S], op0=ALU.mult, op1=ALU.add))

            dve.wait_ge(init, 6)
            dve.wait_ge(lora_in, 48)
            dve.wait_ge(par_in, 16 * 7)
            shift(tw, z3[0], mu_l[:, 0:1], LORA)
            dve.sem_inc(lora_ok, 1)
            shift(zas, z3[1], mu_l[:, 1:2], LORA)
            shift(sg, z3[2], mu[:, RW_IN // P - 1:RW_IN // P])
            dve.sem_inc(lora_ok, 2)
            dve.sem_inc(z_used, 1)
            chunks = lambda t: t[:, :].rearrange("p (c t) -> p c t", t=CH)
            with dve.Fori(0, PAIRS) as i:
                v.loop(i, 20)
                dve.wait_ge(loads, (i + 1) * 96)
                dve.wait_ge(stored, i * 16 * STORES)
                shift(cum, z3[0], mu[:, bass.ds(i, 1)])
                shift(zk, z3[1], mu[:, bass.ds(i + PAIRS, 1)])
                shift(vt, z3[2], mu[:, bass.ds(i + 2 * PAIRS, 1)])
                v.link(dve.tensor_copy(ar[:, :, 1, :], chunks(cum)))
                dve.sem_inc(z_used, 1)
                v.link(dve.tensor_scalar(kk[:, :], zk[:, :], par[:, K_K, bass.ds(i, 1)], None, ALU.mult))
                dve.sem_inc(kk0_ok, 1)
                dve.wait_ge(acts, i * ACTS + 1)
                v.link(dve.tensor_scalar(lw[:, :], lw[:, :], -DECAY_SCALE, None, ALU.mult))
                v.link(dve.tensor_tensor_scan(cum[:, :], reset[:, :], lw[:, :], 0.0, ALU.mult, ALU.add))
                mid = chunks(cum)[:, :, CH // 2 - 1:CH // 2]
                v.link(dve.tensor_tensor(chunks(cm), chunks(cum), mid.to_broadcast([P, NCH, CH]), ALU.subtract))
                dve.tensor_copy(dec[:, 0, :].rearrange("p (c o) -> p c o", o=1), mid)
                dve.tensor_copy(dec[:, 1, :].rearrange("p (c o) -> p c o", o=1), chunks(cm)[:, :, CH - 1:CH])
                v.link(dve.tensor_tensor(lw[:, :], cm[:, :], lw[:, :], ALU.subtract))
                dve.wait_ge(acts, i * ACTS + 5)
                v.link(dve.tensor_scalar(dif[:, :], e1[:, :], 1e-12, None, ALU.max))
                dve.sem_inc(cm_ok, 1)
                v.link(dve.reciprocal(dif[:, :], dif[:, :]))
                v.link(dve.tensor_tensor(kk[:, :], kk[:, :], dif[:, :], ALU.mult))
                dve.wait_ge(acts, i * ACTS + 2)
                v.link(dve.tensor_scalar(dif[:, :], aa[:, :], -1.0, par[:, K_A, bass.ds(i, 1)], ALU.add, ALU.mult))
                v.link(dve.scalar_tensor_tensor(out=zk[:, :], in0=dif[:, :], scalar=1.0, in1=zk[:, :],
                                                op0=ALU.add, op1=ALU.mult))
                v.link(dve.scalar_tensor_tensor(out=chunks(cum), in0=ar[:, :, 1, :], scalar=par[:, R_K, bass.ds(i, 1)],
                                                in1=chunks(zk), op0=ALU.mult, op1=ALU.mult))
                dve.wait_ge(acts, i * ACTS + 3)
                dve.sem_inc(rk_ok, 1)
                v.mark(dve.tensor_tensor(aa[:, :], kk[:, :], aa[:, :], ALU.mult))
                dve.wait_ge(acts, i * ACTS + 9)
                v.wait()
                dve.tensor_tensor(bt[:, :], aa[:, :], e2[:, :], ALU.mult)
                dve.tensor_tensor(kt[:, :], zk[:, :], e2[:, :], ALU.mult)
                dve.scalar_tensor_tensor(out=ar[:, :, 0, :], in0=chunks(kk), scalar=-1.0, in1=chunks(lw),
                                         op0=ALU.mult, op1=ALU.mult)
                dve.tensor_tensor(ar[:, :, 1, :], ar[:, :, 1, :], chunks(e1), ALU.mult)
                dve.wait_ge(made, (i + 1) * MADE)
                v.link(dve.tensor_tensor(dif[:, :].rearrange("p (n t) -> p n t", n=NB), psW[:, :, :],
                                         vt[:, :].rearrange("p (n t) -> p n t", n=NB), ALU.mult))
                dve.sem_inc(bon_ok, 1)
                dve.sem_inc(out_ok, 1)
                v.end(PAIRS)


LEVELS = 7


def stage_rwkv_scan(nc, A, Z):
    H, HG = RW_HEADS, 4
    with ExitStack() as ctx:
        st = Stage(nc, ctx, "rs")
        ar = st.sb("ar", [HD, 2, H, 2, CH])
        bkv = st.sb("bkv", [HD, 2, 3, H, CH])
        tok = st.sb("tok", [P, 3, H, HD])
        M = st.sb("M", [P, H, 4, CH])
        Lm = st.sb("Lm", [P, 2, HG, CH])
        X = st.sb("X", [P, 2, HG, CH])
        inv = st.sb("inv", [P, 2, HG, CH])
        invT = st.sb("invT", [P, 2, HG, CH])
        Wt, U = st.sb("W", [P, H, HD]), st.sb("U", [P, H, HD])
        state, mid = st.sb("state", [HD, H, HD]), st.sb("mid", [HD, H, HD])
        o = st.sb("o", [HD, H, CH])
        dec = st.sb("dec", [HD, H, 2, NCH])
        ident = st.sb("ident", [P, P])
        row, col, row_s, col_s = (st.sb(n, [P, P], I32) for n in ("row", "col", "row_s", "col_s"))
        upper = st.sb("upper", [P, 4, CH])
        block_of = st.sb("block_of", [P, LEVELS + 1, CH])
        join = st.sb("join", [P, LEVELS, CH])
        bank = st.ps("bank", [P, 8, 512])
        XB, DB, EB, SCORE, WB, UB, OB, SB = (0, 1), (2, 3), (4, 5), (3, 4, 5), 6, 7, (0, 1), 2
        loads = st.sems("loads", 2)
        ld_used, dec_in, id_ok, setup, tables, turned, scored = (
            st.sem(n) for n in ("ld_used", "dec_in", "id_ok", "setup", "tables", "turned", "scored"))
        x_made, d_made, e_made, w_made, u_made, o_made, s_made = (
            st.sem(n) for n in ("x_made", "d_made", "e_made", "w_made", "u_made", "o_made", "s_made"))
        tok_ok, m_ok, l_ok, x_ok, d_ok, e_ok, w_ok, u_ok, o_ok, s_ok, mid_ok = (
            st.sem(n) for n in ("tok_ok", "m_ok", "l_ok", "x_ok", "d_ok", "e_ok", "w_ok", "u_ok", "o_ok", "s_ok", "mid_ok"))
        o_out = st.sem("o_out")
        block = st.block()
        heads = lambda t: t.rearrange("(h d) s -> d h s", h=H)

        @block.sync
        def _(sync):
            sync.dma_start(dec[:, :, :, :], Z["rdec"].rearrange("(h d) a c -> d h a c", h=H)).then_inc(dec_in, 16)
            with sync.Fori(0, NCH // 2) as i:
                for k in range(2):
                    c = 2 * i + k
                    sync.wait_ge(ld_used, c + 1)
                    for h2 in range(2):
                        sync.dma_start(ar[:, k, 4 * h2:4 * h2 + 4, :, :],
                                       Z["rar"].rearrange("(h d) c a t -> d h c a t", h=H)[:, 4 * h2:4 * h2 + 4, bass.ds(c, 1), :, :]
                                       .rearrange("d h c a t -> d h (c a t)")).then_inc(loads[k], 16)
                    for n, name in enumerate(("rb", "rk", "rv")):
                        sync.dma_start(bkv[:, k, n, :, :], heads(Z[name])[:, :, bass.ds(c * CH, CH)]).then_inc(loads[k], 16)

        @block.gpsimd
        def _(pool):
            build_identity(pool, ident, id_ok)
            pool.iota(row[:, :], [[0, P]], base=0, channel_multiplier=1).then_inc(setup, 1)
            pool.iota(col[:, :], [[1, P]], base=0, channel_multiplier=0).then_inc(setup, 1)
            pool.wait_ge(tables, 1)
            with pool.Fori(0, NCH // 2) as i:
                for k in range(2):
                    c = 2 * i + k
                    for lev in range(LEVELS):
                        for g in range(2):
                            if lev == 0:
                                pool.wait_ge(m_ok, 8 * c + 4 * g + 4)
                            pool.wait_ge(x_made, 14 * c + 2 * lev + g)
                            if lev == 1:
                                pool.wait_ge(e_ok, 14 * c + g + 1)
                            pool.tensor_tensor(Lm[:, g, :, :], M[:, 4 * g:4 * g + 4, 0, :],
                                               join[:, lev:lev + 1, :].to_broadcast([P, HG, CH]),
                                               ALU.mult).then_inc(l_ok, 1)

        @block.tensor
        def _(pe):
            pe.sem_inc(ld_used, 2)
            pe.wait_ge(id_ok, 2)
            with pe.Fori(0, NCH // 2) as i:
                for k in range(2):
                    c = 2 * i + k
                    pe.wait_ge(loads[k], (i + 1) * 80)
                    pe.wait_ge(o_ok, c)
                    pe.wait_ge(s_ok, c + 1)
                    steady(pe, Z)
                    for n in range(3):
                        for h in range(H):
                            ins = pe.transpose(bank[:, n, h * HD:(h + 1) * HD], bkv[:, k, n, h, :], ident[0:HD, 0:HD])
                        ins.then_inc(turned, 1)
                    for h in range(H):
                        if h >= 3:
                            pe.wait_ge(m_ok, 8 * c + h - 2)
                        b = SCORE[h % 3]
                        arh = ar[:, k, h, :, :].rearrange("d a t -> d (a t)")
                        pe.matmul(bank[:, b, 0:2 * CH], bkv[:, k, 0, h, :], arh, start=True, stop=True)
                        pe.matmul(bank[:, b, 2 * CH:4 * CH], bkv[:, k, 1, h, :], arh, start=True, stop=True).then_inc(scored, 1)
                    pe.wait_ge(m_ok, 8 * c + 8)
                    for g in range(2):
                        pe.wait_ge(l_ok, 14 * c + g + 1)
                        if g == 0:
                            pe.wait_ge(tok_ok, 3 * c + 3)
                        for h in range(HG):
                            ins = pe.matmul(bank[:, DB[g], h * CH:(h + 1) * CH], Lm[:, g, h, :], ident[:, :],
                                            start=True, stop=True)
                        ins.then_inc(d_made, 1)
                        pe.wait_ge(d_made, 12 * c + g + 1)
                        pe.sem_inc(x_made, 1)
                    for lev in range(1, LEVELS):
                        for g in range(2):
                            pe.wait_ge(l_ok, 14 * c + 2 * lev + g + 1)
                            pe.wait_ge(d_ok, 12 * c + 2 * lev + g - 1)
                            for h in range(HG):
                                ins = pe.matmul(bank[:, XB[g], h * CH:(h + 1) * CH], Lm[:, g, h, :], inv[:, g, h, :],
                                                start=True, stop=True)
                            ins.then_inc(x_made, 1)
                        for g in range(2):
                            pe.wait_ge(x_ok, 12 * c + 2 * lev + g - 1)
                            pe.wait_ge(e_ok, 14 * c + 2 * lev + g - 1)
                            if lev < LEVELS - 1:
                                for h in range(HG):
                                    ins = pe.matmul(bank[:, DB[g], h * CH:(h + 1) * CH], invT[:, g, h, :], X[:, g, h, :],
                                                    start=True, stop=True)
                                ins.then_inc(d_made, 1)
                            for h in range(HG):
                                ins = pe.matmul(bank[:, EB[g], h * CH:(h + 1) * CH], X[:, g, h, :], invT[:, g, h, :],
                                                start=True, stop=True)
                            ins.then_inc(e_made, 1)
                    pe.wait_ge(mid_ok, c + 1)
                    for h in range(H):
                        pe.matmul(bank[:, WB, h * HD:(h + 1) * HD], ar[:, k, h, 0, :], mid[:, h, :], start=True, stop=False)
                        ins = pe.matmul(bank[:, WB, h * HD:(h + 1) * HD], M[:, h, 2, :], tok[:, 2, h, :],
                                        start=False, stop=True)
                    ins.then_inc(w_made, 1)
                    pe.wait_ge(w_ok, c + 1)
                    pe.wait_ge(e_ok, 14 * c + 14)
                    for h in range(H):
                        ins = pe.matmul(bank[:, UB, h * HD:(h + 1) * HD], invT[:, h // HG, h % HG, :], Wt[:, h, :],
                                        start=True, stop=True)
                    ins.then_inc(u_made, 1)
                    pe.wait_ge(u_ok, c + 1)
                    for h in range(H):
                        pe.matmul(bank[0:HD, SB, h * HD:(h + 1) * HD], tok[:, 0, h, :], U[:, h, :], start=True, stop=False)
                        ins = pe.matmul(bank[0:HD, SB, h * HD:(h + 1) * HD], tok[:, 1, h, :], tok[:, 2, h, :],
                                        start=False, stop=True)
                    ins.then_inc(s_made, 1)
                    for h in range(H):
                        dst = bank[0:HD, OB[h // HG], (h % HG) * CH:(h % HG + 1) * CH]
                        pe.matmul(dst, mid[:, h, :], ar[:, k, h, 1, :], start=True, stop=False)
                        pe.matmul(dst, U[:, h, :], M[:, h, 1, :], start=False, stop=False)
                        ins = pe.matmul(dst, tok[:, 2, h, :], M[:, h, 3, :], start=False, stop=True)
                    ins.then_inc(o_made, 1)
                    pe.wait_ge(o_made, c + 1)
                    pe.sem_inc(ld_used, 1)

        @block.scalar
        def _(act):
            with act.Fori(0, NCH // 2) as i:
                for k in range(2):
                    c = 2 * i + k
                    act.wait_ge(o_made, c)
                    for n in range(3):
                        act.wait_ge(turned, 3 * c + n + 1)
                        act.copy(tok[:, n, :, :].rearrange("p h d -> p (h d)"), bank[:, n, :]).then_inc(tok_ok, 1)
                    for lev in range(1, LEVELS):
                        for g in range(2):
                            act.wait_ge(x_made, 14 * c + 2 * lev + g + 1)
                            act.wait_ge(e_made, 12 * c + 2 * lev - 2 + g)
                            act.copy(X[:, g, :, :].rearrange("p h t -> p (h t)"), bank[:, XB[g], :]).then_inc(x_ok, 1)
                    act.wait_ge(w_made, c + 1)
                    act.copy(Wt[:, :, :].rearrange("p h d -> p (h d)"), bank[:, WB, :]).then_inc(w_ok, 1)
                    act.wait_ge(o_made, c + 1)
                    act.wait_ge(o_out, c * 16)
                    act.copy(o[:, :, :].rearrange("p (b h) t -> p b (h t)", b=2), bank[0:HD, 0:2, :]).then_inc(o_ok, 1)
                    act.wait_ge(o_ok, c + 1)
                    act.dma_start(heads(Z["ro"])[:, :, bass.ds(c * CH, CH)], o[:, :, :]).then_inc(o_out, 16)
            act.wait_ge(o_out, NCH * 16)

        @block.vector
        def _(dve):
            v = Chain(dve, setup)
            v.n = 2
            dve.wait_ge(setup, 2)
            for lev in range(LEVELS + 1):
                v.mark(dve.tensor_scalar(row_s[:, :], row[:, :], lev, None, ALU.arith_shift_right))
                v.link(dve.tensor_scalar(col_s[:, :], col[:, :], lev, None, ALU.arith_shift_right))
                v.link(dve.tensor_tensor(block_of[:, lev, :], row_s[:, :], col_s[:, :], ALU.is_equal))
            for n in range(4):
                v.link(dve.tensor_tensor(upper[:, n, :], col[:, :], row[:, :], ALU.is_ge if n % 2 else ALU.is_gt))
            for lev in range(LEVELS):
                v.link(dve.tensor_tensor(join[:, lev, :], block_of[:, lev + 1, :], block_of[:, lev, :], ALU.subtract))
                v.link(dve.tensor_tensor(join[:, lev, :], join[:, lev, :], upper[:, 0, :], ALU.mult))
            v.link(dve.memset(state[:, :, :], 0.0))
            dve.sem_inc(tables, 1)
            dve.sem_inc(s_ok, 1)
            dve.wait_ge(dec_in, 16)
            dve.wait_ge(id_ok, 2)
            eye = ident[:, :].rearrange("p (o t) -> p o t", o=1).to_broadcast([P, HG, CH])
            flat = lambda t: t.rearrange("p h t -> p (h t)")
            in_bank = lambda b: bank[:, b, :].rearrange("p (h t) -> p h t", h=HG)
            with dve.Fori(0, NCH // 2) as i:
                for k in range(2):
                    c = 2 * i + k
                    dve.wait_ge(s_ok, c + 1)
                    dve.wait_ge(o_made, c)
                    dve.tensor_tensor(mid[:, :, :], state[:, :, :],
                                      dec[:, :, 0, bass.ds(c, 1)].to_broadcast([HD, H, HD]), ALU.mult).then_inc(mid_ok, 1)
                    for h in range(H):
                        dve.wait_ge(scored, 8 * c + h + 1)
                        dve.tensor_tensor(M[:, h, :, :].rearrange("p a t -> p (a t)"), bank[:, SCORE[h % 3], :],
                                          upper[:, :, :].rearrange("p a t -> p (a t)"), ALU.mult).then_inc(m_ok, 1)
                    for g in range(2):
                        dve.wait_ge(l_ok, 14 * c + g + 1)
                        dve.tensor_tensor(invT[:, g, :, :], Lm[:, g, :, :], eye, ALU.add).then_inc(e_ok, 1)
                        dve.wait_ge(d_made, 12 * c + g + 1)
                        dve.tensor_tensor(inv[:, g, :, :], in_bank(DB[g]), eye, ALU.add).then_inc(d_ok, 1)
                    for lev in range(1, LEVELS):
                        for g in range(2):
                            dve.wait_ge(d_ok, 12 * c + 2 * lev + g - 1)
                            dve.wait_ge(e_ok, 14 * c + 2 * lev + g - 1)
                            dve.wait_ge(e_made, 12 * c + 2 * lev + g - 1)
                            if lev < LEVELS - 1:
                                dve.tensor_tensor(inv[:, g, :, :], in_bank(DB[g]), inv[:, g, :, :],
                                                  ALU.add).then_inc(d_ok, 1)
                            dve.tensor_tensor(invT[:, g, :, :], in_bank(EB[g]), invT[:, g, :, :],
                                              ALU.add).then_inc(e_ok, 1)
                    dve.wait_ge(u_made, c + 1)
                    dve.tensor_copy(U[:, :, :].rearrange("p h d -> p (h d)"), bank[:, UB, :]).then_inc(u_ok, 1)
                    dve.wait_ge(s_made, c + 1)
                    dve.tensor_tensor(state[:, :, :].rearrange("p h d -> p (h d)"),
                                      mid[:, :, :].rearrange("p h d -> p (h d)"), bank[0:HD, SB, :], ALU.add).then_inc(tables, 1)
                    dve.wait_ge(tables, c + 2)
                    dve.tensor_tensor(state[:, :, :], state[:, :, :],
                                      dec[:, :, 1, bass.ds(c, 1)].to_broadcast([HD, H, HD]), ALU.mult).then_inc(s_ok, 1)


def stage_rwkv_post(nc, A, Z):
    with ExitStack() as ctx:
        st = Stage(nc, ctx, "rn")
        o, bonus, g, sd = (st.sb(n, [P, 2, S]) for n in ("o", "bonus", "g", "sd"))
        sq = st.sb("sq", [P, S])
        average = st.sb("average", [P, P])
        eps = st.sb("eps", [P, 1])
        par = st.sb("par", [P, 2, PAIRS])
        mean, var = st.ps("mean", [P, NB, 512]), st.ps("var", [P, NB, 512])
        loads, stored = st.sems("loads", 2), st.sems("stored", 2)
        init, par_in, mean_made, var_made, centred, squared, rooted, y_ok, steps = (
            st.sem(n) for n in ("init", "par_in", "mean_made", "var_made", "centred", "squared", "rooted", "y_ok", "steps"))
        block = st.block()
        rows = lambda t, c: t[bass.ds(c * P, P), :]
        banks = lambda t: t.rearrange("p (n t) -> p n t", n=NB)

        @block.sync
        def _(sync):
            for n, name in enumerate(("rw_ln_w", "rw_ln_b")):
                sync.dma_start(par[:, n, :], cols(A[name][0], PAIRS)).then_inc(par_in, 16)
            with sync.Fori(0, PAIRS // 2) as i:
                for k in range(2):
                    sync.wait_ge(stored[k], i * 16)
                    for t, name in ((o, "ro"), (bonus, "rbonus"), (g, "rg")):
                        sync.dma_start(t[:, k, :], rows(Z[name], 2 * i + k)).then_inc(loads[k], 16)

        @block.gpsimd
        def _(pool):
            pool.memset(average[:, :], 0.0).then_inc(init, 1)
            pool.wait_ge(init, 1)
            pool.memset(average[0:HD, 0:HD], 1.0 / HD).then_inc(init, 1)
            pool.memset(average[HD:P, HD:P], 1.0 / HD).then_inc(init, 1)
            pool.wait_ge(init, 3)
            pool.memset(eps[:, :], GN_EPS).then_inc(init, 1)
            with pool.Fori(0, PAIRS // 2) as i:
                for k in range(2):
                    pool.wait_ge(y_ok, 2 * i + k + 1)
                    pool.dma_start(rows(Z["yr"], 2 * i + k), o[:, k, :]).then_inc(stored[k], 16)
            for k in range(2):
                pool.wait_ge(stored[k], PAIRS // 2 * 16)

        @block.tensor
        def _(pe):
            pe.wait_ge(init, 4)
            with pe.Fori(0, PAIRS // 2) as i:
                for k in range(2):
                    pe.wait_ge(loads[k], (i + 1) * 48)
                    pe.wait_ge(centred, 2 * i + k)
                    for n in range(NB):
                        ins = pe.matmul(mean[:, n, :], average[:, :], o[:, k, n * 512:(n + 1) * 512], start=True, stop=True)
                    ins.then_inc(mean_made, 1)
                    pe.wait_ge(squared, 2 * i + k + 1)
                    pe.wait_ge(rooted, 2 * i + k)
                    for n in range(NB):
                        ins = pe.matmul(var[:, n, :], average[:, :], sq[:, n * 512:(n + 1) * 512], start=True, stop=True)
                    ins.then_inc(var_made, 1)

        @block.scalar
        def _(act):
            act.wait_ge(init, 4)
            with act.Fori(0, PAIRS // 2) as i:
                for k in range(2):
                    act.wait_ge(centred, 2 * i + k + 1)
                    act.wait_ge(var_made, 2 * i + k)
                    act.activation(sq[:, :], o[:, k, :], ACT.Square).then_inc(squared, 1)
                    act.wait_ge(var_made, 2 * i + k + 1)
                    act.activation(banks(sd[:, k, :]), var[:, :, :], ACT.Sqrt, bias=eps[:, 0:1]).then_inc(rooted, 1)

        @block.vector
        def _(dve):
            v = Chain(dve, steps)
            dve.wait_ge(par_in, 32)
            with dve.Fori(0, PAIRS // 2) as i:
                v.loop(i, 8)
                for k in range(2):
                    dve.wait_ge(mean_made, 2 * i + k + 1)
                    dve.tensor_tensor(banks(o[:, k, :]), banks(o[:, k, :]), mean[:, :, :], ALU.subtract).then_inc(centred, 1)
                    dve.wait_ge(rooted, 2 * i + k + 1)
                    v.link(dve.reciprocal(sd[:, k, :], sd[:, k, :]))
                    v.link(dve.tensor_tensor(o[:, k, :], o[:, k, :], sd[:, k, :], ALU.mult))
                    v.link(dve.tensor_scalar(o[:, k, :], o[:, k, :], par[:, 0, bass.ds(2 * i + k, 1)],
                                             par[:, 1, bass.ds(2 * i + k, 1)], ALU.mult, ALU.add))
                    v.link(dve.tensor_tensor(o[:, k, :], o[:, k, :], bonus[:, k, :], ALU.add))
                    dve.tensor_tensor(o[:, k, :], o[:, k, :], g[:, k, :], ALU.mult).then_inc(y_ok, 1)
                v.end(PAIRS // 2)


CMP_BLOCK, CMP_STRIDE, SEL_BLOCK, N_SELECT, WINDOW = 32, 16, 64, 8, 512
N_CMP = (S - CMP_BLOCK) // CMP_STRIDE + 1
N_SEL = S // SEL_BLOCK
LOWEST = -3e38
STEPS = 58
SLOPES = [2.0 ** (-8.0 * (h + 1) / NSA_HEADS) for h in range(NSA_HEADS)]


def stage_nsa(nc, A, Z):
    G, R = KV_HEADS, Q_PER_KV
    outer = ExitStack()
    with outer:
        kp = Stage(nc, outer, "at")
        ks_t = kp.sb("ks_t", [P, S])
        kw_t = kp.sb("kw_t", [P, WINDOW + S + P])
        vs = kp.sb("vs", [P, NT, P])
        vw = kp.sb("vw", [P, WINDOW // P + NT, P])
        kcmp = kp.sb("kcmp", [P, P])
        vcmp = kp.sb("vcmp", [P, G, HD])
        ident = kp.sb("ident", [P, P])

        with ExitStack() as ctx:
            st = Stage(nc, ctx, "cp")
            kv = st.sb("kv", [HD, 2, G, S])
            w1 = st.sb("w1", [HD, 2, CMP_BLOCK, HD])
            w2_k = st.sb("w2_k", [HD, G, P])
            w2_v = st.sb("w2_v", [HD, HD])
            pos = st.sb("pos", [HD, 2, CMP_BLOCK])
            pos_p = st.sb("pos_p", [HD, 2])
            hid = st.sb("hid", [HD, 2, G, N_CMP])
            v_raw = st.sb("v_raw", [P, 2, S])
            acc = st.ps("acc", [P, 2, 512])
            out = st.ps("out", [P, 512])
            tp = st.ps("tp", [P, 4, 512])
            in_k, in_v, in_w, id_ok, hid_made, pos_ok, hid_ok, out_made, out_ok, turned, tok_ok, zeros, w2_clear = (
                st.sem(n) for n in ("in_k", "in_v", "in_w", "id_ok", "hid_made", "pos_ok", "hid_ok", "out_made",
                                    "out_ok", "turned", "tok_ok", "zeros", "w2_clear"))
            block = st.block()

            @block.sync
            def _(sync):
                for a, (row, n) in enumerate(((ROW_KC, "k"), (ROW_VC, "v"))):
                    sync.dma_start(w1[:, a, :, :], A[f"cmp_{n}_w1"][0].rearrange("(l d) e -> d l e", d=HD)).then_inc(in_w, 16)
                    sync.dma_start(pos[:, a, :], A[f"cmp_pos_{n}"][0].rearrange("l d -> d l")).then_inc(in_w, 16)
                    sync.dma_start(kv[:, a, :, :], Z["z"][row:row + P, :].rearrange("(g d) s -> d g s", g=G)).then_inc(in_w, 16)
                sync.dma_start(w2_v[:, :], A["cmp_v_w2"][0]).then_inc(in_w, 16)
                sync.wait_ge(w2_clear, 1)
                for g in range(G):
                    sync.dma_start(w2_k[:, g, g * HD:(g + 1) * HD], A["cmp_k_w2"][0]).then_inc(in_w, 16)
                sync.dma_start(v_raw[:, 0, :], Z["z"][ROW_VS:ROW_VS + P, :]).then_inc(in_v, 16)
                sync.dma_start(v_raw[:, 1, :], Z["z"][ROW_VW:ROW_VW + P, :]).then_inc(in_v, 16)
                sync.dma_start(ks_t[:, :], Z["z"][ROW_KS:ROW_KS + P, :]).then_inc(in_k, 16)
                sync.dma_start(kw_t[:, WINDOW:WINDOW + S], Z["z"][ROW_KW:ROW_KW + P, :]).then_inc(in_k, 16)
                sync.wait_ge(in_k, 32)

            @block.gpsimd
            def _(pool):
                build_identity(pool, ident, id_ok)
                pool.memset(w2_k[:, :, :], 0.0).then_inc(w2_clear, 1)
                pool.memset(kw_t[:, 0:WINDOW], 0.0).then_inc(zeros, 1)
                pool.memset(kw_t[:, WINDOW + S:WINDOW + S + P], 0.0).then_inc(zeros, 1)
                pool.memset(vw[:, 0:WINDOW // P, :], 0.0).then_inc(zeros, 1)
                pool.wait_ge(zeros, 3)

            @block.tensor
            def _(pe):
                pe.wait_ge(in_w, 16 * 9)
                for a in range(2):
                    for g in range(G):
                        for l in range(CMP_BLOCK):
                            pe.matmul(acc[0:HD, a, g * P:g * P + N_CMP], w1[:, a, l, :],
                                      kv[:, a, g, l:l + CMP_STRIDE * (N_CMP - 1) + 1:CMP_STRIDE],
                                      start=(l == 0), stop=(l == CMP_BLOCK - 1))
                    for l in range(CMP_BLOCK):
                        ins = pe.matmul(acc[0:HD, a, 2 * P:2 * P + 1], w1[:, a, l, :], pos[:, a, l:l + 1],
                                        start=(l == 0), stop=(l == CMP_BLOCK - 1))
                    ins.then_inc(hid_made, 1)
                pe.wait_ge(id_ok, 2)
                pe.wait_ge(in_v, 32)
                for n in range(8):
                    if n >= 4:
                        pe.wait_ge(tok_ok, n - 3)
                    for t in range(4):
                        ins = pe.transpose(tp[:, n % 4, t * P:(t + 1) * P],
                                           v_raw[:, n // 4, (n % 4 * 4 + t) * P:(n % 4 * 4 + t + 1) * P], ident[:, :])
                    ins.then_inc(turned, 1)
                pe.wait_ge(hid_ok, 2 * G)
                for g in range(G):
                    pe.matmul(out[:, 0:N_CMP], w2_k[:, g, :], hid[:, 0, g, :], start=(g == 0), stop=(g == G - 1))
                for g in range(G):
                    ins = pe.matmul(out[0:N_CMP, (2 + g) * P:(2 + g) * P + HD], hid[:, 1, g, :], w2_v[:, :],
                                    start=True, stop=True)
                ins.then_inc(out_made, 1)

            @block.scalar
            def _(act):
                for a in range(2):
                    act.wait_ge(hid_made, a + 1)
                    act.copy(pos_p[:, a:a + 1], acc[0:HD, a, 2 * P:2 * P + 1]).then_inc(pos_ok, 1)
                    act.wait_ge(pos_ok, a + 1)
                    for g in range(G):
                        act.activation(hid[:, a, g, :], acc[0:HD, a, g * P:g * P + N_CMP], ACT.Gelu_apprx_tanh,
                                       bias=pos_p[:, a:a + 1]).then_inc(hid_ok, 1)

            @block.vector
            def _(dve):
                for n in range(8):
                    dve.wait_ge(turned, n + 1)
                    dst = vs[:, n * 4:n * 4 + 4, :] if n < 4 else vw[:, n * 4 - 12:n * 4 - 8, :]
                    dve.tensor_copy(dst, tp[:, n % 4, :].rearrange("p (t c) -> p t c", t=4)).then_inc(tok_ok, 1)
                dve.wait_ge(out_made, 1)
                dve.tensor_copy(kcmp[:, 0:N_CMP], out[:, 0:N_CMP]).then_inc(out_ok, 1)
                for g in range(G):
                    dve.tensor_copy(vcmp[0:N_CMP, g, :], out[0:N_CMP, (2 + g) * P:(2 + g) * P + HD]).then_inc(out_ok, 1)
                dve.wait_ge(out_ok, 3)

        with ExitStack() as ctx:
            st = Stage(nc, ctx, "aq")
            WK = WINDOW + P
            WB = WK // P
            t_sel = st.sb("t_sel", [P, S + 1024])
            t_win, t_win0 = st.sb("t_win", [P, WK]), st.sb("t_win0", [P, WK])
            t_pad = st.sb("t_pad", [P, WINDOW + WK])
            t_cmp, t_cmp_t = st.sb("t_cmp", [P, 256]), st.sb("t_cmp_t", [P, N_CMP])
            rows_ok = st.sb("rows_ok", [P, NT + 1])
            keep_t, force_t = st.sb("keep_t", [P, 64]), st.sb("force_t", [P, 64])
            q_scale = st.sb("q_scale", [P, R])
            gate_b = st.sb("gate_b", [P, N_GATE])
            q_raw = st.sb("q_raw", [P, R, P])
            q = st.sb("q", [P, G, R, P])
            g_raw, gates = st.sb("g_raw", [N_GATE, P]), st.sb("gates", [P, N_GATE])
            pc = st.sb("pc", [P, R, P])
            pct = st.sb("pct", [P, R, P])
            oc = st.sb("oc", [P, G, R, HD])
            cst = st.sb("cst", [P, 4, R])
            psum_c = st.sb("psum_c", [P, P + 4])
            imp, imp2, sel = (st.sb(n, [P, N_SEL]) for n in ("imp", "imp2", "sel"))
            top = st.sb("top", [P, 8])
            tg = st.sb("tg", [P, S])
            sc = st.sb("sc", [P, 2, R, S])
            mxc = st.sb("mxc", [P, 4 * R, 4])
            ust = st.sb("ust", [P, 3, 4 * R])
            pt = st.sb("pt", [P, 2, R, P])
            vwin = st.sb("vwin", [P, WB, P])
            oT = st.sb("oT", [HD, R, P])
            part = st.sb("part", [P, R, HD])
            y, yT = st.sb("y", [P, NSA_W]), st.sb("yT", [P, NSA_W // P, P])
            s_bank, t_bank = st.ps("s_bank", [P, 2, 512]), st.ps("t_bank", [P, 2, 512])
            o_bank, back = st.ps("o_bank", [P, 2, 512]), st.ps("back", [P, 512])
            misc = st.ps("misc", [P, 512])
            tabs, tab_ok, small_in, q_in, q_used, q_ok, g_in, g_used = (
                st.sem(n) for n in ("tabs", "tab_ok", "small_in", "q_in", "q_used", "q_ok", "g_in", "g_used"))
            s_made, s_read, max_ok, exp_ok, turned, pt_a, pt_v, pv_made = (
                st.sem(n) for n in ("s_made", "s_read", "max_ok", "exp_ok", "turned", "pt_a", "pt_v", "pv_made"))
            misc_made, misc_read, cmax_ok, cexp_ok, pc_ok, y_ok, y_out, vec = (
                st.sem(n) for n in ("misc_made", "misc_read", "cmax_ok", "cexp_ok", "pc_ok", "y_ok", "y_out", "vec"))
            gate_ok, gated, ot_ok, back_made, back_read, win_used, win_ok = (
                st.sem(n) for n in ("gate_ok", "gated", "ot_ok", "back_made", "back_read", "win_used", "win_ok"))
            block = st.block()
            UNITS = 2 * G
            FRONT = 3
            MISC = 2 + G * FRONT

            def n_blocks(j, grp):
                return 4 * (grp + 1) if j % 2 else WB

            def runs(j, grp):
                widths = [512] * (grp + 1) if j % 2 else [WINDOW, P]
                return [(h, r, wd) for h in range(R) for r, wd in enumerate(widths)]

            def made_in(j, k, grp):
                rs = runs(j + 1, grp)
                return [(i, run) for i, run in enumerate(rs) if i * (n_blocks(j, grp) - 1) // len(rs) == k]

            def last_run(h, r, j, grp):
                return r == (grp if j % 2 else 1)

            def by_dve(j, k):
                return k % 2 == 1 and (j % 2 == 0 or k >= 5)

            class Tile:

                def __init__(self, grp, tau):
                    def each(f):
                        per = [f(g) for g in range(grp + 1)]
                        return 4 * sum(per[:-1]) + tau * per[-1]

                    flags = lambda g: [by_dve(j, k) for j in range(UNITS) for k in range(n_blocks(j, g))]
                    self.t, self.grp, self.flags = tau + 4 * grp, grp, flags(grp)
                    self.blocks = each(lambda g: len(flags(g)))
                    self.v = each(lambda g: sum(flags(g)))
                    self.a = each(lambda g: len(flags(g)) - sum(flags(g)))
                    self.runs = 2 * R + each(lambda g: sum(len(runs(j + 1, g)) for j in range(UNITS)))
                    self.misc = FRONT + self.t * MISC

                def block(self, j, k):
                    return sum(n_blocks(i, self.grp) for i in range(j)) + k

                def run(self, j, i):
                    return sum(len(runs(n + 1, self.grp)) for n in range(j)) + i

                def wait_taken(self, eng, n):
                    if self.flags[n]:
                        eng.wait_ge(pt_v, self.v + sum(self.flags[:n + 1]))
                    else:
                        eng.wait_ge(pt_a, self.a + n + 1 - sum(self.flags[:n + 1]))

            @block.sync
            def _(sync):
                sync.dma_start(gate_b[:, :], A["nsa_gate_b"][0].partition_broadcast(P)).then_inc(small_in, 16)

                def load_q(t, at):
                    sync.wait_ge(q_used, t + 1)
                    steady(sync, Z)
                    for g in range(G):
                        rows = Z["z"][ROW_Q + g * R * HD:ROW_Q + (g + 1) * R * HD, :].rearrange("(h d) s -> d h s", d=HD)
                        sync.dma_start(q_raw[g * HD:(g + 1) * HD, :, :], rows[:, :, at]).then_inc(q_in, 16)

                with sync.Fori(0, NT) as t:
                    load_q(t, bass.ds(t * P, P))
                    sync.wait_ge(g_used, t + 1)
                    steady(sync, Z)
                    sync.dma_start(g_raw[:, :], Z["gate"][:, bass.ds(t * P, P)]).then_inc(g_in, 16)
                load_q(NT, slice(0, P))

            @block.gpsimd
            def _(pool):
                n = [0]

                def step(ins):
                    ins.then_inc(tabs, 1)
                    n[0] += 1
                    pool.wait_ge(tabs, n[0])

                def masked(t, pattern, base, cm, fill, op=ALU.is_ge, part=slice(0, P)):
                    step(pool.affine_select(out=t[part, :], in_=t[part, :], compare_op=op, fill=fill, base=base,
                                            pattern=pattern, channel_multiplier=cm))

                step(pool.memset(q[:, :, :, :], 0.0))
                step(pool.memset(y[:, :], 0.0))
                w = S + 1024
                step(pool.iota(t_sel[:, :], [[1, w]], base=-S, channel_multiplier=-1, allow_small_or_imprecise_dtypes=True))
                masked(t_sel, [[-1, w]], S, 1, NEG)
                step(pool.iota(t_win[:, :], [[1, WK]], base=-WINDOW, channel_multiplier=-1, allow_small_or_imprecise_dtypes=True))
                masked(t_win, [[-1, WK]], WINDOW, 1, NEG)
                masked(t_win, [[1, WK]], -1, -1, NEG)
                step(pool.memset(t_pad[:, 0:WINDOW], NEG))
                step(pool.memset(t_pad[:, WINDOW:WINDOW + WK], 0.0))
                step(pool.iota(t_cmp[:, :], [[CMP_STRIDE, 256]], base=-S, channel_multiplier=-1, allow_small_or_imprecise_dtypes=True))
                step(pool.tensor_scalar(t_cmp[:, :], t_cmp[:, :], 0.5 * (CMP_BLOCK - 1), 1.0, ALU.add, ALU.mult))
                masked(t_cmp, [[-CMP_STRIDE, 256]], S - (CMP_BLOCK - 1), 1, NEG)
                step(pool.memset(rows_ok[:, :], 1.0))
                masked(rows_ok, [[P, NT + 1]], -(CMP_BLOCK - 1), 1, 0.0)
                step(pool.memset(keep_t[:, :], 1.0))
                step(pool.memset(force_t[:, :], -FORCE))
                for h in range(2):
                    half = slice(h * 64, h * 64 + 64)
                    masked(keep_t, [[-1, 64]], 30 + h, 0, 0.0, part=half)
                    masked(force_t, [[1, 64]], -33 - h, 0, FORCE, part=half)
                    masked(force_t, [[1, 64]], -31 - h, 0, 0.0, part=half)
                for g in range(G):
                    for h in range(R):
                        step(pool.memset(q_scale[g * HD:(g + 1) * HD, h:h + 1], HD ** -0.5 / SLOPES[g * R + h]))
                step(pool.memset(psum_c[:, :], 0.0))
                pool.sem_inc(tab_ok, 1)
                with pool.Fori(0, NT) as t:
                    pool.wait_ge(win_used, t)
                    steady(pool, Z)
                    pool.tensor_copy(vwin[:, :, :], vw[:, bass.ds(t, WB), :]).then_inc(win_ok, 1)

            @block.tensor
            def _(pe):
                def use_misc(n, steps):
                    pe.wait_ge(misc_read, n)
                    for ins in steps:
                        last = ins
                    last.then_inc(misc_made, 1)

                def front(stage, g, f, n):
                    if stage == 0:
                        use_misc(n, (pe.matmul(misc[:, h * P:h * P + N_CMP], q[:, g, h, :], kcmp[:, 0:N_CMP], start=True, stop=True)
                                     for h in range(R)))
                    if stage == 2:
                        pe.wait_ge(pc_ok, f + 1)
                        use_misc(n + 1, (pe.transpose(misc[0:N_CMP, h * P:(h + 1) * P], pc[:, h, 0:N_CMP], ident[:, :])
                                         for h in range(R)))
                    if stage == 3:
                        use_misc(n + 2, (pe.matmul(misc[:, h * HD:(h + 1) * HD], pct[0:N_CMP, h, :], vcmp[0:N_CMP, g, :],
                                                   start=True, stop=True) for h in range(R)))

                def score(j, i, at, run, t):
                    h, r, wd = run
                    keys = ks_t[:, r * 512:r * 512 + wd] if j % 2 else kw_t[:, bass.ds(t * P + r * 512, wd)]
                    pe.matmul(s_bank[:, i % 2, 0:wd], q[:, j // 2, h, :], keys, start=True, stop=True).then_inc(s_made, 1)

                def turn_back(j, t):
                    pe.wait_ge(ot_ok, UNITS * t + j + 1)
                    pe.wait_ge(back_read, UNITS * t + j)
                    steady(pe, Z)
                    for h in range(R):
                        ins = pe.transpose(back[:, h * HD:(h + 1) * HD], oT[:, h, :], ident[0:HD, 0:HD])
                    ins.then_inc(back_made, 1)

                def turn_y(t, n):
                    pe.wait_ge(y_ok, G * t)
                    use_misc(n, (pe.transpose(misc[:, c * P:(c + 1) * P], y[:, c * P:(c + 1) * P], ident[:, :])
                                 for c in range(NSA_W // P)))

                pe.wait_ge(tab_ok, 1)
                pe.wait_ge(q_ok, G)
                front(0, 0, 0, 0)
                for i, run in enumerate(runs(0, 0)):
                    if i >= 2:
                        pe.wait_ge(s_read, i - 1)
                    score(0, i, i, run, 0)
                front(2, 0, 0, 0)
                front(3, 0, 0, 0)
                for grp in range(NT // 4):
                    with pe.Fori(0, 4) as tau:
                        T = Tile(grp, tau)
                        t = T.t
                        for j in range(UNITS):
                            nb = n_blocks(j, grp)
                            for k in range(nb + 1):
                                n = T.block(j, k)
                                if k < nb:
                                    if n >= 2:
                                        T.wait_taken(pe, n - 2)
                                    else:
                                        pe.wait_ge(pt_a, T.a)
                                        pe.wait_ge(pt_v, T.v)
                                    for h in range(R):
                                        if k == 0:
                                            pe.wait_ge(exp_ok, UNITS * R * t + R * j + h + 1)
                                        ins = pe.transpose(t_bank[:, n % 2, h * P:(h + 1) * P],
                                                           sc[:, j % 2, h, k * P:(k + 1) * P], ident[:, :])
                                    ins.then_inc(turned, 1)
                                if k == 0 and j > 0:
                                    turn_back(j - 1, t)
                                if k == 0 and j == 3:
                                    pe.sem_inc(win_used, 1)
                                    pe.wait_ge(q_ok, G * t + 2 * G)
                                if j == 0 and k == 1:
                                    turn_y(t, T.misc)
                                if j == 0 and k == 2:
                                    pe.wait_ge(g_in, t * 16 + 16)
                                    pe.wait_ge(misc_read, T.misc + 1)
                                    steady(pe, Z)
                                    use_misc(T.misc + 1, [pe.transpose(misc[:, 0:N_GATE], g_raw[:, :], ident[0:N_GATE, 0:N_GATE])])
                                if j == 1:
                                    front(k, 1, 2 * t + 1, T.misc + 2)
                                if j == 3:
                                    front(k, 0, 2 * t + 2, T.misc + 2 + FRONT)
                                for i, run in made_in(j, k, grp):
                                    i = T.run(j, i)
                                    pe.wait_ge(s_read, T.runs + i - 1)
                                    score((j + 1) % UNITS, i, i, run, t + (j + 1) // UNITS)
                                if k >= 1:
                                    T.wait_taken(pe, n - 1)
                                    if j == 0 and k == 1:
                                        pe.wait_ge(win_ok, t + 1)
                                    g = j // 2
                                    val = (vs if j % 2 else vwin)[:, k - 1, g * HD:(g + 1) * HD]
                                    pe.matmul(o_bank[0:HD, j % 2, :], val, pt[:, (n - 1) % 2, :, :].rearrange("p h t -> p (h t)"),
                                              start=(k == 1), stop=(k == nb)).then_inc(pv_made, 1)
                        turn_back(UNITS - 1, t)
                turn_y(NT, FRONT + NT * MISC)

            @block.scalar
            def _(act):
                def front(stage, f, n):
                    if stage == 1:
                        act.wait_ge(cmax_ok, f + 1)
                        for h in range(R):
                            ins = act.activation(pc[:, h, 0:N_CMP], pc[:, h, 0:N_CMP], ACT.Exp,
                                                 bias=cst[:, 1, h:h + 1], accum_out=cst[:, 2, h:h + 1])
                        ins.then_inc(cexp_ok, 1)
                    if stage == 2:
                        act.wait_ge(misc_made, n + 2)
                        act.copy(pct[0:N_CMP, :, :].rearrange("p h t -> p (h t)"), misc[0:N_CMP, :]).then_inc(misc_read, 1)

                def exp(j, h, m, width):
                    act.wait_ge(max_ok, m + 1)
                    act.activation(sc[:, j % 2, h, 0:width], sc[:, j % 2, h, 0:width], ACT.Exp,
                                   bias=ust[:, 0, R * j + h:R * j + h + 1],
                                   accum_out=ust[:, 1, R * j + h:R * j + h + 1]).then_inc(exp_ok, 1)

                def store_y(t, n):
                    act.wait_ge(misc_made, n + 1)
                    act.wait_ge(y_out, t * 16)
                    act.copy(yT[:, :, :].rearrange("p c t -> p (c t)"), misc[:, :]).then_inc(misc_read, 1)
                    act.wait_ge(misc_read, n + 1)
                    act.dma_start(Z["yn"].rearrange("(c p) s -> p c s", p=P)[:, :, bass.ds(t * P, P)],
                                  yT[:, :, :]).then_inc(y_out, 16)

                act.wait_ge(tab_ok, 1)
                act.wait_ge(small_in, 16)
                front(1, 0, 0)
                for h in range(R):
                    exp(0, h, h, WK)
                front(2, 0, 0)
                for grp in range(NT // 4):
                    with act.Fori(0, 4) as tau:
                        T = Tile(grp, tau)
                        t = T.t
                        for j in range(UNITS):
                            nb = n_blocks(j, grp)
                            for k in range(nb + 1):
                                n = T.block(j, k)
                                if k < nb and not by_dve(j, k):
                                    act.wait_ge(turned, T.blocks + n + 1)
                                    act.wait_ge(pv_made, T.blocks + max(n - 1, 0))
                                    act.copy(pt[:, n % 2, :, :].rearrange("p h t -> p (h t)"), t_bank[:, n % 2, :]).then_inc(pt_a, 1)
                                if j == 0 and k == 1:
                                    store_y(t, T.misc)
                                if j == 0 and k == 3:
                                    act.wait_ge(gate_ok, t + 1)
                                    act.activation(gates[:, :], gates[:, :], ACT.Tanh, scale=0.5).then_inc(gated, 1)
                                if j == 1:
                                    front(k, 2 * t + 1, T.misc + 2)
                                if j == 3:
                                    front(k, 2 * t + 2, T.misc + 2 + FRONT)
                                for i, (h, r, wd) in made_in(j, k - 1, grp):
                                    if last_run(h, r, j + 1, grp):
                                        exp((j + 1) % UNITS, h, UNITS * R * t + R * (j + 1) + h, WK if j % 2 else 512 * (grp + 1))
                            act.wait_ge(pv_made, T.blocks + T.block(j, nb))
                            act.wait_ge(back_made, UNITS * t + j)
                            act.copy(oT[:, :, :].rearrange("p h t -> p (h t)"), o_bank[0:HD, j % 2, :]).then_inc(ot_ok, 1)
                store_y(NT, FRONT + NT * MISC)
                act.wait_ge(y_out, NT * 16 + 16)

            @block.vector
            def _(dve):
                v = Chain(dve, vec)

                def take_q(t):
                    dve.wait_ge(q_in, t * 32 + 32)
                    for g in range(G):
                        own = slice(g * HD, (g + 1) * HD)
                        dve.tensor_tensor(q[own, g, :, :], q_raw[own, :, :],
                                          q_scale[own, :].rearrange("p (h o) -> p h o", o=1).to_broadcast([HD, R, P]),
                                          ALU.mult).then_inc(q_ok, 1)
                    dve.wait_ge(q_ok, G * t + G)
                    dve.sem_inc(q_used, 1)

                def tables(t, first):
                    steady(dve, Z)
                    v.link(dve.tensor_copy(t_cmp_t[:, :], t_cmp[:, bass.ds(P - t * (P // CMP_STRIDE), N_CMP)]))
                    if first:
                        v.link(dve.tensor_tensor(t_win0[:, :], t_win[:, :], t_pad[:, bass.ds(t * P, WK)], ALU.add))

                def compressed_scores(g, f, n):
                    dve.wait_ge(misc_made, n + 1)
                    steady(dve, Z)
                    for h in range(R):
                        ins = dve.tensor_tensor_reduce(
                            out=pc[:, h, 0:N_CMP], in0=misc[:, h * P:h * P + N_CMP], in1=t_cmp_t[:, :],
                            scale=SLOPES[g * R + h], scalar=LOWEST, op0=ALU.add, op1=ALU.max, accum_out=cst[:, 0, h:h + 1])
                    ins.then_inc(misc_read, 1)
                    dve.wait_ge(misc_read, n + 1)
                    dve.tensor_scalar(cst[:, 1, :], cst[:, 0, :], -1.0, None, ALU.mult).then_inc(cmax_ok, 1)

                def compressed_probs(g, f, t):
                    dve.wait_ge(cexp_ok, f + 1)
                    v.link(dve.reciprocal(cst[:, 3, :], cst[:, 2, :]))
                    v.link(dve.tensor_scalar(cst[:, 3, :], cst[:, 3, :], rows_ok[:, bass.ds(t, 1)], None, ALU.mult))
                    for h in range(R):
                        ins = dve.tensor_scalar(pc[:, h, 0:N_CMP], pc[:, h, 0:N_CMP], cst[:, 3, h:h + 1], None, ALU.mult)
                    ins.then_inc(pc_ok, 1)
                    dve.wait_ge(pc_ok, f + 1)

                def select(t, keys):
                    total = psum_c[:, 1:1 + N_CMP]
                    v.link(dve.tensor_tensor(total, pc[:, 0, 0:N_CMP], pc[:, 1, 0:N_CMP], ALU.add))
                    v.link(dve.tensor_tensor(total, total, pc[:, 2, 0:N_CMP], ALU.add))
                    v.link(dve.tensor_tensor(total, total, pc[:, 3, 0:N_CMP], ALU.add))
                    piece = lambda n: psum_c[:, n:n + P - 3:4]
                    v.mark(dve.tensor_tensor(imp2[:, :], piece(0), piece(4), ALU.add))
                    v.link(dve.tensor_tensor(imp[:, :], piece(1), piece(2), ALU.add))
                    v.link(dve.tensor_tensor(imp[:, :], imp[:, :], piece(3), ALU.add))
                    v.link(dve.scalar_tensor_tensor(out=imp[:, :], in0=imp2[:, :], scalar=0.5, in1=imp[:, :],
                                                    op0=ALU.mult, op1=ALU.add))
                    steady(dve, Z)
                    at = bass.ds(32 - 2 * t, N_SEL)
                    v.link(dve.tensor_tensor(imp[:, :], imp[:, :], keep_t[:, at], ALU.mult))
                    v.link(dve.tensor_tensor(imp[:, :], imp[:, :], force_t[:, at], ALU.add))
                    v.link(dve.memset(imp[:, 0:1], FORCE))
                    steady(dve, Z)
                    v.link(dve.max(top[:, :], imp[:, :]))
                    steady(dve, Z)
                    v.link(dve.match_replace(imp2[:, :], top[:, :], imp[:, :], -LOWEST))
                    v.link(dve.tensor_scalar(sel[:, :], imp2[:, :], -LOWEST, NEG, ALU.not_equal, ALU.mult))
                    n = keys // SEL_BLOCK
                    steady(dve, Z)
                    v.link(dve.tensor_tensor(
                        tg[:, 0:keys].rearrange("p (n b) -> p n b", n=n),
                        t_sel[:, bass.ds(S - t * P, keys)].rearrange("p (n b) -> p n b", n=n),
                        sel[:, 0:n].rearrange("p (n o) -> p n o", o=1).to_broadcast([P, n, SEL_BLOCK]), ALU.add))

                def front(stage, g, f, n, t, keys):
                    if stage == 0:
                        compressed_scores(g, f, n)
                    if stage == 1:
                        compressed_probs(g, f, t)
                    if stage == 2:
                        select(t, keys)
                    if stage == 3:
                        dve.wait_ge(misc_made, n + 3)
                        dve.tensor_copy(oc[:, g, :, :].rearrange("p h d -> p (h d)"), misc[:, 0:R * HD]).then_inc(misc_read, 1)
                        dve.wait_ge(misc_read, n + 3)

                def weigh(j, i, run, seen, m, table, last):
                    h, r, wd = run
                    dve.wait_ge(s_made, seen + 1)
                    steady(dve, Z)
                    dve.tensor_tensor_reduce(
                        out=sc[:, j % 2, h, r * 512:r * 512 + wd], in0=s_bank[:, i % 2, 0:wd],
                        in1=table[:, r * 512:r * 512 + wd], scale=SLOPES[j // 2 * R + h],
                        scalar=LOWEST, op0=ALU.add, op1=ALU.max, accum_out=mxc[:, R * j + h, r:r + 1]).then_inc(s_read, 1)
                    if last:
                        dve.wait_ge(s_read, seen + 1)
                        dve.tensor_reduce(ust[:, 0, R * j + h:R * j + h + 1], mxc[:, R * j + h, 0:r + 1], AX.X, ALU.max,
                                          negate=True).then_inc(max_ok, 1)

                def combine(j, t):
                    g, s = j // 2, ust[:, 2, R * j:R * (j + 1)]
                    gate = lambda b: gates[:, 3 * R * g:3 * R * (g + 1)].rearrange("p (h b) -> p b h", b=3)[:, b, :]
                    wide = lambda a: a.rearrange("p (h o) -> p h o", o=1).to_broadcast([P, R, HD])
                    yg = y[:, g * R * HD:(g + 1) * R * HD].rearrange("p (h d) -> p h d", h=R)
                    v.link(dve.reciprocal(s, ust[:, 1, R * j:R * (j + 1)]))
                    v.link(dve.tensor_tensor(s, s, gate(1 if j % 2 else 2), ALU.mult))
                    if j % 2 == 0:
                        for h in range(R):
                            c = 3 * (g * R + h)
                            v.mark(dve.tensor_scalar(yg[:, h, :], oc[:, g, h, :], gates[:, c:c + 1], None, ALU.mult))
                    dve.wait_ge(back_made, UNITS * t + j + 1)
                    v.link(dve.tensor_tensor(part[:, :, :], back[:, 0:R * HD].rearrange("p (h d) -> p h d", h=R), wide(s), ALU.mult))
                    dve.sem_inc(back_read, 1)
                    v.link(dve.tensor_tensor(yg, yg, part[:, :, :], ALU.add))
                    if j % 2:
                        dve.sem_inc(y_ok, 1)

                dve.wait_ge(tab_ok, 1)
                dve.wait_ge(small_in, 16)
                dve.sem_inc(q_used, 1)
                dve.sem_inc(g_used, 1)
                take_q(0)
                tables(0, True)
                front(0, 0, 0, 0, 0, 0)
                for i, (h, r, wd) in enumerate(runs(0, 0)):
                    weigh(0, i, (h, r, wd), i, 0, t_win0, last_run(h, r, 0, 0))
                for stage in (1, 2, 3):
                    front(stage, 0, 0, 0, 0, 512)
                for grp in range(NT // 4):
                    keys = 512 * (grp + 1)
                    with dve.Fori(0, 4) as tau:
                        v.loop(tau, STEPS + (grp == 0))
                        T = Tile(grp, tau)
                        t = T.t
                        win = t_win0 if grp == 0 else t_win
                        for j in range(UNITS):
                            nb = n_blocks(j, grp)
                            dve.wait_ge(turned, T.blocks + T.block(j, 0))
                            if j == 3:
                                take_q(t + 1)
                                tables(t + 1, grp == 0)
                            for k in range(nb + 1):
                                n = T.block(j, k)
                                if k < nb and by_dve(j, k):
                                    dve.wait_ge(turned, T.blocks + n + 1)
                                    dve.wait_ge(pv_made, T.blocks + n - 1)
                                    dve.tensor_copy(pt[:, n % 2, :, :].rearrange("p h t -> p (h t)"), t_bank[:, n % 2, :]).then_inc(pt_v, 1)
                                if k == 1 and j > 0:
                                    combine(j - 1, t)
                                if j == 0 and k == 2:
                                    dve.wait_ge(misc_made, T.misc + 2)
                                    dve.tensor_tensor(gates[:, :], misc[:, 0:N_GATE], gate_b[:, :], ALU.add).then_inc(gate_ok, 1)
                                    dve.wait_ge(gate_ok, t + 1)
                                    dve.sem_inc(misc_read, 1)
                                    dve.sem_inc(g_used, 1)
                                if j == 0 and k == 4:
                                    dve.wait_ge(gated, t + 1)
                                    v.link(dve.tensor_scalar(gates[:, :], gates[:, :], 0.5, 0.5, ALU.mult, ALU.add))
                                if j == 1 and k == 0:
                                    front(0, 1, 2 * t + 1, T.misc + 2, t, keys)
                                if j == 3 and k == 0:
                                    front(0, 0, 2 * t + 2, T.misc + 2 + FRONT, t + 1, 0)
                                for i, (h, r, wd) in made_in(j, k, grp):
                                    i = T.run(j, i)
                                    weigh((j + 1) % UNITS, i, (h, r, wd), T.runs + i, 0, win if j % 2 else tg,
                                          last_run(h, r, j + 1, grp))
                                if j == 1 and k > 0:
                                    front(k, 1, 2 * t + 1, T.misc + 2, t, keys)
                                if j == 3 and k > 0:
                                    front(k, 0, 2 * t + 2, T.misc + 2 + FRONT, t + 1, min(keys + 512, S))
                        combine(UNITS - 1, t)
                        v.end(4)


def stage_mix(nc, A, Z):
    with ExitStack() as ctx:
        st = Stage(nc, ctx, "mx")
        YC = RW_W // P
        up = st.sb("up", [P, 2, YC, D])
        wo = st.sb("wo", [P, DC, D])
        ys = st.sb("ys", [P, 2, YC, 512])
        mg = st.sb("mg", [P, 2, DC, 512])
        res = st.sb("res", [P, 2, D])
        part = st.sb("part", [P, 2, 2, 512])
        mixed = st.sb("mixed", [P, DC, 512])
        ups = st.ps("ups", [P, 2, 2, 512])
        outs = st.ps("outs", [P, 2, 2, 512])
        w_in, y_in, g_in, res_in = st.sem("w_in"), st.sem("y_in"), st.sem("g_in"), st.sems("res_in", 2)
        ups_made, ups_read, sig_ok, mixed_ok, out_made, out_ok, vec = (
            st.sem(n) for n in ("ups_made", "ups_read", "sig_ok", "mixed_ok", "out_made", "out_ok", "vec"))
        stored = st.sems("stored", 2)
        block = st.block()
        TB = 512 // P

        @block.sync
        def _(sync):
            for n, name in enumerate(("w_up_rwkv", "w_up_nsa")):
                sync.dma_start(up[:, n, :, :], A[name][0].rearrange("(c p) n -> p c n", p=P)).then_inc(w_in, 16)
            sync.dma_start(wo[:, :, :], A["w_out"][0].rearrange("(c p) n -> p c n", p=P)).then_inc(w_in, 16)
            with sync.Fori(0, NB) as i:
                sync.wait_ge(ups_made, i * DC)
                for n, (name, lead) in enumerate((("yr", 0), ("yn", P))):
                    sync.dma_start(ys[:, n, :, :], Z[name].rearrange("(c p) s -> p c s", p=P)[:, :, bass.ds(i * 512 + lead, 512)]).then_inc(y_in, 16)
                sync.wait_ge(ups_read, i * DC)
                for n in range(2):
                    sync.dma_start(mg[:, n, :, :], Z["z"][ROW_MERGE + n * D:ROW_MERGE + (n + 1) * D, :]
                                   .rearrange("(c p) s -> p c s", p=P)[:, :, bass.ds(i * 512, 512)]).then_inc(g_in, 16)
                for t in range(TB):
                    tile = i * TB + t
                    sync.wait_ge(stored[t % 2], (i * (TB // 2) + t // 2) * 16)
                    sync.dma_start(res[:, t % 2, :], A["x"][0][bass.ds(tile * P, P), :]).then_inc(res_in[t % 2], 16)

        @block.tensor
        def _(pe):
            pe.wait_ge(w_in, 48)
            with pe.Fori(0, NB) as i:
                pe.wait_ge(y_in, (i + 1) * 32)
                for d in range(DC):
                    pe.wait_ge(ups_read, i * DC + max(d - 1, 0))
                    for n in range(2):
                        for c in range(YC):
                            ins = pe.matmul(ups[:, d % 2, n, :], up[:, n, c, d * P:(d + 1) * P], ys[:, n, c, :],
                                            start=(c == 0), stop=(c == YC - 1))
                    ins.then_inc(ups_made, 1)
                pe.wait_ge(mixed_ok, (i + 1) * DC)
                for t in range(TB):
                    pe.wait_ge(out_ok, i * TB + max(t - 1, 0))
                    for n in range(2):
                        for c in range(DC):
                            ins = pe.matmul(outs[:, t % 2, n, :], mixed[:, c, t * P:(t + 1) * P], wo[:, c, n * 512:(n + 1) * 512],
                                            start=(c == 0), stop=(c == DC - 1))
                    ins.then_inc(out_made, 1)

        @block.scalar
        def _(act):
            with act.Fori(0, NB) as i:
                act.wait_ge(g_in, (i + 1) * 32)
                for d in range(DC):
                    act.activation(mg[:, :, d, :], mg[:, :, d, :], ACT.Sigmoid).then_inc(sig_ok, 1)

        @block.vector
        def _(dve):
            v = Chain(dve, vec)
            with dve.Fori(0, NB) as i:
                v.loop(i, DC)
                for d in range(DC):
                    dve.wait_ge(ups_made, i * DC + d + 1)
                    dve.wait_ge(sig_ok, i * DC + d + 1)
                    dve.wait_ge(mixed_ok, i * DC + max(d - 1, 0))
                    v.link(dve.tensor_tensor(part[:, d % 2, :, :], ups[:, d % 2, :, :], mg[:, :, d, :], ALU.mult))
                    dve.sem_inc(ups_read, 1)
                    if d == 0:
                        dve.wait_ge(out_made, i * TB)
                    dve.tensor_tensor(mixed[:, d, :], part[:, d % 2, 0, :], part[:, d % 2, 1, :], ALU.add).then_inc(mixed_ok, 1)
                for t in range(TB):
                    dve.wait_ge(out_made, i * TB + t + 1)
                    dve.wait_ge(res_in[t % 2], (i * (TB // 2) + t // 2 + 1) * 16)
                    dve.tensor_tensor(res[:, t % 2, :].rearrange("p (n c) -> p n c", n=2), outs[:, t % 2, :, :],
                                      res[:, t % 2, :].rearrange("p (n c) -> p n c", n=2), ALU.add).then_inc(out_ok, 1)
                v.end(NB)

        @block.gpsimd
        def _(pool):
            with pool.Fori(0, NT // 2) as i:
                for k in range(2):
                    pool.wait_ge(out_ok, 2 * i + k + 1)
                    pool.dma_start(Z["x1"][bass.ds((2 * i + k) * P, P), :], res[:, k, :]).then_inc(stored[k], 16)
            for k in range(2):
                pool.wait_ge(stored[k], NT // 2 * 16)


N_GROUPS, PER_GROUP = 4, 8
N_EXPERTS = N_GROUPS * PER_GROUP
D_EXPERT = 512
MAX_BLOCKS = 2 * S // P + N_EXPERTS
N_LOGITS = N_GROUPS + N_EXPERTS


def stage_route(nc, A, Z, keep):
    lg, weight, dest, ends = keep["lg"], keep["weight"], keep["dest"], keep["ends"]
    with ExitStack() as ctx:
        st = Stage(nc, ctx, "ro")
        x_t, xn = st.sb("x", [P, 2, D]), st.sb("xn", [P, 2, D])
        sq = st.sb("sq", [P, D])
        stat = st.sb("stat", [P, 2, 4])
        hT = st.sb("hT", [P, 2, DC, P])
        g_row = st.sb("g", [P, D])
        w_r = st.sb("w_r", [P, DC, N_LOGITS])
        b_r = st.sb("b_r", [P, N_LOGITS])
        ident = st.sb("ident", [P, P])
        zero_i, tok_id = st.sb("zero_i", [P, MAX_BLOCKS + 1], I32), keep["tok_id"]
        tp, lps = st.ps("tp", [P, 2, 2, 512]), st.ps("lps", [P, 2, 512])
        x_in, h_out = st.sems("x_in", 2), st.sems("h_out", 2)
        x_free, w_in, id_ok, squares, roots, ms_ok, vec = (
            st.sem(n) for n in ("x_free", "w_in", "id_ok", "squares", "roots", "ms_ok", "vec"))
        h_ok, turned, ht_ok, l_made, l_ok, cleared, rows_clear = (
            st.sem(n) for n in ("h_ok", "turned", "ht_ok", "l_made", "l_ok", "cleared", "rows_clear"))
        block = st.block()

        @block.sync
        def _(sync):
            sync.dma_start(g_row[:, :], A["g_ffn"][0].partition_broadcast(P)).then_inc(w_in, 16)
            sync.dma_start(w_r[:, :, 0:N_GROUPS], A["w_group"][0].rearrange("(c p) n -> p c n", p=P)).then_inc(w_in, 16)
            sync.dma_start(w_r[:, :, N_GROUPS:N_LOGITS], A["w_router"][0].rearrange("(c p) n -> p c n", p=P)).then_inc(w_in, 16)
            sync.dma_start(b_r[:, 0:N_GROUPS], A["b_group"][0].partition_broadcast(P)).then_inc(w_in, 16)
            sync.dma_start(b_r[:, N_GROUPS:N_LOGITS], A["b_router"][0].partition_broadcast(P)).then_inc(w_in, 16)
            with sync.Fori(0, NT // 2) as i:
                for k in range(2):
                    sync.wait_ge(x_free, 2 * i + k + 1)
                    sync.dma_start(x_t[:, k, :], Z["x1"][bass.ds((2 * i + k) * P, P), :]).then_inc(x_in[k], 16)

        @block.gpsimd
        def _(pool):
            build_identity(pool, ident, id_ok)
            pool.memset(zero_i[:, :], 0).then_inc(cleared, 1)
            pool.iota(tok_id[:, :], [[P, NT]], base=0, channel_multiplier=1).then_inc(cleared, 1)
            pool.wait_ge(cleared, 2)
            pool.dma_start(Z["row_tok"].rearrange("(p b) o -> p (b o)", p=P), zero_i[:, :]).then_inc(rows_clear, 16)
            pool.wait_ge(rows_clear, 16)
            with pool.Fori(0, NT // 2) as i:
                for k in range(2):
                    pool.wait_ge(h_ok, 2 * i + k + 1)
                    pool.dma_start(Z["h2"][bass.ds((2 * i + k) * P, P), :], xn[:, k, :]).then_inc(h_out[k], 16)
            for k in range(2):
                pool.wait_ge(h_out[k], NT // 2 * 16)

        @block.scalar
        def _(act):
            with act.Fori(0, NT // 2) as i:
                for k in range(2):
                    act.wait_ge(x_in[k], (i + 1) * 16)
                    act.wait_ge(squares, 2 * i + k)
                    act.activation(sq[:, :], x_t[:, k, :], ACT.Square, accum_out=stat[:, k, 0:1]).then_inc(squares, 1)
                for k in range(2):
                    act.wait_ge(ms_ok, 2 * i + k + 1)
                    act.activation(stat[:, k, 2:3], stat[:, k, 1:2], ACT.Sqrt).then_inc(roots, 1)
                for k in range(2):
                    act.wait_ge(turned, 2 * i + k + 1)
                    act.wait_ge(l_made, 2 * i + k)
                    act.copy(hT[:, k, :, :].rearrange("p (b c) t -> p b (c t)", b=2), tp[:, k, :, :]).then_inc(ht_ok, 1)

        @block.vector
        def _(dve):
            v = Chain(dve, vec)
            dve.sem_inc(x_free, 2)
            dve.wait_ge(w_in, 80)
            with dve.Fori(0, NT // 2) as i:
                v.loop(i, 4)
                for k in range(2):
                    dve.wait_ge(squares, 2 * i + k + 1)
                    dve.tensor_scalar(stat[:, k, 1:2], stat[:, k, 0:1], 1.0 / D, NORM_EPS, ALU.mult, ALU.add).then_inc(ms_ok, 1)
                for k in range(2):
                    dve.wait_ge(roots, 2 * i + k + 1)
                    v.link(dve.reciprocal(stat[:, k, 3:4], stat[:, k, 2:3]))
                    dve.wait_ge(turned, 2 * i + k)
                    dve.wait_ge(h_out[k], i * 16)
                    v.link(dve.scalar_tensor_tensor(out=xn[:, k, :], in0=x_t[:, k, :], scalar=stat[:, k, 3:4], in1=g_row[:, :],
                                                    op0=ALU.mult, op1=ALU.mult))
                    dve.sem_inc(h_ok, 1)
                    dve.sem_inc(x_free, 1)
                for k in range(2):
                    dve.wait_ge(l_made, 2 * i + k + 1)
                    dve.tensor_tensor(lg[:, bass.ds(2 * i + k, 1), :].rearrange("p o n -> p (o n)"), lps[:, k, 0:N_LOGITS],
                                      b_r[:, :], ALU.add).then_inc(l_ok, 1)
                v.end(NT // 2)
            dve.wait_ge(l_ok, NT)

        @block.tensor
        def _(pe):
            pe.wait_ge(id_ok, 2)
            pe.wait_ge(w_in, 80)
            with pe.Fori(0, NT // 2) as i:
                for k in range(2):
                    pe.wait_ge(h_ok, 2 * i + k + 1)
                    pe.wait_ge(ht_ok, 2 * i)
                    for c in range(DC):
                        ins = pe.transpose(tp[:, k, c // 4, (c % 4) * P:(c % 4 + 1) * P], xn[:, k, c * P:(c + 1) * P], ident[:, :])
                    ins.then_inc(turned, 1)
                for k in range(2):
                    pe.wait_ge(ht_ok, 2 * i + k + 1)
                    pe.wait_ge(l_ok, 2 * i)
                    for c in range(DC):
                        ins = pe.matmul(lps[:, k, 0:N_LOGITS], hT[:, k, c, :], w_r[:, c, :], start=(c == 0), stop=(c == DC - 1))
                    ins.then_inc(l_made, 1)

    with ExitStack() as ctx:
        st = Stage(nc, ctx, "rt")
        E3 = [P, NT, N_EXPERTS]
        small = lambda n: st.sb(n, [P, NT, 1])
        gmax, gsum, g_at, m1, m2, at, ratio, total = (small(n) for n in ("gmax", "gsum", "g_at", "m1", "m2", "at", "ratio", "total"))
        gd, g_one, le, cand, tmp = (st.sb(n, [P, NT, PER_GROUP]) for n in ("gd", "g_one", "le", "cand", "tmp"))
        one = [st.sb(f"one{n}", [P, NT, PER_GROUP]) for n in range(2)]
        hot = [st.sb(f"hot{n}", E3) for n in range(2)]
        both, tot, base, prod = (st.sb(n, E3) for n in ("both", "tot", "base", "prod"))
        count, ends_f, nb_f = (st.sb(n, [P, N_EXPERTS]) for n in ("count", "ends_f", "nb_f"))
        nb_i = st.sb("nb_i", [P, N_EXPERTS], I32)
        ones_e = st.sb("ones_e", [P, N_EXPERTS])
        iota8, col, row = st.sb("iota8", [P, PER_GROUP]), st.sb("col", [P, P]), st.sb("row", [P, P])
        before, ones_m = st.sb("before", [P, P]), st.sb("ones_m", [P, P])
        pos, sums = st.ps("pos", [P, 512]), st.ps("sums", [P, 512])
        vec, init, soft, hots_ok, made = (st.sem(n) for n in ("vec", "init", "soft", "hots_ok", "made"))
        dest_ok, listed = st.sem("dest_ok"), st.sem("listed")
        block = st.block()

        @block.gpsimd
        def _(pool):
            pool.iota(iota8[:, :], [[1, PER_GROUP]], base=0, channel_multiplier=0, allow_small_or_imprecise_dtypes=True).then_inc(init, 1)
            pool.iota(col[:, :], [[1, P]], base=0, channel_multiplier=0, allow_small_or_imprecise_dtypes=True).then_inc(init, 1)
            pool.iota(row[:, :], [[0, P]], base=0, channel_multiplier=1, allow_small_or_imprecise_dtypes=True).then_inc(init, 1)
            pool.memset(ones_e[:, :], 1.0).then_inc(init, 1)
            pool.memset(ones_m[:, :], 1.0).then_inc(init, 1)
            pool.wait_ge(dest_ok, 1)
            for t in range(NT):
                for n in range(2):
                    pool.indirect_dma_start(out=Z["row_tok"], out_offset=bass.IndirectOffsetOnAxis(ap=dest[:, n, t:t + 1], axis=0),
                                            in_=keep["tok_id"][:, t:t + 1], in_offset=None).then_inc(listed, 16)
            pool.wait_ge(listed, 2 * NT * 16)

        @block.tensor
        def _(pe):
            pe.wait_ge(hots_ok, 1)
            flat = both[:, :, :].rearrange("p t e -> p (t e)")
            pe.matmul(pos[:, :], before[:, :], flat, start=True, stop=True)
            pe.matmul(sums[:, :], ones_m[:, :], flat, start=True, stop=True).then_inc(made, 1)

        @block.scalar
        def _(act):
            act.wait_ge(soft, 1)
            act.activation(gd[:, :, 0:N_GROUPS], gd[:, :, 0:N_GROUPS], ACT.Exp).then_inc(soft, 1)
            act.wait_ge(soft, 3)
            act.activation(ratio[:, :, :], ratio[:, :, :], ACT.Exp).then_inc(soft, 1)

        @block.vector
        def _(dve):
            v = Chain(dve, vec)
            dve.wait_ge(init, 5)
            v.link(dve.tensor_tensor(before[:, :], col[:, :], row[:, :], ALU.is_gt))
            wide = lambda t, n: t.to_broadcast([P, NT, n])
            index = lambda n: iota8[:, 0:n].rearrange("p (o n) -> p o n", o=1).to_broadcast([P, NT, n])

            def first_max(values, n, top, out):
                v.link(dve.tensor_reduce(top, values, AX.X, ALU.max))
                v.link(dve.tensor_tensor(cand[:, :, 0:n], values, wide(top, n), ALU.is_ge))
                v.link(dve.tensor_scalar(cand[:, :, 0:n], cand[:, :, 0:n], -64.0, 64.0, ALU.mult, ALU.add))
                v.link(dve.tensor_tensor(cand[:, :, 0:n], cand[:, :, 0:n], index(n), ALU.add))
                v.link(dve.tensor_reduce(at[:, :, :], cand[:, :, 0:n], AX.X, ALU.min))
                v.link(dve.tensor_tensor(out, index(n), wide(at[:, :, :], n), ALU.is_equal))

            groups = lg[:, :, 0:N_GROUPS]
            first_max(groups, N_GROUPS, gmax[:, :, :], g_one[:, :, 0:N_GROUPS])
            v.link(dve.tensor_tensor(gd[:, :, 0:N_GROUPS], groups, wide(gmax[:, :, :], N_GROUPS), ALU.subtract))
            dve.sem_inc(soft, 1)
            for n in range(N_GROUPS):
                e = lg[:, :, N_GROUPS + n * PER_GROUP:N_GROUPS + (n + 1) * PER_GROUP]
                out = le if n == 0 else tmp
                v.link(dve.tensor_tensor(out[:, :, :], e, wide(g_one[:, :, n:n + 1], PER_GROUP), ALU.mult))
                if n:
                    v.link(dve.tensor_tensor(le[:, :, :], le[:, :, :], tmp[:, :, :], ALU.add))
            first_max(le[:, :, :], PER_GROUP, m1[:, :, :], one[0][:, :, :])
            v.link(dve.scalar_tensor_tensor(out=le[:, :, :], in0=one[0][:, :, :], scalar=NEG, in1=le[:, :, :],
                                            op0=ALU.mult, op1=ALU.add))
            first_max(le[:, :, :], PER_GROUP, m2[:, :, :], one[1][:, :, :])
            dve.wait_ge(soft, 2)
            v.link(dve.tensor_tensor(ratio[:, :, :], m2[:, :, :], m1[:, :, :], ALU.subtract))
            dve.sem_inc(soft, 1)
            v.link(dve.tensor_reduce(gsum[:, :, :], gd[:, :, 0:N_GROUPS], AX.X, ALU.add))
            dve.wait_ge(soft, 4)
            v.link(dve.tensor_scalar(total[:, :, :], ratio[:, :, :], 1.0, None, ALU.add))
            v.link(dve.tensor_tensor(total[:, :, :], total[:, :, :], gsum[:, :, :], ALU.mult))
            v.link(dve.reciprocal(weight[:, 0, :].rearrange("p (t o) -> p t o", o=1), total[:, :, :]))
            v.link(dve.tensor_tensor(weight[:, 1, :].rearrange("p (t o) -> p t o", o=1),
                                     weight[:, 0, :].rearrange("p (t o) -> p t o", o=1), ratio[:, :, :], ALU.mult))
            for n in range(2):
                for g in range(N_GROUPS):
                    ins = dve.tensor_tensor(hot[n][:, :, g * PER_GROUP:(g + 1) * PER_GROUP], one[n][:, :, :],
                                            wide(g_one[:, :, g:g + 1], PER_GROUP), ALU.mult)
                v.link(ins)
            v.link(dve.tensor_tensor(both[:, :, :], hot[0][:, :, :], hot[1][:, :, :], ALU.add))
            dve.sem_inc(hots_ok, 1)
            dve.wait_ge(made, 1)
            three = lambda t: t[:, :].rearrange("p (t e) -> p t e", t=NT)
            v.link(dve.tensor_copy(tot[:, :, :], three(sums)))
            v.link(dve.memset(base[:, 0, :], 0.0))
            for t in range(1, NT):
                v.link(dve.tensor_tensor(base[:, t, :], base[:, t - 1, :], tot[:, t - 1, :], ALU.add))
            v.link(dve.tensor_tensor(count[:, :], base[:, NT - 1, :], tot[:, NT - 1, :], ALU.add))
            v.link(dve.tensor_scalar(count[:, :], count[:, :], float(P - 1), float(P), ALU.add, ALU.max))
            v.link(dve.tensor_copy(nb_i[:, :], count[:, :]))
            v.link(dve.tensor_scalar(nb_i[:, :], nb_i[:, :], 7, None, ALU.arith_shift_right))
            v.link(dve.tensor_copy(nb_f[:, :], nb_i[:, :]))
            v.link(dve.tensor_tensor_scan(ends_f[:, :], ones_e[:, :], nb_f[:, :], 0.0, ALU.mult, ALU.add))
            v.link(dve.tensor_copy(ends[:, 1:1 + N_EXPERTS], ends_f[:, :]))
            v.link(dve.memset(ends[:, 0:1], 0))
            v.link(dve.tensor_scalar(ends[:, 1 + N_EXPERTS:2 + N_EXPERTS], ends_f[:, N_EXPERTS - 1:N_EXPERTS], -1.0,
                                     float(MAX_BLOCKS + 1), ALU.mult, ALU.add))
            v.link(dve.tensor_tensor(nb_f[:, :], ends_f[:, :], nb_f[:, :], ALU.subtract))
            v.link(dve.tensor_scalar(nb_f[:, :], nb_f[:, :], float(P), None, ALU.mult))
            v.link(dve.tensor_tensor(base[:, :, :], base[:, :, :], three(pos), ALU.add))
            v.link(dve.tensor_tensor(base[:, :, :], base[:, :, :],
                                     nb_f[:, :].rearrange("p (o e) -> p o e", o=1).to_broadcast(E3), ALU.add))
            for n in range(2):
                v.link(dve.tensor_tensor(prod[:, :, :], base[:, :, :], hot[n][:, :, :], ALU.mult))
                v.link(dve.tensor_reduce(total[:, :, :], prod[:, :, :], AX.X, ALU.add))
                v.link(dve.tensor_copy(dest[:, n, :].rearrange("p (t o) -> p t o", o=1), total[:, :, :]))
            dve.sem_inc(dest_ok, 1)


def stage_experts(nc, A, Z, keep):
    ends = keep["ends"]
    with ExitStack() as ctx:
        st = Stage(nc, ctx, "ex")
        wgu = st.sb("wgu", [P, 2, DC, 2 * D_EXPERT])
        FC = D_EXPERT // P
        wd = st.sb("wd", [P, 2, FC, D])
        idx = st.sb("idx", [P, 1], I32)
        xg = st.sb("xg", [P, D])
        xT = st.sb("xT", [P, DC, P])
        gate = st.sb("gate", [P, D_EXPERT])
        hid = st.sb("hid", [P, D_EXPERT])
        hidT = st.sb("hidT", [P, FC, P])
        y = st.sb("y", [P, D])
        zeros = st.sb("zeros", [P, D])
        ident = st.sb("ident", [P, P])
        tp, gu, tph, yps = st.ps("tp", [P, 2, 512]), st.ps("gu", [P, 2, 512]), st.ps("tph", [P, 512]), st.ps("yps", [P, 2, 512])
        w_in = st.sems("w_in", 2)
        zeros_ok, z_out = st.sem("zeros_ok"), st.sem("z_out")
        w_used, id_ok, idx_in, x_in, turned, xt_ok, gu_made = (
            st.sem(n) for n in ("w_used", "id_ok", "idx_in", "x_in", "turned", "xt_ok", "gu_made"))
        silu_ok, hid_ok, hid_turned, hidt_ok, y_made, y_ok, y_out = (
            st.sem(n) for n in ("silu_ok", "hid_ok", "hid_turned", "hidt_ok", "y_made", "y_ok", "y_out"))
        block = st.block()
        bound = dict(min_val=1, max_val=MAX_BLOCKS)

        @block.sync
        def _(sync):
            WGU = A["w_exp_gate_up"][0].rearrange("e (c p) n -> e p c n", p=P)
            WD = A["w_exp_down"][0].rearrange("e (c p) n -> e p c n", p=P)
            sync.wait_ge(zeros_ok, 1)
            spare = sync.value_load(ends[0:1, 1 + N_EXPERTS:2 + N_EXPERTS], **bound)
            with sync.Fori(0, spare) as b:
                sync.dma_start(Z["rows"][bass.ds((MAX_BLOCKS - b) * P, P), :], zeros[:, :]).then_inc(z_out, 16)
            sync.wait_ge(z_out, spare * 16)
            steady(sync, Z)
            with sync.Fori(0, N_EXPERTS // 2) as i:
                for k in range(2):
                    sync.wait_ge(w_used, 2 * i + k + 1)
                    sync.dma_start(wgu[:, k, :, :], WGU[bass.ds(2 * i + k, 1), :, :, :].rearrange("e p c n -> p (e c) n")).then_inc(w_in[k], 16)
                    sync.dma_start(wd[:, k, :, :], WD[bass.ds(2 * i + k, 1), :, :, :].rearrange("e p c n -> p (e c) n")).then_inc(w_in[k], 16)

        @block.gpsimd
        def _(pool):
            build_identity(pool, ident, id_ok)
            pool.memset(zeros[:, :], 0.0).then_inc(zeros_ok, 1)
            pool.sem_inc(w_used, 2)
            n = pool.value_load(ends[0:1, N_EXPERTS:N_EXPERTS + 1], **bound)
            with pool.Fori(0, n + 1) as b:
                pool.wait_ge(x_in, b * 16)
                pool.dma_start(idx[:, :], Z["row_tok"][bass.ds(b * P, P), :]).then_inc(idx_in, 16)
                pool.wait_ge(idx_in, (b + 1) * 16)
                pool.wait_ge(turned, b)
                steady(pool, Z)
                pool.indirect_dma_start(out=xg[:, :], out_offset=None, in_=Z["h2"],
                                        in_offset=bass.IndirectOffsetOnAxis(ap=idx[:, 0:1], axis=0)).then_inc(x_in, 16)
            pool.wait_ge(turned, n + 1)
            pool.wait_ge(x_in, n * 16 + 16)

        @block.tensor
        def _(pe):
            def turn_rows(b):
                pe.wait_ge(x_in, b * 16 + 16)
                pe.wait_ge(xt_ok, b)
                for c in range(DC):
                    ins = pe.transpose(tp[:, c // 4, (c % 4) * P:(c % 4 + 1) * P], xg[:, c * P:(c + 1) * P], ident[:, :])
                ins.then_inc(turned, 1)

            pe.wait_ge(id_ok, 2)
            turn_rows(0)
            with pe.Fori(0, N_EXPERTS // 2) as i:
                for k in range(2):
                    first = pe.value_load(ends[0:1, bass.ds(2 * i + k, 1)], min_val=0, max_val=MAX_BLOCKS)
                    last = pe.value_load(ends[0:1, bass.ds(2 * i + k + 1, 1)], **bound)
                    pe.wait_ge(w_in[k], (i + 1) * 32)
                    steady(pe, Z)
                    with pe.Fori(first, last) as b:
                        pe.wait_ge(xt_ok, b + 1)
                        pe.wait_ge(hid_ok, b)
                        for n in range(2):
                            for c in range(DC):
                                ins = pe.matmul(gu[:, n, :], xT[:, c, :], wgu[:, k, c, n * 512:(n + 1) * 512],
                                                start=(c == 0), stop=(c == DC - 1))
                            ins.then_inc(gu_made, 1)
                        turn_rows(b + 1)
                        pe.wait_ge(hid_ok, b + 1)
                        pe.wait_ge(hidt_ok, b)
                        for c in range(FC):
                            ins = pe.transpose(tph[:, c * P:(c + 1) * P], hid[:, c * P:(c + 1) * P], ident[:, :])
                        ins.then_inc(hid_turned, 1)
                        pe.wait_ge(hidt_ok, b + 1)
                        pe.wait_ge(y_ok, b)
                        for n in range(2):
                            for c in range(FC):
                                ins = pe.matmul(yps[:, n, :], hidT[:, c, :], wd[:, k, c, n * 512:(n + 1) * 512],
                                                start=(c == 0), stop=(c == FC - 1))
                        ins.then_inc(y_made, 1)
                    pe.wait_ge(y_made, last)
                    pe.sem_inc(w_used, 1)

        @block.scalar
        def _(act):
            n = act.value_load(ends[0:1, N_EXPERTS:N_EXPERTS + 1], **bound)
            with act.Fori(0, n) as b:
                act.wait_ge(gu_made, b * 2 + 1)
                act.wait_ge(hid_ok, b)
                act.activation(gate[:, :], gu[:, 0, :], ACT.Silu).then_inc(silu_ok, 1)
                act.wait_ge(hid_turned, b + 1)
                act.copy(hidT[:, :, :].rearrange("p c t -> p (c t)"), tph[:, :]).then_inc(hidt_ok, 1)
                act.wait_ge(y_made, b + 1)
                act.wait_ge(y_out, b * 16)
                act.copy(y[:, :].rearrange("p (n c) -> p n c", n=2), yps[:, :, :]).then_inc(y_ok, 1)
                act.wait_ge(y_ok, b + 1)
                act.dma_start(Z["rows"][bass.ds(b * P, P), :], y[:, :]).then_inc(y_out, 16)
            act.wait_ge(y_out, n * 16)
            steady(act, Z)

        @block.vector
        def _(dve):
            n = dve.value_load(ends[0:1, N_EXPERTS:N_EXPERTS + 1], **bound)
            dve.wait_ge(turned, 1)
            dve.tensor_copy(xT[:, :, :].rearrange("p (b c) t -> p b (c t)", b=2), tp[:, :, :]).then_inc(xt_ok, 1)
            with dve.Fori(0, n) as b:
                dve.wait_ge(gu_made, b * 2 + 2)
                dve.wait_ge(silu_ok, b + 1)
                dve.wait_ge(hid_turned, b)
                dve.tensor_tensor(hid[:, :], gate[:, :], gu[:, 1, :], ALU.mult).then_inc(hid_ok, 1)
                dve.wait_ge(turned, b + 2)
                dve.tensor_copy(xT[:, :, :].rearrange("p (b c) t -> p b (c t)", b=2), tp[:, :, :]).then_inc(xt_ok, 1)


def stage_moe(nc, A, Z):
    with ExitStack() as ctx:
        st = Stage(nc, ctx, "mo")
        keep = dict(lg=st.sb("lg", [P, NT, N_LOGITS]), weight=st.sb("weight", [P, 2, NT]), dest=st.sb("dest", [P, 2, NT], I32),
                    ends=st.sb("ends", [P, 2 + N_EXPERTS], I32), tok_id=st.sb("tok_id", [P, NT], I32))
        stage_route(nc, A, Z, keep)
        stage_experts(nc, A, Z, keep)
        stage_final(nc, A, Z, keep)


PLE = 256


def stage_final(nc, A, Z, keep):
    dest, weight = keep["dest"], keep["weight"]
    with ExitStack() as ctx:
        st = Stage(nc, ctx, "fi")
        PC = PLE // P
        w_g, w_p = st.sb("w_g", [P, DC, D]), st.sb("w_p", [P, PC, D])
        g_in = st.sb("g_in", [P, DC])
        g_e, g_y = st.sb("g_e", [P, D]), st.sb("g_y", [P, D])
        x = st.sb("x", [P, 2, D])
        r = st.sb("r", [P, 2, 2, D])
        p_t = st.sb("p_t", [P, 2, PLE])
        idx = st.sb("idx", [P, 2, 2], I32)
        xn, sg, e = (st.sb(n, [P, D]) for n in ("xn", "sg", "e"))
        junk = st.sb("junk", [P, D])
        out_t = st.sb("out_t", [P, 2, D])
        xT, pT = st.sb("xT", [P, DC, P]), st.sb("pT", [P, PC, P])
        stat = st.sb("stat", [P, 3, 4])
        ident = st.sb("ident", [P, P])
        tp, gps = st.ps("tp", [P, 2, 512]), st.ps("gps", [P, 2, 512])
        pps, eps = st.ps("pps", [P, 512]), st.ps("eps", [P, 2, 512])
        x_in, r_in, y_out = st.sems("x_in", 2), st.sems("r_in", 2), st.sems("y_out", 2)
        w_in, id_ok, idx_ok, x_used, summed, ms_ok, roots = (
            st.sem(n) for n in ("w_in", "id_ok", "idx_ok", "x_used", "summed", "ms_ok", "roots"))
        xn_ok, turned, xt_ok, made, sig_ok, y_ok, vec = (
            st.sem(n) for n in ("xn_ok", "turned", "xt_ok", "made", "sig_ok", "y_ok", "vec"))
        p_turned, pt_ok, e_made = st.sem("p_turned"), st.sem("pt_ok"), st.sem("e_made")
        block = st.block()
        MIX, EMB, OUT = range(3)

        @block.sync
        def _(sync):
            sync.dma_start(w_g[:, :, :], A["w_ple_gate"][0].rearrange("(c p) n -> p c n", p=P)).then_inc(w_in, 16)
            sync.dma_start(w_p[:, :, :], A["w_ple_proj"][0].rearrange("(c p) n -> p c n", p=P)).then_inc(w_in, 16)
            sync.dma_start(g_in[:, :], cols(A["g_ple_gate_in"][0], DC)).then_inc(w_in, 16)
            sync.dma_start(g_e[:, :], A["g_ple_norm"][0].partition_broadcast(P)).then_inc(w_in, 16)
            sync.dma_start(g_y[:, :], A["g_final"].partition_broadcast(P)).then_inc(w_in, 16)
            with sync.Fori(0, NT // 2) as i:
                for k in range(2):
                    t = 2 * i + k
                    sync.wait_ge(x_used, t + 1)
                    sync.dma_start(x[:, k, :], Z["x1"][bass.ds(t * P, P), :]).then_inc(x_in[k], 16)
                    sync.dma_start(p_t[:, k, :], A["p"][0][0][bass.ds(t * P, P), :]).then_inc(x_in[k], 16)

        @block.gpsimd
        def _(pool):
            build_identity(pool, ident, id_ok)
            with pool.Fori(0, NT // 2) as i:
                for k in range(2):
                    t = 2 * i + k
                    pool.wait_ge(x_used, t + 1)
                    pool.wait_ge(r_in[k], i * 32)
                    pool.tensor_copy(idx[:, k, :].rearrange("p (n o) -> p n o", o=1), dest[:, :, bass.ds(t, 1)]).then_inc(idx_ok, 1)
                    pool.wait_ge(idx_ok, t + 1)
                    steady(pool, Z)
                    for n in range(2):
                        pool.indirect_dma_start(out=r[:, k, n, :], out_offset=None, in_=Z["rows"],
                                                in_offset=bass.IndirectOffsetOnAxis(ap=idx[:, k, n:n + 1], axis=0)).then_inc(r_in[k], 16)

        @block.tensor
        def _(pe):
            pe.wait_ge(id_ok, 2)
            pe.wait_ge(w_in, 80)
            with pe.Fori(0, NT // 2) as i:
                for k in range(2):
                    t = 2 * i + k
                    pe.wait_ge(x_in[k], (i + 1) * 32)
                    pe.wait_ge(pt_ok, t)
                    for c in range(PC):
                        ins = pe.transpose(pps[:, c * P:(c + 1) * P], p_t[:, k, c * P:(c + 1) * P], ident[:, :])
                    ins.then_inc(p_turned, 1)
                    pe.wait_ge(pt_ok, t + 1)
                    pe.wait_ge(y_ok, t)
                    for n in range(2):
                        for c in range(PC):
                            ins = pe.matmul(eps[:, n, :], pT[:, c, :], w_p[:, c, n * 512:(n + 1) * 512],
                                            start=(c == 0), stop=(c == PC - 1))
                    ins.then_inc(e_made, 1)
                    pe.wait_ge(xn_ok, t + 1)
                    for c in range(DC):
                        ins = pe.transpose(tp[:, c // 4, (c % 4) * P:(c % 4 + 1) * P], xn[:, c * P:(c + 1) * P], ident[:, :])
                    ins.then_inc(turned, 1)
                    pe.wait_ge(xt_ok, t + 1)
                    pe.wait_ge(sig_ok, t)
                    for n in range(2):
                        for c in range(DC):
                            ins = pe.matmul(gps[:, n, :], xT[:, c, :], w_g[:, c, n * 512:(n + 1) * 512],
                                            start=(c == 0), stop=(c == DC - 1))
                    ins.then_inc(made, 1)

        @block.scalar
        def _(act):
            def root(which, n):
                act.wait_ge(ms_ok, n)
                act.activation(stat[:, which, 2:3], stat[:, which, 1:2], ACT.Sqrt).then_inc(roots, 1)

            with act.Fori(0, NT // 2) as i:
                for k in range(2):
                    t = 2 * i + k
                    act.wait_ge(p_turned, t + 1)
                    act.wait_ge(e_made, t)
                    act.copy(pT[:, :, :].rearrange("p c t -> p (c t)"), pps[:, 0:PLE]).then_inc(pt_ok, 1)
                    act.wait_ge(e_made, t + 1)
                    act.wait_ge(summed, 3 * t)
                    act.activation(junk[:, :].rearrange("p (n c) -> p n c", n=2), eps[:, :, :], ACT.Square,
                                   accum_out=stat[:, EMB, 0:1]).then_inc(summed, 1)
                    root(EMB, 3 * t + 1)
                    act.wait_ge(vec, t * 8 + 2)
                    act.wait_ge(summed, 3 * t + 1)
                    act.activation(junk[:, :], x[:, k, :], ACT.Square, accum_out=stat[:, MIX, 0:1]).then_inc(summed, 1)
                    root(MIX, 3 * t + 2)
                    act.wait_ge(made, t + 1)
                    act.activation(sg[:, :].rearrange("p (n c) -> p n c", n=2), gps[:, :, :], ACT.Sigmoid).then_inc(sig_ok, 1)
                    act.wait_ge(vec, t * 8 + 7)
                    act.wait_ge(summed, 3 * t + 2)
                    act.activation(junk[:, :], x[:, k, :], ACT.Square, accum_out=stat[:, OUT, 0:1]).then_inc(summed, 1)
                    root(OUT, 3 * t + 3)
                    act.wait_ge(y_ok, t + 1)
                    act.dma_start(Z["y"][0][bass.ds(t * P, P), :], out_t[:, k, :]).then_inc(y_out[k], 16)
            for k in range(2):
                act.wait_ge(y_out[k], NT // 2 * 16)

        @block.vector
        def _(dve):
            v = Chain(dve, vec)

            def mean_square(which, n):
                dve.wait_ge(summed, n)
                dve.tensor_scalar(stat[:, which, 1:2], stat[:, which, 0:1], 1.0 / D, NORM_EPS, ALU.mult, ALU.add).then_inc(ms_ok, 1)
                dve.wait_ge(roots, n)
                v.link(dve.reciprocal(stat[:, which, 3:4], stat[:, which, 2:3]))

            dve.sem_inc(x_used, 2)
            dve.wait_ge(w_in, 80)
            halves = lambda a: a.rearrange("p (n c) -> p n c", n=2)
            with dve.Fori(0, NT // 2) as i:
                v.loop(i, 16)
                for k in range(2):
                    t = 2 * i + k
                    dve.wait_ge(x_in[k], (i + 1) * 32)
                    dve.wait_ge(r_in[k], (i + 1) * 32)
                    for n in range(2):
                        v.link(dve.scalar_tensor_tensor(out=x[:, k, :], in0=r[:, k, n, :], scalar=weight[:, n, bass.ds(t, 1)],
                                                        in1=x[:, k, :], op0=ALU.mult, op1=ALU.add))
                    mean_square(EMB, 3 * t + 1)
                    v.link(dve.scalar_tensor_tensor(out=halves(e[:, :]), in0=eps[:, :, :], scalar=stat[:, EMB, 3:4],
                                                    in1=halves(g_e[:, :]), op0=ALU.mult, op1=ALU.mult))
                    mean_square(MIX, 3 * t + 2)
                    dve.wait_ge(turned, t)
                    dve.tensor_scalar(xn[:, :], x[:, k, :], stat[:, MIX, 3:4], None, ALU.mult).then_inc(xn_ok, 1)
                    dve.wait_ge(turned, t + 1)
                    dve.wait_ge(made, t)
                    for b in range(2):
                        ins = dve.tensor_tensor(xT[:, 4 * b:4 * b + 4, :], tp[:, b, :].rearrange("p (c t) -> p c t", c=4),
                                                g_in[:, 4 * b:4 * b + 4].rearrange("p (c o) -> p c o", o=1).to_broadcast([P, 4, P]),
                                                ALU.mult)
                    ins.then_inc(xt_ok, 1)
                    dve.wait_ge(sig_ok, t + 1)
                    v.link(dve.tensor_tensor(e[:, :], e[:, :], sg[:, :], ALU.mult))
                    v.link(dve.tensor_tensor(x[:, k, :], x[:, k, :], e[:, :], ALU.add))
                    mean_square(OUT, 3 * t + 3)
                    dve.wait_ge(y_out[k], i * 16)
                    dve.scalar_tensor_tensor(out=out_t[:, k, :], in0=x[:, k, :], scalar=stat[:, OUT, 3:4], in1=g_y[:, :],
                                             op0=ALU.mult, op1=ALU.mult).then_inc(y_ok, 1)
                    dve.wait_ge(y_ok, t + 1)
                    dve.sem_inc(x_used, 1)
                v.end(NT // 2)


_IN_NAMES = ["x", "p", "g_mix", "w_in", "mu_shift", "rw_w0", "rw_w2", "rw_a0", "rw_a2", "rw_g2", "rw_k_k", "rw_k_a",
             "rw_r_k", "rw_ln_w", "rw_ln_b", "cmp_pos_k", "cmp_pos_v", "cmp_k_w1", "cmp_k_w2", "cmp_v_w1", "cmp_v_w2",
             "nsa_gate_b", "w_up_rwkv", "w_up_nsa", "w_out", "g_ffn", "w_group", "b_group", "w_router", "b_router",
             "w_exp_gate_up", "w_exp_down", "w_ple_proj", "g_ple_norm", "g_ple_gate_in", "w_ple_gate", "g_final"]

_SCRATCH = {
    "z": ((Z_ROWS, S), F32), "gate": ((N_GATE, S), F32),
    "rar": ((RW_W, NCH, 2, CH), F32), "rb": ((RW_W, S), F32), "rk": ((RW_W, S), F32), "rv": ((RW_W, S), F32),
    "rdec": ((RW_W, 2, NCH), F32), "rbonus": ((RW_W, S), F32), "rg": ((RW_W, S), F32), "ro": ((RW_W, S), F32),
    "yr": ((RW_W, S), F32), "yn": ((NSA_W, P + S), F32), "x1": ((S, D), F32), "h2": ((S, D), F32),
    "row_tok": (((MAX_BLOCKS + 1) * P, 1), I32), "rows": (((MAX_BLOCKS + 1) * P, D), F32),
}


def build_program(nc, A, out):
    Z = {n: nc.dram_tensor(f"s_{n}", shape, dt).ap() for n, (shape, dt) in _SCRATCH.items()}
    Z["y"] = out
    with ExitStack() as whole, nc.semaphore("passed") as passed, \
            nc.allow_non_contiguous_dma(reason="vectors of parameters, a few KB each"):
        Z["passed"], Z["whole"] = passed, whole
        stage_project(nc, A, Z)
        stage_rwkv_prep(nc, A, Z)
        stage_rwkv_scan(nc, A, Z)
        stage_rwkv_post(nc, A, Z)
        stage_nsa(nc, A, Z)
        stage_mix(nc, A, Z)
        stage_moe(nc, A, Z)


def kernel(**inputs):
    import concourse.bacc as bacc
    from concourse.bass_utils import run_bass_kernel_spmd

    nc = bacc.Bacc("TRN2", target_bir_lowering=False, num_devices=1)
    arrays, A = {}, {}
    for name in _IN_NAMES:
        a = np.ascontiguousarray(inputs[name])
        arrays[f"in_{name}"] = a
        A[name] = nc.dram_tensor(f"in_{name}", a.shape, mybir.dt.from_np(a.dtype), kind="ExternalInput").ap()
    out = nc.dram_tensor("out_y", (1, S, D), F32, kind="ExternalOutput").ap()
    build_program(nc, A, out)
    r = run_bass_kernel_spmd(nc, [arrays], core_ids=[0])
    return r.results[0]["out_y"]
```

```python
from contextlib import ExitStack
import math

import numpy as np

import concourse.bass as bass
from concourse import mybir

F32 = mybir.dt.float32
F32R = mybir.dt.float32r
I32 = mybir.dt.int32
ALU = mybir.AluOpType
ACT = mybir.ActivationFunctionType
AX = mybir.AxisListType

P = 128
D = 1024
S = 2048
DC = D // P
NT = S // P
NB = S // 512
HD = 64
RW_HEADS, RW_W = 8, 512
LORA, GATE_LORA = 64, 128
GN_EPS = 64e-5
NORM_EPS = 1e-6
RW_IN = 3 * RW_W + 2 * LORA + GATE_LORA
NSA_HEADS, KV_HEADS = 8, 2
Q_PER_KV = NSA_HEADS // KV_HEADS
NSA_W = 512
N_IN = RW_IN + NSA_W + 6 * KV_HEADS * HD + 3 * NSA_HEADS + 2 * D
GATE_ROW = RW_IN + NSA_W + 6 * KV_HEADS * HD
N_GATE = 3 * NSA_HEADS
MERGE_COL = GATE_ROW + N_GATE
NEG = -1e30
FORCE = 1e6
DECAY_SCALE = math.exp(-0.5)

ROW_R, ROW_K, ROW_V = 0, RW_W, 2 * RW_W
ROW_W, ROW_A, ROW_G = 3 * RW_W, 3 * RW_W + LORA, 3 * RW_W + 2 * LORA
ROW_Q = RW_IN
ROW_KC, ROW_VC, ROW_KS, ROW_VS, ROW_KW, ROW_VW = (RW_IN + NSA_W + 128 * n for n in range(6))
ROW_MERGE = GATE_ROW
Z_ROWS = ROW_MERGE + 2 * D


class Chain:

    def __init__(self, eng, sem):
        self.eng, self.sem, self.base, self.n = eng, sem, 0, 0

    def mark(self, ins):
        ins.then_inc(self.sem, 1)
        self.n += 1
        return ins

    def wait(self):
        self.eng.wait_ge(self.sem, self.base + self.n)

    def link(self, ins):
        self.mark(ins)
        self.wait()

    def loop(self, i, per):
        self.before, self.per = self.n, per
        self.base, self.n = i * per + self.n, 0

    def end(self, trips):
        assert self.n == self.per, (self.n, self.per)
        self.base, self.n = 0, self.before + trips * self.per


class Stage:

    def __init__(self, nc, ctx, name):
        self.nc, self.ctx, self.name, self.numbers = nc, ctx, name, []

    def sb(self, name, shape, dt=F32):
        return self.ctx.enter_context(self.nc.sbuf_tensor(f"{self.name}_{name}", shape, dt))

    def ps(self, name, shape, dt=F32):
        return self.ctx.enter_context(self.nc.psum_tensor(f"{self.name}_{name}", shape, dt))

    def sem(self, name):
        sem = self.ctx.enter_context(self.nc.semaphore(f"{self.name}_{name}"))
        self.numbers.append(sem.num)
        return sem

    def lasting_sem(self, name, whole):
        return whole.enter_context(self.nc.semaphore(f"{self.name}_{name}"))

    def sems(self, name, n):
        return [self.sem(f"{name}{k}") for k in range(n)]

    def zero(self):
        numbers = sorted(self.numbers)
        firsts = [n for n in numbers if n - 1 not in numbers]
        lasts = [n for n in numbers if n + 1 not in numbers]
        with self.nc.Block() as block:
            @block.gpsimd
            def _(pool):
                for first, last in zip(firsts, lasts):
                    pool.sem_clear(range(first, last + 1))

    def block(self):
        self.ctx.callback(self.zero)
        return self.ctx.enter_context(self.nc.Block())


def steady(eng, Z):
    eng.sem_inc(Z["passed"], 1)


def split(v, whole, high, rest):
    v.link(v.eng.tensor_copy(high.bitcast(F32R), whole))
    return v.eng.tensor_tensor(rest.bitcast(F32R), whole, high, ALU.subtract)


def products(pe, dst, lhsT, rhs, start, stop):
    one = lambda a, b, first, last: pe.matmul(dst, a.bitcast(F32R), b.bitcast(F32R), start=first, stop=last)
    one(lhsT[0], rhs[0], start, False)
    one(lhsT[0], rhs[1], False, False)
    return one(lhsT[1], rhs[0], False, stop)


def cols(v, c):
    return v.rearrange("(c p) -> p c", c=c)


def build_identity(pool, ident, seen):
    pool.memset(ident[:, :], 0.0).then_inc(seen, 1)
    pool.wait_ge(seen, 1)
    pool.affine_select(out=ident[:, :], in_=ident[:, :], compare_op=ALU.not_equal, fill=1.0, base=0,
                       pattern=[[-1, P]], channel_multiplier=1).then_inc(seen, 1)


def stage_project(nc, A, Z):
    outer = ExitStack()
    with outer:
        keep = Stage(nc, outer, "pr")
        hT, hT_r = keep.sb("hT", [P, DC, S]), keep.sb("hT_r", [P, DC, S])

        with ExitStack() as ctx:
            st = Stage(nc, ctx, "nm")
            x_t = st.sb("x", [P, 2, D])
            sq = st.sb("sq", [P, D])
            stat = st.sb("stat", [P, 2, 4])
            xn = st.sb("xn", [P, 2, D])
            hw = st.sb("hw", [P, 2, DC, P])
            g_c = st.sb("g", [P, DC])
            ident = st.sb("ident", [P, P])
            tp = st.ps("tp", [P, 2, 2, 512])
            x_in = st.sems("x_in", 2)
            x_free, g_in, id_ok = (st.sem(n) for n in ("x_free", "g_in", "id_ok"))
            squares, roots, steps = (st.sem(n) for n in ("squares", "roots", "steps"))
            ms_ok, xn_ok, turned, taken = (st.sem(n) for n in ("ms_ok", "xn_ok", "turned", "taken"))
            block = st.block()

            @block.sync
            def _(sync):
                sync.dma_start(g_c[:, :], cols(A["g_mix"][0], DC)).then_inc(g_in, 16)
                with sync.Fori(0, NT // 2) as i:
                    for k in range(2):
                        sync.wait_ge(x_free, 2 * i + k + 1)
                        sync.dma_start(x_t[:, k, :], A["x"][0][bass.ds((2 * i + k) * P, P), :]).then_inc(x_in[k], 16)

            @block.gpsimd
            def _(pool):
                build_identity(pool, ident, id_ok)

            @block.scalar
            def _(act):
                with act.Fori(0, NT // 2) as i:
                    for k in range(2):
                        act.wait_ge(x_in[k], (i + 1) * 16)
                        act.wait_ge(squares, 2 * i + k)
                        act.activation(sq[:, :], x_t[:, k, :], ACT.Square,
                                       accum_out=stat[:, k, 0:1]).then_inc(squares, 1)
                    for k in range(2):
                        act.wait_ge(ms_ok, 2 * i + k + 1)
                        act.activation(stat[:, k, 2:3], stat[:, k, 1:2], ACT.Sqrt).then_inc(roots, 1)

            @block.vector
            def _(dve):
                v = Chain(dve, steps)
                dve.sem_inc(x_free, 2)
                dve.sem_inc(taken, 2)
                dve.wait_ge(g_in, 16)
                with dve.Fori(0, NT // 2) as i:
                    v.loop(i, 10)
                    for k in range(2):
                        dve.wait_ge(squares, 2 * i + k + 1)
                        dve.tensor_scalar(stat[:, k, 1:2], stat[:, k, 0:1], 1.0 / D, NORM_EPS,
                                          ALU.mult, ALU.add).then_inc(ms_ok, 1)
                    for k in range(2):
                        dve.wait_ge(roots, 2 * i + k + 1)
                        v.link(dve.reciprocal(stat[:, k, 3:4], stat[:, k, 2:3]))
                        dve.wait_ge(turned, 2 * i + k)
                        dve.tensor_scalar(xn[:, k, :], x_t[:, k, :], stat[:, k, 3:4], None,
                                          ALU.mult).then_inc(xn_ok, 1)
                        dve.wait_ge(xn_ok, 2 * i + k + 1)
                        dve.sem_inc(x_free, 1)
                    for k in range(2):
                        dve.wait_ge(turned, 2 * i + k + 1)
                        at = bass.ds((2 * i + k) * P, P)
                        for c in range(2):
                            ins = dve.tensor_tensor(
                                hw[:, k, 4 * c:4 * c + 4, :],
                                tp[:, k, c, :].rearrange("p (c t) -> p c t", c=4),
                                g_c[:, 4 * c:4 * c + 4].rearrange("p (c o) -> p c o", o=1).to_broadcast([P, 4, P]),
                                ALU.mult)
                            v.mark(ins)
                        v.wait()
                        dve.sem_inc(taken, 1)
                        steady(dve, Z)
                        v.mark(split(v, hw[:, k, :, :], hT[:, :, at], hT_r[:, :, at]))
                    v.end(NT // 2)

            @block.tensor
            def _(pe):
                pe.wait_ge(id_ok, 2)
                with pe.Fori(0, NT // 2) as i:
                    for k in range(2):
                        pe.wait_ge(xn_ok, 2 * i + k + 1)
                        pe.wait_ge(taken, 2 * i + k + 1)
                        for c in range(DC):
                            ins = pe.transpose(tp[:, k, c // 4, (c % 4) * P:(c % 4 + 1) * P],
                                               xn[:, k, c * P:(c + 1) * P], ident[:, :])
                        ins.then_inc(turned, 1)

        with ExitStack() as ctx:
            st = Stage(nc, ctx, "zp")
            w, w_h, w_r = (st.sb(n, [P, 2, DC, P]) for n in ("w", "w_h", "w_r"))
            zs = st.sb("zs", [P, 2, S])
            acc = st.ps("acc", [P, 2, NB, 512])
            w_in, z_out = st.sems("w_in", 2), [st.lasting_sem(f"z_out{k}", Z["whole"]) for k in range(2)]
            w_free, made, half_a, half_v, w_ok, steps = (
                st.sem(n) for n in ("w_free", "made", "half_a", "half_v", "w_ok", "steps"))
            n_lead = GATE_ROW // P
            n_all = Z_ROWS // P
            W = A["w_in"][0].rearrange("(c p) n -> p c n", p=P)
            block = st.block()

            @block.sync
            def _(sync):
                def load(i, k, col):
                    sync.wait_ge(w_free, 2 * i + k + 1)
                    sync.dma_start(w[:, k, :, :], W[:, :, bass.ds(col, P)]).then_inc(w_in[k], 16)

                with sync.Fori(0, n_lead // 2) as i:
                    for k in range(2):
                        load(i, k, (2 * i + k) * P)
                with sync.Fori(n_lead // 2, n_all // 2) as i:
                    for k in range(2):
                        load(i, k, (2 * i + k) * P + N_GATE)
                sync.wait_ge(w_free, n_all + 1)
                sync.dma_start(w[:, 0, :, 0:N_GATE], W[:, :, GATE_ROW:MERGE_COL]).then_inc(w_in[0], 16)

            @block.tensor
            def _(pe):
                pe.sem_inc(w_free, 2)
                with pe.Fori(0, n_all // 2) as i:
                    for k in range(2):
                        pe.wait_ge(w_ok, 2 * i + k + 1)
                        pe.wait_ge(half_a, 2 * i + k + 1)
                        pe.wait_ge(half_v, 2 * i + k + 1)
                        for n in range(NB):
                            for c in range(DC):
                                at = slice(n * 512, (n + 1) * 512)
                                ins = products(pe, acc[:, k, n, :], (w_h[:, k, c, :], w_r[:, k, c, :]),
                                               (hT[:, c, at], hT_r[:, c, at]), c == 0, c == DC - 1)
                        ins.then_inc(made, 1)
                        pe.wait_ge(made, 2 * i + k + 1)
                        pe.sem_inc(w_free, 1)
                pe.wait_ge(w_ok, n_all + 1)
                pe.wait_ge(half_a, n_all + 1)
                pe.wait_ge(half_v, n_all + 1)
                for n in range(NB):
                    for c in range(DC):
                        at = slice(n * 512, (n + 1) * 512)
                        ins = products(pe, acc[0:N_GATE, 0, n, :], (w_h[:, 0, c, 0:N_GATE], w_r[:, 0, c, 0:N_GATE]),
                                       (hT[:, c, at], hT_r[:, c, at]), c == 0, c == DC - 1)
                ins.then_inc(made, 1)

            @block.scalar
            def _(act):
                act.sem_inc(half_a, 2)
                with act.Fori(0, n_all // 2) as i:
                    for k in range(2):
                        act.wait_ge(made, 2 * i + k + 1)
                        act.wait_ge(z_out[k], i * 16)
                        act.copy(zs[:, k, 0:1024].rearrange("p (n t) -> p n t", n=2),
                                 acc[:, k, 0:2, :]).then_inc(half_a, 1)
                act.wait_ge(made, n_all + 1)
                act.wait_ge(z_out[0], n_all // 2 * 16)
                act.copy(zs[0:N_GATE, 0, 0:1024].rearrange("p (n t) -> p n t", n=2),
                         acc[0:N_GATE, 0, 0:2, :]).then_inc(half_a, 1)

            @block.vector
            def _(dve):
                v = Chain(dve, steps)

                def split_w(k, loaded):
                    dve.wait_ge(w_in[k], loaded * 16)
                    split(v, w[:, k, :, :], w_h[:, k, :, :], w_r[:, k, :, :]).then_inc(w_ok, 1)

                dve.sem_inc(half_v, 2)
                split_w(0, 1)
                with dve.Fori(0, n_all // 2) as i:
                    v.loop(i, 2)
                    for k in range(2):
                        split_w(1 - k, i + 1 + k)
                        dve.wait_ge(made, 2 * i + k + 1)
                        dve.wait_ge(z_out[k], i * 16)
                        dve.tensor_copy(zs[:, k, 1024:2048].rearrange("p (n t) -> p n t", n=2),
                                        acc[:, k, 2:4, :]).then_inc(half_v, 1)
                    v.end(n_all // 2)
                dve.wait_ge(made, n_all + 1)
                dve.wait_ge(z_out[0], n_all // 2 * 16)
                dve.tensor_copy(zs[0:N_GATE, 0, 1024:2048].rearrange("p (n t) -> p n t", n=2),
                                acc[0:N_GATE, 0, 2:4, :]).then_inc(half_v, 1)

            @block.gpsimd
            def _(pool):
                with pool.Fori(0, n_all // 2) as i:
                    for k in range(2):
                        pool.wait_ge(half_a, 2 * i + k + 3)
                        pool.wait_ge(half_v, 2 * i + k + 3)
                        pool.dma_start(Z["z"][bass.ds((2 * i + k) * P, P), :], zs[:, k, :]).then_inc(z_out[k], 16)
                pool.wait_ge(half_a, n_all + 3)
                pool.wait_ge(half_v, n_all + 3)
                pool.dma_start(Z["gate"], zs[0:N_GATE, 0, :]).then_inc(z_out[0], 16)
                pool.wait_ge(z_out[0], (n_all // 2 + 1) * 16)
                pool.wait_ge(z_out[1], n_all // 2 * 16)


CH = P
NCH = S // CH
PAIRS = RW_W // P


def stage_rwkv_prep(nc, A, Z):
    with ExitStack() as ctx:
        st = Stage(nc, ctx, "rp")
        z3 = [st.sb(f"z{n}", [P, 1 + S]) for n in range(3)]
        dif = st.sb("dif", [P, S])
        zk, tw, zas, sg = (st.sb(n, [P, S]) for n in ("zk", "tw", "zas", "sg"))
        lw, cum, cm, aa, e1, e2 = (st.sb(n, [P, S]) for n in ("lw", "cum", "cm", "aa", "e1", "e2"))
        kk, sq = st.sb("kk", [P, S]), st.sb("sq", [P, S])
        ar = st.sb("ar", [P, NCH, 2, CH])
        bt, kt, vt = (st.sb(n, [P, S]) for n in ("bt", "kt", "vt"))
        go = sq
        same = st.sb("same", [P, P])
        reset = st.sb("reset", [P, S])
        dec = st.sb("dec", [P, 2, NCH])
        wl = st.sb("wl", [P, 3, P])
        mu = st.sb("mu", [P, RW_IN // P])
        mu_l = st.sb("mu_l", [HD, 2])
        par = st.sb("par", [P, 5, PAIRS])
        psW, psA = st.ps("psW", [P, NB, 512]), st.ps("psA", [P, NB, 512])
        lora_in, par_in, loads, z_used, w_used = (
            st.sem(n) for n in ("lora_in", "par_in", "loads", "z_used", "w_used"))
        init, lora_ok, lora_act, made, acts, vec = (
            st.sem(n) for n in ("init", "lora_ok", "lora_act", "made", "acts", "vec"))
        kk0_ok, rk_ok, cm_ok, out_ok = (
            st.sem(n) for n in ("kk0_ok", "rk_ok", "cm_ok", "out_ok"))
        stored = st.lasting_sem("stored", Z["whole"])
        bon_ok, small, g_free = st.sem("bon_ok"), st.sem("small"), st.sem("g_free")
        MADE, ACTS, STORES = 5, 9, 6
        W0, A0, K_K, K_A, R_K = range(5)
        z, Zc = Z["z"], lambda row: Z["z"][bass.ds(row, P), :]
        block = st.block()

        @block.sync
        def _(sync):
            sync.wait_ge(init, 4)
            sync.dma_start(z3[0][0:LORA, 1:1 + S], z[ROW_W:ROW_W + LORA, :]).then_inc(lora_in, 16)
            sync.dma_start(z3[1][0:LORA, 1:1 + S], z[ROW_A:ROW_A + LORA, :]).then_inc(lora_in, 16)
            sync.dma_start(z3[2][:, 1:1 + S], z[ROW_G:ROW_G + P, :]).then_inc(lora_in, 16)
            sync.dma_start(mu[:, :], cols(A["mu_shift"][0], RW_IN // P)).then_inc(par_in, 16)
            sync.dma_start(mu_l[:, :], A["mu_shift"][0][ROW_W:ROW_G].rearrange("(c p) -> p c", c=2)).then_inc(par_in, 16)
            for n, name in enumerate(("rw_w0", "rw_a0", "rw_k_k", "rw_k_a")):
                sync.dma_start(par[:, n, :], cols(A[name][0], PAIRS)).then_inc(par_in, 16)
            sync.dma_start(par[:, R_K, :], cols(A["rw_r_k"][0].rearrange("h d -> (h d)"), PAIRS)).then_inc(par_in, 16)
            with sync.Fori(0, PAIRS) as i:
                sync.wait_ge(z_used, i + 1)
                for n, row in enumerate((ROW_R, ROW_K, ROW_V)):
                    sync.dma_start(z3[n][:, 1:1 + S], Zc(i * P + row)).then_inc(loads, 16)
                sync.wait_ge(w_used, i + 1)
                steady(sync, Z)
                sync.dma_start(wl[0:LORA, 0, :], A["rw_w2"][0][:, bass.ds(i * P, P)]).then_inc(loads, 16)
                sync.dma_start(wl[0:LORA, 1, :], A["rw_a2"][0][:, bass.ds(i * P, P)]).then_inc(loads, 16)
                sync.dma_start(wl[:, 2, :], A["rw_g2"][0][:, bass.ds(i * P, P)]).then_inc(loads, 16)
            sync.wait_ge(g_free, PAIRS * 16)

        @block.gpsimd
        def _(pool):
            for t in z3:
                pool.memset(t[:, 0:1], 0.0).then_inc(init, 1)
            pool.memset(reset[:, :], 1.0).then_inc(small, 1)
            pool.wait_ge(small, 1)
            pool.memset(reset[:, :].rearrange("p (c t) -> p c t", t=CH)[:, :, 0:1], 0.0).then_inc(init, 1)
            pool.memset(same[:, :], 0.0).then_inc(small, 1)
            pool.wait_ge(small, 2)
            pool.memset(same[0:HD, 0:HD], 1.0).then_inc(init, 1)
            pool.memset(same[HD:P, HD:P], 1.0).then_inc(init, 1)
            with pool.Fori(0, PAIRS) as i:
                pool.wait_ge(out_ok, i + 1)
                steady(pool, Z)
                pool.dma_start(Z["rar"][bass.ds(i * P, P), :, :, :], ar[:, :, :, :]).then_inc(stored, 16)
                pool.dma_start(Z["rb"][bass.ds(i * P, P), :], bt[:, :]).then_inc(stored, 16)
                pool.dma_start(Z["rk"][bass.ds(i * P, P), :], kt[:, :]).then_inc(stored, 16)
                pool.dma_start(Z["rv"][bass.ds(i * P, P), :], vt[:, :]).then_inc(stored, 16)
                pool.dma_start(Z["rdec"][bass.ds(i * P, P), :, :], dec[:, :, :]).then_inc(stored, 16)
                pool.dma_start(Z["rbonus"][bass.ds(i * P, P), :], dif[:, :]).then_inc(stored, 16)
                pool.wait_ge(stored, (i + 1) * 16 * STORES)
                steady(pool, Z)

        @block.tensor
        def _(pe):
            def product(dst, lhsT, rhs, k):
                for n in range(NB):
                    ins = pe.matmul(dst[:, n, :], lhsT, rhs[0:k, n * 512:(n + 1) * 512], start=True, stop=True)
                ins.then_inc(made, 1)

            pe.sem_inc(w_used, 1)
            pe.wait_ge(init, 6)
            pe.wait_ge(lora_act, 2)
            pe.wait_ge(lora_ok, 3)
            with pe.Fori(0, PAIRS) as i:
                pe.wait_ge(loads, (i + 1) * 96)
                pe.wait_ge(bon_ok, i)
                product(psW, wl[0:LORA, 0, :], tw, LORA)
                product(psA, wl[0:LORA, 1, :], zas, LORA)
                pe.wait_ge(acts, i * ACTS + 1)
                product(psW, wl[:, 2, :], sg, P)
                pe.wait_ge(acts, i * ACTS + 4)
                product(psA, same[:, :], sq, P)
                pe.wait_ge(made, i * MADE + 4)
                pe.sem_inc(w_used, 1)
                pe.wait_ge(rk_ok, i + 1)
                product(psW, same[:, :], cum, P)

        @block.scalar
        def _(act):
            a = Chain(act, acts)
            act.wait_ge(lora_ok, 1)
            act.activation(tw[0:LORA, :], tw[0:LORA, :], ACT.Tanh).then_inc(lora_act, 1)
            act.wait_ge(lora_ok, 3)
            act.activation(sg[:, :], sg[:, :], ACT.Sigmoid).then_inc(lora_act, 1)
            banks = lambda t: t[:, :].rearrange("p (n t) -> p n t", n=NB)
            with act.Fori(0, PAIRS) as i:
                a.loop(i, ACTS)
                act.wait_ge(made, i * MADE + 1)
                a.mark(act.activation(banks(lw), psW[:, :, :], ACT.Sigmoid, bias=par[:, W0, bass.ds(i, 1)]))
                act.wait_ge(made, i * MADE + 2)
                a.mark(act.activation(banks(aa), psA[:, :, :], ACT.Sigmoid, bias=par[:, A0, bass.ds(i, 1)]))
                act.wait_ge(made, i * MADE + 3)
                act.wait_ge(g_free, i * 16)
                a.link(act.copy(banks(go), psW[:, :, :]))
                act.dma_start(Z["rg"][bass.ds(i * P, P), :], go[:, :]).then_inc(g_free, 16)
                act.wait_ge(kk0_ok, i + 1)
                act.wait_ge(g_free, (i + 1) * 16)
                a.mark(act.activation(sq[:, :], kk[:, :], ACT.Square))
                act.wait_ge(made, i * MADE + 4)
                a.link(act.activation(banks(e1), psA[:, :, :], ACT.Sqrt))
                act.wait_ge(cm_ok, i + 1)
                a.mark(act.activation(e1[:, :], cm[:, :], ACT.Exp))
                a.mark(act.activation(e2[:, :], cm[:, :], ACT.Exp, scale=-1.0))
                a.mark(act.activation(lw[:, :], lw[:, :], ACT.Exp))
                act.activation(dec[:, 0, :], dec[:, 0, :], ACT.Exp)
                a.mark(act.activation(dec[:, 1, :], dec[:, 1, :], ACT.Exp))
                a.end(PAIRS)

        @block.vector
        def _(dve):
            v = Chain(dve, vec)

            def shift(out, src, m, n=P):
                v.link(dve.tensor_tensor(dif[0:n, :], src[0:n, 0:S], src[0:n, 1:1 + S], ALU.subtract))
                v.link(dve.scalar_tensor_tensor(out=out[0:n, :], in0=dif[0:n, :], scalar=m,
                                                in1=src[0:n, 1:1 + S], op0=ALU.mult, op1=ALU.add))

            dve.wait_ge(init, 6)
            dve.wait_ge(lora_in, 48)
            dve.wait_ge(par_in, 16 * 7)
            shift(tw, z3[0], mu_l[:, 0:1], LORA)
            dve.sem_inc(lora_ok, 1)
            shift(zas, z3[1], mu_l[:, 1:2], LORA)
            shift(sg, z3[2], mu[:, RW_IN // P - 1:RW_IN // P])
            dve.sem_inc(lora_ok, 2)
            dve.sem_inc(z_used, 1)
            chunks = lambda t: t[:, :].rearrange("p (c t) -> p c t", t=CH)
            with dve.Fori(0, PAIRS) as i:
                v.loop(i, 20)
                dve.wait_ge(loads, (i + 1) * 96)
                dve.wait_ge(stored, i * 16 * STORES)
                shift(cum, z3[0], mu[:, bass.ds(i, 1)])
                shift(zk, z3[1], mu[:, bass.ds(i + PAIRS, 1)])
                shift(vt, z3[2], mu[:, bass.ds(i + 2 * PAIRS, 1)])
                v.link(dve.tensor_copy(ar[:, :, 1, :], chunks(cum)))
                dve.sem_inc(z_used, 1)
                v.link(dve.tensor_scalar(kk[:, :], zk[:, :], par[:, K_K, bass.ds(i, 1)], None, ALU.mult))
                dve.sem_inc(kk0_ok, 1)
                dve.wait_ge(acts, i * ACTS + 1)
                v.link(dve.tensor_scalar(lw[:, :], lw[:, :], -DECAY_SCALE, None, ALU.mult))
                v.link(dve.tensor_tensor_scan(cum[:, :], reset[:, :], lw[:, :], 0.0, ALU.mult, ALU.add))
                mid = chunks(cum)[:, :, CH // 2 - 1:CH // 2]
                v.link(dve.tensor_tensor(chunks(cm), chunks(cum), mid.to_broadcast([P, NCH, CH]), ALU.subtract))
                dve.tensor_copy(dec[:, 0, :].rearrange("p (c o) -> p c o", o=1), mid)
                dve.tensor_copy(dec[:, 1, :].rearrange("p (c o) -> p c o", o=1), chunks(cm)[:, :, CH - 1:CH])
                v.link(dve.tensor_tensor(lw[:, :], cm[:, :], lw[:, :], ALU.subtract))
                dve.wait_ge(acts, i * ACTS + 5)
                v.link(dve.tensor_scalar(dif[:, :], e1[:, :], 1e-12, None, ALU.max))
                dve.sem_inc(cm_ok, 1)
                v.link(dve.reciprocal(dif[:, :], dif[:, :]))
                v.link(dve.tensor_tensor(kk[:, :], kk[:, :], dif[:, :], ALU.mult))
                dve.wait_ge(acts, i * ACTS + 2)
                v.link(dve.tensor_scalar(dif[:, :], aa[:, :], -1.0, par[:, K_A, bass.ds(i, 1)], ALU.add, ALU.mult))
                v.link(dve.scalar_tensor_tensor(out=zk[:, :], in0=dif[:, :], scalar=1.0, in1=zk[:, :],
                                                op0=ALU.add, op1=ALU.mult))
                v.link(dve.scalar_tensor_tensor(out=chunks(cum), in0=ar[:, :, 1, :], scalar=par[:, R_K, bass.ds(i, 1)],
                                                in1=chunks(zk), op0=ALU.mult, op1=ALU.mult))
                dve.wait_ge(acts, i * ACTS + 3)
                dve.sem_inc(rk_ok, 1)
                v.mark(dve.tensor_tensor(aa[:, :], kk[:, :], aa[:, :], ALU.mult))
                dve.wait_ge(acts, i * ACTS + 9)
                v.wait()
                dve.tensor_tensor(bt[:, :], aa[:, :], e2[:, :], ALU.mult)
                dve.tensor_tensor(kt[:, :], zk[:, :], e2[:, :], ALU.mult)
                dve.scalar_tensor_tensor(out=ar[:, :, 0, :], in0=chunks(kk), scalar=-1.0, in1=chunks(lw),
                                         op0=ALU.mult, op1=ALU.mult)
                dve.tensor_tensor(ar[:, :, 1, :], ar[:, :, 1, :], chunks(e1), ALU.mult)
                dve.wait_ge(made, (i + 1) * MADE)
                v.link(dve.tensor_tensor(dif[:, :].rearrange("p (n t) -> p n t", n=NB), psW[:, :, :],
                                         vt[:, :].rearrange("p (n t) -> p n t", n=NB), ALU.mult))
                dve.sem_inc(bon_ok, 1)
                dve.sem_inc(out_ok, 1)
                v.end(PAIRS)


LEVELS = 7


def stage_rwkv_scan(nc, A, Z):
    H, HG = RW_HEADS, 4
    with ExitStack() as ctx:
        st = Stage(nc, ctx, "rs")
        ar = st.sb("ar", [HD, 2, H, 2, CH])
        bkv = st.sb("bkv", [HD, 2, 3, H, CH])
        tok = st.sb("tok", [P, 3, H, HD])
        M = st.sb("M", [P, H, 4, CH])
        Lm = st.sb("Lm", [P, 2, HG, CH])
        X = st.sb("X", [P, 2, HG, CH])
        inv = st.sb("inv", [P, 2, HG, CH])
        invT = st.sb("invT", [P, 2, HG, CH])
        Wt, U = st.sb("W", [P, H, HD]), st.sb("U", [P, H, HD])
        state, mid = st.sb("state", [HD, H, HD]), st.sb("mid", [HD, H, HD])
        o = st.sb("o", [HD, H, CH])
        dec = st.sb("dec", [HD, H, 2, NCH])
        ident = st.sb("ident", [P, P])
        row, col, row_s, col_s = (st.sb(n, [P, P], I32) for n in ("row", "col", "row_s", "col_s"))
        upper = st.sb("upper", [P, 4, CH])
        block_of = st.sb("block_of", [P, LEVELS + 1, CH])
        join = st.sb("join", [P, LEVELS, CH])
        bank = st.ps("bank", [P, 8, 512])
        XB, DB, EB, SCORE, WB, UB, OB, SB = (0, 1), (2, 3), (4, 5), (3, 4, 5), 6, 7, (0, 1), 2
        loads = st.sems("loads", 2)
        ld_used, dec_in, id_ok, setup, tables, turned, scored = (
            st.sem(n) for n in ("ld_used", "dec_in", "id_ok", "setup", "tables", "turned", "scored"))
        x_made, d_made, e_made, w_made, u_made, o_made, s_made = (
            st.sem(n) for n in ("x_made", "d_made", "e_made", "w_made", "u_made", "o_made", "s_made"))
        tok_ok, m_ok, l_ok, x_ok, d_ok, e_ok, w_ok, u_ok, o_ok, s_ok, mid_ok = (
            st.sem(n) for n in ("tok_ok", "m_ok", "l_ok", "x_ok", "d_ok", "e_ok", "w_ok", "u_ok", "o_ok", "s_ok", "mid_ok"))
        o_out = st.sem("o_out")
        block = st.block()
        heads = lambda t: t.rearrange("(h d) s -> d h s", h=H)

        @block.sync
        def _(sync):
            sync.dma_start(dec[:, :, :, :], Z["rdec"].rearrange("(h d) a c -> d h a c", h=H)).then_inc(dec_in, 16)
            with sync.Fori(0, NCH // 2) as i:
                for k in range(2):
                    c = 2 * i + k
                    sync.wait_ge(ld_used, c + 1)
                    for h2 in range(2):
                        sync.dma_start(ar[:, k, 4 * h2:4 * h2 + 4, :, :],
                                       Z["rar"].rearrange("(h d) c a t -> d h c a t", h=H)[:, 4 * h2:4 * h2 + 4, bass.ds(c, 1), :, :]
                                       .rearrange("d h c a t -> d h (c a t)")).then_inc(loads[k], 16)
                    for n, name in enumerate(("rb", "rk", "rv")):
                        sync.dma_start(bkv[:, k, n, :, :], heads(Z[name])[:, :, bass.ds(c * CH, CH)]).then_inc(loads[k], 16)

        @block.gpsimd
        def _(pool):
            build_identity(pool, ident, id_ok)
            pool.iota(row[:, :], [[0, P]], base=0, channel_multiplier=1).then_inc(setup, 1)
            pool.iota(col[:, :], [[1, P]], base=0, channel_multiplier=0).then_inc(setup, 1)
            pool.wait_ge(tables, 1)
            with pool.Fori(0, NCH // 2) as i:
                for k in range(2):
                    c = 2 * i + k
                    for lev in range(LEVELS):
                        for g in range(2):
                            if lev == 0:
                                pool.wait_ge(m_ok, 8 * c + 4 * g + 4)
                            pool.wait_ge(x_made, 14 * c + 2 * lev + g - 1 if lev else 14 * c)
                            if lev == 1:
                                pool.wait_ge(e_ok, 14 * c + g + 1)
                            pool.tensor_tensor(Lm[:, g, :, :], M[:, 4 * g:4 * g + 4, 0, :],
                                               join[:, lev:lev + 1, :].to_broadcast([P, HG, CH]),
                                               ALU.mult).then_inc(l_ok, 1)

        @block.tensor
        def _(pe):
            pe.sem_inc(ld_used, 2)
            pe.wait_ge(id_ok, 2)
            with pe.Fori(0, NCH // 2) as i:
                for k in range(2):
                    c = 2 * i + k
                    pe.wait_ge(loads[k], (i + 1) * 80)
                    pe.wait_ge(o_ok, c)
                    pe.wait_ge(s_ok, c + 1)
                    steady(pe, Z)
                    for n in range(3):
                        for h in range(H):
                            ins = pe.transpose(bank[:, n, h * HD:(h + 1) * HD], bkv[:, k, n, h, :], ident[0:HD, 0:HD])
                        ins.then_inc(turned, 1)
                    for h in range(H):
                        if h >= 3:
                            pe.wait_ge(m_ok, 8 * c + h - 2)
                        b = SCORE[h % 3]
                        arh = ar[:, k, h, :, :].rearrange("d a t -> d (a t)")
                        pe.matmul(bank[:, b, 0:2 * CH], bkv[:, k, 0, h, :], arh, start=True, stop=True)
                        pe.matmul(bank[:, b, 2 * CH:4 * CH], bkv[:, k, 1, h, :], arh, start=True, stop=True).then_inc(scored, 1)
                    pe.wait_ge(m_ok, 8 * c + 8)
                    for g in range(2):
                        pe.wait_ge(l_ok, 14 * c + g + 1)
                        if g == 0:
                            pe.wait_ge(tok_ok, 3 * c + 3)
                        for h in range(HG):
                            ins = pe.matmul(bank[:, DB[g], h * CH:(h + 1) * CH], Lm[:, g, h, :], ident[:, :],
                                            start=True, stop=True)
                        ins.then_inc(d_made, 1)
                        pe.wait_ge(d_made, 12 * c + g + 1)
                        pe.sem_inc(x_made, 1)
                    for lev in range(1, LEVELS):
                        for g in range(2):
                            pe.wait_ge(l_ok, 14 * c + 2 * lev + g + 1)
                            pe.wait_ge(d_ok, 12 * c + 2 * lev + g - 1)
                            for h in range(HG):
                                ins = pe.matmul(bank[:, XB[g], h * CH:(h + 1) * CH], Lm[:, g, h, :], inv[:, g, h, :],
                                                start=True, stop=True)
                            ins.then_inc(x_made, 1)
                        for g in range(2):
                            pe.wait_ge(x_ok, 12 * c + 2 * lev + g - 1)
                            pe.wait_ge(e_ok, 14 * c + 2 * lev + g - 1)
                            if lev < LEVELS - 1:
                                for h in range(HG):
                                    ins = pe.matmul(bank[:, DB[g], h * CH:(h + 1) * CH], invT[:, g, h, :], X[:, g, h, :],
                                                    start=True, stop=True)
                                ins.then_inc(d_made, 1)
                            for h in range(HG):
                                ins = pe.matmul(bank[:, EB[g], h * CH:(h + 1) * CH], X[:, g, h, :], invT[:, g, h, :],
                                                start=True, stop=True)
                            ins.then_inc(e_made, 1)
                    pe.wait_ge(mid_ok, c + 1)
                    for h in range(H):
                        pe.matmul(bank[:, WB, h * HD:(h + 1) * HD], ar[:, k, h, 0, :], mid[:, h, :], start=True, stop=False)
                        ins = pe.matmul(bank[:, WB, h * HD:(h + 1) * HD], M[:, h, 2, :], tok[:, 2, h, :],
                                        start=False, stop=True)
                    ins.then_inc(w_made, 1)
                    pe.wait_ge(w_ok, c + 1)
                    pe.wait_ge(e_ok, 14 * c + 14)
                    for h in range(H):
                        ins = pe.matmul(bank[:, UB, h * HD:(h + 1) * HD], invT[:, h // HG, h % HG, :], Wt[:, h, :],
                                        start=True, stop=True)
                    ins.then_inc(u_made, 1)
                    pe.wait_ge(u_ok, c + 1)
                    for h in range(H):
                        pe.matmul(bank[0:HD, SB, h * HD:(h + 1) * HD], tok[:, 0, h, :], U[:, h, :], start=True, stop=False)
                        ins = pe.matmul(bank[0:HD, SB, h * HD:(h + 1) * HD], tok[:, 1, h, :], tok[:, 2, h, :],
                                        start=False, stop=True)
                    ins.then_inc(s_made, 1)
                    for h in range(H):
                        dst = bank[0:HD, OB[h // HG], (h % HG) * CH:(h % HG + 1) * CH]
                        pe.matmul(dst, mid[:, h, :], ar[:, k, h, 1, :], start=True, stop=False)
                        pe.matmul(dst, U[:, h, :], M[:, h, 1, :], start=False, stop=False)
                        ins = pe.matmul(dst, tok[:, 2, h, :], M[:, h, 3, :], start=False, stop=True)
                    ins.then_inc(o_made, 1)
                    pe.wait_ge(o_made, c + 1)
                    pe.sem_inc(ld_used, 1)

        @block.scalar
        def _(act):
            with act.Fori(0, NCH // 2) as i:
                for k in range(2):
                    c = 2 * i + k
                    act.wait_ge(o_made, c)
                    for n in range(3):
                        act.wait_ge(turned, 3 * c + n + 1)
                        act.copy(tok[:, n, :, :].rearrange("p h d -> p (h d)"), bank[:, n, :]).then_inc(tok_ok, 1)
                    for lev in range(1, LEVELS):
                        for g in range(2):
                            act.wait_ge(x_made, 14 * c + 2 * lev + g + 1)
                            act.wait_ge(e_made, 12 * c + 2 * lev - 2 + g)
                            act.copy(X[:, g, :, :].rearrange("p h t -> p (h t)"), bank[:, XB[g], :]).then_inc(x_ok, 1)
                    act.wait_ge(w_made, c + 1)
                    act.copy(Wt[:, :, :].rearrange("p h d -> p (h d)"), bank[:, WB, :]).then_inc(w_ok, 1)
                    act.wait_ge(o_made, c + 1)
                    act.wait_ge(o_out, c * 16)
                    act.copy(o[:, :, :].rearrange("p (b h) t -> p b (h t)", b=2), bank[0:HD, 0:2, :]).then_inc(o_ok, 1)
                    act.wait_ge(o_ok, c + 1)
                    act.dma_start(heads(Z["ro"])[:, :, bass.ds(c * CH, CH)], o[:, :, :]).then_inc(o_out, 16)
            act.wait_ge(o_out, NCH * 16)

        @block.vector
        def _(dve):
            v = Chain(dve, setup)
            v.n = 2
            dve.wait_ge(setup, 2)
            for lev in range(LEVELS + 1):
                v.mark(dve.tensor_scalar(row_s[:, :], row[:, :], lev, None, ALU.arith_shift_right))
                v.link(dve.tensor_scalar(col_s[:, :], col[:, :], lev, None, ALU.arith_shift_right))
                v.link(dve.tensor_tensor(block_of[:, lev, :], row_s[:, :], col_s[:, :], ALU.is_equal))
            for n in range(4):
                v.link(dve.tensor_tensor(upper[:, n, :], col[:, :], row[:, :], ALU.is_ge if n % 2 else ALU.is_gt))
            for lev in range(LEVELS):
                v.link(dve.tensor_tensor(join[:, lev, :], block_of[:, lev + 1, :], block_of[:, lev, :], ALU.subtract))
                v.link(dve.tensor_tensor(join[:, lev, :], join[:, lev, :], upper[:, 0, :], ALU.mult))
            v.link(dve.memset(state[:, :, :], 0.0))
            dve.sem_inc(tables, 1)
            dve.sem_inc(s_ok, 1)
            dve.wait_ge(dec_in, 16)
            dve.wait_ge(id_ok, 2)
            eye = ident[:, :].rearrange("p (o t) -> p o t", o=1).to_broadcast([P, HG, CH])
            flat = lambda t: t.rearrange("p h t -> p (h t)")
            in_bank = lambda b: bank[:, b, :].rearrange("p (h t) -> p h t", h=HG)
            with dve.Fori(0, NCH // 2) as i:
                for k in range(2):
                    c = 2 * i + k
                    dve.wait_ge(s_ok, c + 1)
                    dve.wait_ge(o_made, c)
                    dve.tensor_tensor(mid[:, :, :], state[:, :, :],
                                      dec[:, :, 0, bass.ds(c, 1)].to_broadcast([HD, H, HD]), ALU.mult).then_inc(mid_ok, 1)
                    for h in range(H):
                        dve.wait_ge(scored, 8 * c + h + 1)
                        dve.tensor_tensor(M[:, h, :, :].rearrange("p a t -> p (a t)"), bank[:, SCORE[h % 3], :],
                                          upper[:, :, :].rearrange("p a t -> p (a t)"), ALU.mult).then_inc(m_ok, 1)
                    for g in range(2):
                        dve.wait_ge(l_ok, 14 * c + g + 1)
                        dve.tensor_tensor(invT[:, g, :, :], Lm[:, g, :, :], eye, ALU.add).then_inc(e_ok, 1)
                        dve.wait_ge(d_made, 12 * c + g + 1)
                        dve.tensor_tensor(inv[:, g, :, :], in_bank(DB[g]), eye, ALU.add).then_inc(d_ok, 1)
                    for lev in range(1, LEVELS):
                        for g in range(2):
                            dve.wait_ge(d_ok, 12 * c + 2 * lev + g - 1)
                            dve.wait_ge(e_ok, 14 * c + 2 * lev + g - 1)
                            dve.wait_ge(e_made, 12 * c + 2 * lev + g - 1)
                            if lev < LEVELS - 1:
                                dve.tensor_tensor(inv[:, g, :, :], in_bank(DB[g]), inv[:, g, :, :],
                                                  ALU.add).then_inc(d_ok, 1)
                            dve.tensor_tensor(invT[:, g, :, :], in_bank(EB[g]), invT[:, g, :, :],
                                              ALU.add).then_inc(e_ok, 1)
                    dve.wait_ge(u_made, c + 1)
                    dve.tensor_copy(U[:, :, :].rearrange("p h d -> p (h d)"), bank[:, UB, :]).then_inc(u_ok, 1)
                    dve.wait_ge(s_made, c + 1)
                    dve.tensor_tensor(state[:, :, :].rearrange("p h d -> p (h d)"),
                                      mid[:, :, :].rearrange("p h d -> p (h d)"), bank[0:HD, SB, :], ALU.add).then_inc(tables, 1)
                    dve.wait_ge(tables, c + 2)
                    dve.tensor_tensor(state[:, :, :], state[:, :, :],
                                      dec[:, :, 1, bass.ds(c, 1)].to_broadcast([HD, H, HD]), ALU.mult).then_inc(s_ok, 1)


def stage_rwkv_post(nc, A, Z):
    with ExitStack() as ctx:
        st = Stage(nc, ctx, "rn")
        o, bonus, g, sd = (st.sb(n, [P, 2, S]) for n in ("o", "bonus", "g", "sd"))
        sq = st.sb("sq", [P, S])
        average = st.sb("average", [P, P])
        eps = st.sb("eps", [P, 1])
        par = st.sb("par", [P, 2, PAIRS])
        mean, var = st.ps("mean", [P, NB, 512]), st.ps("var", [P, NB, 512])
        loads, stored = st.sems("loads", 2), st.sems("stored", 2)
        init, par_in, mean_made, var_made, centred, squared, rooted, y_ok, steps = (
            st.sem(n) for n in ("init", "par_in", "mean_made", "var_made", "centred", "squared", "rooted", "y_ok", "steps"))
        block = st.block()
        rows = lambda t, c: t[bass.ds(c * P, P), :]
        banks = lambda t: t.rearrange("p (n t) -> p n t", n=NB)

        @block.sync
        def _(sync):
            for n, name in enumerate(("rw_ln_w", "rw_ln_b")):
                sync.dma_start(par[:, n, :], cols(A[name][0], PAIRS)).then_inc(par_in, 16)
            with sync.Fori(0, PAIRS // 2) as i:
                for k in range(2):
                    sync.wait_ge(stored[k], i * 16)
                    for t, name in ((o, "ro"), (bonus, "rbonus"), (g, "rg")):
                        sync.dma_start(t[:, k, :], rows(Z[name], 2 * i + k)).then_inc(loads[k], 16)

        @block.gpsimd
        def _(pool):
            pool.memset(average[:, :], 0.0).then_inc(init, 1)
            pool.wait_ge(init, 1)
            pool.memset(average[0:HD, 0:HD], 1.0 / HD).then_inc(init, 1)
            pool.memset(average[HD:P, HD:P], 1.0 / HD).then_inc(init, 1)
            pool.wait_ge(init, 3)
            pool.memset(eps[:, :], GN_EPS).then_inc(init, 1)
            with pool.Fori(0, PAIRS // 2) as i:
                for k in range(2):
                    pool.wait_ge(y_ok, 2 * i + k + 1)
                    pool.dma_start(rows(Z["yr"], 2 * i + k), o[:, k, :]).then_inc(stored[k], 16)
            for k in range(2):
                pool.wait_ge(stored[k], PAIRS // 2 * 16)

        @block.tensor
        def _(pe):
            pe.wait_ge(init, 4)
            with pe.Fori(0, PAIRS // 2) as i:
                for k in range(2):
                    pe.wait_ge(loads[k], (i + 1) * 48)
                    pe.wait_ge(centred, 2 * i + k)
                    for n in range(NB):
                        ins = pe.matmul(mean[:, n, :], average[:, :], o[:, k, n * 512:(n + 1) * 512], start=True, stop=True)
                    ins.then_inc(mean_made, 1)
                for k in range(2):
                    pe.wait_ge(squared, 2 * i + k + 1)
                    pe.wait_ge(rooted, 2 * i + k)
                    for n in range(NB):
                        ins = pe.matmul(var[:, n, :], average[:, :], sq[:, n * 512:(n + 1) * 512], start=True, stop=True)
                    ins.then_inc(var_made, 1)

        @block.scalar
        def _(act):
            act.wait_ge(init, 4)
            with act.Fori(0, PAIRS // 2) as i:
                for k in range(2):
                    act.wait_ge(centred, 2 * i + k + 1)
                    act.wait_ge(var_made, 2 * i + k)
                    act.activation(sq[:, :], o[:, k, :], ACT.Square).then_inc(squared, 1)
                    act.wait_ge(var_made, 2 * i + k + 1)
                    act.activation(banks(sd[:, k, :]), var[:, :, :], ACT.Sqrt, bias=eps[:, 0:1]).then_inc(rooted, 1)

        @block.vector
        def _(dve):
            v = Chain(dve, steps)
            dve.wait_ge(par_in, 32)
            with dve.Fori(0, PAIRS // 2) as i:
                v.loop(i, 8)
                for k in range(2):
                    dve.wait_ge(mean_made, 2 * i + k + 1)
                    dve.tensor_tensor(banks(o[:, k, :]), banks(o[:, k, :]), mean[:, :, :], ALU.subtract).then_inc(centred, 1)
                for k in range(2):
                    dve.wait_ge(rooted, 2 * i + k + 1)
                    v.link(dve.reciprocal(sd[:, k, :], sd[:, k, :]))
                    v.link(dve.tensor_tensor(o[:, k, :], o[:, k, :], sd[:, k, :], ALU.mult))
                    v.link(dve.tensor_scalar(o[:, k, :], o[:, k, :], par[:, 0, bass.ds(2 * i + k, 1)],
                                             par[:, 1, bass.ds(2 * i + k, 1)], ALU.mult, ALU.add))
                    v.link(dve.tensor_tensor(o[:, k, :], o[:, k, :], bonus[:, k, :], ALU.add))
                    dve.tensor_tensor(o[:, k, :], o[:, k, :], g[:, k, :], ALU.mult).then_inc(y_ok, 1)
                v.end(PAIRS // 2)


CMP_BLOCK, CMP_STRIDE, SEL_BLOCK, N_SELECT, WINDOW = 32, 16, 64, 8, 512
N_CMP = (S - CMP_BLOCK) // CMP_STRIDE + 1
N_SEL = S // SEL_BLOCK
LOWEST = -3e38
STEPS = 59
SLOPES = [2.0 ** (-8.0 * (h + 1) / NSA_HEADS) for h in range(NSA_HEADS)]


def stage_nsa(nc, A, Z):
    G, R = KV_HEADS, Q_PER_KV
    outer = ExitStack()
    with outer:
        kp = Stage(nc, outer, "at")
        ks_h, ks_r = (kp.sb(n, [P, S]) for n in ("ks_h", "ks_r"))
        kw_h, kw_r = (kp.sb(n, [P, WINDOW + S + P]) for n in ("kw_h", "kw_r"))
        vs = kp.sb("vs", [P, NT, P])
        vw = kp.sb("vw", [P, WINDOW // P + NT, P])
        kcmp = kp.sb("kcmp", [P, P])
        vcmp = kp.sb("vcmp", [P, G, HD])
        ident = kp.sb("ident", [P, P])

        with ExitStack() as ctx:
            st = Stage(nc, ctx, "cp")
            kv = st.sb("kv", [HD, 2, G, S])
            w1 = st.sb("w1", [HD, 2, CMP_BLOCK, HD])
            w2_k = st.sb("w2_k", [HD, G, P])
            w2_v = st.sb("w2_v", [HD, HD])
            pos = st.sb("pos", [HD, 2, CMP_BLOCK])
            pos_p = st.sb("pos_p", [HD, 2])
            hid = st.sb("hid", [HD, 2, G, N_CMP])
            v_raw = st.sb("v_raw", [P, 2, S])
            ks_t = st.sb("ks_t", [P, S])
            kw_t = st.sb("kw_t", [P, WINDOW + S + P])
            key_steps = st.sem("key_steps")
            acc = st.ps("acc", [P, 2, 512])
            out = st.ps("out", [P, 512])
            tp = st.ps("tp", [P, 4, 512])
            in_k, in_v, in_w, id_ok, hid_made, pos_ok, hid_ok, out_made, out_ok, turned, tok_ok, zeros, w2_clear = (
                st.sem(n) for n in ("in_k", "in_v", "in_w", "id_ok", "hid_made", "pos_ok", "hid_ok", "out_made",
                                    "out_ok", "turned", "tok_ok", "zeros", "w2_clear"))
            block = st.block()

            @block.sync
            def _(sync):
                for a, (row, n) in enumerate(((ROW_KC, "k"), (ROW_VC, "v"))):
                    sync.dma_start(w1[:, a, :, :], A[f"cmp_{n}_w1"][0].rearrange("(l d) e -> d l e", d=HD)).then_inc(in_w, 16)
                    sync.dma_start(pos[:, a, :], A[f"cmp_pos_{n}"][0].rearrange("l d -> d l")).then_inc(in_w, 16)
                    sync.dma_start(kv[:, a, :, :], Z["z"][row:row + P, :].rearrange("(g d) s -> d g s", g=G)).then_inc(in_w, 16)
                sync.dma_start(w2_v[:, :], A["cmp_v_w2"][0]).then_inc(in_w, 16)
                sync.wait_ge(w2_clear, 1)
                for g in range(G):
                    sync.dma_start(w2_k[:, g, g * HD:(g + 1) * HD], A["cmp_k_w2"][0]).then_inc(in_w, 16)
                sync.dma_start(v_raw[:, 0, :], Z["z"][ROW_VS:ROW_VS + P, :]).then_inc(in_v, 16)
                sync.dma_start(v_raw[:, 1, :], Z["z"][ROW_VW:ROW_VW + P, :]).then_inc(in_v, 16)
                sync.dma_start(ks_t[:, :], Z["z"][ROW_KS:ROW_KS + P, :]).then_inc(in_k, 16)
                sync.dma_start(kw_t[:, WINDOW:WINDOW + S], Z["z"][ROW_KW:ROW_KW + P, :]).then_inc(in_k, 16)
                sync.wait_ge(in_k, 32)

            @block.gpsimd
            def _(pool):
                build_identity(pool, ident, id_ok)
                pool.memset(w2_k[:, :, :], 0.0).then_inc(w2_clear, 1)
                pool.memset(kw_t[:, 0:WINDOW], 0.0).then_inc(zeros, 1)
                pool.memset(kw_t[:, WINDOW + S:WINDOW + S + P], 0.0).then_inc(zeros, 1)
                pool.memset(vw[:, 0:WINDOW // P, :], 0.0).then_inc(zeros, 1)
                pool.wait_ge(zeros, 3)

            @block.tensor
            def _(pe):
                pe.wait_ge(in_w, 16 * 9)
                for a in range(2):
                    for g in range(G):
                        for l in range(CMP_BLOCK):
                            pe.matmul(acc[0:HD, a, g * P:g * P + N_CMP], w1[:, a, l, :],
                                      kv[:, a, g, l:l + CMP_STRIDE * (N_CMP - 1) + 1:CMP_STRIDE],
                                      start=(l == 0), stop=(l == CMP_BLOCK - 1))
                    for l in range(CMP_BLOCK):
                        ins = pe.matmul(acc[0:HD, a, 2 * P:2 * P + 1], w1[:, a, l, :], pos[:, a, l:l + 1],
                                        start=(l == 0), stop=(l == CMP_BLOCK - 1))
                    ins.then_inc(hid_made, 1)
                pe.wait_ge(id_ok, 2)
                pe.wait_ge(in_v, 32)
                for n in range(8):
                    if n >= 4:
                        pe.wait_ge(tok_ok, n - 3)
                    for t in range(4):
                        ins = pe.transpose(tp[:, n % 4, t * P:(t + 1) * P],
                                           v_raw[:, n // 4, (n % 4 * 4 + t) * P:(n % 4 * 4 + t + 1) * P], ident[:, :])
                    ins.then_inc(turned, 1)
                pe.wait_ge(hid_ok, 2 * G)
                for g in range(G):
                    pe.matmul(out[:, 0:N_CMP], w2_k[:, g, :], hid[:, 0, g, :], start=(g == 0), stop=(g == G - 1))
                for g in range(G):
                    ins = pe.matmul(out[0:N_CMP, (2 + g) * P:(2 + g) * P + HD], hid[:, 1, g, :], w2_v[:, :],
                                    start=True, stop=True)
                ins.then_inc(out_made, 1)

            @block.scalar
            def _(act):
                for a in range(2):
                    act.wait_ge(hid_made, a + 1)
                    act.copy(pos_p[:, a:a + 1], acc[0:HD, a, 2 * P:2 * P + 1]).then_inc(pos_ok, 1)
                    act.wait_ge(pos_ok, a + 1)
                    for g in range(G):
                        act.activation(hid[:, a, g, :], acc[0:HD, a, g * P:g * P + N_CMP], ACT.Gelu_apprx_tanh,
                                       bias=pos_p[:, a:a + 1]).then_inc(hid_ok, 1)

            @block.vector
            def _(dve):
                v = Chain(dve, key_steps)
                dve.wait_ge(in_k, 32)
                dve.wait_ge(zeros, 3)
                v.mark(split(v, ks_t[:, :], ks_h[:, :], ks_r[:, :]))
                v.link(split(v, kw_t[:, :], kw_h[:, :], kw_r[:, :]))
                for n in range(8):
                    dve.wait_ge(turned, n + 1)
                    dst = vs[:, n * 4:n * 4 + 4, :] if n < 4 else vw[:, n * 4 - 12:n * 4 - 8, :]
                    dve.tensor_copy(dst, tp[:, n % 4, :].rearrange("p (t c) -> p t c", t=4)).then_inc(tok_ok, 1)
                dve.wait_ge(out_made, 1)
                dve.tensor_copy(kcmp[:, 0:N_CMP], out[:, 0:N_CMP]).then_inc(out_ok, 1)
                for g in range(G):
                    dve.tensor_copy(vcmp[0:N_CMP, g, :], out[0:N_CMP, (2 + g) * P:(2 + g) * P + HD]).then_inc(out_ok, 1)
                dve.wait_ge(out_ok, 3)

        with ExitStack() as ctx:
            st = Stage(nc, ctx, "aq")
            WK = WINDOW + P
            WB = WK // P
            t_sel = st.sb("t_sel", [P, S + 1024])
            t_win, t_win0 = st.sb("t_win", [P, WK]), st.sb("t_win0", [P, WK])
            t_pad = st.sb("t_pad", [P, WINDOW + WK])
            t_cmp, t_cmp_t = st.sb("t_cmp", [P, 256]), st.sb("t_cmp_t", [P, N_CMP])
            rows_ok = st.sb("rows_ok", [P, NT + 1])
            keep_t, force_t = st.sb("keep_t", [P, 64]), st.sb("force_t", [P, 64])
            q_scale = st.sb("q_scale", [P, R])
            gate_b = st.sb("gate_b", [P, N_GATE])
            q_raw = st.sb("q_raw", [P, R, P])
            q, q_h, q_r = (st.sb(n, [P, G, R, P]) for n in ("q", "q_h", "q_r"))
            g_raw, gates = st.sb("g_raw", [N_GATE, P]), st.sb("gates", [P, N_GATE])
            pc = st.sb("pc", [P, R, P])
            pct = st.sb("pct", [P, R, P])
            oc = st.sb("oc", [P, G, R, HD])
            cst = st.sb("cst", [P, 4, R])
            psum_c = st.sb("psum_c", [P, P + 4])
            imp, imp2, sel = (st.sb(n, [P, N_SEL]) for n in ("imp", "imp2", "sel"))
            top = st.sb("top", [P, 8])
            tg = st.sb("tg", [P, S])
            sc = st.sb("sc", [P, 2, R, S])
            mxc = st.sb("mxc", [P, 4 * R, 4])
            ust = st.sb("ust", [P, 3, 4 * R])
            pt = st.sb("pt", [P, 2, R, P])
            vwin = st.sb("vwin", [P, WB, P])
            oT = st.sb("oT", [HD, R, P])
            part = st.sb("part", [P, R, HD])
            y, yT = st.sb("y", [P, NSA_W]), st.sb("yT", [P, NSA_W // P, P])
            s_bank, t_bank = st.ps("s_bank", [P, 2, 512]), st.ps("t_bank", [P, 2, 512])
            o_bank, back = st.ps("o_bank", [P, 2, 512]), st.ps("back", [P, 512])
            misc = st.ps("misc", [P, 512])
            tabs, tab_ok, small_in, q_in, q_used, q_ok, g_in, g_used = (
                st.sem(n) for n in ("tabs", "tab_ok", "small_in", "q_in", "q_used", "q_ok", "g_in", "g_used"))
            s_made, s_read, max_ok, exp_ok, turned, pt_a, pt_v, pv_made = (
                st.sem(n) for n in ("s_made", "s_read", "max_ok", "exp_ok", "turned", "pt_a", "pt_v", "pv_made"))
            misc_made, misc_read, cmax_ok, cexp_ok, pc_ok, y_ok, y_out, vec = (
                st.sem(n) for n in ("misc_made", "misc_read", "cmax_ok", "cexp_ok", "pc_ok", "y_ok", "y_out", "vec"))
            gate_ok, gated, ot_ok, back_made, back_read, win_used, win_ok = (
                st.sem(n) for n in ("gate_ok", "gated", "ot_ok", "back_made", "back_read", "win_used", "win_ok"))
            block = st.block()
            UNITS = 2 * G
            FRONT = 3
            MISC = 2 + G * FRONT

            def n_blocks(j, grp):
                return 4 * (grp + 1) if j % 2 else WB

            def runs(j, grp):
                widths = [512] * (grp + 1) if j % 2 else [WINDOW, P]
                return [(h, r, wd) for h in range(R) for r, wd in enumerate(widths)]

            def made_in(j, k, grp):
                rs = runs(j + 1, grp)
                return [(i, run) for i, run in enumerate(rs) if i * (n_blocks(j, grp) - 1) // len(rs) == k]

            def last_run(h, r, j, grp):
                return r == (grp if j % 2 else 1)

            def by_dve(j, k):
                return k % 2 == 1 and (j % 2 == 0 or k >= 5)

            class Tile:

                def __init__(self, grp, tau):
                    def each(f):
                        per = [f(g) for g in range(grp + 1)]
                        return 4 * sum(per[:-1]) + tau * per[-1]

                    flags = lambda g: [by_dve(j, k) for j in range(UNITS) for k in range(n_blocks(j, g))]
                    self.t, self.grp, self.flags = tau + 4 * grp, grp, flags(grp)
                    self.blocks = each(lambda g: len(flags(g)))
                    self.v = each(lambda g: sum(flags(g)))
                    self.a = each(lambda g: len(flags(g)) - sum(flags(g)))
                    self.runs = 2 * R + each(lambda g: sum(len(runs(j + 1, g)) for j in range(UNITS)))
                    self.misc = FRONT + self.t * MISC

                def block(self, j, k):
                    return sum(n_blocks(i, self.grp) for i in range(j)) + k

                def run(self, j, i):
                    return sum(len(runs(n + 1, self.grp)) for n in range(j)) + i

                def wait_taken(self, eng, n):
                    if self.flags[n]:
                        eng.wait_ge(pt_v, self.v + sum(self.flags[:n + 1]))
                    else:
                        eng.wait_ge(pt_a, self.a + n + 1 - sum(self.flags[:n + 1]))

            @block.sync
            def _(sync):
                sync.dma_start(gate_b[:, :], A["nsa_gate_b"][0].partition_broadcast(P)).then_inc(small_in, 16)

                def load_q(t, at):
                    sync.wait_ge(q_used, t + 1)
                    steady(sync, Z)
                    for g in range(G):
                        rows = Z["z"][ROW_Q + g * R * HD:ROW_Q + (g + 1) * R * HD, :].rearrange("(h d) s -> d h s", d=HD)
                        sync.dma_start(q_raw[g * HD:(g + 1) * HD, :, :], rows[:, :, at]).then_inc(q_in, 16)

                with sync.Fori(0, NT) as t:
                    load_q(t, bass.ds(t * P, P))
                    sync.wait_ge(g_used, t + 1)
                    steady(sync, Z)
                    sync.dma_start(g_raw[:, :], Z["gate"][:, bass.ds(t * P, P)]).then_inc(g_in, 16)
                load_q(NT, slice(0, P))

            @block.gpsimd
            def _(pool):
                n = [0]

                def step(ins):
                    ins.then_inc(tabs, 1)
                    n[0] += 1
                    pool.wait_ge(tabs, n[0])

                def masked(t, pattern, base, cm, fill, op=ALU.is_ge, part=slice(0, P)):
                    step(pool.affine_select(out=t[part, :], in_=t[part, :], compare_op=op, fill=fill, base=base,
                                            pattern=pattern, channel_multiplier=cm))

                step(pool.memset(q[:, :, :, :], 0.0))
                step(pool.memset(y[:, :], 0.0))
                w = S + 1024
                step(pool.iota(t_sel[:, :], [[1, w]], base=-S, channel_multiplier=-1, allow_small_or_imprecise_dtypes=True))
                masked(t_sel, [[-1, w]], S, 1, NEG)
                step(pool.iota(t_win[:, :], [[1, WK]], base=-WINDOW, channel_multiplier=-1, allow_small_or_imprecise_dtypes=True))
                masked(t_win, [[-1, WK]], WINDOW, 1, NEG)
                masked(t_win, [[1, WK]], -1, -1, NEG)
                step(pool.memset(t_pad[:, 0:WINDOW], NEG))
                step(pool.memset(t_pad[:, WINDOW:WINDOW + WK], 0.0))
                step(pool.iota(t_cmp[:, :], [[CMP_STRIDE, 256]], base=-S, channel_multiplier=-1, allow_small_or_imprecise_dtypes=True))
                step(pool.tensor_scalar(t_cmp[:, :], t_cmp[:, :], 0.5 * (CMP_BLOCK - 1), 1.0, ALU.add, ALU.mult))
                masked(t_cmp, [[-CMP_STRIDE, 256]], S - (CMP_BLOCK - 1), 1, NEG)
                step(pool.memset(rows_ok[:, :], 1.0))
                masked(rows_ok, [[P, NT + 1]], -(CMP_BLOCK - 1), 1, 0.0)
                step(pool.memset(keep_t[:, :], 1.0))
                step(pool.memset(force_t[:, :], -FORCE))
                for h in range(2):
                    half = slice(h * 64, h * 64 + 64)
                    masked(keep_t, [[-1, 64]], 30 + h, 0, 0.0, part=half)
                    masked(force_t, [[1, 64]], -33 - h, 0, FORCE, part=half)
                    masked(force_t, [[1, 64]], -31 - h, 0, 0.0, part=half)
                for g in range(G):
                    for h in range(R):
                        step(pool.memset(q_scale[g * HD:(g + 1) * HD, h:h + 1], HD ** -0.5 / SLOPES[g * R + h]))
                step(pool.memset(psum_c[:, :], 0.0))
                pool.sem_inc(tab_ok, 1)
                with pool.Fori(0, NT) as t:
                    pool.wait_ge(win_used, t)
                    steady(pool, Z)
                    pool.tensor_copy(vwin[:, :, :], vw[:, bass.ds(t, WB), :]).then_inc(win_ok, 1)

            @block.tensor
            def _(pe):
                def use_misc(n, steps):
                    pe.wait_ge(misc_read, n)
                    for ins in steps:
                        last = ins
                    last.then_inc(misc_made, 1)

                def front(stage, g, f, n):
                    if stage == 0:
                        use_misc(n, (pe.matmul(misc[:, h * P:h * P + N_CMP], q[:, g, h, :], kcmp[:, 0:N_CMP], start=True, stop=True)
                                     for h in range(R)))
                    if stage == 2:
                        pe.wait_ge(pc_ok, f + 1)
                        use_misc(n + 1, (pe.transpose(misc[0:N_CMP, h * P:(h + 1) * P], pc[:, h, 0:N_CMP], ident[:, :])
                                         for h in range(R)))
                    if stage == 3:
                        use_misc(n + 2, (pe.matmul(misc[:, h * HD:(h + 1) * HD], pct[0:N_CMP, h, :], vcmp[0:N_CMP, g, :],
                                                   start=True, stop=True) for h in range(R)))

                def score(j, i, at, run, t):
                    h, r, wd = run
                    at = slice(r * 512, r * 512 + wd) if j % 2 else bass.ds(t * P + r * 512, wd)
                    high, rest = (ks_h, ks_r) if j % 2 else (kw_h, kw_r)
                    products(pe, s_bank[:, i % 2, 0:wd], (q_h[:, j // 2, h, :], q_r[:, j // 2, h, :]),
                             (high[:, at], rest[:, at]), True, True).then_inc(s_made, 1)

                def turn_back(j, t):
                    pe.wait_ge(ot_ok, UNITS * t + j + 1)
                    pe.wait_ge(back_read, UNITS * t + j)
                    steady(pe, Z)
                    for h in range(R):
                        ins = pe.transpose(back[:, h * HD:(h + 1) * HD], oT[:, h, :], ident[0:HD, 0:HD])
                    ins.then_inc(back_made, 1)

                def turn_y(t, n):
                    pe.wait_ge(y_ok, G * t)
                    use_misc(n, (pe.transpose(misc[:, c * P:(c + 1) * P], y[:, c * P:(c + 1) * P], ident[:, :])
                                 for c in range(NSA_W // P)))

                pe.wait_ge(tab_ok, 1)
                pe.wait_ge(q_ok, G + 1)
                front(0, 0, 0, 0)
                for i, run in enumerate(runs(0, 0)):
                    if i >= 2:
                        pe.wait_ge(s_read, i - 1)
                    score(0, i, i, run, 0)
                front(2, 0, 0, 0)
                front(3, 0, 0, 0)
                for grp in range(NT // 4):
                    with pe.Fori(0, 4) as tau:
                        T = Tile(grp, tau)
                        t = T.t
                        for j in range(UNITS):
                            nb = n_blocks(j, grp)
                            for k in range(nb + 1):
                                n = T.block(j, k)
                                if k < nb:
                                    if n >= 2:
                                        T.wait_taken(pe, n - 2)
                                    else:
                                        pe.wait_ge(pt_a, T.a)
                                        pe.wait_ge(pt_v, T.v)
                                    for h in range(R):
                                        if k == 0:
                                            pe.wait_ge(exp_ok, UNITS * R * t + R * j + h + 1)
                                        ins = pe.transpose(t_bank[:, n % 2, h * P:(h + 1) * P],
                                                           sc[:, j % 2, h, k * P:(k + 1) * P], ident[:, :])
                                    ins.then_inc(turned, 1)
                                if k == 0 and j > 0:
                                    turn_back(j - 1, t)
                                if k == 0 and j == 3:
                                    pe.sem_inc(win_used, 1)
                                    pe.wait_ge(q_ok, (G + 1) * t + 2 * (G + 1))
                                if j == 0 and k == 1:
                                    turn_y(t, T.misc)
                                if j == 0 and k == 2:
                                    pe.wait_ge(g_in, t * 16 + 16)
                                    pe.wait_ge(misc_read, T.misc + 1)
                                    steady(pe, Z)
                                    use_misc(T.misc + 1, [pe.transpose(misc[:, 0:N_GATE], g_raw[:, :], ident[0:N_GATE, 0:N_GATE])])
                                if j == 1:
                                    front(k, 1, 2 * t + 1, T.misc + 2)
                                if j == 3:
                                    front(k, 0, 2 * t + 2, T.misc + 2 + FRONT)
                                for i, run in made_in(j, k, grp):
                                    i = T.run(j, i)
                                    pe.wait_ge(s_read, T.runs + i - 1)
                                    score((j + 1) % UNITS, i, i, run, t + (j + 1) // UNITS)
                                if k >= 1:
                                    T.wait_taken(pe, n - 1)
                                    if j == 0 and k == 1:
                                        pe.wait_ge(win_ok, t + 1)
                                    g = j // 2
                                    val = (vs if j % 2 else vwin)[:, k - 1, g * HD:(g + 1) * HD]
                                    pe.matmul(o_bank[0:HD, j % 2, :], val, pt[:, (n - 1) % 2, :, :].rearrange("p h t -> p (h t)"),
                                              start=(k == 1), stop=(k == nb)).then_inc(pv_made, 1)
                        turn_back(UNITS - 1, t)
                turn_y(NT, FRONT + NT * MISC)

            @block.scalar
            def _(act):
                def front(stage, f, n):
                    if stage == 1:
                        act.wait_ge(cmax_ok, f + 1)
                        for h in range(R):
                            ins = act.activation(pc[:, h, 0:N_CMP], pc[:, h, 0:N_CMP], ACT.Exp,
                                                 bias=cst[:, 1, h:h + 1], accum_out=cst[:, 2, h:h + 1])
                        ins.then_inc(cexp_ok, 1)
                    if stage == 2:
                        act.wait_ge(misc_made, n + 2)
                        act.copy(pct[0:N_CMP, :, :].rearrange("p h t -> p (h t)"), misc[0:N_CMP, :]).then_inc(misc_read, 1)

                def exp(j, h, m, width):
                    act.wait_ge(max_ok, m + 1)
                    act.activation(sc[:, j % 2, h, 0:width], sc[:, j % 2, h, 0:width], ACT.Exp,
                                   bias=ust[:, 0, R * j + h:R * j + h + 1],
                                   accum_out=ust[:, 1, R * j + h:R * j + h + 1]).then_inc(exp_ok, 1)

                def store_y(t, n):
                    act.wait_ge(misc_made, n + 1)
                    act.wait_ge(y_out, t * 16)
                    act.copy(yT[:, :, :].rearrange("p c t -> p (c t)"), misc[:, :]).then_inc(misc_read, 1)
                    act.wait_ge(misc_read, n + 1)
                    act.dma_start(Z["yn"].rearrange("(c p) s -> p c s", p=P)[:, :, bass.ds(t * P, P)],
                                  yT[:, :, :]).then_inc(y_out, 16)

                act.wait_ge(tab_ok, 1)
                act.wait_ge(small_in, 16)
                front(1, 0, 0)
                for h in range(R):
                    exp(0, h, h, WK)
                front(2, 0, 0)
                for grp in range(NT // 4):
                    with act.Fori(0, 4) as tau:
                        T = Tile(grp, tau)
                        t = T.t
                        for j in range(UNITS):
                            nb = n_blocks(j, grp)
                            for k in range(nb + 1):
                                n = T.block(j, k)
                                if k < nb and not by_dve(j, k):
                                    act.wait_ge(turned, T.blocks + n + 1)
                                    act.wait_ge(pv_made, T.blocks + max(n - 1, 0))
                                    act.copy(pt[:, n % 2, :, :].rearrange("p h t -> p (h t)"), t_bank[:, n % 2, :]).then_inc(pt_a, 1)
                                if j == 0 and k == 1:
                                    store_y(t, T.misc)
                                if j == 0 and k == 3:
                                    act.wait_ge(gate_ok, t + 1)
                                    act.activation(gates[:, :], gates[:, :], ACT.Tanh, scale=0.5).then_inc(gated, 1)
                                if j == 1:
                                    front(k, 2 * t + 1, T.misc + 2)
                                if j == 3:
                                    front(k, 2 * t + 2, T.misc + 2 + FRONT)
                                for i, (h, r, wd) in made_in(j, k - 1, grp):
                                    if last_run(h, r, j + 1, grp):
                                        exp((j + 1) % UNITS, h, UNITS * R * t + R * (j + 1) + h, WK if j % 2 else 512 * (grp + 1))
                            act.wait_ge(pv_made, T.blocks + T.block(j, nb))
                            act.wait_ge(back_made, UNITS * t + j)
                            act.copy(oT[:, :, :].rearrange("p h t -> p (h t)"), o_bank[0:HD, j % 2, :]).then_inc(ot_ok, 1)
                store_y(NT, FRONT + NT * MISC)
                act.wait_ge(y_out, NT * 16 + 16)

            @block.vector
            def _(dve):
                v = Chain(dve, vec)

                def take_q(t):
                    dve.wait_ge(q_in, t * 32 + 32)
                    for g in range(G):
                        own = slice(g * HD, (g + 1) * HD)
                        dve.tensor_tensor(q[own, g, :, :], q_raw[own, :, :],
                                          q_scale[own, :].rearrange("p (h o) -> p h o", o=1).to_broadcast([HD, R, P]),
                                          ALU.mult).then_inc(q_ok, 1)
                    dve.wait_ge(q_ok, (G + 1) * t + G)
                    dve.sem_inc(q_used, 1)
                    every = lambda a: a[:, :, :, :].rearrange("p g h t -> p (g h t)")
                    split(v, every(q), every(q_h), every(q_r)).then_inc(q_ok, 1)

                def tables(t, first):
                    steady(dve, Z)
                    v.link(dve.tensor_copy(t_cmp_t[:, :], t_cmp[:, bass.ds(P - t * (P // CMP_STRIDE), N_CMP)]))
                    if first:
                        v.link(dve.tensor_tensor(t_win0[:, :], t_win[:, :], t_pad[:, bass.ds(t * P, WK)], ALU.add))

                def compressed_scores(g, f, n):
                    dve.wait_ge(misc_made, n + 1)
                    steady(dve, Z)
                    for h in range(R):
                        ins = dve.tensor_tensor_reduce(
                            out=pc[:, h, 0:N_CMP], in0=misc[:, h * P:h * P + N_CMP], in1=t_cmp_t[:, :],
                            scale=SLOPES[g * R + h], scalar=LOWEST, op0=ALU.add, op1=ALU.max, accum_out=cst[:, 0, h:h + 1])
                    ins.then_inc(misc_read, 1)
                    dve.wait_ge(misc_read, n + 1)
                    dve.tensor_scalar(cst[:, 1, :], cst[:, 0, :], -1.0, None, ALU.mult).then_inc(cmax_ok, 1)

                def compressed_probs(g, f, t):
                    dve.wait_ge(cexp_ok, f + 1)
                    v.link(dve.reciprocal(cst[:, 3, :], cst[:, 2, :]))
                    v.link(dve.tensor_scalar(cst[:, 3, :], cst[:, 3, :], rows_ok[:, bass.ds(t, 1)], None, ALU.mult))
                    for h in range(R):
                        ins = dve.tensor_scalar(pc[:, h, 0:N_CMP], pc[:, h, 0:N_CMP], cst[:, 3, h:h + 1], None, ALU.mult)
                    ins.then_inc(pc_ok, 1)
                    dve.wait_ge(pc_ok, f + 1)

                def select(t, keys):
                    total = psum_c[:, 1:1 + N_CMP]
                    v.link(dve.tensor_tensor(total, pc[:, 0, 0:N_CMP], pc[:, 1, 0:N_CMP], ALU.add))
                    v.link(dve.tensor_tensor(total, total, pc[:, 2, 0:N_CMP], ALU.add))
                    v.link(dve.tensor_tensor(total, total, pc[:, 3, 0:N_CMP], ALU.add))
                    piece = lambda n: psum_c[:, n:n + P - 3:4]
                    v.mark(dve.tensor_tensor(imp2[:, :], piece(0), piece(4), ALU.add))
                    v.link(dve.tensor_tensor(imp[:, :], piece(1), piece(2), ALU.add))
                    v.link(dve.tensor_tensor(imp[:, :], imp[:, :], piece(3), ALU.add))
                    v.link(dve.scalar_tensor_tensor(out=imp[:, :], in0=imp2[:, :], scalar=0.5, in1=imp[:, :],
                                                    op0=ALU.mult, op1=ALU.add))
                    steady(dve, Z)
                    at = bass.ds(32 - 2 * t, N_SEL)
                    v.link(dve.tensor_tensor(imp[:, :], imp[:, :], keep_t[:, at], ALU.mult))
                    v.link(dve.tensor_tensor(imp[:, :], imp[:, :], force_t[:, at], ALU.add))
                    v.link(dve.memset(imp[:, 0:1], FORCE))
                    steady(dve, Z)
                    v.link(dve.max(top[:, :], imp[:, :]))
                    steady(dve, Z)
                    v.link(dve.match_replace(imp2[:, :], top[:, :], imp[:, :], -LOWEST))
                    v.link(dve.tensor_scalar(sel[:, :], imp2[:, :], -LOWEST, NEG, ALU.not_equal, ALU.mult))
                    n = keys // SEL_BLOCK
                    steady(dve, Z)
                    v.link(dve.tensor_tensor(
                        tg[:, 0:keys].rearrange("p (n b) -> p n b", n=n),
                        t_sel[:, bass.ds(S - t * P, keys)].rearrange("p (n b) -> p n b", n=n),
                        sel[:, 0:n].rearrange("p (n o) -> p n o", o=1).to_broadcast([P, n, SEL_BLOCK]), ALU.add))

                def front(stage, g, f, n, t, keys):
                    if stage == 0:
                        compressed_scores(g, f, n)
                    if stage == 1:
                        compressed_probs(g, f, t)
                    if stage == 2:
                        select(t, keys)
                    if stage == 3:
                        dve.wait_ge(misc_made, n + 3)
                        dve.tensor_copy(oc[:, g, :, :].rearrange("p h d -> p (h d)"), misc[:, 0:R * HD]).then_inc(misc_read, 1)
                        dve.wait_ge(misc_read, n + 3)

                def weigh(j, i, run, seen, m, table, last):
                    h, r, wd = run
                    dve.wait_ge(s_made, seen + 1)
                    steady(dve, Z)
                    dve.tensor_tensor_reduce(
                        out=sc[:, j % 2, h, r * 512:r * 512 + wd], in0=s_bank[:, i % 2, 0:wd],
                        in1=table[:, r * 512:r * 512 + wd], scale=SLOPES[j // 2 * R + h],
                        scalar=LOWEST, op0=ALU.add, op1=ALU.max, accum_out=mxc[:, R * j + h, r:r + 1]).then_inc(s_read, 1)
                    if last:
                        dve.wait_ge(s_read, seen + 1)
                        dve.tensor_reduce(ust[:, 0, R * j + h:R * j + h + 1], mxc[:, R * j + h, 0:r + 1], AX.X, ALU.max,
                                          negate=True).then_inc(max_ok, 1)

                def combine(j, t):
                    g, s = j // 2, ust[:, 2, R * j:R * (j + 1)]
                    gate = lambda b: gates[:, 3 * R * g:3 * R * (g + 1)].rearrange("p (h b) -> p b h", b=3)[:, b, :]
                    wide = lambda a: a.rearrange("p (h o) -> p h o", o=1).to_broadcast([P, R, HD])
                    yg = y[:, g * R * HD:(g + 1) * R * HD].rearrange("p (h d) -> p h d", h=R)
                    v.link(dve.reciprocal(s, ust[:, 1, R * j:R * (j + 1)]))
                    v.link(dve.tensor_tensor(s, s, gate(1 if j % 2 else 2), ALU.mult))
                    if j % 2 == 0:
                        for h in range(R):
                            c = 3 * (g * R + h)
                            v.mark(dve.tensor_scalar(yg[:, h, :], oc[:, g, h, :], gates[:, c:c + 1], None, ALU.mult))
                    dve.wait_ge(back_made, UNITS * t + j + 1)
                    v.link(dve.tensor_tensor(part[:, :, :], back[:, 0:R * HD].rearrange("p (h d) -> p h d", h=R), wide(s), ALU.mult))
                    dve.sem_inc(back_read, 1)
                    v.link(dve.tensor_tensor(yg, yg, part[:, :, :], ALU.add))
                    if j % 2:
                        dve.sem_inc(y_ok, 1)

                dve.wait_ge(tab_ok, 1)
                dve.wait_ge(small_in, 16)
                dve.sem_inc(q_used, 1)
                dve.sem_inc(g_used, 1)
                take_q(0)
                tables(0, True)
                front(0, 0, 0, 0, 0, 0)
                for i, (h, r, wd) in enumerate(runs(0, 0)):
                    weigh(0, i, (h, r, wd), i, 0, t_win0, last_run(h, r, 0, 0))
                for stage in (1, 2, 3):
                    front(stage, 0, 0, 0, 0, 512)
                for grp in range(NT // 4):
                    keys = 512 * (grp + 1)
                    with dve.Fori(0, 4) as tau:
                        v.loop(tau, STEPS + (grp == 0))
                        T = Tile(grp, tau)
                        t = T.t
                        win = t_win0 if grp == 0 else t_win
                        for j in range(UNITS):
                            nb = n_blocks(j, grp)
                            dve.wait_ge(turned, T.blocks + T.block(j, 0))
                            if j == 3:
                                take_q(t + 1)
                                tables(t + 1, grp == 0)
                            for k in range(nb + 1):
                                n = T.block(j, k)
                                if k < nb and by_dve(j, k):
                                    dve.wait_ge(turned, T.blocks + n + 1)
                                    dve.wait_ge(pv_made, T.blocks + n - 1)
                                    dve.tensor_copy(pt[:, n % 2, :, :].rearrange("p h t -> p (h t)"), t_bank[:, n % 2, :]).then_inc(pt_v, 1)
                                if k == 1 and j > 0:
                                    combine(j - 1, t)
                                if j == 0 and k == 2:
                                    dve.wait_ge(misc_made, T.misc + 2)
                                    dve.tensor_tensor(gates[:, :], misc[:, 0:N_GATE], gate_b[:, :], ALU.add).then_inc(gate_ok, 1)
                                    dve.wait_ge(gate_ok, t + 1)
                                    dve.sem_inc(misc_read, 1)
                                    dve.sem_inc(g_used, 1)
                                if j == 0 and k == 4:
                                    dve.wait_ge(gated, t + 1)
                                    v.link(dve.tensor_scalar(gates[:, :], gates[:, :], 0.5, 0.5, ALU.mult, ALU.add))
                                if j == 1 and k == 0:
                                    front(0, 1, 2 * t + 1, T.misc + 2, t, keys)
                                if j == 3 and k == 0:
                                    front(0, 0, 2 * t + 2, T.misc + 2 + FRONT, t + 1, 0)
                                for i, (h, r, wd) in made_in(j, k, grp):
                                    i = T.run(j, i)
                                    weigh((j + 1) % UNITS, i, (h, r, wd), T.runs + i, 0, win if j % 2 else tg,
                                          last_run(h, r, j + 1, grp))
                                if j == 1 and k > 0:
                                    front(k, 1, 2 * t + 1, T.misc + 2, t, keys)
                                if j == 3 and k > 0:
                                    front(k, 0, 2 * t + 2, T.misc + 2 + FRONT, t + 1, min(keys + 512, S))
                        combine(UNITS - 1, t)
                        v.end(4)


def stage_mix(nc, A, Z):
    with ExitStack() as ctx:
        st = Stage(nc, ctx, "mx")
        YC = RW_W // P
        TW = 256
        up, up_h = (st.sb(n, [P, 2, YC, D]) for n in ("up", "up_h"))
        wo, wo_h = (st.sb(n, [P, DC, D]) for n in ("wo", "wo_h"))

        with ExitStack() as loading:
            ld = Stage(nc, loading, "mw")
            raw = ld.sb("raw", [P, 2, YC, D])
            raw_in, quarter, steps = ld.sems("raw_in", 2), ld.sem("quarter"), ld.sem("steps")
            block = ld.block()
            quarters = [(A[n][0], up[:, i, :, :], up_h[:, i, :, :]) for i, n in enumerate(("w_up_rwkv", "w_up_nsa"))]
            quarters += [(A["w_out"][0][i * YC * P:(i + 1) * YC * P, :], wo[:, i * YC:(i + 1) * YC, :],
                          wo_h[:, i * YC:(i + 1) * YC, :]) for i in range(2)]

            @block.sync
            def _(sync):
                for n, (src, _, _) in enumerate(quarters):
                    if n >= 2:
                        sync.wait_ge(quarter, n - 1)
                    sync.dma_start(raw[:, n % 2, :, :], src.rearrange("(c p) n -> p c n", p=P)).then_inc(raw_in[n % 2], 16)

            @block.vector
            def _(dve):
                v = Chain(dve, steps)
                for n, (_, rest, high) in enumerate(quarters):
                    dve.wait_ge(raw_in[n % 2], 16 * (n // 2 + 1))
                    split(v, raw[:, n % 2, :, :], high, rest).then_inc(quarter, 1)
                dve.wait_ge(quarter, 4)

        y_raw, ys, ys_h = (st.sb(n, [P, 2, YC, TW]) for n in ("y_raw", "ys", "ys_h"))
        m_raw = st.sb("m_raw", [P, TW])
        mg = st.sb("mg", [P, 2, DC, TW])
        res = st.sb("res", [P, 2, D])
        part = st.sb("part", [P, 2, 2, TW])
        mixed, mixed_h = (st.sb(n, [P, DC, TW]) for n in ("mixed", "mixed_h"))
        ups = st.ps("ups", [P, 2, 2, 512])
        outs = st.ps("outs", [P, 2, 2, 512])
        y_in, g_in, res_in, ys_ok = st.sem("y_in"), st.sem("g_in"), st.sems("res_in", 2), st.sem("ys_ok")
        ups_made, ups_read, sig_ok, mixed_ok, out_made, out_ok, vec = (
            st.sem(n) for n in ("ups_made", "ups_read", "sig_ok", "mixed_ok", "out_made", "out_ok", "vec"))
        stored = st.sems("stored", 2)
        block = st.block()
        TB = TW // P
        N_BLOCKS = S // TW

        @block.sync
        def _(sync):
            with sync.Fori(0, N_BLOCKS // 2) as i:
                for k in range(2):
                    b = 2 * i + k
                    sync.wait_ge(ups_read, b * DC)
                    for n in range(2):
                        sync.dma_start(mg[:, n, :, :], Z["z"][ROW_MERGE + n * D:ROW_MERGE + (n + 1) * D, :]
                                       .rearrange("(c p) s -> p c s", p=P)[:, :, bass.ds(b * TW, TW)]).then_inc(g_in, 16)
                    for t in range(TB):
                        sync.wait_ge(stored[t], b * 16)
                        sync.dma_start(res[:, t, :], A["x"][0][bass.ds((b * TB + t) * P, P), :]).then_inc(res_in[t], 16)

        @block.tensor
        def _(pe):
            with pe.Fori(0, N_BLOCKS // 2) as i:
                for k in range(2):
                    b = 2 * i + k
                    pe.wait_ge(ys_ok, b + 1)
                    for d in range(DC):
                        pe.wait_ge(ups_read, b * DC + max(d - 1, 0))
                        own = slice(d * P, (d + 1) * P)
                        for n in range(2):
                            for c in range(YC):
                                ins = products(pe, ups[:, d % 2, n, 0:TW], (up_h[:, n, c, own], up[:, n, c, own]),
                                               (ys_h[:, n, c, :], ys[:, n, c, :]), c == 0, c == YC - 1)
                        ins.then_inc(ups_made, 1)
                    pe.wait_ge(mixed_ok, (b + 1) * DC)
                    for t in range(TB):
                        pe.wait_ge(out_ok, b * TB + t - 1 if t else b * TB)
                        own = slice(t * P, (t + 1) * P)
                        for n in range(2):
                            half = slice(n * 512, (n + 1) * 512)
                            for c in range(DC):
                                ins = products(pe, outs[:, t, n, :], (mixed_h[:, c, own], mixed[:, c, own]),
                                               (wo_h[:, c, half], wo[:, c, half]), c == 0, c == DC - 1)
                        ins.then_inc(out_made, 1)

        @block.scalar
        def _(act):
            def load_ys(b):
                for n, (name, lead) in enumerate((("yr", 0), ("yn", P))):
                    act.dma_start(y_raw[:, n, :, :], Z[name].rearrange("(c p) s -> p c s", p=P)[:, :, bass.ds(b * TW + lead, TW)]).then_inc(y_in, 16)

            def gates(b):
                act.wait_ge(g_in, (b + 1) * 32)
                for d in range(DC):
                    act.activation(mg[:, :, d, :], mg[:, :, d, :], ACT.Sigmoid).then_inc(sig_ok, 1)

            load_ys(0)
            with act.Fori(0, N_BLOCKS - 1) as b:
                gates(b)
                act.wait_ge(ys_ok, b + 1)
                steady(act, Z)
                load_ys(b + 1)
            gates(N_BLOCKS - 1)

        @block.vector
        def _(dve):
            v = Chain(dve, vec)

            def split_ys(b):
                dve.wait_ge(y_in, b * 32 + 32)
                split(v, y_raw[:, :, :, :], ys_h[:, :, :, :], ys[:, :, :, :]).then_inc(ys_ok, 1)

            split_ys(0)
            def pair(i, last):
                for k in range(2):
                    b = 2 * i + k
                    for d in range(DC):
                        dve.wait_ge(ups_made, b * DC + d + 1)
                        dve.wait_ge(sig_ok, b * DC + d + 1)
                        v.link(dve.tensor_tensor(part[:, d % 2, :, :], ups[:, d % 2, :, 0:TW], mg[:, :, d, :], ALU.mult))
                        dve.sem_inc(ups_read, 1)
                        if d == 0:
                            dve.wait_ge(out_made, b * TB)
                        v.link(dve.tensor_tensor(m_raw[:, :], part[:, d % 2, 0, :], part[:, d % 2, 1, :], ALU.add))
                        split(v, m_raw[:, :], mixed_h[:, d, :], mixed[:, d, :]).then_inc(mixed_ok, 1)
                        dve.wait_ge(mixed_ok, b * DC + d + 1)
                    if not (last and k):
                        split_ys(b + 1)
                    for t in range(TB):
                        dve.wait_ge(out_made, b * TB + t + 1)
                        dve.wait_ge(res_in[t], (b + 1) * 16)
                        dve.tensor_tensor(res[:, t, :].rearrange("p (n c) -> p n c", n=2), outs[:, t, :, :],
                                          res[:, t, :].rearrange("p (n c) -> p n c", n=2), ALU.add).then_inc(out_ok, 1)
            with dve.Fori(0, N_BLOCKS // 2 - 1) as i:
                v.loop(i, 2 * (3 * DC + 1))
                pair(i, False)
                v.end(N_BLOCKS // 2 - 1)
            pair(N_BLOCKS // 2 - 1, True)

        @block.gpsimd
        def _(pool):
            with pool.Fori(0, N_BLOCKS) as b:
                for k in range(TB):
                    pool.wait_ge(out_ok, TB * b + k + 1)
                    pool.dma_start(Z["x1"][bass.ds((TB * b + k) * P, P), :], res[:, k, :]).then_inc(stored[k], 16)
            for k in range(TB):
                pool.wait_ge(stored[k], N_BLOCKS * 16)


N_GROUPS, PER_GROUP = 4, 8
N_EXPERTS = N_GROUPS * PER_GROUP
D_EXPERT = 512
MAX_BLOCKS = 2 * S // P + N_EXPERTS
N_LOGITS = N_GROUPS + N_EXPERTS
FINAL = N_EXPERTS + 2


def stage_route(nc, A, Z, keep):
    lg, weight, dest, ends = keep["lg"], keep["weight"], keep["dest"], keep["ends"]
    with ExitStack() as ctx:
        st = Stage(nc, ctx, "ro")
        x_t, xn = st.sb("x", [P, 2, D]), st.sb("xn", [P, 2, D])
        sq = st.sb("sq", [P, D])
        stat = st.sb("stat", [P, 2, 4])
        hT = st.sb("hT", [P, 2, DC, P])
        g_row = st.sb("g", [P, D])
        w_r = st.sb("w_r", [P, DC, N_LOGITS])
        b_r = st.sb("b_r", [P, N_LOGITS])
        ident = st.sb("ident", [P, P])
        zero_i, tok_id = st.sb("zero_i", [P, MAX_BLOCKS + 1], I32), keep["tok_id"]
        tp, lps = st.ps("tp", [P, 2, 2, 512]), st.ps("lps", [P, 2, 512])
        x_in, h_out = st.sems("x_in", 2), st.sems("h_out", 2)
        x_free, w_in, id_ok, squares, roots, ms_ok, vec = (
            st.sem(n) for n in ("x_free", "w_in", "id_ok", "squares", "roots", "ms_ok", "vec"))
        h_ok, turned, ht_ok, l_made, l_ok, cleared, rows_clear = (
            st.sem(n) for n in ("h_ok", "turned", "ht_ok", "l_made", "l_ok", "cleared", "rows_clear"))
        block = st.block()

        @block.sync
        def _(sync):
            sync.dma_start(g_row[:, :], A["g_ffn"][0].partition_broadcast(P)).then_inc(w_in, 16)
            sync.dma_start(w_r[:, :, 0:N_GROUPS], A["w_group"][0].rearrange("(c p) n -> p c n", p=P)).then_inc(w_in, 16)
            sync.dma_start(w_r[:, :, N_GROUPS:N_LOGITS], A["w_router"][0].rearrange("(c p) n -> p c n", p=P)).then_inc(w_in, 16)
            sync.dma_start(b_r[:, 0:N_GROUPS], A["b_group"][0].partition_broadcast(P)).then_inc(w_in, 16)
            sync.dma_start(b_r[:, N_GROUPS:N_LOGITS], A["b_router"][0].partition_broadcast(P)).then_inc(w_in, 16)
            with sync.Fori(0, NT // 2) as i:
                for k in range(2):
                    sync.wait_ge(x_free, 2 * i + k + 1)
                    sync.dma_start(x_t[:, k, :], Z["x1"][bass.ds((2 * i + k) * P, P), :]).then_inc(x_in[k], 16)

        @block.gpsimd
        def _(pool):
            build_identity(pool, ident, id_ok)
            pool.memset(zero_i[:, :], 0).then_inc(cleared, 1)
            pool.iota(tok_id[:, :], [[P, NT]], base=0, channel_multiplier=1).then_inc(cleared, 1)
            pool.wait_ge(cleared, 2)
            pool.dma_start(Z["row_tok"].rearrange("(p b) o -> p (b o)", p=P), zero_i[:, :]).then_inc(rows_clear, 16)
            pool.wait_ge(rows_clear, 16)
            with pool.Fori(0, NT // 2) as i:
                for k in range(2):
                    pool.wait_ge(h_ok, 2 * i + k + 1)
                    pool.dma_start(Z["h2"][bass.ds((2 * i + k) * P, P), :], xn[:, k, :]).then_inc(h_out[k], 16)
            for k in range(2):
                pool.wait_ge(h_out[k], NT // 2 * 16)

        @block.scalar
        def _(act):
            with act.Fori(0, NT // 2) as i:
                for k in range(2):
                    act.wait_ge(x_in[k], (i + 1) * 16)
                    act.wait_ge(squares, 2 * i + k)
                    act.activation(sq[:, :], x_t[:, k, :], ACT.Square, accum_out=stat[:, k, 0:1]).then_inc(squares, 1)
                for k in range(2):
                    act.wait_ge(ms_ok, 2 * i + k + 1)
                    act.activation(stat[:, k, 2:3], stat[:, k, 1:2], ACT.Sqrt).then_inc(roots, 1)
                for k in range(2):
                    act.wait_ge(turned, 2 * i + k + 1)
                    act.wait_ge(l_made, 2 * i + k)
                    act.copy(hT[:, k, :, :].rearrange("p (b c) t -> p b (c t)", b=2), tp[:, k, :, :]).then_inc(ht_ok, 1)

        @block.vector
        def _(dve):
            v = Chain(dve, vec)
            dve.sem_inc(x_free, 2)
            dve.wait_ge(w_in, 80)
            with dve.Fori(0, NT // 2) as i:
                v.loop(i, 4)
                for k in range(2):
                    dve.wait_ge(squares, 2 * i + k + 1)
                    dve.tensor_scalar(stat[:, k, 1:2], stat[:, k, 0:1], 1.0 / D, NORM_EPS, ALU.mult, ALU.add).then_inc(ms_ok, 1)
                for k in range(2):
                    dve.wait_ge(roots, 2 * i + k + 1)
                    v.link(dve.reciprocal(stat[:, k, 3:4], stat[:, k, 2:3]))
                    dve.wait_ge(turned, 2 * i + k)
                    dve.wait_ge(h_out[k], i * 16)
                    v.link(dve.scalar_tensor_tensor(out=xn[:, k, :], in0=x_t[:, k, :], scalar=stat[:, k, 3:4], in1=g_row[:, :],
                                                    op0=ALU.mult, op1=ALU.mult))
                    dve.sem_inc(h_ok, 1)
                    dve.sem_inc(x_free, 1)
                for k in range(2):
                    dve.wait_ge(l_made, 2 * i + k + 1)
                    dve.tensor_tensor(lg[:, bass.ds(2 * i + k, 1), :].rearrange("p o n -> p (o n)"), lps[:, k, 0:N_LOGITS],
                                      b_r[:, :], ALU.add).then_inc(l_ok, 1)
                v.end(NT // 2)
            dve.wait_ge(l_ok, NT)

        @block.tensor
        def _(pe):
            pe.wait_ge(id_ok, 2)
            pe.wait_ge(w_in, 80)
            with pe.Fori(0, NT // 2) as i:
                for k in range(2):
                    pe.wait_ge(h_ok, 2 * i + k + 1)
                    pe.wait_ge(ht_ok, 2 * i)
                    for c in range(DC):
                        ins = pe.transpose(tp[:, k, c // 4, (c % 4) * P:(c % 4 + 1) * P], xn[:, k, c * P:(c + 1) * P], ident[:, :])
                    ins.then_inc(turned, 1)
                for k in range(2):
                    pe.wait_ge(ht_ok, 2 * i + k + 1)
                    pe.wait_ge(l_ok, 2 * i)
                    for c in range(DC):
                        ins = pe.matmul(lps[:, k, 0:N_LOGITS], hT[:, k, c, :], w_r[:, c, :], start=(c == 0), stop=(c == DC - 1))
                    ins.then_inc(l_made, 1)

    with ExitStack() as ctx:
        st = Stage(nc, ctx, "rt")
        E3 = [P, NT, N_EXPERTS]
        small = lambda n: st.sb(n, [P, NT, 1])
        gmax, gsum, g_at, m1, m2, at, ratio, total = (small(n) for n in ("gmax", "gsum", "g_at", "m1", "m2", "at", "ratio", "total"))
        gd, g_one, le, cand, tmp = (st.sb(n, [P, NT, PER_GROUP]) for n in ("gd", "g_one", "le", "cand", "tmp"))
        one = [st.sb(f"one{n}", [P, NT, PER_GROUP]) for n in range(2)]
        hot = [st.sb(f"hot{n}", E3) for n in range(2)]
        both, tot, base, prod = (st.sb(n, E3) for n in ("both", "tot", "base", "prod"))
        count, ends_f, nb_f = (st.sb(n, [P, N_EXPERTS]) for n in ("count", "ends_f", "nb_f"))
        nb_i = st.sb("nb_i", [P, N_EXPERTS], I32)
        ones_e = st.sb("ones_e", [P, N_EXPERTS])
        iota8, col, row = st.sb("iota8", [P, PER_GROUP]), st.sb("col", [P, P]), st.sb("row", [P, P])
        before, ones_m = st.sb("before", [P, P]), st.sb("ones_m", [P, P])
        pos, sums = st.ps("pos", [P, 512]), st.ps("sums", [P, 512])
        vec, init, soft, hots_ok, made = (st.sem(n) for n in ("vec", "init", "soft", "hots_ok", "made"))
        dest_ok, listed = st.sem("dest_ok"), st.sem("listed")
        block = st.block()

        @block.gpsimd
        def _(pool):
            pool.iota(iota8[:, :], [[1, PER_GROUP]], base=0, channel_multiplier=0, allow_small_or_imprecise_dtypes=True).then_inc(init, 1)
            pool.iota(col[:, :], [[1, P]], base=0, channel_multiplier=0, allow_small_or_imprecise_dtypes=True).then_inc(init, 1)
            pool.iota(row[:, :], [[0, P]], base=0, channel_multiplier=1, allow_small_or_imprecise_dtypes=True).then_inc(init, 1)
            pool.memset(ones_e[:, :], 1.0).then_inc(init, 1)
            pool.memset(ones_m[:, :], 1.0).then_inc(init, 1)
            pool.wait_ge(dest_ok, 1)
            for t in range(NT):
                for n in range(2):
                    pool.indirect_dma_start(out=Z["row_tok"], out_offset=bass.IndirectOffsetOnAxis(ap=dest[:, n, t:t + 1], axis=0),
                                            in_=keep["tok_id"][:, t:t + 1], in_offset=None).then_inc(listed, 16)
            pool.wait_ge(listed, 2 * NT * 16)

        @block.tensor
        def _(pe):
            pe.wait_ge(hots_ok, 1)
            flat = both[:, :, :].rearrange("p t e -> p (t e)")
            pe.matmul(pos[:, :], before[:, :], flat, start=True, stop=True)
            pe.matmul(sums[:, :], ones_m[:, :], flat, start=True, stop=True).then_inc(made, 1)

        @block.scalar
        def _(act):
            act.wait_ge(soft, 1)
            act.activation(gd[:, :, 0:N_GROUPS], gd[:, :, 0:N_GROUPS], ACT.Exp).then_inc(soft, 1)
            act.wait_ge(soft, 3)
            act.activation(ratio[:, :, :], ratio[:, :, :], ACT.Exp).then_inc(soft, 1)

        @block.vector
        def _(dve):
            v = Chain(dve, vec)
            dve.wait_ge(init, 5)
            v.link(dve.tensor_tensor(before[:, :], col[:, :], row[:, :], ALU.is_gt))
            wide = lambda t, n: t.to_broadcast([P, NT, n])
            index = lambda n: iota8[:, 0:n].rearrange("p (o n) -> p o n", o=1).to_broadcast([P, NT, n])

            def first_max(values, n, top, out):
                v.link(dve.tensor_reduce(top, values, AX.X, ALU.max))
                v.link(dve.tensor_tensor(cand[:, :, 0:n], values, wide(top, n), ALU.is_ge))
                v.link(dve.tensor_scalar(cand[:, :, 0:n], cand[:, :, 0:n], -64.0, 64.0, ALU.mult, ALU.add))
                v.link(dve.tensor_tensor(cand[:, :, 0:n], cand[:, :, 0:n], index(n), ALU.add))
                v.link(dve.tensor_reduce(at[:, :, :], cand[:, :, 0:n], AX.X, ALU.min))
                v.link(dve.tensor_tensor(out, index(n), wide(at[:, :, :], n), ALU.is_equal))

            groups = lg[:, :, 0:N_GROUPS]
            first_max(groups, N_GROUPS, gmax[:, :, :], g_one[:, :, 0:N_GROUPS])
            v.link(dve.tensor_tensor(gd[:, :, 0:N_GROUPS], groups, wide(gmax[:, :, :], N_GROUPS), ALU.subtract))
            dve.sem_inc(soft, 1)
            for n in range(N_GROUPS):
                e = lg[:, :, N_GROUPS + n * PER_GROUP:N_GROUPS + (n + 1) * PER_GROUP]
                out = le if n == 0 else tmp
                v.link(dve.tensor_tensor(out[:, :, :], e, wide(g_one[:, :, n:n + 1], PER_GROUP), ALU.mult))
                if n:
                    v.link(dve.tensor_tensor(le[:, :, :], le[:, :, :], tmp[:, :, :], ALU.add))
            first_max(le[:, :, :], PER_GROUP, m1[:, :, :], one[0][:, :, :])
            v.link(dve.scalar_tensor_tensor(out=le[:, :, :], in0=one[0][:, :, :], scalar=NEG, in1=le[:, :, :],
                                            op0=ALU.mult, op1=ALU.add))
            first_max(le[:, :, :], PER_GROUP, m2[:, :, :], one[1][:, :, :])
            dve.wait_ge(soft, 2)
            v.link(dve.tensor_tensor(ratio[:, :, :], m2[:, :, :], m1[:, :, :], ALU.subtract))
            dve.sem_inc(soft, 1)
            v.link(dve.tensor_reduce(gsum[:, :, :], gd[:, :, 0:N_GROUPS], AX.X, ALU.add))
            dve.wait_ge(soft, 4)
            v.link(dve.tensor_scalar(total[:, :, :], ratio[:, :, :], 1.0, None, ALU.add))
            v.link(dve.tensor_tensor(total[:, :, :], total[:, :, :], gsum[:, :, :], ALU.mult))
            v.link(dve.reciprocal(weight[:, 0, :].rearrange("p (t o) -> p t o", o=1), total[:, :, :]))
            v.link(dve.tensor_tensor(weight[:, 1, :].rearrange("p (t o) -> p t o", o=1),
                                     weight[:, 0, :].rearrange("p (t o) -> p t o", o=1), ratio[:, :, :], ALU.mult))
            for n in range(2):
                for g in range(N_GROUPS):
                    ins = dve.tensor_tensor(hot[n][:, :, g * PER_GROUP:(g + 1) * PER_GROUP], one[n][:, :, :],
                                            wide(g_one[:, :, g:g + 1], PER_GROUP), ALU.mult)
                v.link(ins)
            v.link(dve.tensor_tensor(both[:, :, :], hot[0][:, :, :], hot[1][:, :, :], ALU.add))
            dve.sem_inc(hots_ok, 1)
            dve.wait_ge(made, 1)
            three = lambda t: t[:, :].rearrange("p (t e) -> p t e", t=NT)
            v.link(dve.tensor_copy(tot[:, :, :], three(sums)))
            v.link(dve.memset(base[:, 0, :], 0.0))
            for t in range(1, NT):
                v.link(dve.tensor_tensor(base[:, t, :], base[:, t - 1, :], tot[:, t - 1, :], ALU.add))
            v.link(dve.tensor_tensor(count[:, :], base[:, NT - 1, :], tot[:, NT - 1, :], ALU.add))
            v.link(dve.tensor_scalar(count[:, :], count[:, :], float(P - 1), float(P), ALU.add, ALU.max))
            v.link(dve.tensor_copy(nb_i[:, :], count[:, :]))
            v.link(dve.tensor_scalar(nb_i[:, :], nb_i[:, :], 7, None, ALU.arith_shift_right))
            v.link(dve.tensor_copy(nb_f[:, :], nb_i[:, :]))
            v.link(dve.tensor_tensor_scan(ends_f[:, :], ones_e[:, :], nb_f[:, :], 0.0, ALU.mult, ALU.add))
            v.link(dve.tensor_copy(ends[:, 1:1 + N_EXPERTS], ends_f[:, :]))
            v.link(dve.memset(ends[:, 0:1], 0))
            v.link(dve.tensor_scalar(ends[:, FINAL:FINAL + N_EXPERTS], ends_f[:, :], -1.0, None, ALU.add))
            v.link(dve.tensor_scalar(ends[:, 1 + N_EXPERTS:2 + N_EXPERTS], ends_f[:, N_EXPERTS - 1:N_EXPERTS], -1.0,
                                     float(MAX_BLOCKS + 1), ALU.mult, ALU.add))
            v.link(dve.tensor_tensor(nb_f[:, :], ends_f[:, :], nb_f[:, :], ALU.subtract))
            v.link(dve.tensor_scalar(nb_f[:, :], nb_f[:, :], float(P), None, ALU.mult))
            v.link(dve.tensor_tensor(base[:, :, :], base[:, :, :], three(pos), ALU.add))
            v.link(dve.tensor_tensor(base[:, :, :], base[:, :, :],
                                     nb_f[:, :].rearrange("p (o e) -> p o e", o=1).to_broadcast(E3), ALU.add))
            for n in range(2):
                v.link(dve.tensor_tensor(prod[:, :, :], base[:, :, :], hot[n][:, :, :], ALU.mult))
                v.link(dve.tensor_reduce(total[:, :, :], prod[:, :, :], AX.X, ALU.add))
                v.link(dve.tensor_copy(dest[:, n, :].rearrange("p (t o) -> p t o", o=1), total[:, :, :]))
            dve.sem_inc(dest_ok, 1)


def stage_experts(nc, A, Z, keep):
    ends = keep["ends"]
    with ExitStack() as ctx:
        st = Stage(nc, ctx, "ex")
        FC = D_EXPERT // P
        PART = DC * D_EXPERT
        raw = st.sb("raw", [P, 3, PART])
        gate_w, up_w = (st.sb(n, [P, 2, DC, D_EXPERT]) for n in ("gate_w", "up_w"))
        down_w = st.sb("down_w", [P, 2, 2, FC, D])
        idx = st.sb("idx", [P, 1], I32)
        xg = st.sb("xg", [P, D])
        xT = st.sb("xT", [P, 2, DC, P])
        gate = st.sb("gate", [P, D_EXPERT])
        hid = st.sb("hid", [P, D_EXPERT])
        hidT = st.sb("hidT", [P, 2, FC, P])
        y, zeros = st.sb("y", [P, D]), st.sb("zeros", [P, D])
        ident = st.sb("ident", [P, P])
        tp, gu, tph, yps = st.ps("tp", [P, 2, 512]), st.ps("gu", [P, 2, 512]), st.ps("tph", [P, 512]), st.ps("yps", [P, 2, 512])
        raw_in = st.sems("raw_in", 3)
        zeros_ok, z_out, high_ok, parts_ok = (st.sem(n) for n in ("zeros_ok", "z_out", "high_ok", "parts_ok"))
        id_ok, idx_in, x_in, turned, xh_ok, xt_ok, gate_made, up_made = (
            st.sem(n) for n in ("id_ok", "idx_in", "x_in", "turned", "xh_ok", "xt_ok", "gate_made", "up_made"))
        silu_ok, hid_ok, hid_turned, hh_ok, hidt_ok, y_made, y_ok, y_out = (
            st.sem(n) for n in ("silu_ok", "hid_ok", "hid_turned", "hh_ok", "hidt_ok", "y_made", "y_ok", "y_out"))
        block = st.block()
        bound = dict(min_val=1, max_val=MAX_BLOCKS)
        GATE, UP, DOWN = range(3)
        READY = 3

        def part(p, k):
            t = (gate_w[:, :, :, :], up_w[:, :, :, :], down_w[:, k, :, :, :])[p]
            return [t[:, n, :, :].rearrange("p c n -> p (c n)") for n in range(2)]

        def buffer_of(i, k, p):
            return p, 2 * i + k + 1

        def experts(eng, one):
            with eng.Fori(0, N_EXPERTS // 2 - 1) as i:
                one(i, 0, (i, 1))
                one(i, 1, (i + 1, 0))
            i = N_EXPERTS // 2 - 1
            one(i, 0, (i, 1))
            one(i, 1, None)

        def blocks(eng, e, body):
            steady(eng, Z)
            first = eng.value_load(ends[0:1, bass.ds(e, 1)], min_val=0, max_val=MAX_BLOCKS - 1)
            final = eng.value_load(ends[0:1, bass.ds(e + FINAL, 1)], min_val=0, max_val=MAX_BLOCKS - 1)
            with eng.If(first < final):
                with eng.Fori(first, final) as b:
                    body(b, False)
            body(final, True)

        @block.sync
        def _(sync):
            WGU = A["w_exp_gate_up"][0].rearrange("e (c p) n -> e p c n", p=P)
            WD = A["w_exp_down"][0].rearrange("e (c p) n -> e p c n", p=P)
            with sync.Fori(0, N_EXPERTS // 2) as i:
                for k in range(2):
                    for p in (GATE, UP, DOWN):
                        e, n = 2 * i + k, buffer_of(i, k, p)[0]
                        sync.wait_ge(parts_ok, 3 * e + p + 1)
                        steady(sync, Z)
                        if p == DOWN:
                            sync.dma_start(raw[:, n, :].rearrange("p (c n) -> p c n", c=FC),
                                           WD[bass.ds(e, 1), :, :, :].rearrange("e p c n -> p (e c) n")).then_inc(raw_in[n], 16)
                        else:
                            sync.dma_start(raw[:, n, :].rearrange("p (c n) -> p c n", c=DC),
                                           WGU[bass.ds(e, 1), :, :, p * D_EXPERT:(p + 1) * D_EXPERT]
                                           .rearrange("e p c n -> p (e c) n")).then_inc(raw_in[n], 16)
            sync.wait_ge(zeros_ok, 1)
            spare = sync.value_load(ends[0:1, 1 + N_EXPERTS:2 + N_EXPERTS], **bound)
            with sync.Fori(0, spare) as b:
                sync.dma_start(Z["rows"][bass.ds((MAX_BLOCKS - b) * P, P), :], zeros[:, :]).then_inc(z_out, 16)
            sync.wait_ge(z_out, spare * 16)
            steady(sync, Z)

        @block.gpsimd
        def _(pool):
            build_identity(pool, ident, id_ok)
            pool.memset(zeros[:, :], 0.0).then_inc(zeros_ok, 1)
            n = pool.value_load(ends[0:1, N_EXPERTS:N_EXPERTS + 1], **bound)
            with pool.Fori(0, n + 1) as b:
                pool.wait_ge(x_in, b * 16)
                pool.dma_start(idx[:, :], Z["row_tok"][bass.ds(b * P, P), :]).then_inc(idx_in, 16)
                pool.wait_ge(idx_in, (b + 1) * 16)
                pool.wait_ge(turned, b)
                steady(pool, Z)
                pool.indirect_dma_start(out=xg[:, :], out_offset=None, in_=Z["h2"],
                                        in_offset=bass.IndirectOffsetOnAxis(ap=idx[:, 0:1], axis=0)).then_inc(x_in, 16)
            pool.wait_ge(turned, n + 1)
            pool.wait_ge(x_in, n * 16 + 16)

        @block.tensor
        def _(pe):
            pair = lambda t, c, at: (t[:, 0, c, at], t[:, 1, c, at])
            ALL = slice(0, P)

            def turn_rows(b):
                pe.wait_ge(x_in, b * 16 + 16)
                pe.wait_ge(xt_ok, b)
                for c in range(DC):
                    ins = pe.transpose(tp[:, c // 4, (c % 4) * P:(c % 4 + 1) * P], xg[:, c * P:(c + 1) * P], ident[:, :])
                ins.then_inc(turned, 1)

            def project(n, w, done):
                for c in range(DC):
                    ins = products(pe, gu[:, n, :], pair(xT, c, ALL), pair(w, c, slice(0, D_EXPERT)), c == 0, c == DC - 1)
                ins.then_inc(done, 1)

            def gate_product(b, e):
                pe.wait_ge(xt_ok, b + 1)
                pe.wait_ge(silu_ok, b)
                pe.wait_ge(parts_ok, READY + 3 * e + GATE + 1)
                project(0, gate_w, gate_made)

            def expert(i, k, after):
                e = 2 * i + k

                def one(b, is_last):
                    pe.wait_ge(hid_ok, b)
                    pe.wait_ge(parts_ok, READY + 3 * e + UP + 1)
                    project(1, up_w, up_made)
                    turn_rows(b + 1)
                    pe.wait_ge(hid_ok, b + 1)
                    pe.wait_ge(hidt_ok, b)
                    for c in range(FC):
                        ins = pe.transpose(tph[:, c * P:(c + 1) * P], hid[:, c * P:(c + 1) * P], ident[:, :])
                    ins.then_inc(hid_turned, 1)
                    pe.wait_ge(hidt_ok, b + 1)
                    pe.wait_ge(y_ok, b)
                    pe.wait_ge(parts_ok, READY + 3 * e + DOWN + 1)
                    for n in range(2):
                        for c in range(FC):
                            ins = products(pe, yps[:, n, :], pair(hidT, c, ALL), pair(down_w[:, k, :, :, :], c, slice(n * 512, n * 512 + 512)),
                                           c == 0, c == FC - 1)
                    ins.then_inc(y_made, 1)
                    if after or not is_last:
                        gate_product(b + 1, e + 1 if is_last else e)

                blocks(pe, e, one)

            pe.wait_ge(id_ok, 2)
            turn_rows(0)
            gate_product(0, 0)
            experts(pe, expert)

        @block.scalar
        def _(act):
            def high(i, k, p):
                n, loaded = buffer_of(i, k, p)
                act.wait_ge(raw_in[n], loaded * 16)
                for h in range(2):
                    half = slice(h * PART // 2, (h + 1) * PART // 2)
                    act.copy(part(p, k)[0][:, half].bitcast(F32R), raw[:, n, half]).then_inc(high_ok, 1)

            def x_high(b):
                act.wait_ge(turned, b + 1)
                act.wait_ge(gate_made, b)
                act.wait_ge(up_made, b)
                act.copy(xT[:, 0, :, :].rearrange("p (b c) t -> p b (c t)", b=2).bitcast(F32R), tp[:, :, :]).then_inc(xh_ok, 1)

            def expert(i, k, after):
                def one(b, is_last):
                    act.wait_ge(gate_made, b + 1)
                    act.wait_ge(hid_ok, b)
                    act.activation(gate[:, :], gu[:, 0, :], ACT.Silu).then_inc(silu_ok, 1)
                    if is_last and after:
                        high(*after, GATE)
                    act.wait_ge(up_made, b + 1)
                    x_high(b + 1)
                    act.wait_ge(hid_turned, b + 1)
                    act.wait_ge(y_made, b)
                    act.copy(hidT[:, 0, :, :].rearrange("p c t -> p (c t)").bitcast(F32R), tph[:, :]).then_inc(hh_ok, 1)
                    if is_last and after:
                        high(*after, UP)
                        high(*after, DOWN)
                    act.wait_ge(y_made, b + 1)
                    act.wait_ge(y_out, b * 16)
                    act.copy(y[:, :].rearrange("p (n c) -> p n c", n=2), yps[:, :, :]).then_inc(y_ok, 1)
                    act.wait_ge(y_ok, b + 1)
                    act.dma_start(Z["rows"][bass.ds(b * P, P), :], y[:, :]).then_inc(y_out, 16)

                blocks(act, 2 * i + k, one)

            n = act.value_load(ends[0:1, N_EXPERTS:N_EXPERTS + 1], **bound)
            for p in (GATE, UP, DOWN):
                high(0, 0, p)
            x_high(0)
            experts(act, expert)
            act.wait_ge(y_out, n * 16)
            steady(act, Z)

        @block.vector
        def _(dve):
            def rest(i, k, p, halves=(0, 1)):
                e, n = 2 * i + k, buffer_of(i, k, p)[0]
                for h in halves:
                    half = slice(h * PART // 2, (h + 1) * PART // 2)
                    dve.wait_ge(high_ok, 2 * (3 * e + p) + h + 1)
                    hi, lo = part(p, k)
                    ins = dve.tensor_tensor(lo[:, half].bitcast(F32R), raw[:, n, half], hi[:, half], ALU.subtract)
                if 1 in halves:
                    ins.then_inc(parts_ok, 1)

            def x_rest(b):
                dve.wait_ge(xh_ok, b + 1)
                dve.tensor_tensor(xT[:, 1, :, :].rearrange("p (b c) t -> p b (c t)", b=2).bitcast(F32R), tp[:, :, :],
                                  xT[:, 0, :, :].rearrange("p (b c) t -> p b (c t)", b=2), ALU.subtract).then_inc(xt_ok, 1)

            def expert(i, k, after):
                def one(b, is_last):
                    if is_last and after:
                        rest(*after, GATE, halves=(0,))
                    dve.wait_ge(up_made, b + 1)
                    dve.wait_ge(silu_ok, b + 1)
                    dve.wait_ge(hid_turned, b)
                    dve.tensor_tensor(hid[:, :], gate[:, :], gu[:, 1, :], ALU.mult).then_inc(hid_ok, 1)
                    x_rest(b + 1)
                    dve.wait_ge(hh_ok, b + 1)
                    dve.tensor_tensor(hidT[:, 1, :, :].rearrange("p c t -> p (c t)").bitcast(F32R), tph[:, :],
                                      hidT[:, 0, :, :].rearrange("p c t -> p (c t)"), ALU.subtract).then_inc(hidt_ok, 1)
                    if is_last and after:
                        rest(*after, GATE, halves=(1,))
                        rest(*after, UP)
                        rest(*after, DOWN)

                blocks(dve, 2 * i + k, one)

            dve.sem_inc(parts_ok, READY)
            for p in (GATE, UP, DOWN):
                rest(0, 0, p)
            x_rest(0)
            experts(dve, expert)


def stage_moe(nc, A, Z):
    with ExitStack() as ctx:
        st = Stage(nc, ctx, "mo")
        keep = dict(lg=st.sb("lg", [P, NT, N_LOGITS]), weight=st.sb("weight", [P, 2, NT]), dest=st.sb("dest", [P, 2, NT], I32),
                    ends=st.sb("ends", [P, FINAL + N_EXPERTS], I32), tok_id=st.sb("tok_id", [P, NT], I32))
        stage_route(nc, A, Z, keep)
        stage_experts(nc, A, Z, keep)
        stage_final(nc, A, Z, keep)


PLE = 256


def stage_final(nc, A, Z, keep):
    dest, weight = keep["dest"], keep["weight"]
    with ExitStack() as ctx:
        st = Stage(nc, ctx, "fi")
        PC = PLE // P
        HC = DC // 2
        w_raw = st.sb("w_raw", [P, HC, D])
        w_g, w_gh = (st.sb(n, [P, DC, D]) for n in ("w_g", "w_gh"))
        w_p, w_ph = (st.sb(n, [P, PC, D]) for n in ("w_p", "w_ph"))
        g_in = st.sb("g_in", [P, DC])
        g_e, g_y = st.sb("g_e", [P, D]), st.sb("g_y", [P, D])
        x1, x = st.sb("x1", [P, 2, D]), st.sb("x", [P, 2, D])
        r = st.sb("r", [P, 2, 2, D])
        p_t = st.sb("p_t", [P, 2, PLE])
        idx = st.sb("idx", [P, 2, 2], I32)
        xn, sg, e = st.sb("xn", [P, D]), st.sb("sg", [P, D]), st.sb("e", [P, 2, D])
        junk = st.sb("junk", [P, D])
        out_t = st.sb("out_t", [P, 2, D])
        xT, xT_h, xT_r = (st.sb(n, [P, DC, P]) for n in ("xT", "xT_h", "xT_r"))
        pT, pT_h, pT_r = (st.sb(n, [P, PC, P]) for n in ("pT", "pT_h", "pT_r"))
        stat = st.sb("stat", [P, 3, 4])
        ident = st.sb("ident", [P, P])
        tp, gps = st.ps("tp", [P, 2, 512]), st.ps("gps", [P, 2, 512])
        pps, eps = st.ps("pps", [P, 512]), st.ps("eps", [P, 2, 512])
        x_in, r_in, y_out = st.sems("x_in", 2), st.sems("r_in", 2), st.sems("y_out", 2)
        summed, ms_ok, roots = st.sems("summed", 3), st.sems("ms_ok", 3), st.sems("roots", 3)
        raw_in = st.sem("raw_in")
        w_in, w_ok, id_ok, idx_ok, x_used, r_used, x2_ok, x3_ok, squares = (
            st.sem(n) for n in ("w_in", "w_ok", "id_ok", "idx_ok", "x_used", "r_used", "x2_ok", "x3_ok", "squares"))
        xn_ok, turned, xt_ok, made, sig_ok, y_ok, vec = (
            st.sem(n) for n in ("xn_ok", "turned", "xt_ok", "made", "sig_ok", "y_ok", "vec"))
        p_turned, pt_ok, pt_split, e_made, e_ok, sg_used = (
            st.sem(n) for n in ("p_turned", "pt_ok", "pt_split", "e_made", "e_ok", "sg_used"))
        block = st.block()
        MIX, EMB, OUT = range(3)

        @block.sync
        def _(sync):
            sync.dma_start(g_in[:, :], cols(A["g_ple_gate_in"][0], DC)).then_inc(w_in, 16)
            sync.dma_start(g_e[:, :], A["g_ple_norm"][0].partition_broadcast(P)).then_inc(w_in, 16)
            sync.dma_start(g_y[:, :], A["g_final"].partition_broadcast(P)).then_inc(w_in, 16)
            gate_w = A["w_ple_gate"][0].rearrange("(c p) n -> p c n", p=P)
            sync.dma_start(w_raw[:, 0:PC, :], A["w_ple_proj"][0].rearrange("(c p) n -> p c n", p=P)).then_inc(raw_in, 16)
            for h in range(2):
                sync.wait_ge(w_ok, h + 1)
                sync.dma_start(w_raw[:, :, :], gate_w[:, h * HC:(h + 1) * HC, :]).then_inc(raw_in, 16)
            with sync.Fori(0, NT // 2) as i:
                for k in range(2):
                    t = 2 * i + k
                    sync.wait_ge(x_used, t + 1)
                    sync.dma_start(x1[:, k, :], Z["x1"][bass.ds(t * P, P), :]).then_inc(x_in[k], 16)
                    sync.dma_start(p_t[:, k, :], A["p"][0][0][bass.ds(t * P, P), :]).then_inc(x_in[k], 16)

        @block.gpsimd
        def _(pool):
            build_identity(pool, ident, id_ok)
            with pool.Fori(0, NT // 2) as i:
                for k in range(2):
                    t = 2 * i + k
                    pool.wait_ge(r_used, t + 1)
                    pool.wait_ge(r_in[k], i * 32)
                    pool.tensor_copy(idx[:, k, :].rearrange("p (n o) -> p n o", o=1), dest[:, :, bass.ds(t, 1)]).then_inc(idx_ok, 1)
                    pool.wait_ge(idx_ok, t + 1)
                    steady(pool, Z)
                    for n in range(2):
                        pool.indirect_dma_start(out=r[:, k, n, :], out_offset=None, in_=Z["rows"],
                                                in_offset=bass.IndirectOffsetOnAxis(ap=idx[:, k, n:n + 1], axis=0)).then_inc(r_in[k], 16)

        @block.tensor
        def _(pe):
            def turn_p(t, k, loaded):
                pe.wait_ge(x_in[k], loaded * 32)
                pe.wait_ge(pt_ok, t)
                steady(pe, Z)
                for c in range(PC):
                    ins = pe.transpose(pps[:, c * P:(c + 1) * P], p_t[:, k, c * P:(c + 1) * P], ident[:, :])
                ins.then_inc(p_turned, 1)

            def tile(i, k, last):
                t = 2 * i + k
                pe.wait_ge(xn_ok, t + 1)
                for c in range(DC):
                    ins = pe.transpose(tp[:, c // 4, (c % 4) * P:(c % 4 + 1) * P], xn[:, c * P:(c + 1) * P], ident[:, :])
                ins.then_inc(turned, 1)
                pe.wait_ge(pt_split, t + 1)
                pe.wait_ge(e_ok, t)
                for n in range(2):
                    half = slice(n * 512, (n + 1) * 512)
                    for c in range(PC):
                        ins = products(pe, eps[:, n, :], (pT_h[:, c, :], pT_r[:, c, :]), (w_ph[:, c, half], w_p[:, c, half]),
                                       c == 0, c == PC - 1)
                ins.then_inc(e_made, 1)
                if not last:
                    turn_p(t + 1, 1 - k, i + 1 + k)
                pe.wait_ge(xt_ok, t + 1)
                pe.wait_ge(sig_ok, t)
                for n in range(2):
                    half = slice(n * 512, (n + 1) * 512)
                    for c in range(DC):
                        ins = products(pe, gps[:, n, :], (xT_h[:, c, :], xT_r[:, c, :]), (w_gh[:, c, half], w_g[:, c, half]),
                                       c == 0, c == DC - 1)
                ins.then_inc(made, 1)

            pe.wait_ge(id_ok, 2)
            turn_p(0, 0, 1)
            pe.wait_ge(w_ok, 3)
            with pe.Fori(0, NT // 2 - 1) as i:
                for k in range(2):
                    tile(i, k, False)
            for k in range(2):
                tile(NT // 2 - 1, k, k == 1)

        @block.scalar
        def _(act):
            a = Chain(act, squares)

            def root(which, t):
                act.wait_ge(ms_ok[which], t + 1)
                act.activation(stat[:, which, 2:3], stat[:, which, 1:2], ACT.Sqrt).then_inc(roots[which], 1)

            def square(which, t, src):
                dst = junk[:, :].rearrange("p (n c) -> p n c", n=2) if which == EMB else junk[:, :]
                a.link(act.activation(dst, src, ACT.Square, accum_out=stat[:, which, 0:1]))
                act.sem_inc(summed[which], 1)

            def before_gate(t, k):
                act.wait_ge(p_turned, t + 1)
                act.wait_ge(e_made, t)
                act.copy(pT[:, :, :].rearrange("p c t -> p (c t)"), pps[:, 0:PLE]).then_inc(pt_ok, 1)
                act.wait_ge(x2_ok, t + 1)
                square(MIX, t, x[:, k, :])
                root(MIX, t)

            def embedding(t):
                act.wait_ge(e_made, t + 1)
                square(EMB, t, eps[:, :, :])
                root(EMB, t)

            def sigmoid(t):
                act.wait_ge(made, t + 1)
                act.wait_ge(sg_used, t)
                act.activation(sg[:, :].rearrange("p (n c) -> p n c", n=2), gps[:, :, :], ACT.Sigmoid).then_inc(sig_ok, 1)

            def output(t, k):
                act.wait_ge(x3_ok, t + 1)
                square(OUT, t, x[:, k, :])
                root(OUT, t)
                act.wait_ge(y_ok, t + 1)
                act.dma_start(Z["y"][0][bass.ds(t * P, P), :], out_t[:, k, :]).then_inc(y_out[k], 16)

            def step(i, k, last):
                t = 2 * i + k
                if not last:
                    before_gate(t + 1, 1 - k)
                sigmoid(t)
                if not last:
                    embedding(t + 1)
                output(t, k)

            before_gate(0, 0)
            embedding(0)
            with act.Fori(0, NT // 2 - 1) as i:
                a.loop(i, 6)
                for k in range(2):
                    step(i, k, False)
                a.end(NT // 2 - 1)
            for k in range(2):
                step(NT // 2 - 1, k, k == 1)
            for k in range(2):
                act.wait_ge(y_out[k], NT // 2 * 16)

        @block.vector
        def _(dve):
            v = Chain(dve, vec)
            halves = lambda a: a.rearrange("p (n c) -> p n c", n=2)

            def mean_square(which, t):
                dve.wait_ge(summed[which], t + 1)
                dve.tensor_scalar(stat[:, which, 1:2], stat[:, which, 0:1], 1.0 / D, NORM_EPS, ALU.mult, ALU.add).then_inc(ms_ok[which], 1)
                dve.wait_ge(roots[which], t + 1)
                v.link(dve.reciprocal(stat[:, which, 3:4], stat[:, which, 2:3]))

            def before_gate(t, k, loaded):
                dve.wait_ge(x_in[k], loaded * 32)
                dve.wait_ge(r_in[k], loaded * 32)
                for n in range(2):
                    v.link(dve.scalar_tensor_tensor(out=x[:, k, :], in0=r[:, k, n, :], scalar=weight[:, n, bass.ds(t, 1)],
                                                    in1=(x if n else x1)[:, k, :], op0=ALU.mult, op1=ALU.add))
                dve.sem_inc(x2_ok, 1)
                dve.sem_inc(r_used, 1)
                dve.wait_ge(pt_ok, t + 1)
                split(v, pT[:, :, :], pT_h[:, :, :], pT_r[:, :, :]).then_inc(pt_split, 1)
                dve.sem_inc(x_used, 1)
                mean_square(MIX, t)
                dve.wait_ge(turned, t)
                dve.tensor_scalar(xn[:, :], x[:, k, :], stat[:, MIX, 3:4], None, ALU.mult).then_inc(xn_ok, 1)

            def gate_input(t):
                dve.wait_ge(turned, t + 1)
                dve.wait_ge(made, t)
                for b in range(2):
                    v.mark(dve.tensor_tensor(xT[:, 4 * b:4 * b + 4, :], tp[:, b, :].rearrange("p (c t) -> p c t", c=4),
                                             g_in[:, 4 * b:4 * b + 4].rearrange("p (c o) -> p c o", o=1).to_broadcast([P, 4, P]),
                                             ALU.mult))
                v.wait()
                split(v, xT[:, :, :], xT_h[:, :, :], xT_r[:, :, :]).then_inc(xt_ok, 1)

            def embedding(t, k):
                mean_square(EMB, t)
                dve.scalar_tensor_tensor(out=halves(e[:, k, :]), in0=eps[:, :, :], scalar=stat[:, EMB, 3:4],
                                         in1=halves(g_e[:, :]), op0=ALU.mult, op1=ALU.mult).then_inc(e_ok, 1)

            def output(t, k, stored):
                dve.wait_ge(sig_ok, t + 1)
                dve.wait_ge(e_ok, t + 1)
                v.link(dve.tensor_tensor(e[:, k, :], e[:, k, :], sg[:, :], ALU.mult))
                dve.sem_inc(sg_used, 1)
                v.link(dve.tensor_tensor(x[:, k, :], x[:, k, :], e[:, k, :], ALU.add))
                dve.sem_inc(x3_ok, 1)
                mean_square(OUT, t)
                dve.wait_ge(y_out[k], stored * 16)
                dve.scalar_tensor_tensor(out=out_t[:, k, :], in0=x[:, k, :], scalar=stat[:, OUT, 3:4], in1=g_y[:, :],
                                         op0=ALU.mult, op1=ALU.mult).then_inc(y_ok, 1)

            def step(i, k, last):
                t = 2 * i + k
                dve.wait_ge(y_ok, t)
                if not last:
                    before_gate(t + 1, 1 - k, i + 1 + k)
                    gate_input(t + 1)
                    embedding(t + 1, 1 - k)
                output(t, k, i)

            dve.sem_inc(x_used, 2)
            dve.sem_inc(r_used, 2)
            dve.wait_ge(w_in, 48)
            dve.wait_ge(raw_in, 16)
            split(v, w_raw[:, 0:PC, :], w_ph[:, :, :], w_p[:, :, :]).then_inc(w_ok, 1)
            for h in range(2):
                own = slice(h * HC, (h + 1) * HC)
                dve.wait_ge(raw_in, 32 + 16 * h)
                split(v, w_raw[:, :, :], w_gh[:, own, :], w_g[:, own, :]).then_inc(w_ok, 1)
            before_gate(0, 0, 1)
            gate_input(0)
            embedding(0, 0)
            with dve.Fori(0, NT // 2 - 1) as i:
                v.loop(i, 22)
                for k in range(2):
                    step(i, k, False)
                v.end(NT // 2 - 1)
            for k in range(2):
                step(NT // 2 - 1, k, k == 1)


_IN_NAMES = ["x", "p", "g_mix", "w_in", "mu_shift", "rw_w0", "rw_w2", "rw_a0", "rw_a2", "rw_g2", "rw_k_k", "rw_k_a",
             "rw_r_k", "rw_ln_w", "rw_ln_b", "cmp_pos_k", "cmp_pos_v", "cmp_k_w1", "cmp_k_w2", "cmp_v_w1", "cmp_v_w2",
             "nsa_gate_b", "w_up_rwkv", "w_up_nsa", "w_out", "g_ffn", "w_group", "b_group", "w_router", "b_router",
             "w_exp_gate_up", "w_exp_down", "w_ple_proj", "g_ple_norm", "g_ple_gate_in", "w_ple_gate", "g_final"]

_SCRATCH = {
    "z": ((Z_ROWS, S), F32), "gate": ((N_GATE, S), F32),
    "rar": ((RW_W, NCH, 2, CH), F32), "rb": ((RW_W, S), F32), "rk": ((RW_W, S), F32), "rv": ((RW_W, S), F32),
    "rdec": ((RW_W, 2, NCH), F32), "rbonus": ((RW_W, S), F32), "rg": ((RW_W, S), F32), "ro": ((RW_W, S), F32),
    "yr": ((RW_W, S), F32), "yn": ((NSA_W, P + S), F32), "x1": ((S, D), F32), "h2": ((S, D), F32),
    "row_tok": (((MAX_BLOCKS + 1) * P, 1), I32), "rows": (((MAX_BLOCKS + 1) * P, D), F32),
}


def build_program(nc, A, out):
    Z = {n: nc.dram_tensor(f"s_{n}", shape, dt).ap() for n, (shape, dt) in _SCRATCH.items()}
    Z["y"] = out
    with ExitStack() as whole, nc.semaphore("passed") as passed, \
            nc.allow_non_contiguous_dma(reason="vectors of parameters, a few KB each"):
        Z["passed"], Z["whole"] = passed, whole
        stage_project(nc, A, Z)
        stage_rwkv_prep(nc, A, Z)
        stage_rwkv_scan(nc, A, Z)
        stage_rwkv_post(nc, A, Z)
        stage_nsa(nc, A, Z)
        stage_mix(nc, A, Z)
        stage_moe(nc, A, Z)


def kernel(**inputs):
    import concourse.bacc as bacc
    from concourse.bass_utils import run_bass_kernel_spmd

    nc = bacc.Bacc("TRN2", target_bir_lowering=False, num_devices=1)
    arrays, A = {}, {}
    for name in _IN_NAMES:
        a = np.ascontiguousarray(inputs[name])
        arrays[f"in_{name}"] = a
        A[name] = nc.dram_tensor(f"in_{name}", a.shape, mybir.dt.from_np(a.dtype), kind="ExternalInput").ap()
    out = nc.dram_tensor("out_y", (1, S, D), F32, kind="ExternalOutput").ap()
    build_program(nc, A, out)
    r = run_bass_kernel_spmd(nc, [arrays], core_ids=[0])
    return r.results[0]["out_y"]
```
